# Optimizing a Trainium2 kernel written in Bass

```python
import jax
import jax.numpy as jnp
from jax import lax
import numpy as np

D_MODEL = 1024
BATCH = 1
SEQ = 256
DEPTH = 2

CTX_LEN = 256
GRID_W = 64
N_EVEN = (DEPTH + 1) // 2
N_ODD = DEPTH // 2
EPS = 1e-6

ML_HEADS = 4
ML_DQK = 128
ML_DV = 128
ML_CHUNK = 64
ML_QK_W = ML_HEADS * ML_DQK
ML_W = ML_HEADS * ML_DV
ML_GATES = 4 * ML_HEADS

GLA_HEADS = 4
GLA_DK = 64
GLA_DV = 128
GLA_LR = 16
GLA_TAU = 16.0
GLA_CHUNK = 32
GLA_QK_W = GLA_HEADS * GLA_DK
GLA_W = GLA_HEADS * GLA_DV

MIX_W = ML_W + GLA_W
IN_SIZES = (ML_QK_W, ML_QK_W, ML_W, ML_W, ML_GATES, GLA_QK_W, GLA_QK_W, GLA_W, GLA_W, 2 * GLA_LR)
IN_WIDTH = sum(IN_SIZES)

RW_HEAD = 64
RW_HEADS = D_MODEL // RW_HEAD
RW_DECAY_LR = 64
RW_A_LR = 64
RW_G_LR = 128
RW_LN_EPS = 64e-5

D_FF = 2816


def split_points(sizes):
    pts, acc = [], 0
    for s in sizes[:-1]:
        acc += s
        pts.append(acc)
    return pts

def rmsnorm(x, g):
    xf = x.astype(jnp.float32)
    y = xf * lax.rsqrt(jnp.mean(xf * xf, axis=-1, keepdims=True) + EPS)
    return (y * g.astype(jnp.float32)).astype(x.dtype)

def head_rmsnorm(y, g, n_heads):
    bn, L, W = y.shape
    d = W // n_heads
    return rmsnorm(y.reshape(bn, L, n_heads, d), g.reshape(n_heads, d)).reshape(bn, L, W)

def head_layernorm(y, w, b, n_heads, out_dtype):
    bn, L, W = y.shape
    yf = y.astype(jnp.float32).reshape(bn, L, n_heads, W // n_heads)
    mu = jnp.mean(yf, axis=-1, keepdims=True)
    var = jnp.mean(jnp.square(yf - mu), axis=-1, keepdims=True)
    yn = ((yf - mu) * lax.rsqrt(var + RW_LN_EPS)).reshape(bn, L, W)
    return (yn * w.astype(jnp.float32) + b.astype(jnp.float32)).astype(out_dtype)

def modulate(h, shift, scale):
    return h * (1 + scale) + shift

def to_heads(t, n_heads):
    bn, L, W = t.shape
    return t.reshape(bn, L, n_heads, W // n_heads).transpose(0, 2, 1, 3)

def from_heads(t):
    bn, H, L, d = t.shape
    return t.transpose(0, 2, 1, 3).reshape(bn, L, H * d)

def to_chunks(t, chunk):
    bn, H, L = t.shape[:3]
    t = t.reshape((bn, H, L // chunk, chunk) + t.shape[3:])
    return jnp.moveaxis(t, 2, 0)

def from_chunks(t):
    t = jnp.moveaxis(t, 0, 2)
    return t.reshape(t.shape[:2] + (-1,) + t.shape[4:])

def short_conv(x, w, b):
    xp = jnp.pad(x, ((0, 0), (1, 1), (0, 0)))
    return xp[:, :-2] * w[0] + xp[:, 1:-1] * w[1] + xp[:, 2:] * w[2] + b

def dwconv_grid(h, w, b, grid):
    rows, width = grid
    bn, L, F = h.shape
    img = h.reshape(bn, rows, width, F)
    out = lax.conv_general_dilated(img, w[:, :, None, :].astype(h.dtype), window_strides=(1, 1), padding="SAME",
                                   dimension_numbers=("NHWC", "HWIO", "NHWC"), feature_group_count=F)
    return out.reshape(bn, L, F) + b

def grid_shift(x, grid):
    rows, width = grid
    bn, L, D = x.shape
    q = D // 4
    p = jnp.pad(x.reshape(bn, rows, width, D), ((0, 0), (1, 1), (1, 1), (0, 0)))
    out = jnp.concatenate([p[:, 1:-1, :-2, :q], p[:, 1:-1, 2:, q:2 * q],
                           p[:, :-2, 1:-1, 2 * q:3 * q], p[:, 2:, 1:-1, 3 * q:]], axis=-1)
    return out.reshape(bn, L, D)

def seq_shift(x):
    D = x.shape[-1]
    q = D // 4
    p = jnp.pad(x, ((0, 0), (1, 1), (0, 0)))
    prv, nxt = p[:, :-2], p[:, 2:]
    return jnp.concatenate([prv[..., :q], nxt[..., q:2 * q], prv[..., 2 * q:3 * q], nxt[..., 3 * q:]], axis=-1)

def bidir_scan(scan_fn, init, ctx_fwd, ctx_bwd, lat_fwd, lat_bwd):
    flip = lambda args: tuple(jnp.flip(a, axis=2) for a in args)
    y_cf, s_f = scan_fn(*ctx_fwd, init)
    y_cb, s_b = scan_fn(*flip(ctx_bwd), init)
    y_lf, _ = scan_fn(*lat_fwd, s_f)
    y_lb, _ = scan_fn(*flip(lat_bwd), s_b)
    return y_cf + jnp.flip(y_cb, axis=2), y_lf + jnp.flip(y_lb, axis=2)

def mlstm_scan(q, k, v, logi, logf, state):
    q, k, v, logi, logf = (t.astype(jnp.float32) for t in (q, k, v, logi, logf))
    mask = jnp.tril(jnp.ones((ML_CHUNK, ML_CHUNK), dtype=bool))

    def step(carry, blk):
        C, n, m = carry
        qc, kc, vc, ic, fc = blk
        b = jnp.cumsum(fc, axis=-1)
        inter = b + m[..., None]
        d = jnp.where(mask, b[..., :, None] - b[..., None, :] + ic[..., None, :], -jnp.inf)
        mt = jnp.maximum(inter, jnp.max(d, axis=-1))
        s = jnp.einsum("bhtd,bhsd->bhts", qc, kc) * jnp.exp(d - mt[..., None])
        wi = jnp.exp(inter - mt)
        num = jnp.einsum("bhts,bhsv->bhtv", s, vc) + wi[..., None] * jnp.einsum("bhtd,bhdv->bhtv", qc, C)
        den = jnp.sum(s, axis=-1) + wi * jnp.einsum("bhtd,bhd->bht", qc, n)
        h = num / jnp.maximum(jnp.abs(den), jnp.exp(-mt))[..., None]
        bl = b[..., -1]
        g = bl[..., None] - b + ic
        m_new = jnp.maximum(bl + m, jnp.max(g, axis=-1))
        ws = jnp.exp(g - m_new[..., None])
        wp = jnp.exp(bl + m - m_new)
        C = wp[..., None, None] * C + jnp.einsum("bhs,bhsd,bhsv->bhdv", ws, kc, vc)
        n = wp[..., None] * n + jnp.einsum("bhs,bhsd->bhd", ws, kc)
        return (C, n, m_new), h

    state, hs = lax.scan(step, state, tuple(to_chunks(t, ML_CHUNK) for t in (q, k, v, logi, logf)))
    return from_chunks(hs), state

def gla_scan(q, k, v, la, S):
    q, k, v, la = (t.astype(jnp.float32) for t in (q, k, v, la))
    mask = jnp.tril(jnp.ones((GLA_CHUNK, GLA_CHUNK), dtype=bool))[:, :, None]

    def step(S, blk):
        qc, kc, vc, ac = blk
        b = jnp.cumsum(ac, axis=2)
        decay = jnp.exp(jnp.where(mask, b[:, :, :, None, :] - b[:, :, None, :, :], -jnp.inf))
        A = jnp.einsum("bhtd,bhsd,bhtsd->bhts", qc, kc, decay)
        o = jnp.einsum("bhts,bhsv->bhtv", A, vc) + jnp.einsum("bhtd,bhdv->bhtv", qc * jnp.exp(b), S)
        bl = b[:, :, -1:, :]
        S = jnp.exp(bl[:, :, 0, :])[..., None] * S + jnp.einsum("bhsd,bhsv->bhdv", kc * jnp.exp(bl - b), vc)
        return S, o

    S, os_ = lax.scan(step, S, tuple(to_chunks(t, GLA_CHUNK) for t in (q, k, v, la)))
    return from_chunks(os_), S

def rwkv7_scan(r, w, k, v, kk, a, S):
    xs = tuple(jnp.moveaxis(t.astype(jnp.float32), 2, 0) for t in (r, w, k, v, kk, a))

    def step(S, inp):
        rt, wt, kt, vt, kkt, at = inp
        sa = jnp.einsum("bhvk,bhk->bhv", S, -kkt)
        S = S * wt[:, :, None, :] + sa[..., None] * (kkt * at)[:, :, None, :] + vt[..., None] * kt[:, :, None, :]
        return S, jnp.einsum("bhvk,bhk->bhv", S, rt)

    S, ys = lax.scan(step, S, xs)
    return jnp.moveaxis(ys, 0, 2), S

def even_project(h, w_in, b_gates, conv_w, conv_b, gla_w2, gla_b):
    bn, L, _ = h.shape
    z = h @ w_in
    mq, mk, mv, mo, mg, gq, gk, gv, gg, glr = jnp.split(z, split_points(IN_SIZES), axis=-1)
    qk = jax.nn.silu(short_conv(jnp.concatenate([mq, mk], axis=-1), conv_w, conv_b))
    mq, mk = jnp.split(qk, 2, axis=-1)
    mg = (mg + b_gates).astype(jnp.float32).reshape(bn, L, 4, ML_HEADS).transpose(2, 0, 3, 1)
    glr = glr.reshape(bn, L, 2, GLA_LR)
    la = jax.nn.log_sigmoid((jnp.einsum("blzr,zrc->zblc", glr, gla_w2) + gla_b[:, None, None, :]).astype(jnp.float32)) / GLA_TAU
    return {
        "mq": to_heads(mq * ML_DQK ** -0.5, ML_HEADS), "mk": to_heads(mk, ML_HEADS), "mv": to_heads(mv, ML_HEADS),
        "i_f": mg[0], "f_f": jax.nn.log_sigmoid(mg[1]), "i_b": mg[2], "f_b": jax.nn.log_sigmoid(mg[3]),
        "gq": to_heads(gq * GLA_DK ** -0.5, GLA_HEADS), "gk": to_heads(gk, GLA_HEADS), "gv": to_heads(gv, GLA_HEADS),
        "la_f": to_heads(la[0], GLA_HEADS), "la_b": to_heads(la[1], GLA_HEADS),
        "mo": mo, "gg": gg,
    }

def even_out(ml_y, gla_y, p, head_g, w_out):
    dt = p["mo"].dtype
    m = head_rmsnorm(from_heads(ml_y).astype(dt), head_g[:ML_W], ML_HEADS) * jax.nn.sigmoid(p["mo"])
    g = head_rmsnorm(from_heads(gla_y).astype(dt), head_g[ML_W:], GLA_HEADS) * jax.nn.silu(p["gg"])
    return jnp.concatenate([m, g], axis=-1) @ w_out

def even_mixer(hc, hl, w_in, b_gates, conv_w, conv_b, gla_w2, gla_b, head_g, w_out, need_ctx):
    pc = even_project(hc, w_in, b_gates, conv_w, conv_b, gla_w2, gla_b)
    pl = even_project(hl, w_in, b_gates, conv_w, conv_b, gla_w2, gla_b)
    bn = hl.shape[0]
    f32 = jnp.float32
    ml_init = (jnp.zeros((bn, ML_HEADS, ML_DQK, ML_DV), f32), jnp.zeros((bn, ML_HEADS, ML_DQK), f32),
               jnp.zeros((bn, ML_HEADS), f32))
    gla_init = jnp.zeros((bn, GLA_HEADS, GLA_DK, GLA_DV), f32)
    ml_args = lambda p: ((p["mq"], p["mk"], p["mv"], p["i_f"], p["f_f"]), (p["mq"], p["mk"], p["mv"], p["i_b"], p["f_b"]))
    gla_args = lambda p: ((p["gq"], p["gk"], p["gv"], p["la_f"]), (p["gq"], p["gk"], p["gv"], p["la_b"]))
    ml_c, ml_l = bidir_scan(mlstm_scan, ml_init, *ml_args(pc), *ml_args(pl))
    gla_c, gla_l = bidir_scan(gla_scan, gla_init, *gla_args(pc), *gla_args(pl))
    y_lat = even_out(ml_l, gla_l, pl, head_g, w_out)
    y_ctx = even_out(ml_c, gla_c, pc, head_g, w_out) if need_ctx else None
    return y_ctx, y_lat

def rwkv_project(h, shifted, mu, w_rkv, w0, w1, w2, a0, a1, a2, g1, g2, kvec):
    xx = shifted - h
    xr, xw, xk, xv, xa, xg = (h + xx * mu[i] for i in range(6))
    r = xr @ w_rkv[0]
    k = xk @ w_rkv[1]
    v = xv @ w_rkv[2]
    lw = jnp.einsum("zblr,zrd->zbld", jnp.tanh(jnp.einsum("bld,zdr->zblr", xw, w1)), w2) + w0[:, None, None, :]
    decay = jnp.exp(-jnp.exp(-jax.nn.softplus(-lw.astype(jnp.float32)) - 0.5))
    a = jax.nn.sigmoid(a0 + (xa @ a1) @ a2)
    g = jax.nn.sigmoid(xg @ g1) @ g2
    kk = to_heads(k * kvec[0], RW_HEADS).astype(jnp.float32)
    kk = kk / jnp.maximum(jnp.sqrt(jnp.sum(kk * kk, axis=-1, keepdims=True)), 1e-12)
    k = k * (1 + (a - 1) * kvec[1])
    return {"r": r, "k": k, "v": v, "a": a, "g": g, "decay": decay, "kk": kk}

def rwkv_out(y, p, kvec, lnx, w_o):
    r, k, v, g = p["r"], p["k"], p["v"], p["g"]
    bn, L, D = r.shape
    y = head_layernorm(from_heads(y), lnx[0], lnx[1], RW_HEADS, r.dtype)
    bonus = jnp.sum((r * k * kvec[2]).reshape(bn, L, RW_HEADS, RW_HEAD), axis=-1, keepdims=True) * v.reshape(bn, L, RW_HEADS, RW_HEAD)
    return ((y + bonus.reshape(bn, L, D)) * g) @ w_o

def rwkv_mixer(hc, hl, lat_grid, mu, w_rkv, w_o, w0, w1, w2, a0, a1, a2, g1, g2, kvec, lnx, need_ctx):
    pc = rwkv_project(hc, seq_shift(hc), mu, w_rkv, w0, w1, w2, a0, a1, a2, g1, g2, kvec)
    pl = rwkv_project(hl, grid_shift(hl, lat_grid), mu, w_rkv, w0, w1, w2, a0, a1, a2, g1, g2, kvec)
    init = jnp.zeros((hl.shape[0], RW_HEADS, RW_HEAD, RW_HEAD), jnp.float32)

    def scan_args(p):
        r, k, v, a = (to_heads(p[n], RW_HEADS) for n in ("r", "k", "v", "a"))
        return ((r, to_heads(p["decay"][0], RW_HEADS), k, v, p["kk"], a),
                (r, to_heads(p["decay"][1], RW_HEADS), k, v, p["kk"], a))

    y_c, y_l = bidir_scan(rwkv7_scan, init, *scan_args(pc), *scan_args(pl))
    out_l = rwkv_out(y_l, pl, kvec, lnx, w_o)
    out_c = rwkv_out(y_c, pc, kvec, lnx, w_o) if need_ctx else None
    return out_c, out_l

def conv_ffn(h, w_up, conv_w, conv_b, w_down, grid):
    gate, up = jnp.split(h @ w_up, 2, axis=-1)
    gate = dwconv_grid(gate, conv_w, conv_b, grid)
    return (jax.nn.gelu(gate, approximate=True) * up) @ w_down

def first_inputs(seed: int = 0) -> dict:
    key = jax.random.key(seed)
    keys = iter(jax.random.split(key, 48))

    def nrm(shape, scale):
        return jax.random.normal(next(keys), shape, jnp.float32) * scale

    def unif(shape, lo, hi):
        return jax.random.uniform(next(keys), shape, jnp.float32, lo, hi)

    D = D_MODEL
    gate_i = nrm((N_EVEN, 2, 1, ML_HEADS), 0.1)
    gate_f = jnp.linspace(3.0, 6.0, ML_HEADS, dtype=jnp.float32) + nrm((N_EVEN, 2, 1, ML_HEADS), 0.1)
    return {
        "x": nrm((BATCH, SEQ, D), 1.0),
        "c": nrm((BATCH, D), 1.0),
        "ctx": nrm((BATCH, CTX_LEN, D), 1.0),
        "c_ctx": nrm((D,), 1.0),
        "w_mod": nrm((DEPTH, D, 6 * D), 0.5 * D ** -0.5),
        "b_mod": nrm((DEPTH, 6 * D), 0.02),
        "norm_g": 1.0 + nrm((DEPTH, 4, D), 0.02),
        "ffn_w_up": nrm((DEPTH, D, 2 * D_FF), D ** -0.5),
        "ffn_conv_w": nrm((DEPTH, 3, 3, D_FF), 1.0 / 3.0),
        "ffn_conv_b": nrm((DEPTH, D_FF), 0.02),
        "ffn_w_down": nrm((DEPTH, D_FF, D), D_FF ** -0.5),
        "ev_w_in": nrm((N_EVEN, D, IN_WIDTH), D ** -0.5),
        "ev_b_gates": jnp.concatenate([gate_i, gate_f], axis=2).reshape(N_EVEN, ML_GATES),
        "ev_conv_w": nrm((N_EVEN, 3, 2 * ML_QK_W), 3 ** -0.5),
        "ev_conv_b": nrm((N_EVEN, 2 * ML_QK_W), 0.02),
        "ev_gla_w2": nrm((N_EVEN, 2, GLA_LR, GLA_QK_W), GLA_LR ** -0.5),
        "ev_gla_b": nrm((N_EVEN, 2, GLA_QK_W), 0.1),
        "ev_head_g": 1.0 + nrm((N_EVEN, MIX_W), 0.02),
        "ev_w_out": nrm((N_EVEN, MIX_W, D), MIX_W ** -0.5),
        "rw_mu": unif((N_ODD, 6, D), 0.0, 1.0),
        "rw_w_rkv": nrm((N_ODD, 3, D, D), D ** -0.5),
        "rw_w_o": nrm((N_ODD, D, D), D ** -0.5),
        "rw_w0": unif((N_ODD, 2, D), -6.0, 1.0),
        "rw_w1": nrm((N_ODD, 2, D, RW_DECAY_LR), D ** -0.5),
        "rw_w2": nrm((N_ODD, 2, RW_DECAY_LR, D), 0.1 * RW_DECAY_LR ** -0.5),
        "rw_a0": nrm((N_ODD, D), 0.1),
        "rw_a1": nrm((N_ODD, D, RW_A_LR), D ** -0.5),
        "rw_a2": nrm((N_ODD, RW_A_LR, D), 0.1 * RW_A_LR ** -0.5),
        "rw_g1": nrm((N_ODD, D, RW_G_LR), D ** -0.5),
        "rw_g2": nrm((N_ODD, RW_G_LR, D), RW_G_LR ** -0.5),
        "rw_kvec": jnp.stack([0.85 + nrm((N_ODD, D), 0.02), 1.0 + nrm((N_ODD, D), 0.02), nrm((N_ODD, D), 0.1)], axis=1),
        "rw_lnx": jnp.stack([1.0 + nrm((N_ODD, D), 0.02), nrm((N_ODD, D), 0.02)], axis=1),
    }

def first_block(x, c, ctx, c_ctx, w_mod, b_mod, norm_g, ffn_w_up, ffn_conv_w, ffn_conv_b, ffn_w_down,
              ev_w_in, ev_b_gates, ev_conv_w, ev_conv_b, ev_gla_w2, ev_gla_b, ev_head_g, ev_w_out,
              rw_mu, rw_w_rkv, rw_w_o, rw_w0, rw_w1, rw_w2, rw_a0, rw_a1, rw_a2, rw_g1, rw_g2, rw_kvec, rw_lnx):
    rows = x.shape[1] // GRID_W
    lat_grid = (rows, GRID_W)
    ctx_grid = (1, ctx.shape[1])
    xl, xc = x, ctx
    for layer in range(DEPTH):
        last = layer == DEPTH - 1
        j = layer // 2
        mod_l = jnp.split((jax.nn.silu(c) @ w_mod[layer] + b_mod[layer])[:, None, :], 6, axis=-1)
        mod_c = jnp.split((jax.nn.silu(c_ctx) @ w_mod[layer] + b_mod[layer])[None, None, :], 6, axis=-1)
        hl = modulate(rmsnorm(xl, norm_g[layer, 0]), mod_l[0], mod_l[1])
        hc = modulate(rmsnorm(xc, norm_g[layer, 0]), mod_c[0], mod_c[1])
        if layer % 2 == 0:
            yc, yl = even_mixer(hc, hl, ev_w_in[j], ev_b_gates[j], ev_conv_w[j], ev_conv_b[j], ev_gla_w2[j],
                                ev_gla_b[j], ev_head_g[j], ev_w_out[j], not last)
        else:
            yc, yl = rwkv_mixer(hc, hl, lat_grid, rw_mu[j], rw_w_rkv[j], rw_w_o[j], rw_w0[j], rw_w1[j], rw_w2[j],
                                rw_a0[j], rw_a1[j], rw_a2[j], rw_g1[j], rw_g2[j], rw_kvec[j], rw_lnx[j], not last)
        xl = xl + mod_l[2] * rmsnorm(yl, norm_g[layer, 1])
        hl = modulate(rmsnorm(xl, norm_g[layer, 2]), mod_l[3], mod_l[4])
        xl = xl + mod_l[5] * rmsnorm(conv_ffn(hl, ffn_w_up[layer], ffn_conv_w[layer], ffn_conv_b[layer],
                                              ffn_w_down[layer], lat_grid), norm_g[layer, 3])
        if not last:
            xc = xc + mod_c[2] * rmsnorm(yc, norm_g[layer, 1])
            hc = modulate(rmsnorm(xc, norm_g[layer, 2]), mod_c[3], mod_c[4])
            xc = xc + mod_c[5] * rmsnorm(conv_ffn(hc, ffn_w_up[layer], ffn_conv_w[layer], ffn_conv_b[layer],
                                                  ffn_w_down[layer], ctx_grid), norm_g[layer, 3])
    return xl


HEAD_DIM = 64
N_HEADS = D_MODEL // HEAD_DIM
N_KV_HEADS = 4
GROUP = N_HEADS // N_KV_HEADS
ROPE_THETA = 10000.0
RMS_EPS = 1e-6
NEG_INF = -1e30
POS_INF = 1e30
IDX_HEADS = 8
IDX_DIM = HEAD_DIM
DSA_TOPK = 256
DSA_Q_BLOCK = 128
CMP_LEN = 32
CMP_STRIDE = 16
CMP_HIDDEN = 256
SLC_LEN = 64
SLC_TOPN = 16
WINDOW = 512
NSA_Q_BLOCK = 64
N_NSA_BRANCH = 3
D_FF_2 = 256 * ((8 * D_MODEL // 3 + 255) // 256)
N_EXPERTS = 8
TOP_K_EXPERTS = 2
D_FF_EXPERT = 7 * D_MODEL // 2
N_A_LAYERS = max(1, DEPTH // 2)
N_B_LAYERS = DEPTH - N_A_LAYERS
N_DENSE_LAYERS = (DEPTH + 1) // 2
N_MOE_LAYERS = DEPTH // 2
A_WIDTHS = (N_HEADS * HEAD_DIM, N_KV_HEADS * HEAD_DIM, N_KV_HEADS * HEAD_DIM, IDX_HEADS * IDX_DIM, IDX_DIM, IDX_HEADS)
A_IN = sum(A_WIDTHS)
B_IN = N_HEADS * HEAD_DIM + N_NSA_BRANCH * N_HEADS
KV_WIDTH = 2 * N_NSA_BRANCH * N_KV_HEADS * HEAD_DIM


F32 = jnp.float32

def rmsnorm_2(x, g):
    xf = x.astype(F32)
    y = xf * lax.rsqrt(jnp.mean(xf * xf, axis=-1, keepdims=True) + RMS_EPS)
    return (y * g.astype(F32)).astype(x.dtype)

def modulate_2(u, shift, scale):
    return u * (1.0 + scale[:, None, :]) + shift[:, None, :]

def rope_tables(positions, dim):
    inv = 1.0 / (ROPE_THETA ** (jnp.arange(0, dim, 2, dtype=F32) / dim))
    ang = positions.astype(F32)[..., None] * inv
    return jnp.cos(ang), jnp.sin(ang)

def apply_rope(x, cos, sin):
    x1, x2 = jnp.split(x.astype(F32), 2, axis=-1)
    c = cos[:, :, None, :]
    s = sin[:, :, None, :]
    return jnp.concatenate([x1 * c - x2 * s, x2 * c + x1 * s], axis=-1).astype(x.dtype)

def masked_softmax(s, mask):
    p = jax.nn.softmax(jnp.where(mask, s, NEG_INF), axis=-1)
    return jnp.where(mask, p, 0.0)

def swiglu(u, wg, wu, wd):
    return (jax.nn.silu(u @ wg) * (u @ wu)) @ wd

def moe_swiglu(u, w_router, wg, wu, wd):
    bsz, seq, d = u.shape
    xf = u.reshape(bsz * seq, d)
    logits = (xf @ w_router).astype(F32)
    vals, idx = lax.top_k(logits, TOP_K_EXPERTS)
    w = jax.nn.softmax(vals, axis=-1)
    gate = jnp.sum(jax.nn.one_hot(idx, N_EXPERTS, dtype=F32) * w[..., None], axis=1)
    y = jnp.zeros_like(xf)
    for e in range(N_EXPERTS):
        y = y + gate[:, e:e + 1].astype(xf.dtype) * swiglu(xf, wg[e], wu[e], wd[e])
    return y.reshape(bsz, seq, d)

def dsa_mixer(u, cos, sin, w_in, w_out):
    bsz, seq, _ = u.shape
    splits = [int(i) for i in np.cumsum(A_WIDTHS[:-1])]
    q, k, v, iq, ik, iw = jnp.split(u @ w_in, splits, axis=-1)
    q = apply_rope(q.reshape(bsz, seq, N_HEADS, HEAD_DIM), cos, sin)
    k = apply_rope(k.reshape(bsz, seq, N_KV_HEADS, HEAD_DIM), cos, sin)
    v = v.reshape(bsz, seq, N_KV_HEADS, HEAD_DIM)
    iq = apply_rope(iq.reshape(bsz, seq, IDX_HEADS, IDX_DIM), cos, sin).astype(F32)
    ik = apply_rope(ik.reshape(bsz, seq, 1, IDX_DIM), cos, sin)[:, :, 0].astype(F32)
    iw = iw.astype(F32) * (IDX_HEADS ** -0.5 * IDX_DIM ** -0.5)
    n_keep = min(DSA_TOPK, seq // 4)
    key_pos = jnp.arange(seq)
    scale = HEAD_DIM ** -0.5

    def block(i):
        q0 = i * DSA_Q_BLOCK
        t = q0 + jnp.arange(DSA_Q_BLOCK)
        qb = lax.dynamic_slice_in_dim(q, q0, DSA_Q_BLOCK, axis=1)
        iqb = lax.dynamic_slice_in_dim(iq, q0, DSA_Q_BLOCK, axis=1)
        iwb = lax.dynamic_slice_in_dim(iw, q0, DSA_Q_BLOCK, axis=1)
        rel = jax.nn.relu(jnp.einsum('bqhd,bsd->bqhs', iqb, ik))
        score = jnp.einsum('bqh,bqhs->bqs', iwb, rel)
        score = jnp.where(key_pos[None, None, :] <= t[None, :, None], score, NEG_INF)
        _, idx = lax.top_k(score, n_keep)
        kg = jax.vmap(lambda kb, ib: kb[ib])(k, idx)
        vg = jax.vmap(lambda vb, ib: vb[ib])(v, idx)
        qg = qb.reshape(bsz, DSA_Q_BLOCK, N_KV_HEADS, GROUP, HEAD_DIM)
        s = jnp.einsum('bqgrd,bqkgd->bgrqk', qg, kg).astype(F32) * scale
        valid = (idx <= t[None, :, None])[:, None, None]
        p = masked_softmax(s, valid).astype(vg.dtype)
        o = jnp.einsum('bgrqk,bqkgd->bqgrd', p, vg)
        return o.reshape(bsz, DSA_Q_BLOCK, N_HEADS * HEAD_DIM)

    o = lax.map(block, jnp.arange(seq // DSA_Q_BLOCK))
    o = jnp.transpose(o, (1, 0, 2, 3)).reshape(bsz, seq, N_HEADS * HEAD_DIM)
    return o @ w_out

def compress_blocks(x, blk_idx, pe, w1, w2):
    bsz = x.shape[0]
    n_cmp = blk_idx.shape[0]
    xb = x[:, blk_idx] + pe[None, None, :, None, :]
    xb = jnp.transpose(xb, (0, 1, 3, 2, 4)).reshape(bsz, n_cmp, N_KV_HEADS, CMP_LEN * HEAD_DIM)
    return jax.nn.gelu(xb @ w1) @ w2

def nsa_shared_kv(h, c_act, kv_gain, w_kv_ada, b_kv_ada, w_kv, pe_k, w1_k, w2_k, pe_v, w1_v, w2_v, cos, sin):
    bsz, seq, _ = h.shape
    shift, scale = jnp.split(c_act @ w_kv_ada + b_kv_ada, 2, axis=-1)
    u = modulate_2(rmsnorm_2(h, kv_gain), shift, scale)
    kv = (u @ w_kv).reshape(bsz, seq, 2 * N_NSA_BRANCH, N_KV_HEADS, HEAD_DIM)
    k_cmp = apply_rope(kv[:, :, 0], cos, sin)
    v_cmp = kv[:, :, 1]
    k_slc = apply_rope(kv[:, :, 2], cos, sin)
    v_slc = kv[:, :, 3]
    k_win = apply_rope(kv[:, :, 4], cos, sin)
    v_win = kv[:, :, 5]
    n_cmp = (seq - CMP_LEN) // CMP_STRIDE + 1
    blk_idx = np.arange(n_cmp)[:, None] * CMP_STRIDE + np.arange(CMP_LEN)[None, :]
    kc = compress_blocks(k_cmp, blk_idx, pe_k, w1_k, w2_k)
    vc = compress_blocks(v_cmp, blk_idx, pe_v, w1_v, w2_v)
    return kc, vc, k_slc, v_slc, k_win, v_win

def nsa_mixer(u, cos, sin, kc, vc, k_slc, v_slc, k_win, v_win, w_q, w_out):
    bsz, seq, _ = u.shape
    proj = u @ w_q
    q = apply_rope(proj[..., :N_HEADS * HEAD_DIM].reshape(bsz, seq, N_HEADS, HEAD_DIM), cos, sin)
    gates = jax.nn.sigmoid(proj[..., N_HEADS * HEAD_DIM:].astype(F32)).reshape(bsz, seq, N_HEADS, N_NSA_BRANCH)
    n_cmp = kc.shape[1]
    n_slc = seq // SLC_LEN
    n_sel = min(SLC_TOPN, n_slc)
    cmp_start = np.arange(n_cmp) * CMP_STRIDE
    cmp_end = jnp.asarray(cmp_start + CMP_LEN - 1)
    slc_start = np.arange(n_slc) * SLC_LEN
    ov = np.minimum(cmp_start[:, None] + CMP_LEN, slc_start[None, :] + SLC_LEN) - np.maximum(cmp_start[:, None], slc_start[None, :])
    agg = jnp.asarray(np.clip(ov, 0, None) / CMP_LEN, dtype=F32)
    ks_blk = jnp.transpose(k_slc.reshape(bsz, n_slc, SLC_LEN, N_KV_HEADS, HEAD_DIM), (0, 3, 1, 2, 4))
    vs_blk = jnp.transpose(v_slc.reshape(bsz, n_slc, SLC_LEN, N_KV_HEADS, HEAD_DIM), (0, 3, 1, 2, 4))
    kw_pad = jnp.pad(k_win, ((0, 0), (WINDOW, 0), (0, 0), (0, 0)))
    vw_pad = jnp.pad(v_win, ((0, 0), (WINDOW, 0), (0, 0), (0, 0)))
    blk = jnp.arange(n_slc)
    in_blk = jnp.arange(SLC_LEN)
    scale = HEAD_DIM ** -0.5

    def block(i):
        q0 = i * NSA_Q_BLOCK
        t = q0 + jnp.arange(NSA_Q_BLOCK)
        qb = lax.dynamic_slice_in_dim(q, q0, NSA_Q_BLOCK, axis=1)
        qb = jnp.transpose(qb.reshape(bsz, NSA_Q_BLOCK, N_KV_HEADS, GROUP, HEAD_DIM), (0, 2, 3, 1, 4))
        gb = lax.dynamic_slice_in_dim(gates, q0, NSA_Q_BLOCK, axis=1)
        gb = jnp.transpose(gb.reshape(bsz, NSA_Q_BLOCK, N_KV_HEADS, GROUP, N_NSA_BRANCH), (0, 2, 3, 1, 4))
        sc = jnp.einsum('bgrqd,bngd->bgrqn', qb, kc).astype(F32) * scale
        pc = masked_softmax(sc, cmp_end[None, :] <= t[:, None])
        oc = jnp.einsum('bgrqn,bngd->bgrqd', pc.astype(vc.dtype), vc)
        imp = jnp.einsum('bgrqn,nj->bgqj', pc, agg)
        jt = t // SLC_LEN
        valid_b = blk[None, :] * SLC_LEN <= t[:, None]
        forced = (blk[None, :] == 0) | (blk[None, :] == jt[:, None]) | (blk[None, :] == jt[:, None] - 1)
        imp = jnp.where(valid_b, jnp.where(forced, POS_INF, imp), NEG_INF)
        _, sel = lax.top_k(imp, n_sel)
        kg = jax.vmap(jax.vmap(lambda kb, sb: kb[sb]))(ks_blk, sel)
        vg = jax.vmap(jax.vmap(lambda vb, sb: vb[sb]))(vs_blk, sel)
        tok = sel[..., None] * SLC_LEN + in_blk
        ss = jnp.einsum('bgrqd,bgqnld->bgrqnl', qb, kg).astype(F32) * scale
        ss = ss.reshape(bsz, N_KV_HEADS, GROUP, NSA_Q_BLOCK, n_sel * SLC_LEN)
        ms = (tok <= t[None, None, :, None, None]).reshape(bsz, N_KV_HEADS, 1, NSA_Q_BLOCK, n_sel * SLC_LEN)
        ps = masked_softmax(ss, ms)
        os_ = jnp.einsum('bgrqm,bgqmd->bgrqd', ps.astype(vg.dtype), vg.reshape(bsz, N_KV_HEADS, NSA_Q_BLOCK, n_sel * SLC_LEN, HEAD_DIM))
        kwb = lax.dynamic_slice_in_dim(kw_pad, q0, NSA_Q_BLOCK + WINDOW, axis=1)
        vwb = lax.dynamic_slice_in_dim(vw_pad, q0, NSA_Q_BLOCK + WINDOW, axis=1)
        s_pos = q0 - WINDOW + jnp.arange(NSA_Q_BLOCK + WINDOW)
        mw = (s_pos[None, :] >= 0) & (s_pos[None, :] <= t[:, None]) & (s_pos[None, :] > t[:, None] - WINDOW)
        sw = jnp.einsum('bgrqd,bkgd->bgrqk', qb, kwb).astype(F32) * scale
        pw = masked_softmax(sw, mw)
        ow = jnp.einsum('bgrqk,bkgd->bgrqd', pw.astype(vwb.dtype), vwb)
        o = gb[..., 0:1] * oc.astype(F32) + gb[..., 1:2] * os_.astype(F32) + gb[..., 2:3] * ow.astype(F32)
        return jnp.transpose(o, (0, 3, 1, 2, 4)).reshape(bsz, NSA_Q_BLOCK, N_HEADS * HEAD_DIM).astype(u.dtype)

    o = lax.map(block, jnp.arange(seq // NSA_Q_BLOCK))
    o = jnp.transpose(o, (1, 0, 2, 3)).reshape(bsz, seq, N_HEADS * HEAD_DIM)
    return o @ w_out

def second_inputs(seed: int = 0) -> dict:
    key = jax.random.key(seed)
    ks = jax.random.split(key, 32)
    d = D_MODEL

    def nrm(k, shape, scale):
        return jax.random.normal(k, shape, F32) * scale

    offset = jax.random.randint(ks[2], (BATCH, 1), 0, 1024, dtype=jnp.int32)
    positions = (offset + jnp.arange(SEQ, dtype=jnp.int32)[None, :]).astype(jnp.int32)
    return {
        'x': nrm(ks[0], (BATCH, SEQ, d), 1.0),
        'c': nrm(ks[1], (BATCH, d), 1.0),
        'positions': positions,
        'attn_gain': 1.0 + nrm(ks[3], (DEPTH, d), 0.05),
        'ffn_gain': 1.0 + nrm(ks[4], (DEPTH, d), 0.05),
        'w_ada': nrm(ks[5], (DEPTH, d, 6 * d), 0.5 * d ** -0.5),
        'b_ada': nrm(ks[6], (DEPTH, 6 * d), 0.01),
        'a_w_in': nrm(ks[7], (N_A_LAYERS, d, A_IN), d ** -0.5),
        'a_w_out': nrm(ks[8], (N_A_LAYERS, N_HEADS * HEAD_DIM, d), (N_HEADS * HEAD_DIM) ** -0.5),
        'b_w_q': nrm(ks[9], (N_B_LAYERS, d, B_IN), d ** -0.5),
        'b_w_out': nrm(ks[10], (N_B_LAYERS, N_HEADS * HEAD_DIM, d), (N_HEADS * HEAD_DIM) ** -0.5),
        'kv_gain': 1.0 + nrm(ks[11], (d,), 0.05),
        'w_kv_ada': nrm(ks[12], (d, 2 * d), 0.5 * d ** -0.5),
        'b_kv_ada': nrm(ks[13], (2 * d,), 0.01),
        'w_kv': nrm(ks[14], (d, KV_WIDTH), d ** -0.5),
        'cmp_pe_k': nrm(ks[15], (CMP_LEN, HEAD_DIM), 0.5),
        'cmp_w1_k': nrm(ks[16], (CMP_LEN * HEAD_DIM, CMP_HIDDEN), (CMP_LEN * HEAD_DIM) ** -0.5),
        'cmp_w2_k': nrm(ks[17], (CMP_HIDDEN, HEAD_DIM), CMP_HIDDEN ** -0.5),
        'cmp_pe_v': nrm(ks[18], (CMP_LEN, HEAD_DIM), 0.5),
        'cmp_w1_v': nrm(ks[19], (CMP_LEN * HEAD_DIM, CMP_HIDDEN), (CMP_LEN * HEAD_DIM) ** -0.5),
        'cmp_w2_v': nrm(ks[20], (CMP_HIDDEN, HEAD_DIM), CMP_HIDDEN ** -0.5),
        'ffn_w_gate': nrm(ks[21], (N_DENSE_LAYERS, d, D_FF_2), d ** -0.5),
        'ffn_w_up': nrm(ks[22], (N_DENSE_LAYERS, d, D_FF_2), d ** -0.5),
        'ffn_w_down': nrm(ks[23], (N_DENSE_LAYERS, D_FF_2, d), D_FF_2 ** -0.5),
        'moe_w_router': nrm(ks[24], (N_MOE_LAYERS, d, N_EXPERTS), d ** -0.5),
        'moe_w_gate': nrm(ks[25], (N_MOE_LAYERS, N_EXPERTS, d, D_FF_EXPERT), d ** -0.5),
        'moe_w_up': nrm(ks[26], (N_MOE_LAYERS, N_EXPERTS, d, D_FF_EXPERT), d ** -0.5),
        'moe_w_down': nrm(ks[27], (N_MOE_LAYERS, N_EXPERTS, D_FF_EXPERT, d), D_FF_EXPERT ** -0.5),
        'final_gain': 1.0 + nrm(ks[28], (d,), 0.05),
    }

def second_block(x, c, positions, attn_gain, ffn_gain, w_ada, b_ada, a_w_in, a_w_out, b_w_q, b_w_out,
              kv_gain, w_kv_ada, b_kv_ada, w_kv, cmp_pe_k, cmp_w1_k, cmp_w2_k, cmp_pe_v, cmp_w1_v, cmp_w2_v,
              ffn_w_gate, ffn_w_up, ffn_w_down, moe_w_router, moe_w_gate, moe_w_up, moe_w_down, final_gain):
    cos, sin = rope_tables(positions, HEAD_DIM)
    c_act = jax.nn.silu(c)
    h = x
    kc = vc = k_slc = v_slc = k_win = v_win = None
    for layer in range(DEPTH):
        mod = c_act @ w_ada[layer] + b_ada[layer]
        a_shift, a_scale, a_gate, f_shift, f_scale, f_gate = jnp.split(mod, 6, axis=-1)
        if layer == N_A_LAYERS:
            kc, vc, k_slc, v_slc, k_win, v_win = nsa_shared_kv(
                h, c_act, kv_gain, w_kv_ada, b_kv_ada, w_kv,
                cmp_pe_k, cmp_w1_k, cmp_w2_k, cmp_pe_v, cmp_w1_v, cmp_w2_v, cos, sin)
        u = modulate_2(rmsnorm_2(h, attn_gain[layer]), a_shift, a_scale)
        if layer < N_A_LAYERS:
            mix = dsa_mixer(u, cos, sin, a_w_in[layer], a_w_out[layer])
        else:
            j = layer - N_A_LAYERS
            mix = nsa_mixer(u, cos, sin, kc, vc, k_slc, v_slc, k_win, v_win, b_w_q[j], b_w_out[j])
        h = h + a_gate[:, None, :] * mix
        u = modulate_2(rmsnorm_2(h, ffn_gain[layer]), f_shift, f_scale)
        if layer % 2 == 0:
            ff = swiglu(u, ffn_w_gate[layer // 2], ffn_w_up[layer // 2], ffn_w_down[layer // 2])
        else:
            m = layer // 2
            ff = moe_swiglu(u, moe_w_router[m], moe_w_gate[m], moe_w_up[m], moe_w_down[m])
        h = h + f_gate[:, None, :] * ff
    return rmsnorm_2(h, final_gain)


def setup_inputs(seed=0):
    out = dict(first_inputs(seed))
    for name, value in second_inputs(seed + 1).items():
        if name != "x":
            out[name + "_2"] = value
    return out


def reference(
    x, c, ctx, c_ctx, w_mod, b_mod, norm_g, ffn_w_up, ffn_conv_w, ffn_conv_b, ffn_w_down,
    ev_w_in, ev_b_gates, ev_conv_w, ev_conv_b, ev_gla_w2, ev_gla_b, ev_head_g, ev_w_out, rw_mu,
    rw_w_rkv, rw_w_o, rw_w0, rw_w1, rw_w2, rw_a0, rw_a1, rw_a2, rw_g1, rw_g2, rw_kvec, rw_lnx,
    c_2, positions_2, attn_gain_2, ffn_gain_2, w_ada_2, b_ada_2, a_w_in_2, a_w_out_2, b_w_q_2,
    b_w_out_2, kv_gain_2, w_kv_ada_2, b_kv_ada_2, w_kv_2, cmp_pe_k_2, cmp_w1_k_2, cmp_w2_k_2,
    cmp_pe_v_2, cmp_w1_v_2, cmp_w2_v_2, ffn_w_gate_2, ffn_w_up_2, ffn_w_down_2, moe_w_router_2,
    moe_w_gate_2, moe_w_up_2, moe_w_down_2, final_gain_2,
):
    x = first_block(
        x, c, ctx, c_ctx, w_mod, b_mod, norm_g, ffn_w_up, ffn_conv_w, ffn_conv_b, ffn_w_down,
        ev_w_in, ev_b_gates, ev_conv_w, ev_conv_b, ev_gla_w2, ev_gla_b, ev_head_g, ev_w_out,
        rw_mu, rw_w_rkv, rw_w_o, rw_w0, rw_w1, rw_w2, rw_a0, rw_a1, rw_a2, rw_g1, rw_g2,
        rw_kvec, rw_lnx,
    )
    return second_block(
        x, c_2, positions_2, attn_gain_2, ffn_gain_2, w_ada_2, b_ada_2, a_w_in_2, a_w_out_2,
        b_w_q_2, b_w_out_2, kv_gain_2, w_kv_ada_2, b_kv_ada_2, w_kv_2, cmp_pe_k_2, cmp_w1_k_2,
        cmp_w2_k_2, cmp_pe_v_2, cmp_w1_v_2, cmp_w2_v_2, ffn_w_gate_2, ffn_w_up_2, ffn_w_down_2,
        moe_w_router_2, moe_w_gate_2, moe_w_up_2, moe_w_down_2, final_gain_2,
    )


_drawn_inputs = setup_inputs


def setup_inputs(seed=0):
    import zlib

    import numpy as np

    out = dict(_drawn_inputs(seed))
    spreads = {}
    factors = {'ffn_conv_b': 3.788,
     'ev_conv_b': 8.0,
     'ev_gla_b': 3.965,
     'ev_head_g': 6.499,
     'rw_w1': 8.0,
     'rw_w2': 8.0,
     'rw_a0': 3.484,
     'rw_a1': 3.522,
     'rw_a2': 3.384,
     'attn_gain_2': 3.242,
     'b_ada_2': 2.955,
     'kv_gain_2': 8.0,
     'b_kv_ada_2': 8.0,
     'cmp_pe_k_2': 5.463}
    for name, (base, spread) in spreads.items():
        noise = np.random.default_rng([zlib.crc32(name.encode()), seed]).standard_normal(out[name].shape)
        drawn = base * np.exp(spread * noise) if base else spread * noise
        out[name] = jnp.asarray(drawn.astype(out[name].dtype))
    for name, factor in factors.items():
        out[name] = (out[name] * factor).astype(out[name].dtype)
    return out
```

```python
from contextlib import ExitStack, contextmanager

import numpy as np

import concourse.bass as bass
from concourse import mybir

F32 = mybir.dt.float32
I32 = mybir.dt.int32
U32 = mybir.dt.uint32
ALU = mybir.AluOpType
ACT = mybir.ActivationFunctionType
AX = mybir.AxisListType.X
ds = bass.ds

P = 128
D = 1024
DC = D // P
CTX = 256
LAT = 256
TT = CTX + LAT
GRID_W = 64
GRID_H = LAT // GRID_W
SEGS = {"ctx": slice(0, CTX), "lat": slice(CTX, TT)}
EPS = 1e-6

ML_HEADS = 4
ML_DK = 128
GLA_HEADS = 4
GLA_DK = 64
GLA_LR = 16
GLA_TAU = 16.0
RW_HEADS = 16
RW_HEAD = 64
RW_CHUNK = 64
RW_LN_EPS = 64e-5
RW_DECAY = -float(np.exp(-0.5))
FF = 2816
FC = FF // P

HEADS = 16
HD = 64
KV_HEADS = 4
IDX_HEADS = 8
DSA_KEEP = min(256, LAT // 4)
CMP_LEN = 32
CMP_STRIDE = 16
CMP_HIDDEN = 256
N_CMP = (LAT - CMP_LEN) // CMP_STRIDE + 1
SLC_LEN = 64
assert min(16, LAT // SLC_LEN) * SLC_LEN == LAT
assert LAT <= 512
EXPERTS = 8
FE = 3584
FEC = FE // P
NEG = -1e30
GONE = -3e38


LEVELS = 8


def level_mask(level, backward):
    s, t = np.arange(P)[:, None], np.arange(P)[None, :]
    if level == 0:
        return (s == t).astype(np.float32)
    h = 1 << (level - 1)
    late, early = (s, t) if backward else (t, s)
    return ((s // (2 * h) == t // (2 * h)) & (late // h % 2 == 1) & (early // h % 2 == 0)).astype(np.float32)


def constant_table():
    s, t = np.arange(P)[:, None], np.arange(P)[None, :]
    block = (s // RW_CHUNK == t // RW_CHUNK)
    parts = {"ident": np.eye(P), "ones": np.ones((P, P)), "head_ones": block}
    rot = np.zeros((P, P))
    for m in range(P):
        if m % HD < HD // 2:
            rot[m + HD // 2, m] = -1.0
        else:
            rot[m - HD // 2, m] = 1.0
    parts["rot"] = rot
    parts["neg_after"] = np.where(t <= s, 0.0, NEG)
    parts["neg_before"] = np.where(t >= s, 0.0, NEG)
    u, c = np.arange(P)[:, None] % RW_CHUNK, np.arange(RW_CHUNK)[None, :]
    for back in (0, 1):
        first, then = (c, u) if back else (u, c)
        parts[f"before_{back}"] = first < then
        parts[f"upto_{back}"] = first <= then
        for level in range(1, 7):
            m = level_mask(level, back)[:RW_CHUNK, :RW_CHUNK]
            parts[f"pair{level}_{back}"] = np.concatenate([m, m])
    parts["pair_ident"] = u == c
    for back in (0, 1):
        for level in range(LEVELS):
            parts[f"level{level}_{back}"] = level_mask(level, back)
    token = np.arange(LAT).reshape(2, P).T
    end = np.arange(CMP_STRIDE) * CMP_STRIDE + CMP_LEN - 1
    seen = (end[None, None, :] <= token[:, :, None]) & (np.arange(CMP_STRIDE) < N_CMP)[None, None, :]
    parts["cmp_seen"] = seen.reshape(P, -1)
    parts["cmp_neg"] = np.where(seen, 0.0, NEG).reshape(P, -1)
    start = (np.arange(TT) % RW_CHUNK != 0)
    parts["keep_fwd"] = np.broadcast_to(start, (P, TT))
    stop = (np.arange(TT) % RW_CHUNK != RW_CHUNK - 1)
    parts["keep_bwd"] = np.broadcast_to(stop, (P, TT))
    inv = np.float32(1.0) / np.power(np.float32(10000.0), np.arange(0, HD, 2, dtype=np.float32) / np.float32(HD)).astype(np.float32)
    parts["inv_freq"] = np.concatenate([inv] * (P // len(inv)))[:, None]
    at, columns = {}, 0
    for name, a in parts.items():
        at[name] = (columns, columns + a.shape[1])
        columns += a.shape[1]
    return np.ascontiguousarray(np.concatenate([np.asarray(a, np.float32) for a in parts.values()], axis=1)), at


CONST, CONST_AT = constant_table()


def vector_rows(shapes):
    names = ("c", "c_ctx", "c_2", "b_mod", "norm_g", "ffn_conv_w", "ffn_conv_b", "ev_conv_w", "ev_conv_b", "ev_gla_b",
             "ev_head_g", "rw_mu", "rw_w0", "rw_a0", "rw_kvec", "rw_lnx", "b_ada_2", "attn_gain_2", "ffn_gain_2",
             "kv_gain_2", "b_kv_ada_2", "final_gain_2", "cmp_pe_k_2", "cmp_pe_v_2")
    at, row = {}, 0
    for n in names:
        k = int(np.prod(shapes[n])) // P
        at[n] = (row, k)
        row += k
    return at, row


class Counter:

    def __init__(self, nc, ctx, name):
        self.sem = ctx.enter_context(nc.semaphore(name))
        self.base = 0
        self.n = 0

    def at(self, n):
        return self.base + n

    def count(self, ins, by=1):
        ins.then_inc(self.sem, by)
        self.n += by
        return ins

    def settle(self):
        self.base += self.n
        self.n = 0


class Core:

    def __init__(self, nc, ctx):
        self.nc = nc
        self.ctx = ctx
        self.counters = {}
        self.spare = []
        self.psum = [ctx.enter_context(nc.psum_tensor(f"bank_pair{i}", [P, 1024], F32)) for i in range(4)]
        self.stage_no = 0

    def bank(self, i):
        return self.psum[i // 2][:, (i % 2) * 512:(i % 2 + 1) * 512]

    def counter(self, name, keep=False):
        if name not in self.counters:
            s = self.spare.pop() if self.spare and not keep else Counter(self.nc, self.ctx, name if keep else f"{name}_{self.stage_no}")
            s.keep = keep
            self.counters[name] = s
        return self.counters[name]

    def sb(self, name, shape, dtype=F32, ctx=None):
        return (ctx or self.ctx).enter_context(self.nc.sbuf_tensor(f"{name}_{self.stage_no}" if ctx else name, shape, dtype))

    @contextmanager
    def engines_block(self):
        with self.nc.Block() as block:
            yield block
        for name, s in list(self.counters.items()):
            s.settle()
            if not s.keep:
                self.spare.append(self.counters.pop(name))
        self.stage_no += 1


class Chain:

    def __init__(self, eng, signal, it=None, per=0):
        self.eng, self.counter, self.it, self.per, self.k = eng, signal, it, per, signal.n if it is None else 0
        self.start = signal.n

    def ended(self, ins):
        ins.then_inc(self.counter.sem, 1)
        self.k += 1
        if self.it is None:
            self.counter.n += 1
            self.eng.wait_ge(self.counter.sem, self.counter.at(self.k))
        else:
            self.eng.wait_ge(self.counter.sem, self.counter.at(self.start + self.it * self.per + self.k))

    def settle(self, rounds):
        assert self.k == self.per, (self.k, self.per)
        self.counter.n += rounds * self.per


class Gemm:

    def __init__(self, core, ctx, key, tiles, banks, width):
        self.core, self.sources = core, tiles
        nc = core.nc
        kc = max(t[2] for t in tiles)
        self.ring = core.sb(f"ring_{key}", [P, len(tiles), kc, width], ctx=ctx)
        self.banks = {o: core.bank(b) for o, b in banks.items()}
        self.landed = [core.counter(f"{key}_tile{s}_landed", True) for s in range(len(tiles))]
        self.used = [core.counter(f"{key}_tile{s}_used", True) for s in range(len(tiles))]
        self.free = {o: core.counter(f"{key}_bank{o}_free", True) for o in banks}
        self.first = {o: min(s for s, t in enumerate(tiles) if o in t[3]) for o in banks}
        self.last = {o: max(s for s, t in enumerate(tiles) if o in t[3]) for o in banks}

    def fetch_round(self, sp, it, first=False, where=None):
        for s, (src, _, kc, outs) in enumerate(self.sources):
            if not first:
                sp.wait_ge(self.used[s].sem, self.used[s].at(it))
            ap = src(it if where is None else where)
            sp.dma_start(self.ring[:, s, 0:kc, 0:ap.shape[2]], ap).then_inc(self.landed[s].sem, 16)

    def matmul_round(self, pe, it, rhs, first=False):
        for s, (_, k0, kc, outs) in enumerate(self.sources):
            pe.wait_ge(self.landed[s].sem, self.landed[s].at(16 * it + 16))
            for j, o in enumerate(outs):
                if s == self.first[o] and not first:
                    pe.wait_ge(self.free[o].sem, self.free[o].at(it))
                for k in range(kc):
                    x = rhs(k0 + k)
                    ins = self.core.nc.tensor.matmul(self.banks[o][:, 0:x.shape[1]], self.ring[:, s, k, j * P:(j + 1) * P], x,
                                                     start=(s == self.first[o] and k == 0),
                                                     stop=(s == self.last[o] and k == kc - 1))
            ins.then_inc(self.used[s].sem, 1)

    def wait_bank(self, eng, o, it):
        s = self.last[o]
        eng.wait_ge(self.used[s].sem, self.used[s].at(it + 1))
        return self.banks[o]

    def bank_taken(self, ins, o):
        ins.then_inc(self.free[o].sem, 1)

    def settle(self, rounds):
        for s in self.landed:
            s.n += 16 * rounds
        for s in (*self.used, *self.free.values()):
            s.n += rounds


def rounds(eng, n, body):
    body(0, True)
    if n > 1:
        with eng.Fori(1, n) as it:
            body(it, False)


def k_tiles(w, width, splits, outs, col=lambda it: None):
    v = w.rearrange("(k p) n -> p k n", p=P)
    kc = v.shape[1]
    edges = [kc * i // splits for i in range(splits + 1)]
    return [((lambda it, a=a, b=b: v[:, a:b, ds(col(it), width)]), a, b - a, outs) for a, b in zip(edges, edges[1:])]


class Store:

    def __init__(self, core, A):
        sb = core.sb
        self.A = A
        self.rows_at, self.n_rows = vector_rows({n: a.shape for n, a in A.items()})
        self.const = sb("const", [P, CONST.shape[1]])
        self.vec = sb("vec", [P, -(-self.n_rows // P) * P])
        self.X = sb("X", [P, DC, TT])
        self.H = sb("H", [P, DC, TT])
        self.Y = sb("Y", [P, DC, TT])
        self.act = sb("act", [P, DC, 4])
        self.mod = sb("mod", [P, 48, 2])
        self.coef = sb("coef", [P, 2, 4, DC])
        self.cos = sb("cos", [P, LAT])
        self.sin = sb("sin", [P, LAT])

    def C(self, name):
        a, b = CONST_AT[name]
        return self.const[:, a:b]

    def V(self, name, i=0, n=1):
        r, k = self.rows_at[name]
        assert i + n <= k
        return self.vec[:, r + i:r + i + n]


def setup_stage(core, st):
    nc, A = core.nc, st.A
    n_tiles = -(-st.n_rows // P)
    with ExitStack() as ctx, core.engines_block() as block:
        rows = core.sb("rows", [P, n_tiles, P], ctx=ctx)
        tokens = core.sb("tokens", [P, 4, D], ctx=ctx)
        pos_i = core.sb("pos_i", [P, LAT], I32, ctx=ctx)
        ang = core.sb("ang", [P, LAT], ctx=ctx)
        turn = core.sb("turn", [P, 2, LAT], ctx=ctx)
        rest = core.sb("rest", [P, 2, LAT], ctx=ctx)
        sig = core.sb("sig", [P, DC, 4], ctx=ctx)
        const_in, rows_in, tokens_in, pos_in = (core.counter(n) for n in ("const_in", "rows_in", "tokens_in", "pos_in"))
        turned, copied = core.counter("turned"), core.counter("turned_copied")
        vec_chain, angle_ready, sig_ready = core.counter("vector_chain"), core.counter("angle_ready"), core.counter("sig_ready")
        groups = [("rows", t, min(4, n_tiles - t)) for t in range(0, n_tiles, 4)]
        groups += [("tokens", b, k) for b in range(4) for k in (0, 4)]

        @block.sync
        def _(sp):
            const_in.count(sp.dma_start(st.const[:], A["const"]), 16)
            for name, (r, k) in st.rows_at.items():
                axes = " ".join("abcdef"[:len(A[name].shape)])
                src = A[name].rearrange(f"{axes} -> ({axes})").rearrange("(r p) -> r p", p=P)
                done = 0
                while done < k:
                    at = r + done
                    n = min(k - done, P - at % P)
                    rows_in.count(sp.dma_start(rows[at % P:at % P + n, at // P, :], src[done:done + n, :]), 16)
                    done += n

        @block.scalar
        def _(act):
            for b, (name, t) in enumerate((("ctx", 0), ("ctx", 1), ("x", 0), ("x", 1))):
                tokens_in.count(act.dma_start(tokens[:, b, :], A[name][0, t * P:(t + 1) * P, :]), 16)
            pos_in.count(act.dma_start(pos_i[:], A["positions_2"].rearrange("a t -> (a t)").partition_broadcast(P)), 16)
            act.wait_ge(copied.sem, copied.at(1))
            for i, name in enumerate(("c", "c_ctx", "c_2", "c_2")):
                ins = nc.scalar.activation(sig[:, :, i], st.V(name, 0, DC), ACT.Sigmoid)
            sig_ready.count(ins)
            for i, table in enumerate((st.sin, st.cos)):
                act.wait_ge(angle_ready.sem, angle_ready.at(i + 1))
                nc.scalar.activation(table[:], rest[:, i, :], ACT.Sin)

        @block.tensor
        def _(pe):
            pe.wait_ge(const_in.sem, const_in.at(16))
            pe.wait_ge(rows_in.sem, rows_in.at(rows_in.n))
            for g, (kind, a, b) in enumerate(groups):
                if g >= 4:
                    pe.wait_ge(copied.sem, copied.at(g - 3))
                bank = core.bank(g % 4)
                if kind == "rows":
                    for j in range(b):
                        n = min(P, st.n_rows - (a + j) * P)
                        ins = nc.tensor.transpose(bank[:, j * P:j * P + n], rows[0:n, a + j, :], st.C("ident")[0:n, 0:n])
                else:
                    pe.wait_ge(tokens_in.sem, tokens_in.at(64))
                    for j in range(4):
                        ins = nc.tensor.transpose(bank[:, j * P:(j + 1) * P], tokens[:, a, (b + j) * P:(b + j + 1) * P], st.C("ident"))
                turned.count(ins)

        @block.vector
        def _(dve):
            for g, (kind, a, b) in enumerate(groups):
                dve.wait_ge(turned.sem, turned.at(g + 1))
                bank = core.bank(g % 4)
                if kind == "rows":
                    n = min(b * P, st.n_rows - a * P)
                    ins = nc.vector.tensor_copy(st.vec[:, a * P:a * P + n], bank[:, 0:n])
                else:
                    ins = nc.vector.tensor_copy(st.X[:, b:b + 4, a * P:(a + 1) * P], bank.rearrange("p (k t) -> p k t", k=4))
                copied.count(ins)
            c = Chain(dve, vec_chain)
            dve.wait_ge(sig_ready.sem, sig_ready.at(1))
            for i, name in enumerate(("c", "c_ctx", "c_2", "c_2")):
                nc.vector.tensor_tensor(st.act[:, :, i], sig[:, :, i], st.V(name, 0, DC), ALU.mult)
            dve.wait_ge(pos_in.sem, pos_in.at(16))
            c.ended(nc.vector.tensor_copy(ang[:], pos_i[:]))
            c.ended(nc.vector.tensor_scalar(ang[:], ang[:], st.C("inv_freq"), None, ALU.mult))
            for i, quarter in enumerate((0.0, 0.25)):
                n, r = turn[:, i, :], rest[:, i, :]
                c.ended(nc.vector.tensor_scalar(n, ang[:], float(1 / (2 * np.pi)), quarter, ALU.mult, ALU.add))
                c.ended(nc.vector.tensor_scalar(n, n, 12582912.0, None, ALU.add))
                c.ended(nc.vector.tensor_scalar(n, n, -12582912.0, None, ALU.add))
                c.ended(nc.vector.scalar_tensor_tensor(r, n, -6.28125, ang[:], ALU.mult, ALU.add))
                c.ended(nc.vector.scalar_tensor_tensor(r, n, -0.00193500518798828125, r, ALU.mult, ALU.add))
                c.ended(nc.vector.scalar_tensor_tensor(r, n, -3.0199159819e-07, r, ALU.mult, ALU.add))
                c.ended(nc.vector.tensor_scalar(r, r, quarter * float(2 * np.pi), 3.1415925, ALU.add, ALU.min))
                angle_ready.count(nc.vector.tensor_scalar(r, r, -3.1415925, None, ALU.max))


def mod_stage(core, st, w, bias, vecs, n_chunks):
    nc = core.nc
    n_it = n_chunks // 4
    v0, nv = vecs
    with ExitStack() as ctx, core.engines_block() as block:
        g = Gemm(core, ctx, "mod", k_tiles(w, 512, 4, (0, 1, 2, 3), lambda it: it * 512), {o: o for o in range(4)}, 512)
        r0 = st.rows_at[bias[0]][0] + bias[1]

        @block.sync
        def _(sp):
            rounds(sp, n_it, lambda it, first: g.fetch_round(sp, it, first))

        @block.tensor
        def _(pe):
            rounds(pe, n_it, lambda it, first: g.matmul_round(pe, it, lambda k: st.act[:, k, v0:v0 + nv], first))

        @block.vector
        def _(dve):
            def body(it, first):
                for o in range(4):
                    bank = g.wait_bank(dve, o, it)
                    b = st.vec[:, ds(r0 + it * 4 + o, 1)]
                    g.bank_taken(nc.vector.tensor_scalar(st.mod[:, ds(it * 4 + o, 1), 0:nv].rearrange("p a v -> p (a v)"),
                                                    bank[:, 0:nv], b, None, ALU.add), o)
            rounds(dve, n_it, body)
        g.settle(n_it)


def coef_stage(core, st, jobs):
    nc = core.nc
    chain = core.counter("vector_chain")
    with core.engines_block() as block:
        @block.vector
        def _(dve):
            for v, slot, gain, m, one in jobs:
                c = Chain(dve, chain)
                out = st.coef[:, v, slot, :]
                c.ended(nc.vector.tensor_scalar(out, st.mod[:, m:m + DC, v], float(one), None, ALU.add))
                if gain is not None:
                    nc.vector.tensor_tensor(out, out, st.V(gain[0], gain[1], DC), ALU.mult)


def norm_stage(core, st, jobs, T=LAT):
    nc = core.nc
    with ExitStack() as ctx, core.engines_block() as block:
        square = core.sb("square", [P, len(jobs), DC, T], ctx=ctx)
        var = core.sb("var", [P, len(jobs), T], ctx=ctx)
        rstd = core.sb("rstd", [P, len(jobs), T], ctx=ctx)
        unit = core.sb("unit", [P, 2, T], ctx=ctx)
        squared, summed, var_ready, std_ready = (core.counter(n) for n in ("squared", "summed", "var_ready", "std_ready"))
        chain = core.counter("vector_chain")

        @block.scalar
        def _(act):
            for j, (x, *_) in enumerate(jobs):
                for k in range(DC):
                    ins = nc.scalar.activation(square[:, j, k], x(k), ACT.Square)
                squared.count(ins)
            for j in range(len(jobs)):
                act.wait_ge(var_ready.sem, var_ready.at(j + 1))
                std_ready.count(nc.scalar.activation(rstd[:, j], var[:, j], ACT.Sqrt))

        @block.tensor
        def _(pe):
            for j in range(len(jobs)):
                pe.wait_ge(squared.sem, squared.at(j + 1))
                for k in range(DC):
                    ins = nc.tensor.matmul(core.bank(j)[:, 0:T], st.C("ones"), square[:, j, k], start=k == 0, stop=k == DC - 1)
                summed.count(ins)

        @block.vector
        def _(dve):
            c = Chain(dve, chain)
            for j in range(len(jobs)):
                dve.wait_ge(summed.sem, summed.at(j + 1))
                var_ready.count(nc.vector.tensor_scalar(var[:, j], core.bank(j)[:, 0:T], 1.0 / D, EPS, ALU.mult, ALU.add))
            for j, (x, mul, add, dst) in enumerate(jobs):
                dve.wait_ge(std_ready.sem, std_ready.at(j + 1))
                c.ended(nc.vector.reciprocal(rstd[:, j], rstd[:, j]))
                for k in range(DC):
                    u = unit[:, k % 2]
                    c.ended(nc.vector.tensor_tensor(u, x(k), rstd[:, j], ALU.mult))
                    a = add(k) if add else None
                    if a is None:
                        nc.vector.tensor_scalar(dst(k), u, mul(k), None, ALU.mult)
                    elif a.shape[1] == 1:
                        nc.vector.tensor_scalar(dst(k), u, mul(k), a, ALU.mult, ALU.add)
                    else:
                        nc.vector.scalar_tensor_tensor(dst(k), u, mul(k), a, ALU.mult, ALU.add)


def gemm_stage(core, st, key, w, n_cols, rhs, store, width=512, splits=4, sections=None, mix=None, engine="scalar"):
    nc = core.nc
    n_it = len(sections) if sections else n_cols // width
    outs = tuple(range(width // P))
    col = (lambda it: sections[it]) if sections else (lambda it: it * width)
    with ExitStack() as ctx, core.engines_block() as block:
        g = Gemm(core, ctx, key, k_tiles(w, width, splits, outs, col), {o: o for o in outs}, width)

        def each(eng, body):
            if sections:
                for it in range(n_it):
                    body(it, it == 0)
            else:
                rounds(eng, n_it, body)

        @block.sync
        def _(sp):
            each(sp, lambda it, first: g.fetch_round(sp, it, first))

        mixed = core.counter("mixed")
        if mix:
            @block.vector
            def _(dve):
                mixed.count(mix())

        @block.tensor
        def _(pe):
            if mix:
                pe.wait_ge(mixed.sem, mixed.at(1))
            each(pe, lambda it, first: g.matmul_round(pe, it, rhs, first))

        def take(eng):
            def body(it, first):
                for o in outs:
                    bank = g.wait_bank(eng, o, it)
                    g.bank_taken(store(eng, it * len(outs) + o, bank), o)
            each(eng, body)

        if engine == "scalar":
            @block.scalar
            def _(act):
                take(act)
        else:
            @block.vector
            def _(dve):
                take(dve)
        g.settle(n_it)


def chunk_of(tensor, n, tokens=slice(None)):
    return tensor[:, ds(n, 1), tokens].rearrange("p a t -> p (a t)")



IN_MQK, IN_MV, IN_MO, IN_MG, IN_GQK, IN_GV, IN_GG, IN_LR = 0, 1024, 1536, 2048, 2064, 2576, 3088, 3600


class Even:
    def __init__(self, core, ctx):
        sb = lambda name, shape: core.sb(name, shape, ctx=ctx)
        self.q = sb("ml_q", [P, 4, TT])
        self.k = sb("ml_k", [P, 4, TT])
        self.o = sb("ml_o", [P, 4, TT])
        self.gqk = sb("gla_qk", [P, 4, TT])
        self.gg = sb("gla_g", [P, 4, TT])
        self.v = sb("values", [P, 2, 4, 512])
        self.gap = sb("gap", [P, 4, 2, 4])
        self.rowmax = [sb(f"rowmax{d}", [4, TT]) for d in (0, 1)]
        self.floor = [sb(f"floor{d}", [4, TT]) for d in (0, 1)]
        self.decay = sb("decay", [P, 2, 2, TT])


def even_project(core, st, ev):
    nc, w = core.nc, st.A["ev_w_in"][0]

    def store(act, c, bank):
        i, j = c // 4, c % 4
        dst = (ev.q, ev.k, ev.o, ev.gqk, ev.gg)[i][:, j]
        if i == 2:
            return nc.scalar.activation(dst, bank, ACT.Sigmoid)
        return nc.scalar.activation(dst, bank, ACT.Copy, scale=GLA_DK ** -0.5 if i == 3 and j < 2 else 1.0)
    gemm_stage(core, st, "in", w, None, lambda k: st.H[:, k], store, sections=[IN_MQK, IN_MQK + 512, IN_MO, IN_GQK, IN_GG])

    with ExitStack() as ctx, core.engines_block() as block:
        wv = (st.Y, core.sb("wv", [P, DC, 512], ctx=ctx))
        wg = core.sb("wg", [P, DC, 4 * ML_HEADS], ctx=ctx)
        wl = core.sb("wl", [P, DC, 2 * GLA_LR], ctx=ctx)
        w2 = core.sb("gla_w2", [GLA_LR, 2, 256], ctx=ctx)
        bg = core.sb("b_gates", [4, 4], ctx=ctx)
        low = core.sb("low", [GLA_LR, 2, TT], ctx=ctx)
        gate = [core.sb(f"gate{i}", [4, TT], ctx=ctx) for i in range(4)]
        soft = [core.sb(f"soft{i}", [4, TT], ctx=ctx) for i in range(2)]
        raw = ev.decay
        soft2 = core.sb("soft2", [P, 2, 2, TT], ctx=ctx)
        gap = [core.sb(f"gap_rows{d}", [4, TT], ctx=ctx) for d in (0, 1)]
        one = core.sb("one_row", [P, TT], ctx=ctx)
        nul = core.sb("nul_row", [4, TT], ctx=ctx)
        conv = core.sb("conv", [P, 2, TT], ctx=ctx)
        load = [core.counter(f"even_weights{i}") for i in range(3)]
        low_ready, low_copied = core.counter("low_ready"), core.counter("low_copied")
        gates_ready, values_ready, values_copied = core.counter("gates_ready"), core.counter("values_ready"), core.counter("values_copied")
        la_ready, raw_ready, soft_ready = core.counter("la_ready"), core.counter("raw_ready"), core.counter("soft_ready")
        gap_ready, gap_turned, floor_ready = core.counter("gap_ready"), core.counter("gap_turned"), core.counter("floor_ready")
        act_chain, vec_chain, conv_ready = core.counter("scalar_chain"), core.counter("vector_chain"), core.counter("conv_ready")

        @block.sync
        def _(sp):
            v = w.rearrange("(k p) n -> p k n", p=P)
            load[0].count(sp.dma_start(wg[:], v[:, :, IN_MG:IN_MG + 16]), 16)
            load[0].count(sp.dma_start(wl[:], v[:, :, IN_LR:IN_LR + 32]), 16)
            load[0].count(sp.dma_start(w2[:], st.A["ev_gla_w2"][0].rearrange("z r c -> r z c")), 16)
            load[0].count(sp.dma_start(bg[:], st.A["ev_b_gates"][0].rearrange("(g h) -> h g", h=4), allow_slow_non_contiguous=True), 16)
            for i, col in enumerate((IN_MV, IN_GV)):
                load[1 + i].count(sp.dma_start(wv[i][:], v[:, :, col:col + 512]), 16)

        @block.tensor
        def _(pe):
            pe.wait_ge(load[0].sem, load[0].at(64))
            for z in (0, 1):
                for k in range(DC):
                    ins = nc.tensor.matmul(core.bank(4 + z)[0:GLA_LR, :], wl[:, k, z * GLA_LR:(z + 1) * GLA_LR], st.H[:, k],
                                           start=k == 0, stop=k == DC - 1)
                low_ready.count(ins)
            for i in range(4):
                for k in range(DC):
                    ins = nc.tensor.matmul(core.bank(i)[0:4, :], wg[:, k, i * 4:(i + 1) * 4], st.H[:, k], start=k == 0, stop=k == DC - 1)
                gates_ready.count(ins)
            for z in (0, 1):
                pe.wait_ge(low_copied.sem, low_copied.at(2))
                for c in (0, 1):
                    b = 4 + z * 2 + c
                    la_ready.count(nc.tensor.matmul(core.bank(b), w2[:, z, c * P:(c + 1) * P], low[:, z], start=True, stop=True))
            for i in (0, 1):
                pe.wait_ge(load[1 + i].sem, load[1 + i].at(16))
                for t in range(4):
                    n = i * 4 + t
                    if n < 4:
                        pe.wait_ge(raw_ready.sem, raw_ready.at(4))
                    else:
                        pe.wait_ge(values_copied.sem, values_copied.at(n - 3))
                    for k in range(DC):
                        ins = nc.tensor.matmul(core.bank(n % 4), st.H[:, k, t * P:(t + 1) * P], wv[i][:, k], start=k == 0, stop=k == DC - 1)
                    values_ready.count(ins)
            for d in (0, 1):
                pe.wait_ge(gap_ready.sem, gap_ready.at(d + 1))
                if d == 0:
                    pe.wait_ge(raw_ready.sem, raw_ready.at(8))
                for b in range(4):
                    ins = nc.tensor.transpose(core.bank(4)[:, (b * 2 + d) * 4:(b * 2 + d) * 4 + 4], gap[d][:, b * P:(b + 1) * P],
                                              st.C("ident")[0:4, 0:4])
                gap_turned.count(ins)

        @block.scalar
        def _(act):
            c = Chain(act, act_chain)
            act.wait_ge(low_ready.sem, low_ready.at(2))
            for z in (0, 1):
                ins = nc.scalar.activation(low[:, z], core.bank(4 + z)[0:GLA_LR, :], ACT.Copy)
                low_copied.count(ins)
            act.wait_ge(raw_ready.sem, raw_ready.at(4))
            for d in (0, 1):
                s = soft[d][:]
                c.ended(nc.scalar.activation(s, gate[2 * d + 1][:], ACT.Abs))
                c.ended(nc.scalar.activation(s, s, ACT.Exp, scale=-1.0))
                soft_ready.count(nc.scalar.activation(s, s, ACT.Ln, bias=1.0))
            act.wait_ge(raw_ready.sem, raw_ready.at(8))
            c.ended(nc.scalar.activation(soft2[:], raw[:], ACT.Abs))
            c.ended(nc.scalar.activation(soft2[:], soft2[:], ACT.Exp, scale=-1.0))
            soft_ready.count(nc.scalar.activation(soft2[:], soft2[:], ACT.Ln, bias=1.0))
            for i in (0, 1):
                for t in range(4):
                    act.wait_ge(values_ready.sem, values_ready.at(i * 4 + t + 1))
                    values_copied.count(nc.scalar.activation(ev.v[:, i, t], core.bank(t), ACT.Copy))
            for d in (0, 1):
                act.wait_ge(floor_ready.sem, floor_ready.at(d + 1))
                nc.scalar.activation(ev.floor[d][:], ev.floor[d][:], ACT.Exp, scale=-1.0)
            for n in range(8):
                x = (ev.q, ev.k)[n // 4][:, n % 4]
                act.wait_ge(conv_ready.sem, conv_ready.at(n + 1))
                c.ended(nc.scalar.activation(x, conv[:, n % 2], ACT.Silu))

        @block.vector
        def _(dve):
            c = Chain(dve, vec_chain)
            c.ended(nc.vector.memset(one[:], 1.0))
            c.ended(nc.vector.memset(nul[:], 0.0))
            dve.wait_ge(load[0].sem, load[0].at(64))
            for i in range(4):
                dve.wait_ge(gates_ready.sem, gates_ready.at(i + 1))
                raw_ready.count(nc.vector.tensor_scalar(gate[i][:], core.bank(i)[0:4, :], bg[:, i:i + 1], None, ALU.add))
            for z in (0, 1):
                for k in (0, 1):
                    dve.wait_ge(la_ready.sem, la_ready.at(z * 2 + k + 1))
                    raw_ready.count(nc.vector.tensor_scalar(raw[:, z, k], core.bank(4 + z * 2 + k), st.V("ev_gla_b", z * 2 + k), None, ALU.add))
            for d in (0, 1):
                i_gate, f_gate = gate[2 * d][:], gate[2 * d + 1][:]
                dve.wait_ge(soft_ready.sem, soft_ready.at(d + 1))
                c.ended(nc.vector.scalar_tensor_tensor(f_gate, f_gate, 0.0, soft[d][:], ALU.min, ALU.subtract))
                total = soft[d]
                for part in scan_parts(d):
                    c.ended(nc.vector.tensor_tensor_scan(total[:, part[0]], one[0:4, part[0]], f_gate[:, part[0]],
                                                        total[:, part[1]:part[1] + 1] if part[1] is not None else 0.0, ALU.mult, ALU.add))
                gap_ready.count(nc.vector.tensor_tensor(gap[d][:], i_gate, total[:], ALU.subtract))
                dve.wait_ge(gap_ready.sem, gap_ready.at(d + 1))
                for part in scan_parts(d):
                    c.ended(nc.vector.tensor_tensor_scan(ev.rowmax[d][:, part[0]], nul[:, part[0]], gap[d][:, part[0]],
                                                        ev.rowmax[d][:, part[1]:part[1] + 1] if part[1] is not None else 0.0, ALU.max, ALU.max))
                floor_ready.count(nc.vector.tensor_tensor(ev.floor[d][:], total[:], ev.rowmax[d][:], ALU.add))
            dve.wait_ge(soft_ready.sem, soft_ready.at(3))
            for z in (0, 1):
                c.ended(nc.vector.scalar_tensor_tensor(raw[:, z], raw[:, z], 0.0, soft2[:, z], ALU.min, ALU.subtract))
                c.ended(nc.vector.tensor_scalar(raw[:, z], raw[:, z], 1.0 / GLA_TAU, None, ALU.mult))
                for k in (0, 1):
                    for part in scan_parts(z):
                        c.ended(nc.vector.tensor_tensor_scan(ev.decay[:, z, k, part[0]], one[:, part[0]], raw[:, z, k, part[0]],
                                                            ev.decay[:, z, k, part[1]:part[1] + 1] if part[1] is not None else 0.0, ALU.mult, ALU.add))
            dve.wait_ge(gap_turned.sem, gap_turned.at(2))
            c.ended(nc.vector.tensor_copy(ev.gap[:], core.bank(4)[:, 0:32].rearrange("p (b d h) -> p b d h", b=4, d=2)))
            for n in range(8):
                x, y = (ev.q, ev.k)[n // 4][:, n % 4].rearrange("p (s t) -> p s t", s=2), conv[:, n % 2].rearrange("p (s t) -> p s t", s=2)
                if n >= 2:
                    dve.wait_ge(act_chain.sem, act_chain.at(6 + n - 1))
                c.ended(nc.vector.tensor_scalar(y, x, st.V("ev_conv_w", 8 + n), st.V("ev_conv_b", n), ALU.mult, ALU.add))
                c.ended(nc.vector.scalar_tensor_tensor(y[:, :, 1:], x[:, :, :-1], st.V("ev_conv_w", n), y[:, :, 1:], ALU.mult, ALU.add))
                conv_ready.count(nc.vector.scalar_tensor_tensor(y[:, :, :-1], x[:, :, 1:], st.V("ev_conv_w", 16 + n), y[:, :, :-1], ALU.mult, ALU.add))


def scan_parts(backward):
    if backward:
        return [(slice(CTX - 1, None, -1), None), (slice(TT - 1, CTX - 1, -1), 0)]
    return [(slice(0, TT), None)]


def key_blocks(backward):
    if backward:
        return [(1, [(0, 4)]), (0, [(0, 1), (2, 4)]), (3, [(2, 4)]), (2, [(2, 3)])]
    return [(s, [(s, 4)]) for s in range(4)]


def mlstm_stage(core, st, ev):
    nc = core.nc
    units = [(h, d) for h in range(ML_HEADS) for d in (0, 1)]
    items = [(u, s, runs) for u, (h, d) in enumerate(units) for s, runs in key_blocks(d)]
    with ExitStack() as ctx, core.engines_block() as block:
        masked = core.sb("masked", [P, 2, P], ctx=ctx)
        weight = core.sb("weight", [P, 2, TT], ctx=ctx)
        pt = core.sb("pt", [P, 2, TT], ctx=ctx)
        den = core.sb("den", [P, TT], ctx=ctx)
        res = core.sb("res", [P, TT], ctx=ctx)
        names = ("rows_spread", "scores_ready", "masked_ready", "weights_ready", "pt_ready", "pt_used", "den_ready", "unit_done")
        spread, scores, masked_ready, weights, pt_ready, pt_used, den_ready, unit_done = (core.counter("ml_" + n) for n in names)
        chain = core.counter("vector_chain")
        MAXB, FLOORB, NUM, DEN = core.bank(0), core.bank(1), core.bank(4), core.bank(5)
        SC = [core.bank(2), core.bank(3)]

        @block.tensor
        def _(pe):
            for u, (h, d) in enumerate(units):
                if u:
                    pe.wait_ge(unit_done.sem, unit_done.at(u))
                sel = st.C("ident")[0:4, h:h + 1].to_broadcast([4, P])
                nc.tensor.matmul(MAXB, sel, ev.rowmax[d][:], start=True, stop=True)
                spread.count(nc.tensor.matmul(FLOORB, sel, ev.floor[d][:], start=True, stop=True))
                mine = [(n, s, runs) for n, (uu, s, runs) in enumerate(items) if uu == u]

                def score(n, s):
                    if n >= 2:
                        pe.wait_ge(pt_ready.sem, pt_ready.at(n - 1))
                    scores.count(nc.tensor.matmul(SC[n % 2], ev.k[:, h, s * P:(s + 1) * P], ev.q[:, h], start=True, stop=True))
                score(*mine[0][:2])
                for j, (n, s, runs) in enumerate(mine):
                    if j + 1 < len(mine):
                        score(*mine[j + 1][:2])
                    pe.wait_ge(pt_ready.sem, pt_ready.at(n + 1))
                    for r, (a, b) in enumerate(runs):
                        x = pt[:, n % 2, a * P:b * P]
                        flags = dict(start=j == 0 and r == 0, stop=j == 3, skip_group_check=True)
                        nc.tensor.matmul(NUM[:, a * P:b * P], ev.v[:, 0, s, h * P:(h + 1) * P], x, **flags)
                        ins = nc.tensor.matmul(DEN[:, a * P:b * P], st.C("ones"), x, **flags)
                    pt_used.count(ins)

        @block.scalar
        def _(act):
            for n, (u, s, runs) in enumerate(items):
                h, d = units[u]
                bias = ev.gap[:, s, d, h:h + 1]
                act.wait_ge(masked_ready.sem, masked_ready.at(n + 1))
                if n >= 2:
                    act.wait_ge(pt_ready.sem, pt_ready.at(n - 1))
                w = weight[:, n % 2]
                for a, b in runs:
                    for i, j in ((a, s), (s + 1, b)) if a <= s < b else ((a, b),):
                        if i < j:
                            nc.scalar.activation(w[:, i * P:j * P], MAXB[:, i * P:j * P], ACT.Exp, bias=bias, scale=-1.0)
                weights.count(nc.scalar.activation(w[:, s * P:(s + 1) * P], masked[:, n % 2], ACT.Exp, bias=bias))
                if n % 4 == 3:
                    act.wait_ge(pt_used.sem, pt_used.at(n + 1))
                    if u:
                        act.wait_ge(unit_done.sem, unit_done.at(u))
                    den_ready.count(nc.scalar.activation(den[:], DEN, ACT.Abs))

        @block.vector
        def _(dve):
            c = Chain(dve, chain)
            for n, (u, s, runs) in enumerate(items):
                h, d = units[u]
                dve.wait_ge(spread.sem, spread.at(u + 1))
                if n >= 2:
                    dve.wait_ge(weights.sem, weights.at(n - 1))
                masked_ready.count(nc.vector.scalar_tensor_tensor(masked[:, n % 2], MAXB[:, s * P:(s + 1) * P], -1.0,
                                                                st.C("neg_after" if d else "neg_before"), ALU.mult, ALU.add))
                dve.wait_ge(scores.sem, scores.at(n + 1))
                dve.wait_ge(weights.sem, weights.at(n + 1))
                if n >= 2:
                    dve.wait_ge(pt_used.sem, pt_used.at(n - 1))
                for a, b in runs:
                    ins = nc.vector.scalar_tensor_tensor(pt[:, n % 2, a * P:b * P], SC[n % 2][:, a * P:b * P], ML_DK ** -0.5,
                                                         weight[:, n % 2, a * P:b * P], ALU.mult, ALU.mult)
                pt_ready.count(ins)
                if n % 4 == 3:
                    dve.wait_ge(den_ready.sem, den_ready.at(u + 1))
                    c.ended(nc.vector.tensor_tensor(den[:], den[:], FLOORB, ALU.max))
                    c.ended(nc.vector.reciprocal(den[:], den[:]))
                    if d == 0:
                        unit_done.count(nc.vector.tensor_tensor(st.Y[:, h], NUM, den[:], ALU.mult))
                    else:
                        c.ended(nc.vector.tensor_tensor(res[:], NUM, den[:], ALU.mult))
                        unit_done.count(nc.vector.tensor_tensor(st.Y[:, h], st.Y[:, h], res[:], ALU.add))


def gla_stage(core, st, ev):
    nc = core.nc
    units = [(c, d) for c in (0, 1) for d in (0, 1)]
    n_lv = LEVELS + 2
    with ExitStack() as ctx, core.engines_block() as block:
        eq = core.sb("eq", [P, 2, TT], ctx=ctx)
        ek = core.sb("ek", [P, 2, TT], ctx=ctx)
        qs = core.sb("qs", [P, 2, TT], ctx=ctx)
        ks = core.sb("ks", [P, 2, TT], ctx=ctx)
        att = core.sb("att", [P, 2, TT], ctx=ctx)
        part = core.sb("part", [P, 2, TT], ctx=ctx)
        near = core.sb("near", [P, 2, 2 * P], ctx=ctx)
        far = core.sb("far", [P, 2, 2, CTX], ctx=ctx)
        exps_in, exps, scaled, scored, summed, pv = (core.counter("gla_" + n) for n in ("shifts", "exps", "scaled", "scored", "summed", "pv"))
        far_copied, out_taken = core.counter("gla_far_copied"), core.counter("gla_out_taken")
        chain = core.counter("vector_chain")
        OUT = [core.bank(4), core.bank(5)]

        def halves(x, level, d):
            h = 1 << (level - 1)
            v = x.rearrange("p (n two h) -> p n two h", two=2, h=h)
            late, early = (0, 1) if d and h < CTX else (1, 0)
            ref = v[:, :, early, 0:1] if d else v[:, :, early, h - 1:h]
            return v[:, :, late], v[:, :, early], ref.to_broadcast([P, TT // (2 * h), h])

        @block.vector
        def _(dve):
            c = Chain(dve, chain)
            c.ended(nc.vector.memset(qs[:], 0.0))
            c.ended(nc.vector.memset(ks[:], 0.0))
            for u, (ch, d) in enumerate(units):
                b, q, k = ev.decay[:, d, ch], ev.gqk[:, ch], ev.gqk[:, 2 + ch]

                def scale(l):
                    n = u * n_lv + l
                    p = n % 2
                    if n >= 2:
                        dve.wait_ge(scored.sem, scored.at(n - 1))
                    if l == 0:
                        nc.vector.tensor_copy(qs[:, p], q)
                        scaled.count(nc.vector.tensor_copy(ks[:, p], k))
                        return
                    bq, bk, ref = halves(b, l, d)
                    shift_q, _, _ = halves(eq[:, p], l, d)
                    _, shift_k, _ = halves(ek[:, p], l, d)
                    nc.vector.tensor_tensor(shift_q, bq, ref, ALU.subtract)
                    exps_in.count(nc.vector.tensor_tensor(shift_k, ref, bk, ALU.subtract))
                    dve.wait_ge(exps.sem, exps.at(u * (n_lv - 1) + l))
                    nc.vector.tensor_tensor(halves(qs[:, p], l, d)[0], halves(q, l, d)[0], shift_q, ALU.mult)
                    scaled.count(nc.vector.tensor_tensor(halves(ks[:, p], l, d)[1], halves(k, l, d)[1], shift_k, ALU.mult))

                def add_up(l):
                    n = u * n_lv + l
                    dve.wait_ge(scored.sem, scored.at(n + 1))
                    mask = st.C(f"level{l}_{d}").unsqueeze(1).to_broadcast([P, 4, P])
                    if l == 0 and u:
                        dve.wait_ge(pv.sem, pv.at(u))
                    for hh in (0, 1):
                        bank = core.bank((n % 2) * 2 + hh).rearrange("p (b t) -> p b t", b=4)
                        dst = att if l == 0 else part
                        ins = nc.vector.tensor_tensor(dst[:, hh].rearrange("p (b t) -> p b t", b=4), bank, mask, ALU.mult)
                    if l:
                        c.ended(ins)
                        ins = nc.vector.tensor_tensor(att[:], att[:], part[:], ALU.add)
                    summed.count(ins)
                    dve.wait_ge(summed.sem, summed.at(u * LEVELS + l + 1))

                scale(0)
                for l in range(n_lv):
                    if l + 1 < n_lv:
                        scale(l + 1)
                    if l < LEVELS:
                        add_up(l)
                if d:
                    dve.wait_ge(pv.sem, pv.at(u + 1))
                    for hh in (0, 1):
                        ins = nc.vector.tensor_copy(st.Y[:, 4 + 2 * ch + hh], OUT[hh])
                    out_taken.count(ins)

        @block.scalar
        def _(act):
            for u, (ch, d) in enumerate(units):
                for l in range(n_lv):
                    n = u * n_lv + l
                    p = n % 2
                    if l:
                        act.wait_ge(exps_in.sem, exps_in.at(u * (n_lv - 1) + l))
                        x, y = halves(eq[:, p], l, d)[0], halves(ek[:, p], l, d)[1]
                        nc.scalar.activation(x, x, ACT.Exp)
                        exps.count(nc.scalar.activation(y, y, ACT.Exp))
                    if l >= LEVELS + 1:
                        if u:
                            act.wait_ge(pv.sem, pv.at(u))
                        for up in (LEVELS, LEVELS + 1):
                            m = u * n_lv + up
                            act.wait_ge(scored.sem, scored.at(m + 1))
                            for hh in (0, 1):
                                bank = core.bank((m % 2) * 2 + hh)
                                if up == LEVELS:
                                    ins = nc.scalar.activation(near[:, hh], bank[:, 0:2 * P], ACT.Copy)
                                else:
                                    ins = nc.scalar.activation(far[:, hh], bank.rearrange("p (b t) -> p b t", b=2), ACT.Copy)
                            far_copied.count(ins)

        @block.tensor
        def _(pe):
            for u, (ch, d) in enumerate(units):
                for l in range(n_lv):
                    n = u * n_lv + l
                    pe.wait_ge(scaled.sem, scaled.at(n + 1))
                    if n >= 2:
                        m = n - 2
                        if m % n_lv < LEVELS:
                            pe.wait_ge(summed.sem, summed.at(m // n_lv * LEVELS + m % n_lv + 1))
                        else:
                            pe.wait_ge(far_copied.sem, far_copied.at(m // n_lv * 2 + m % n_lv - LEVELS + 1))
                    for hh in (0, 1):
                        bank = core.bank((n % 2) * 2 + hh)
                        k, q = ks[hh * 64:hh * 64 + 64, n % 2], qs[hh * 64:hh * 64 + 64, n % 2]
                        if l < LEVELS:
                            tiles = [(b * P, b * P, b * P, P) for b in range(4)]
                        elif l == LEVELS:
                            tiles = [(i * P, (2 * i + d) * P, (2 * i + 1 - d) * P, P) for i in (0, 1)]
                        else:
                            tiles = [(i * CTX, i * P, CTX, LAT) for i in (0, 1)]
                        for at, s, t, w in tiles:
                            ins = nc.tensor.matmul(bank[:, at:at + w], k[:, s:s + P], q[:, t:t + w], start=True, stop=True)
                    scored.count(ins)
                pe.wait_ge(summed.sem, summed.at((u + 1) * LEVELS))
                pe.wait_ge(far_copied.sem, far_copied.at(2 * u + 2))
                if u == 2:
                    pe.wait_ge(out_taken.sem, out_taken.at(1))
                for hh in (0, 1):
                    v = lambda s: ev.v[:, 1, s, (2 * ch + hh) * P:(2 * ch + hh + 1) * P]
                    prods = [(s, att[:, hh, s * P:(s + 1) * P], s * P, P) for s in range(4)]
                    prods += [(2 * i + d, near[:, hh, i * P:(i + 1) * P], (2 * i + 1 - d) * P, P) for i in (0, 1)]
                    prods += [(i, far[:, hh, i], CTX, LAT) for i in (0, 1)]
                    for j, (s, x, t, w) in enumerate(prods):
                        ins = nc.tensor.matmul(OUT[hh][:, t:t + w], v(s), x, start=d == 0 and j == 0,
                                               stop=d == 1 and j == len(prods) - 1, skip_group_check=True)
                pv.count(ins)


def even_gate_stage(core, st, ev):
    nc = core.nc
    with ExitStack() as ctx, core.engines_block() as block:
        square = core.sb("square", [P, DC, TT], ctx=ctx)
        var = core.sb("var", [P, 2, TT], ctx=ctx)
        unit = core.sb("unit", [P, 2, TT], ctx=ctx)
        squared, summed, var_ready, std_ready, done = (core.counter(n) for n in ("squared", "summed", "var_ready", "std_ready", "head_done"))
        chain = core.counter("vector_chain")

        @block.scalar
        def _(act):
            for k in range(DC):
                squared.count(nc.scalar.activation(square[:, k], st.Y[:, k], ACT.Square))
            for k in range(4):
                ins = nc.scalar.activation(ev.gg[:, k], ev.gg[:, k], ACT.Silu)
            for k in range(DC):
                act.wait_ge(var_ready.sem, var_ready.at(k + 1))
                std_ready.count(nc.scalar.activation(var[:, k % 2], var[:, k % 2], ACT.Sqrt))

        @block.tensor
        def _(pe):
            for k in range(DC):
                pe.wait_ge(squared.sem, squared.at(k + 1))
                summed.count(nc.tensor.matmul(core.bank(k), st.C("ones"), square[:, k], start=True, stop=True))

        @block.vector
        def _(dve):
            c = Chain(dve, chain)

            def spread(k):
                dve.wait_ge(summed.sem, summed.at(k + 1))
                var_ready.count(nc.vector.tensor_scalar(var[:, k % 2], core.bank(k), 1.0 / P, EPS, ALU.mult, ALU.add))
            spread(0)
            for k in range(DC):
                if k + 1 < DC:
                    spread(k + 1)
                dve.wait_ge(std_ready.sem, std_ready.at(k + 1))
                v = var[:, k % 2]
                c.ended(nc.vector.reciprocal(v, v))
                u = unit[:, k % 2]
                c.ended(nc.vector.scalar_tensor_tensor(u, st.Y[:, k], st.V("ev_head_g", k), v, ALU.mult, ALU.mult))
                nc.vector.tensor_tensor(st.Y[:, k], u, (ev.o if k < 4 else ev.gg)[:, k % 4], ALU.mult)


def ffn_stage(core, st, layer, T, t0):
    nc, A = core.nc, st.A
    with ExitStack() as outer:
        h = core.sb("ffn_h", [P, FC, T], ctx=outer)
        n_it = FC // 2
        with ExitStack() as ctx, core.engines_block() as block:
            up = A["ffn_w_up"][layer]
            tiles = k_tiles(up, 256, 2, (0, 1), lambda it: it * 256) + k_tiles(up, 256, 2, (2, 3), lambda it: it * 256 + FF)
            g = Gemm(core, ctx, "up", tiles, {o: o for o in range(4)}, 256)
            taps = core.sb("taps", [P, 2, 10], ctx=ctx)
            conv = core.sb("conv", [P, 2, T], ctx=ctx)
            gelu = core.sb("gelu", [P, 2, T], ctx=ctx)
            conv_ready, gelu_ready, chain = core.counter("conv_ready"), core.counter("gelu_ready"), core.counter("vector_chain")
            w0, b0 = st.rows_at["ffn_conv_w"][0] + layer * 9 * FC, st.rows_at["ffn_conv_b"][0] + layer * FC
            tap_order = [(dy, dx) for dy in (-1, 0, 1) for dx in (-1, 0, 1) if (dy, dx) != (0, 0)]
            per = 2 * (1 + len(tap_order)) + (2 * 2 if T == TT else 0)

            @block.sync
            def _(sp):
                rounds(sp, n_it, lambda it, first: g.fetch_round(sp, it, first))

            @block.tensor
            def _(pe):
                rounds(pe, n_it, lambda it, first: g.matmul_round(pe, it, lambda k: st.H[:, k, t0:t0 + T], first))

            @block.vector
            def _(dve):
                def body(it, first):
                    c = Chain(dve, chain, it, per)
                    for o in (0, 1):
                        n = it * 2 + o
                        nc.vector.tensor_copy(taps[:, o, 0:9].unsqueeze(2), st.vec[:, w0:w0 + 9 * FC].rearrange("p (w f) -> p w f", f=FC)[:, :, ds(n, 1)])
                        c.ended(nc.vector.tensor_copy(taps[:, o, 9:10], st.vec[:, ds(b0 + n, 1)]))
                        bank = g.wait_bank(dve, o, it)
                        if not first:
                            dve.wait_ge(gelu_ready.sem, gelu_ready.at(it * 2 + o - 1))
                        y = conv[:, o]
                        c.ended(nc.vector.tensor_scalar(y, bank[:, 0:T], taps[:, o, 4:5], taps[:, o, 9:10], ALU.mult, ALU.add))
                        if T == TT:
                            c.ended(nc.vector.scalar_tensor_tensor(y[:, 1:CTX], bank[:, 0:CTX - 1], taps[:, o, 3:4], y[:, 1:CTX], ALU.mult, ALU.add))
                            c.ended(nc.vector.scalar_tensor_tensor(y[:, 0:CTX - 1], bank[:, 1:CTX], taps[:, o, 5:6], y[:, 0:CTX - 1], ALU.mult, ALU.add))
                        yg = y[:, T - LAT:T].rearrange("p (r w) -> p r w", w=GRID_W)
                        xg = bank[:, T - LAT:T].rearrange("p (r w) -> p r w", w=GRID_W)
                        for i, (dy, dx) in enumerate(tap_order):
                            rows = [slice(max(0, -s), n - max(0, s)) for s, n in ((dy, GRID_H), (dx, GRID_W))]
                            from_ = [slice(r.start + s, r.stop + s) for r, s in zip(rows, (dy, dx))]
                            w = (dy + 1) * 3 + dx + 1
                            ins = nc.vector.scalar_tensor_tensor(yg[:, rows[0], rows[1]], xg[:, from_[0], from_[1]], taps[:, o, w:w + 1],
                                                                 yg[:, rows[0], rows[1]], ALU.mult, ALU.add)
                            if i + 1 < len(tap_order):
                                c.ended(ins)
                        g.bank_taken(ins, o)
                    for o in (0, 1):
                        bank = g.wait_bank(dve, 2 + o, it)
                        dve.wait_ge(gelu_ready.sem, gelu_ready.at(it * 2 + o + 1))
                        g.bank_taken(nc.vector.tensor_tensor(chunk_of(h, it * 2 + o), gelu[:, o], bank[:, 0:T], ALU.mult), 2 + o)
                    return c
                c = [None]

                def run(it, first):
                    c[0] = body(it, first)
                rounds(dve, n_it, run)
                c[0].settle(n_it)

            @block.scalar
            def _(act):
                def body(it, first):
                    for o in (0, 1):
                        act.wait_ge(g.free[o].sem, g.free[o].at(it + 1))
                        if not first:
                            act.wait_ge(g.free[2 + o].sem, g.free[2 + o].at(it))
                        nc.scalar.activation(gelu[:, o], conv[:, o], ACT.Gelu_apprx_tanh).then_inc(gelu_ready.sem, 1)
                rounds(act, n_it, body)
            gelu_ready.n += 2 * n_it
            g.settle(n_it)
        gemm_stage(core, st, "down", A["ffn_w_down"][layer], D, lambda k: h[:, k],
                   lambda act, c, bank: nc.scalar.activation(chunk_of(st.Y, c, slice(t0, t0 + T)), bank[:, 0:T], ACT.Copy), width=256)


class Rwkv:
    def __init__(self, core, st, ctx):
        sb = lambda name: core.sb(name, [P, DC, TT], ctx=ctx)
        self.k, self.v, self.kk, self.b = sb("rw_k"), sb("rw_v"), sb("rw_kk"), sb("rw_b")
        self.decay = [sb("rw_decay0"), sb("rw_decay1")]
        self.r = st.X[:, :, 0:CTX]
        self.g = st.Y[:, :, 0:CTX]
        self.y = st.Y[:, :, CTX:TT]


def rwkv_shift_stage(core, st):
    nc = core.nc
    with core.engines_block() as block:
        @block.vector
        def _(dve):
            for quarter in range(4):
                k = slice(2 * quarter, 2 * quarter + 2)
                h, y = st.H[:, k], st.Y[:, k]
                back = quarter % 2 == 0
                to, of, edge = (slice(1, CTX), slice(0, CTX - 1), slice(0, 1)) if back else (slice(0, CTX - 1), slice(1, CTX), slice(CTX - 1, CTX))
                nc.vector.tensor_tensor(y[:, :, to], h[:, :, of], h[:, :, to], ALU.subtract)
                nc.vector.tensor_scalar(y[:, :, edge], h[:, :, edge], -1.0, None, ALU.mult)
                for c in (0, 1):
                    hg, yg = (x[:, c, CTX:TT].rearrange("p (r w) -> p r w", w=GRID_W) for x in (h, y))
                    n = GRID_W if quarter < 2 else GRID_H
                    to, of, edge = (slice(1, n), slice(0, n - 1), slice(0, 1)) if back else (slice(0, n - 1), slice(1, n), slice(n - 1, n))
                    cut = (lambda x, s: x[:, :, s]) if quarter < 2 else (lambda x, s: x[:, s, :])
                    nc.vector.tensor_tensor(cut(yg, to), cut(hg, of), cut(hg, to), ALU.subtract)
                    nc.vector.tensor_scalar(cut(yg, edge), cut(hg, edge), -1.0, None, ALU.mult)


def rwkv_low_rank_stage(core, st, rw, mu, w1_parts, rank, func, w2, parts, store, tokens):
    nc = core.nc
    T = tokens.stop - tokens.start
    with ExitStack() as ctx, core.engines_block() as block:
        w1s = core.sb("w1s", [P, DC, rank], ctx=ctx)
        w2s = core.sb("w2s", [rank, D], ctx=ctx)
        hidden = core.sb("hidden", [rank, T], ctx=ctx)
        loaded, mixed, hid, hid_done, out, taken = (core.counter("low_" + n) for n in ("loaded", "mixed", "hidden", "hidden_done", "out", "taken"))

        @block.sync
        def _(sp):
            each = rank // len(w1_parts)
            for i, w in enumerate(w1_parts):
                loaded.count(sp.dma_start(w1s[:, :, i * each:(i + 1) * each], w.rearrange("(k p) r -> p k r", p=P)), 16)
            loaded.count(sp.dma_start(w2s[:], w2), 16)

        @block.vector
        def _(dve):
            mixed.count(rwkv_mix(core, st, rw, mu, tokens))

        @block.tensor
        def _(pe):
            pe.wait_ge(mixed.sem, mixed.at(1))
            pe.wait_ge(loaded.sem, loaded.at(loaded.n))
            for k in range(DC):
                ins = nc.tensor.matmul(core.bank(0)[0:rank, 0:T], w1s[:, k], rw.kk[:, k, tokens], start=k == 0, stop=k == DC - 1)
            hid.count(ins)
            pe.wait_ge(hid_done.sem, hid_done.at(1))
            for i, rows in enumerate(parts):
                for n in range(DC):
                    m = i * DC + n
                    if m >= 4:
                        pe.wait_ge(taken.sem, taken.at(m - 3))
                    out.count(nc.tensor.matmul(core.bank(4 + m % 4)[:, 0:T], w2s[rows, n * P:(n + 1) * P], hidden[rows], start=True, stop=True))

        @block.scalar
        def _(act):
            act.wait_ge(hid.sem, hid.at(1))
            hid_done.count(nc.scalar.activation(hidden[:], core.bank(0)[0:rank, 0:T], func))
            for m in range(len(parts) * DC):
                act.wait_ge(out.sem, out.at(m + 1))
                taken.count(store(m // DC, m % DC, core.bank(4 + m % 4)[:, 0:T]))


def rwkv_mix(core, st, rw, mu, tokens):
    for k in range(DC):
        ins = core.nc.vector.scalar_tensor_tensor(rw.kk[:, k, tokens], st.Y[:, k, tokens], st.V("rw_mu", mu * DC + k), st.H[:, k, tokens],
                                                  ALU.mult, ALU.add)
    return ins


def rwkv_project(core, st, rw):
    nc, A = core.nc, st.A
    lat, all_ = slice(CTX, TT), slice(0, TT)
    rwkv_shift_stage(core, st)
    copy = lambda dst: lambda act, c, bank: nc.scalar.activation(chunk_of(dst, c), bank[:, 0:dst.shape[2]], ACT.Copy)
    for i, (mu, dst, tokens) in enumerate(((0, rw.r, lat), (2, rw.k, all_), (3, rw.v, all_))):
        gemm_stage(core, st, "in", A["rw_w_rkv"][0, i], D, lambda k, t=tokens: rw.kk[:, k, t], copy(dst),
                   mix=lambda mu=mu, t=tokens: rwkv_mix(core, st, rw, mu, t))
    rwkv_low_rank_stage(core, st, rw, 4, [A["rw_a1"][0]], 64, ACT.Copy, A["rw_a2"][0], [slice(0, 64)],
                        lambda i, n, bank: nc.scalar.activation(rw.b[:, n], bank, ACT.Sigmoid, bias=st.V("rw_a0", n)), all_)
    rwkv_low_rank_stage(core, st, rw, 1, [A["rw_w1"][0, 0], A["rw_w1"][0, 1]], 128, ACT.Tanh, A["rw_w2"][0].rearrange("z r d -> (z r) d"),
                        [slice(0, 64), slice(64, 128)],
                        lambda i, n, bank: nc.scalar.activation(rw.decay[i][:, n], bank, ACT.Sigmoid, bias=st.V("rw_w0", i * DC + n)), all_)
    rwkv_low_rank_stage(core, st, rw, 5, [A["rw_g1"][0]], 128, ACT.Sigmoid, A["rw_g2"][0], [slice(0, 128)],
                        lambda i, n, bank: nc.scalar.activation(rw.g[:, n], bank, ACT.Copy), lat)

    with ExitStack() as ctx, core.engines_block() as block:
        square = core.sb("square", [P, 2, TT], ctx=ctx)
        norm = core.sb("norm", [P, 2, TT], ctx=ctx)
        blend = core.sb("blend", [P, TT], ctx=ctx)
        rest = core.sb("rest", [P, DC], ctx=ctx)
        scaled, squared, summed, rooted = (core.counter("kk_" + n) for n in ("scaled", "squared", "summed", "rooted"))
        chain = core.counter("vector_chain")

        @block.scalar
        def _(act):
            for n in range(DC):
                act.wait_ge(scaled.sem, scaled.at(n + 1))
                squared.count(nc.scalar.activation(square[:, n % 2], rw.kk[:, n], ACT.Square))
                act.wait_ge(summed.sem, summed.at(n + 1))
                if n >= 2:
                    act.wait_ge(scaled.sem, scaled.at(n + 1))
                rooted.count(nc.scalar.activation(norm[:, n % 2], core.bank(n), ACT.Sqrt))

        @block.tensor
        def _(pe):
            for n in range(DC):
                pe.wait_ge(squared.sem, squared.at(n + 1))
                summed.count(nc.tensor.matmul(core.bank(n), st.C("head_ones"), square[:, n % 2], start=True, stop=True))

        @block.vector
        def _(dve):
            c = Chain(dve, chain)
            c.ended(nc.vector.tensor_scalar(rest[:], st.V("rw_kvec", DC, DC), -1.0, 1.0, ALU.mult, ALU.add))
            scale = lambda n: scaled.count(nc.vector.tensor_scalar(rw.kk[:, n], rw.k[:, n], st.V("rw_kvec", n), None, ALU.mult))
            scale(0)
            for n in range(DC):
                if n + 1 < DC:
                    scale(n + 1)
                nc.vector.tensor_tensor_scan(rw.decay[0][:, n], st.C("keep_fwd"), rw.decay[0][:, n], 0.0, ALU.mult, ALU.add)
                nc.vector.tensor_tensor_scan(rw.decay[1][:, n, ::-1], st.C("keep_bwd")[:, ::-1], rw.decay[1][:, n, ::-1], 0.0, ALU.mult, ALU.add)
                c.ended(nc.vector.tensor_scalar(blend[:], rw.b[:, n], st.V("rw_kvec", DC + n), rest[:, n:n + 1], ALU.mult, ALU.add))
                c.ended(nc.vector.tensor_tensor(rw.k[:, n], rw.k[:, n], blend[:], ALU.mult))
                dve.wait_ge(rooted.sem, rooted.at(n + 1))
                v = norm[:, n % 2]
                c.ended(nc.vector.tensor_scalar(v, v, 1e-12, None, ALU.max))
                c.ended(nc.vector.reciprocal(v, v))
                c.ended(nc.vector.tensor_tensor(rw.kk[:, n], rw.kk[:, n], v, ALU.mult))
                c.ended(nc.vector.tensor_tensor(rw.b[:, n], rw.b[:, n], rw.kk[:, n], ALU.mult))


def rwkv_steps(latent):
    levels = range(2, 7)
    out = ["RK", "RB"] if latent else []
    pe = ["V", "K", "B", "C", "CT", "LK"] + out
    for l in levels:
        pe += [f"Y{l}", f"E{l}"] + ([f"D{l}"] if l < 6 else [])
    pe += ["W", "U"] + (["O"] if latent else []) + ["S"]
    act = ["exp", "V", "K", "B", "C"] + [f"Y{l}" for l in levels] + ["W", "U"]
    dve = ["prep", "CT", "D1", "LK"] + out
    for l in levels:
        dve += [f"E{l}"] + ([f"D{l}"] if l < 6 else [])
    dve += (["O"] if latent else []) + ["S"]
    return pe, act, dve


def rwkv_scan_stage(core, st, rw):
    nc = core.nc
    n_chunks = CTX // RW_CHUNK
    C = RW_CHUNK
    with ExitStack() as ctx, core.engines_block() as block:
        taken_h = iter(range(DC))

        def buf(name):
            k = next(taken_h, None)
            t = st.H[:, k] if k is not None else core.sb(name, [P, DC * C], ctx=ctx)[:]
            return t.rearrange("p (n t) -> p n t", n=DC)
        names = ("alpha", "rho", "beta", "kappa", "val", "kappa_t", "beta_t", "val_t", "c", "e", "grow", "fall", "state")
        B = [{n: buf(f"{n}{d}") for n in names} for d in (0, 1)]
        for b in B:
            b.update(lk=b["grow"], rk=b["fall"], rb=b["kappa"], y=b["beta"], w=b["beta"], u=b["c"], d=b["val"])
        last = [core.sb(f"last{d}", [P, DC], ctx=ctx) for d in (0, 1)]
        pe_s, act_s, dve_s = ([core.counter(f"rw_{e}_step{d}") for d in (0, 1)] for e in ("tensor", "scalar", "vector"))
        chain = core.counter("vector_chain")
        passed = core.counter("rw_tensor_passed"), core.counter("rw_vector_passed")
        phases = [(False, 0), (True, CTX)]
        H2 = [slice(0, 64), slice(64, 128)]

        def value(sig, order, off, it, step):
            return sig.at(off + it * len(order) + order.index(step) + 1)

        def start_of(it, d, t0):
            return t0 + (it * C if d == 0 else (n_chunks - 1) * C - it * C)

        offs = []
        off = [1, 1, 1]
        for latent, _ in phases:
            offs.append(list(off))
            off = [o + n_chunks * len(x) for o, x in zip(off, rwkv_steps(latent))]

        @block.tensor
        def _(pe):
            for d in (0, 1):
                pe.sem_inc(pe_s[d].sem, 1)
            for (latent, t0), (po, ao, do) in zip(phases, offs):
                order, act_order, dve_order = rwkv_steps(latent)
                a, v = "act", "dve"
                need = {"V": [(v, "prep"), (a, "exp")], "Y2": [(a, "C"), (v, "CT")], "E2": [(a, "Y2"), (v, "D1")], "W": [(v, "LK"), (a, "V")],
                        "U": [(a, "W"), (v, "E6")], "O": [(a, "U"), (v, "RB")], "S": [(a, "U")]}
                for l in range(3, 7):
                    need[f"Y{l}"] = [(v, f"E{l - 1}")]
                    need[f"E{l}"] = [(a, f"Y{l}"), (v, f"D{l - 1}")]
                with pe.Fori(0, n_chunks) as it:
                    for n, step in enumerate(order):
                        for d in (0, 1):
                            b, bank = B[d], core.bank(4 * d + n % 4).rearrange("p (n t) -> p n t", n=DC)
                            wait = list(need.get(step, []))
                            if n >= 4:
                                p = order[n - 4]
                                wait.append(("act" if p in act_order else "dve", p))
                            on_act = [s for eng, s in wait if eng == "act"]
                            on_dve = [s for eng, s in wait if eng == "dve"]
                            if on_act:
                                pe.wait_ge(act_s[d].sem, value(act_s[d], act_order, ao, it, max(on_act, key=act_order.index)))
                            if on_dve:
                                pe.wait_ge(dve_s[d].sem, value(dve_s[d], dve_order, do, it, max(on_dve, key=dve_order.index)))
                            pe.sem_inc(passed[0].sem, 1)
                            kind = step.rstrip("123456")
                            ident = st.C("ident")
                            for i in range(DC):
                                for h in H2:
                                    turn = ident[h, h]
                                    x = {"V": [("val", turn)], "K": [("kappa", turn)], "B": [("beta", turn)], "C": [("alpha", "beta")],
                                         "CT": [("beta", "alpha")], "LK": [("kappa", "alpha")], "RK": [("kappa", "rho")], "RB": [("beta", "rho")],
                                         "Y": [("c", "e")], "E": [("d", "y")], "D": [("y", "d")], "W": [("alpha", "state"), ("lk", "val_t")],
                                         "U": [("e", "w")], "O": [("state", "rho"), ("val_t", "rk"), ("u", "rb")],
                                         "S": [("kappa_t", "val_t"), ("beta_t", "u")]}[kind]
                                    for j, (lhs, rhs) in enumerate(x):
                                        moving = b[rhs][h, i] if isinstance(rhs, str) else rhs
                                        ins = nc.tensor.matmul(bank[h, i], b[lhs][h, i], moving, start=j == 0, stop=j == len(x) - 1)
                            ins.then_inc(pe_s[d].sem, 1)

        @block.scalar
        def _(act):
            for d in (0, 1):
                act.sem_inc(act_s[d].sem, 1)
            for (latent, t0), (po, ao, do) in zip(phases, offs):
                pe_order, order, _ = rwkv_steps(latent)
                with act.Fori(0, n_chunks) as it:
                    for step in order:
                        for d in (0, 1):
                            b = B[d]
                            if step == "exp":
                                act.wait_ge(pe_s[d].sem, pe_s[d].at(po + it * len(pe_order)))
                                at = ds(start_of(it, d, t0), C)
                                nc.scalar.activation(b["grow"], rw.decay[d][:, :, at], ACT.Exp, scale=RW_DECAY)
                                nc.scalar.activation(b["fall"], rw.decay[d][:, :, at], ACT.Exp, scale=-RW_DECAY)
                                ins = nc.scalar.activation(b["val"], rw.v[:, :, at], ACT.Copy)
                            else:
                                act.wait_ge(pe_s[d].sem, value(pe_s[d], pe_order, po, it, step))
                                bank = core.bank(4 * d + pe_order.index(step) % 4).rearrange("p (n t) -> p n t", n=DC)
                                dst = {"V": "val_t", "K": "kappa_t", "B": "beta_t", "C": "c", "W": "w", "U": "u"}.get(step, "y")
                                ins = nc.scalar.activation(b[dst], bank, ACT.Copy)
                            ins.then_inc(act_s[d].sem, 1)

        @block.vector
        def _(dve):
            for d in (0, 1):
                nc.vector.memset(B[d]["state"], 0.0).then_inc(dve_s[d].sem, 1)
            nc.vector.memset(rw.y, 0.0).then_inc(chain.sem, 1)
            chain.n += 1
            for (latent, t0), (po, ao, do) in zip(phases, offs):
                pe_order, act_order, order = rwkv_steps(latent)
                done = 0
                per = 4
                base = chain.n
                with dve.Fori(0, n_chunks) as it:
                    for step in order:
                        for d in (0, 1):
                            b = B[d]
                            mask = lambda name, u=False: (st.C(name).bitcast(U32) if u else st.C(name)).unsqueeze(1).to_broadcast([P, DC, C])
                            if step == "prep":
                                dve.wait_ge(act_s[d].sem, value(act_s[d], act_order, ao, it, "exp"))
                                dve.wait_ge(dve_s[d].sem, dve_s[d].at(do + it * len(order)))
                                t = start_of(it, d, t0)
                                at = ds(t, C)
                                edge, inner, before = (C - 1, slice(0, C - 1), slice(1, C)) if d else (0, slice(1, C), slice(0, C - 1))
                                shift = 0 if d else 1
                                nc.vector.tensor_copy(last[d][:].unsqueeze(2), b["grow"][:, :, (0 if d else C - 1):(1 if d else C)])
                                nc.vector.scalar_tensor_tensor(b["alpha"][:, :, inner], rw.kk[:, :, ds(t + shift, C - 1)], -1.0,
                                                               b["grow"][:, :, before], ALU.mult, ALU.mult)
                                nc.vector.tensor_scalar(b["alpha"][:, :, edge:edge + 1], rw.kk[:, :, ds(t + edge, 1)], -1.0, None, ALU.mult)
                                if latent:
                                    nc.vector.tensor_tensor(b["rho"], rw.r[:, :, ds(t - CTX, C)], b["grow"], ALU.mult)
                                nc.vector.tensor_tensor(b["beta"], rw.b[:, :, at], b["fall"], ALU.mult)
                                ins = nc.vector.tensor_tensor(b["kappa"], rw.k[:, :, at], b["fall"], ALU.mult)
                            elif step == "D1":
                                dve.wait_ge(act_s[d].sem, value(act_s[d], act_order, ao, it, "C"))
                                nc.vector.tensor_copy(b["d"], mask("pair_ident")).then_inc(chain.sem, 1)
                                done += 1
                                dve.wait_ge(chain.sem, chain.at(base + it * 6 + done))
                                dve.sem_inc(passed[1].sem, 1)
                                ins = nc.vector.copy_predicated(b["d"], mask(f"pair1_{1 - d}", True), b["c"])
                            else:
                                bank = core.bank(4 * d + pe_order.index(step) % 4).rearrange("p (n t) -> p n t", n=DC)
                                if step == "CT":
                                    nc.vector.tensor_copy(b["e"], mask("pair_ident")).then_inc(chain.sem, 1)
                                    done += 1
                                    dve.wait_ge(chain.sem, chain.at(base + it * 6 + done))
                                dve.wait_ge(pe_s[d].sem, value(pe_s[d], pe_order, po, it, step))
                                if step == "CT" or step[0] in "ED":
                                    dve.sem_inc(passed[1].sem, 1)
                                if step == "CT":
                                    ins = nc.vector.copy_predicated(b["e"], mask(f"pair1_{d}", True), bank)
                                elif step in ("LK", "RK", "RB"):
                                    m = "before" if step == "LK" else "upto"
                                    ins = nc.vector.tensor_tensor(b[step.lower()], bank, mask(f"{m}_{d}"), ALU.mult)
                                elif step[0] in "ED":
                                    l = int(step[1])
                                    ins = nc.vector.copy_predicated(b[step[0].lower()], mask(f"pair{l}_{d if step[0] == 'E' else 1 - d}", True), bank)
                                elif step == "O":
                                    y = rw.y[:, :, ds(start_of(it, d, 0), C)]
                                    ins = nc.vector.tensor_tensor(y, y, bank, ALU.add)
                                elif step == "S":
                                    nc.vector.tensor_tensor(b["state"], b["state"], bank, ALU.add).then_inc(chain.sem, 1)
                                    done += 1
                                    dve.wait_ge(chain.sem, chain.at(base + it * 6 + done))
                                    ins = nc.vector.tensor_tensor(b["state"], b["state"], last[d][:].unsqueeze(2).to_broadcast([P, DC, C]), ALU.mult)
                            ins.then_inc(dve_s[d].sem, 1)
                assert done == 6
                chain.n += 6 * n_chunks
        for sigs, n in zip((pe_s, act_s, dve_s), off):
            for s in sigs:
                s.n += n
        for s, per in zip(passed, (lambda x: 2 * len(x[0]), lambda x: 2 * sum(y[0] in "ED" or y == "CT" for y in x[2]))):
            s.n += n_chunks * sum(per(rwkv_steps(latent)) for latent, _ in phases)


def rwkv_out_stage(core, st, rw):
    nc = core.nc
    lat = slice(CTX, TT)
    with ExitStack() as ctx, core.engines_block() as block:
        cen = core.sb("cen", [P, DC, LAT], ctx=ctx)
        square = core.sb("square", [P, DC, LAT], ctx=ctx)
        std = core.sb("std", [P, DC, LAT], ctx=ctx)
        rk = core.sb("rk", [P, DC, LAT], ctx=ctx)
        names = ("rk", "mean", "centred", "squared", "summed", "var", "rooted", "bonus")
        rk_s, mean, centred, squared, summed, var, rooted, bonus = (core.counter("out_" + n) for n in names)
        chain = core.counter("vector_chain")

        def half(i, n):
            return core.bank(i * 4 + n // 2)[:, n % 2 * LAT:(n % 2 + 1) * LAT]

        @block.tensor
        def _(pe):
            for n in range(DC):
                mean.count(nc.tensor.matmul(half(0, n), st.C("head_ones"), rw.y[:, n], start=True, stop=True))
            for n in range(DC):
                pe.wait_ge(rk_s.sem, rk_s.at(n + 1))
                bonus.count(nc.tensor.matmul(half(1, n), st.C("head_ones"), rk[:, n], start=True, stop=True))
            for n in range(DC):
                pe.wait_ge(squared.sem, squared.at(DC))
                summed.count(nc.tensor.matmul(half(0, n), st.C("head_ones"), square[:, n], start=True, stop=True))

        @block.scalar
        def _(act):
            for n in range(DC):
                act.wait_ge(centred.sem, centred.at(n + 1))
                squared.count(nc.scalar.activation(square[:, n], cen[:, n], ACT.Square))
            for n in range(DC):
                act.wait_ge(var.sem, var.at(n + 1))
                rooted.count(nc.scalar.activation(std[:, n], std[:, n], ACT.Sqrt))

        @block.vector
        def _(dve):
            c = Chain(dve, chain)
            for n in range(DC):
                rk_s.count(nc.vector.scalar_tensor_tensor(rk[:, n], rw.r[:, n], st.V("rw_kvec", 2 * DC + n), rw.k[:, n, lat], ALU.mult, ALU.mult))
            for n in range(DC):
                dve.wait_ge(mean.sem, mean.at(n // 2 * 2 + 2))
                centred.count(nc.vector.scalar_tensor_tensor(cen[:, n], half(0, n), -1.0 / RW_HEAD, rw.y[:, n], ALU.mult, ALU.add))
            for n in range(DC):
                dve.wait_ge(summed.sem, summed.at(n // 2 * 2 + 2))
                var.count(nc.vector.tensor_scalar(std[:, n], half(0, n), 1.0 / RW_HEAD, RW_LN_EPS, ALU.mult, ALU.add))
            for n in range(DC):
                dve.wait_ge(rooted.sem, rooted.at(n + 1))
                c.ended(nc.vector.reciprocal(std[:, n], std[:, n]))
                c.ended(nc.vector.tensor_tensor(cen[:, n], cen[:, n], std[:, n], ALU.mult))
                c.ended(nc.vector.tensor_scalar(cen[:, n], cen[:, n], st.V("rw_lnx", n), st.V("rw_lnx", DC + n), ALU.mult, ALU.add))
                dve.wait_ge(bonus.sem, bonus.at(n // 2 * 2 + 2))
                c.ended(nc.vector.tensor_tensor(rk[:, n], half(1, n), rw.v[:, n, lat], ALU.mult))
                c.ended(nc.vector.tensor_tensor(cen[:, n], cen[:, n], rk[:, n], ALU.add))
                nc.vector.tensor_tensor(st.H[:, n, lat], cen[:, n], rw.g[:, n], ALU.mult)


def rwkv_layer(core, st):
    nc, A = core.nc, st.A
    lat = slice(CTX, TT)
    modulations(core, st, 1, (0, 1))
    norm_in(core, st, 0, 0, (0, 1))
    with ExitStack() as scope:
        rw = Rwkv(core, st, scope)
        rwkv_project(core, st, rw)
        rwkv_scan_stage(core, st, rw)
        rwkv_out_stage(core, st, rw)
    gemm_stage(core, st, "in", A["rw_w_o"][0], D, lambda k: st.H[:, k, lat],
               lambda act, c, bank: nc.scalar.activation(chunk_of(st.Y, c, lat), bank[:, 0:LAT], ACT.Copy))
    norm_out(core, st, 1, st.Y, (0,))
    norm_in(core, st, 2, 24, (0,))
    ffn_stage(core, st, 1, LAT, CTX)
    norm_out(core, st, 3, st.Y, (0,))


LATS = slice(CTX, TT)


def ada(core, st, layer):
    mod_stage(core, st, st.A["w_ada_2"][layer], ("b_ada_2", layer * 48), (2, 2), 48)
    coef_stage(core, st, [(0, 0, ("attn_gain_2", layer * DC), 8, 1), (0, 2, ("ffn_gain_2", layer * DC), 32, 1)])


def add_gated(core, st, key, w, rhs, gate, width=512):
    nc = core.nc

    def store(dve, c, bank):
        x = chunk_of(st.X, c, LATS)
        return nc.vector.scalar_tensor_tensor(x, bank[:, 0:LAT], st.mod[:, ds(gate + c, 1), 0], x, ALU.mult, ALU.add)
    gemm_stage(core, st, key, w, D, rhs, store, width=width, engine="vector")


def small_stage(core, st, w, jobs):
    nc = core.nc
    v = w.rearrange("(k p) n -> p k n", p=P)
    with ExitStack() as ctx, core.engines_block() as block:
        ws, outs = [], []
        for i, (kind, col, n, dst, *more) in enumerate(jobs):
            if kind == "pair":
                t = core.sb(f"w_pair{i}", [P, DC, n, 2, HD], ctx=ctx)
                for g in range(n):
                    outs.append((i, lambda k, t=t, g=g: (t[:, k, g].rearrange("p a d -> p (a d)"), st.H[:, k, LATS]), LAT,
                                 lambda bank, dst=dst, g=g: nc.scalar.activation(dst[:, g], bank, ACT.Copy)))
            else:
                width = n * HD if kind == "values" else n
                t = core.sb(f"w_tokens{i}", [P, DC, width], ctx=ctx)
                for b in (0, 1):
                    if kind == "values":
                        take = lambda bank, dst=dst, b=b, n=n: nc.scalar.activation(dst[:, b, :, HD:2 * HD], bank.rearrange("p (g d) -> p g d", g=n), ACT.Copy)
                    else:
                        take = lambda bank, dst=dst, b=b, more=more: nc.scalar.activation(dst[:, b], bank, more[0], scale=more[1])
                    outs.append((i, lambda k, t=t, b=b: (st.H[:, k, CTX + b * P:CTX + (b + 1) * P], t[:, k]), width, take))
            ws.append(t)
        loaded = [core.counter(f"small_weights{i}") for i in range(len(jobs))]
        ready, taken, zeroed = core.counter("small_ready"), core.counter("small_taken"), core.counter("small_zeroed")

        @block.sync
        def _(sp):
            for i, (kind, col, n, *_) in enumerate(jobs):
                if kind == "pair":
                    for k in range(DC):
                        for a in (0, 1):
                            loaded[i].count(sp.dma_start(ws[i][:, k, :, a], v[:, k, col:col + n * HD].rearrange("p (g d) -> p g d", d=HD)), 16)
                else:
                    width = n * HD if kind == "values" else n
                    loaded[i].count(sp.dma_start(ws[i][:], v[:, :, col:col + width]), 16)

        @block.vector
        def _(dve):
            for kind, _, _, dst, *_ in jobs:
                if kind == "values":
                    zeroed.count(nc.vector.memset(dst[:], 0.0))

        @block.tensor
        def _(pe):
            for m, (i, operands, width, _) in enumerate(outs):
                pe.wait_ge(loaded[i].sem, loaded[i].at(loaded[i].n))
                if m >= 4:
                    pe.wait_ge(taken.sem, taken.at(m - 3))
                for k in range(DC):
                    lhs, rhs = operands(k)
                    ins = nc.tensor.matmul(core.bank(m % 4)[:, 0:width], lhs, rhs, start=k == 0, stop=k == DC - 1)
                ready.count(ins)

        @block.scalar
        def _(act):
            if zeroed.n:
                act.wait_ge(zeroed.sem, zeroed.at(zeroed.n))
            for m, (i, _, width, take) in enumerate(outs):
                act.wait_ge(ready.sem, ready.at(m + 1))
                taken.count(take(core.bank(m % 4)[:, 0:width]))


def rope_stage(core, st, chunks):
    nc = core.nc
    with ExitStack() as ctx, core.engines_block() as block:
        turned = core.sb("turned", [P, 2, LAT], ctx=ctx)
        straight = core.sb("straight", [P, 2, LAT], ctx=ctx)
        swapped, done, chain = core.counter("rope_swapped"), core.counter("rope_done"), core.counter("vector_chain")

        @block.tensor
        def _(pe):
            for i, x in enumerate(chunks):
                if i >= 4:
                    pe.wait_ge(done.sem, done.at(i - 3))
                swapped.count(nc.tensor.matmul(core.bank(i % 4)[:, 0:LAT], st.C("rot"), x, start=True, stop=True))

        @block.vector
        def _(dve):
            c = Chain(dve, chain)
            for i, x in enumerate(chunks):
                nc.vector.tensor_tensor(straight[:, i % 2], x, st.cos[:], ALU.mult)
                dve.wait_ge(swapped.sem, swapped.at(i + 1))
                c.ended(nc.vector.tensor_tensor(turned[:, i % 2], core.bank(i % 4)[:, 0:LAT], st.sin[:], ALU.mult))
                done.count(nc.vector.tensor_tensor(x, straight[:, i % 2], turned[:, i % 2], ALU.add))


def causal_stage(core, st, seen):
    nc = core.nc
    with core.engines_block() as block:
        @block.vector
        def _(dve):
            nc.vector.memset(seen[:, 0, P:LAT], NEG)
            nc.vector.memset(seen[:, 1, 0:P], 0.0)
            for b in (0, 1):
                nc.vector.tensor_copy(seen[:, b, b * P:(b + 1) * P], st.C("neg_after"))


def indexer_stage(core, st, iq, ik, iw, seen, keep):
    nc = core.nc
    with ExitStack() as ctx, core.engines_block() as block:
        score = core.sb("score", [P, 2, LAT], ctx=ctx)
        left = [core.sb(f"left{i}", [P, 2, LAT], ctx=ctx) for i in (0, 1)]
        part = core.sb("part", [P, 2, LAT], ctx=ctx)
        top = core.sb("top", [P, 2, 2, 8], ctx=ctx)
        dots, weighed, chain = core.counter("idx_dots"), core.counter("idx_weighed"), core.counter("vector_chain")

        @block.tensor
        def _(pe):
            for b in (0, 1):
                for h in range(IDX_HEADS):
                    n = b * IDX_HEADS + h
                    if n >= 4:
                        pe.wait_ge(weighed.sem, weighed.at(n - 3))
                    half = slice(h % 2 * HD, (h % 2 + 1) * HD)
                    dots.count(nc.tensor.matmul(core.bank(n % 4)[:, 0:LAT], iq[half, h // 2, b * P:(b + 1) * P], ik[half, 0], start=True, stop=True))

        @block.vector
        def _(dve):
            c = Chain(dve, chain)
            for b in (0, 1):
                for h in range(IDX_HEADS):
                    n = b * IDX_HEADS + h
                    dve.wait_ge(dots.sem, dots.at(n + 1))
                    ins = nc.vector.tensor_scalar(score[:, b] if h == 0 else part[:, h % 2], core.bank(n % 4)[:, 0:LAT], 0.0, iw[:, b, h:h + 1], ALU.max, ALU.mult)
                    weighed.count(ins)
                    dve.wait_ge(weighed.sem, weighed.at(n + 1))
                    if h:
                        c.ended(nc.vector.tensor_tensor(score[:, b], score[:, b], part[:, h % 2], ALU.add))
            c.ended(nc.vector.tensor_tensor(left[0][:], score[:], seen[:], ALU.add))
            for r in range(DSA_KEEP // 8):
                x, y = left[r % 2], left[1 - r % 2]
                for b in (0, 1):
                    ins = nc.vector.max(top[:, b, r % 2], x[:, b])
                c.ended(ins)
                for b in (0, 1):
                    ins = nc.vector.match_replace(y[:, b], top[:, b, r % 2], x[:, b], GONE)
                c.ended(ins)
            x = left[DSA_KEEP // 8 % 2]
            c.ended(nc.vector.tensor_scalar(keep[:], x[:], GONE / 2, NEG, ALU.is_ge, ALU.mult))
            nc.vector.tensor_tensor(keep[:], keep[:], seen[:], ALU.add)


def attention_stage(core, st, q, kd, v, neg, out, n_keys=LAT, gate=None, some=None, add=False):
    nc = core.nc
    items = [(b, hp) for b in (0, 1) for hp in range(HEADS // 2)]
    N = len(items)
    group = HEADS // KV_HEADS
    with ExitStack() as ctx, core.engines_block() as block:
        s = core.sb("scores", [P, 2, 2, n_keys], ctx=ctx)
        low = core.sb("low", [P, 2, 2], ctx=ctx)
        total = core.sb("total", [P, 2, 2], ctx=ctx)
        pt = core.sb("pt", [P, 2, 4, P], ctx=ctx)
        names = ("scored", "masked", "exped", "normed", "turned", "pt_ready", "summed", "out_taken")
        scored, masked, exped, normed, turned, pt_ready, summed, out_taken = (core.counter("at_" + n) for n in names)
        chain = core.counter("vector_chain")
        keys = lambda b: min(n_keys, (b + 1) * P)
        blocks = lambda b: [(i * P, min(P, keys(b) - i * P)) for i in range(-(-keys(b) // P))]
        SC = [core.psum[i].rearrange("p (h s) -> p h s", h=2) for i in (0, 1)]
        TR, OUT = [core.bank(4), core.bank(5)], [core.bank(6), core.bank(7)]

        @block.tensor
        def _(pe):
            for n in range(N + 2):
                if n < N:
                    b, hp = items[n]
                    if n >= 2:
                        pe.wait_ge(masked.sem, masked.at(n - 1))
                    for h in (0, 1):
                        half = slice(h * HD, (h + 1) * HD)
                        ins = nc.tensor.matmul(SC[n % 2][:, h, 0:keys(b)], q[half, hp, b * P:(b + 1) * P],
                                               kd[half, hp * 2 // group, 0:keys(b)], start=True, stop=True)
                    scored.count(ins)
                if 0 <= n - 1 < N:
                    m = n - 1
                    b, hp = items[m]
                    pe.wait_ge(normed.sem, normed.at(m + 1))
                    if m >= 2:
                        pe.wait_ge(pt_ready.sem, pt_ready.at(m - 1))
                    for h in (0, 1):
                        for i, (at, w) in enumerate(blocks(b)):
                            ins = nc.tensor.transpose(TR[m % 2][0:w, (h * 2 + i) * P:(h * 2 + i + 1) * P], s[:, m % 2, h, at:at + w], st.C("ident"))
                    turned.count(ins)
                if 0 <= n - 2:
                    m = n - 2
                    b, hp = items[m]
                    pe.wait_ge(pt_ready.sem, pt_ready.at(m + 1))
                    if m >= 2:
                        pe.wait_ge(out_taken.sem, out_taken.at(m - 1))
                    parts = [(h, i, w) for h in (0, 1) for i, (_, w) in enumerate(blocks(b))]
                    for j, (h, i, w) in enumerate(parts):
                        ins = nc.tensor.matmul(OUT[m % 2][:, 0:P], v[0:w, i, hp * 2 // group, (1 - h) * HD:(1 - h) * HD + P], pt[0:w, m % 2, h * 2 + i],
                                               start=j == 0, stop=j == len(parts) - 1)
                    summed.count(ins)

        @block.scalar
        def _(act):
            for n in range(N + 2):
                if n < N:
                    b, hp = items[n]
                    act.wait_ge(masked.sem, masked.at(n + 1))
                    if n >= 2:
                        act.wait_ge(normed.sem, normed.at(n - 1))
                    for h in (0, 1):
                        x = s[:, n % 2, h, 0:keys(b)]
                        ins = nc.scalar.activation(x, x, ACT.Exp, bias=low[:, n % 2, h:h + 1], accum_out=total[:, n % 2, h:h + 1])
                    exped.count(ins)
                if 0 <= n - 1 < N:
                    m = n - 1
                    b, hp = items[m]
                    act.wait_ge(turned.sem, turned.at(m + 1))
                    if m >= 2:
                        act.wait_ge(summed.sem, summed.at(m - 1))
                    nb, w = len(blocks(b)), blocks(b)[0][1]
                    ins = nc.scalar.activation(pt[0:w, m % 2].rearrange("p (h i) t -> p h i t", h=2)[:, :, 0:nb],
                                               TR[m % 2][0:w].rearrange("p (h i t) -> p h i t", h=2, i=2)[:, :, 0:nb], ACT.Copy)
                    pt_ready.count(ins)
                if 0 <= n - 2 and not add:
                    m = n - 2
                    b, hp = items[m]
                    act.wait_ge(summed.sem, summed.at(m + 1))
                    out_taken.count(nc.scalar.activation(out[:, hp, b * P:(b + 1) * P], OUT[m % 2][:, 0:P], ACT.Copy))

        @block.vector
        def _(dve):
            c = Chain(dve, chain)
            for n in range(N + 3):
                if n < N:
                    b, hp = items[n]
                    K = keys(b)
                    x = s[:, n % 2, :, 0:K]
                    dve.wait_ge(scored.sem, scored.at(n + 1))
                    if n >= 2:
                        dve.wait_ge(turned.sem, turned.at(n - 1))
                    c.ended(nc.vector.scalar_tensor_tensor(x, SC[n % 2][:, :, 0:K], HD ** -0.5,
                                                          neg[:, b, 0:K].unsqueeze(1).to_broadcast([P, 2, K]), ALU.mult, ALU.add))
                    masked.count(nc.vector.tensor_reduce(low[:, n % 2], x, AX, ALU.max, negate=True))
                if 0 <= n - 1 < N:
                    m = n - 1
                    b, hp = items[m]
                    K = keys(b)
                    x = s[:, m % 2, :, 0:K]
                    r = total[:, m % 2]
                    dve.wait_ge(exped.sem, exped.at(m + 1))
                    c.ended(nc.vector.reciprocal(r, r))
                    if gate is not None:
                        c.ended(nc.vector.tensor_tensor(r, r, gate[:, b, 2 * hp:2 * hp + 2], ALU.mult))
                    if some is not None:
                        c.ended(nc.vector.tensor_tensor(x, x, some[:, b, 0:K].unsqueeze(1).to_broadcast([P, 2, K]), ALU.mult))
                    normed.count(nc.vector.tensor_tensor(x, x, r.unsqueeze(2).to_broadcast([P, 2, K]), ALU.mult))
                if 0 <= n - 3 and add:
                    m = n - 3
                    b, hp = items[m]
                    dve.wait_ge(summed.sem, summed.at(m + 1))
                    y = out[:, hp, b * P:(b + 1) * P]
                    out_taken.count(nc.vector.tensor_tensor(y, y, OUT[m % 2][:, 0:P], ALU.add))


def swiglu_stage(core, st, wg, wu, wd):
    nc = core.nc
    fc = wg.shape[1] // P
    n_it = fc // 2
    with ExitStack() as outer:
        h = core.sb("swiglu_h", [P, fc, LAT], ctx=outer)
        with ExitStack() as ctx, core.engines_block() as block:
            tiles = k_tiles(wg, 256, 2, (0, 1), lambda it: it * 256) + k_tiles(wu, 256, 2, (2, 3), lambda it: it * 256)
            g = Gemm(core, ctx, "up", tiles, {o: o for o in range(4)}, 256)
            silu = core.sb("silu", [P, 2, LAT], ctx=ctx)

            @block.sync
            def _(sp):
                rounds(sp, n_it, lambda it, first: g.fetch_round(sp, it, first))

            @block.tensor
            def _(pe):
                rounds(pe, n_it, lambda it, first: g.matmul_round(pe, it, lambda k: st.H[:, k, LATS], first))

            @block.scalar
            def _(act):
                def body(it, first):
                    for o in (0, 1):
                        bank = g.wait_bank(act, o, it)
                        if not first:
                            act.wait_ge(g.free[2 + o].sem, g.free[2 + o].at(it))
                        g.bank_taken(nc.scalar.activation(silu[:, o], bank[:, 0:LAT], ACT.Silu), o)
                rounds(act, n_it, body)

            @block.vector
            def _(dve):
                def body(it, first):
                    for o in (0, 1):
                        bank = g.wait_bank(dve, 2 + o, it)
                        dve.wait_ge(g.free[o].sem, g.free[o].at(it + 1))
                        g.bank_taken(nc.vector.tensor_tensor(chunk_of(h, it * 2 + o), silu[:, o], bank[:, 0:LAT], ALU.mult), 2 + o)
                rounds(dve, n_it, body)
            g.settle(n_it)
        add_gated(core, st, "down", wd, lambda k: h[:, k], 40, width=256)


def sparse_layer(core, st):
    nc, A = core.nc, st.A
    ada(core, st, 0)
    norm_in(core, st, 0, 0, (0,))
    with ExitStack() as scope:
        sb = lambda name, shape: core.sb(name, shape, ctx=scope)
        q, kd, v = sb("q", [P, HEADS // 2, LAT]), sb("kd", [P, KV_HEADS, LAT]), sb("v", [P, 2, KV_HEADS, 3 * HD])
        iq, ik, iw = sb("iq", [P, IDX_HEADS // 2, LAT]), sb("ik", [P, 1, LAT]), sb("iw", [P, 2, IDX_HEADS])
        seen, keep = sb("seen", [P, 2, LAT]), sb("keep", [P, 2, LAT])
        w = A["a_w_in_2"][0]
        at = np.cumsum([0, HEADS * HD, KV_HEADS * HD, KV_HEADS * HD, IDX_HEADS * HD, HD])
        gemm_stage(core, st, "in", w, None, lambda k: st.H[:, k, LATS],
                   lambda act, c, bank: nc.scalar.activation(q[:, c] if c < 8 else iq[:, c - 8], bank[:, 0:LAT], ACT.Copy),
                   sections=[0, 512, int(at[3])])
        small_stage(core, st, w, [("pair", int(at[1]), KV_HEADS, kd), ("values", int(at[2]), KV_HEADS, v), ("pair", int(at[4]), 1, ik),
                                  ("tokens", int(at[5]), IDX_HEADS, iw, ACT.Copy, IDX_HEADS ** -0.5 * HD ** -0.5)])
        rope_stage(core, st, [q[:, i] for i in range(8)] + [kd[:, i] for i in range(4)] + [iq[:, i] for i in range(4)] + [ik[:, 0]])
        causal_stage(core, st, seen)
        indexer_stage(core, st, iq, ik, iw, seen, keep)
        attention_stage(core, st, q, kd, v, keep, st.Y[:, :, LATS])
        add_gated(core, st, "in", A["a_w_out_2"][0], lambda k: st.Y[:, k, LATS], 16)
    norm_in(core, st, 2, 24, (0,))
    swiglu_stage(core, st, A["ffn_w_gate_2"][0], A["ffn_w_up_2"][0], A["ffn_w_down_2"][0])


def compress_stage(core, st, jobs):
    nc = core.nc
    n_l = CMP_LEN // 2
    with ExitStack() as ctx, core.engines_block() as block:
        loaded = [core.counter(f"cmp_weights{i}") for i in (0, 1)]
        unfolded, hid, hid_done, out, zeroed = (core.counter("cmp_" + n) for n in ("unfolded", "hidden", "hidden_done", "out", "zeroed"))
        chain = core.counter("vector_chain")
        w1s = [core.sb(f"cmp_w1_{i}", [P, n_l, CMP_HIDDEN], ctx=ctx) for i in (0, 1)]
        w2s = [core.sb(f"cmp_w2_{i}", [P, 2, 2, HD], ctx=ctx) for i in (0, 1)]
        blocks = [core.sb(f"cmp_blocks{i}", [P, n_l, KV_HEADS, N_CMP], ctx=ctx) for i in (0, 1)]
        hidden = [core.sb(f"cmp_hidden{i}", [P, 2, KV_HEADS * N_CMP], ctx=ctx) for i in (0, 1)]

        @block.sync
        def _(sp):
            for i, (x, pe_name, w1, w2, dst, by_token) in enumerate(jobs):
                loaded[i].count(sp.dma_start(w1s[i][:], w1.rearrange("(l p) n -> p l n", p=P)), 16)
                for a in (0, 1):
                    loaded[i].count(sp.dma_start(w2s[i][:, :, a], w2.rearrange("(c p) d -> p c d", p=P)), 16)

        @block.vector
        def _(dve):
            c = Chain(dve, chain)
            for i, (x, pe_name, *_, dst, by_token) in enumerate(jobs):
                if by_token:
                    nc.vector.memset(dst[:], 0.0)
                else:
                    nc.vector.memset(dst[:], 0.0)
                for half in (0, 1):
                    rows = slice(half * HD, (half + 1) * HD)
                    for l in range(n_l):
                        at = 2 * l + half
                        src = x[rows, :, at:at + (N_CMP - 1) * CMP_STRIDE + 1:CMP_STRIDE]
                        ins = nc.vector.tensor_scalar(blocks[i][rows, l], src, st.V(pe_name, l)[rows], None, ALU.add)
                unfolded.count(ins)

        @block.tensor
        def _(pe):
            for i, (*_, dst, by_token) in enumerate(jobs):
                pe.wait_ge(loaded[i].sem, loaded[i].at(48))
                pe.wait_ge(unfolded.sem, unfolded.at(i + 1))
                for c in (0, 1):
                    for l in range(n_l):
                        ins = nc.tensor.matmul(core.bank(2 * i + c)[:, 0:KV_HEADS * N_CMP], w1s[i][:, l, c * P:(c + 1) * P],
                                               blocks[i][:, l].rearrange("p g n -> p (g n)"), start=l == 0, stop=l == n_l - 1)
                hid.count(ins)
            for i, (*_, dst, by_token) in enumerate(jobs):
                pe.wait_ge(hid_done.sem, hid_done.at(i + 1))
                bank = core.bank(4 + i)
                if not by_token:
                    for c in (0, 1):
                        ins = nc.tensor.matmul(bank[:, 0:KV_HEADS * N_CMP], w2s[i][:, c].rearrange("p a d -> p (a d)"), hidden[i][:, c], start=c == 0, stop=c == 1)
                else:
                    for g in range(KV_HEADS):
                        for c in (0, 1):
                            ins = nc.tensor.matmul(bank[0:N_CMP, g * HD:(g + 1) * HD], hidden[i][:, c, g * N_CMP:(g + 1) * N_CMP], w2s[i][:, c, 0],
                                                   start=c == 0, stop=c == 1)
                out.count(ins)

        @block.scalar
        def _(act):
            for i in (0, 1):
                act.wait_ge(hid.sem, hid.at(i + 1))
                for c in (0, 1):
                    ins = nc.scalar.activation(hidden[i][:, c], core.bank(2 * i + c)[:, 0:KV_HEADS * N_CMP], ACT.Gelu_apprx_tanh)
                hid_done.count(ins)
            for i, (*_, dst, by_token) in enumerate(jobs):
                act.wait_ge(out.sem, out.at(i + 1))
                bank = core.bank(4 + i)
                if by_token:
                    nc.scalar.activation(dst[0:N_CMP, 0, :, HD:2 * HD], bank[0:N_CMP, 0:KV_HEADS * HD].rearrange("p (g d) -> p g d", g=KV_HEADS), ACT.Copy)
                else:
                    nc.scalar.activation(dst[:, :, 0:N_CMP], bank[:, 0:KV_HEADS * N_CMP].rearrange("p (g n) -> p g n", g=KV_HEADS), ACT.Copy)


def router_stage(core, st, shares):
    nc = core.nc
    E = EXPERTS
    with ExitStack() as ctx, core.engines_block() as block:
        w = core.sb("w_router", [P, DC, E], ctx=ctx)
        logit, rank, expo = (core.sb(n, [P, 2, E], ctx=ctx) for n in ("logit", "rank", "expo"))
        low, total = (core.sb(n, [P, 2, 1], ctx=ctx) for n in ("low", "total"))
        rows = core.sb("share_rows", [E, LAT], ctx=ctx)
        loaded, logits, low_ready, exped, gated, turned, rows_ready, spread, taken = (
            core.counter("route_" + n) for n in ("loaded", "logits", "low_ready", "exped", "gated", "turned", "rows_ready", "spread", "taken"))
        chain = core.counter("vector_chain")

        @block.sync
        def _(sp):
            loaded.count(sp.dma_start(w[:], st.A["moe_w_router_2"][0].rearrange("(k p) e -> p k e", p=P)), 16)

        @block.tensor
        def _(pe):
            pe.wait_ge(loaded.sem, loaded.at(16))
            for b in (0, 1):
                for k in range(DC):
                    ins = nc.tensor.matmul(core.bank(b)[:, 0:E], st.H[:, k, CTX + b * P:CTX + (b + 1) * P], w[:, k], start=k == 0, stop=k == DC - 1)
            logits.count(ins)
            pe.wait_ge(gated.sem, gated.at(1))
            for b in (0, 1):
                ins = nc.tensor.transpose(core.bank(2)[0:E, b * P:(b + 1) * P], expo[:, b], st.C("ident"))
            turned.count(ins)
            pe.wait_ge(rows_ready.sem, rows_ready.at(1))
            for e in range(E):
                if e >= 4:
                    pe.wait_ge(taken.sem, taken.at(e - 3))
                spread.count(nc.tensor.matmul(core.bank(4 + e % 4)[:, 0:LAT], st.C("ident")[0:E, e:e + 1].to_broadcast([E, P]), rows[:], start=True, stop=True))

        @block.scalar
        def _(act):
            act.wait_ge(low_ready.sem, low_ready.at(1))
            for b in (0, 1):
                ins = nc.scalar.activation(expo[:, b], logit[:, b], ACT.Exp, bias=low[:, b])
            exped.count(ins)
            act.wait_ge(turned.sem, turned.at(1))
            rows_ready.count(nc.scalar.activation(rows[:], core.bank(2)[0:E, 0:LAT], ACT.Copy))
            for e in range(E):
                act.wait_ge(spread.sem, spread.at(e + 1))
                taken.count(nc.scalar.activation(shares[:, e], core.bank(4 + e % 4)[:, 0:LAT], ACT.Copy))

        @block.vector
        def _(dve):
            c = Chain(dve, chain)
            dve.wait_ge(logits.sem, logits.at(1))
            nc.vector.memset(rank[:], 0.0)
            for b in (0, 1):
                c.ended(nc.vector.tensor_copy(logit[:, b], core.bank(b)[:, 0:E]))
            low_ready.count(nc.vector.tensor_reduce(low[:], logit[:], AX, ALU.max, negate=True))
            for j in range(E):
                for b in (0, 1):
                    x = logit[:, b, j:j + 1]
                    ins = nc.vector.scalar_tensor_tensor(rank[:, b], logit[:, b], x, rank[:, b], ALU.is_lt, ALU.add)
                c.ended(ins)
                if j + 1 < E:
                    for b in (0, 1):
                        x, later = logit[:, b, j:j + 1], rank[:, b, j + 1:]
                        ins = nc.vector.scalar_tensor_tensor(later, logit[:, b, j + 1:], x, later, ALU.is_equal, ALU.add)
                    c.ended(ins)
            c.ended(nc.vector.tensor_scalar(rank[:], rank[:], 2.0, None, ALU.is_lt))
            dve.wait_ge(exped.sem, exped.at(1))
            c.ended(nc.vector.tensor_tensor(expo[:], expo[:], rank[:], ALU.mult))
            c.ended(nc.vector.tensor_reduce(total[:], expo[:], AX, ALU.add))
            c.ended(nc.vector.reciprocal(total[:], total[:]))
            gated.count(nc.vector.tensor_tensor(expo[:], expo[:], total[:].to_broadcast([P, 2, E]), ALU.mult))


def moe_stage(core, st, shares):
    nc, A = core.nc, st.A
    n_up, n_down = FEC // 2, DC // 2
    with ExitStack() as ctx, core.engines_block() as block:
        h = core.sb("moe_h", [P, FEC, LAT], ctx=ctx)
        silu = core.sb("silu", [P, 2, LAT], ctx=ctx)
        shared = core.sb("shared", [P, 2, LAT], ctx=ctx)

        def tiles(w, splits, outs):
            v = w.rearrange("e (k p) n -> p e k n", p=P)
            kc = v.shape[2]
            edges = [kc * i // splits for i in range(splits + 1)]
            return [((lambda at, a=a, b=b: v[:, ds(at[0], 1), a:b, ds(at[1] * 256, 256)].rearrange("p e k n -> p (e k) n")), a, b - a, outs)
                    for a, b in zip(edges, edges[1:])]
        up = Gemm(core, ctx, "up", tiles(A["moe_w_gate_2"][0], 2, (0, 1)) + tiles(A["moe_w_up_2"][0], 2, (2, 3)), {o: o for o in range(4)}, 256)
        down = Gemm(core, ctx, "down", tiles(A["moe_w_down_2"][0], 4, (0, 1)), {0: 4, 1: 5}, 256)
        h_ready, y_zero, chain = core.counter("moe_h_ready"), core.counter("moe_y_zero"), core.counter("vector_chain")
        silu_shared, passed = core.counter("moe_silu_shared"), core.counter("moe_h_passed")

        @block.sync
        def _(sp):
            with sp.Fori(0, EXPERTS) as e:
                with sp.Fori(0, n_up) as i:
                    up.fetch_round(sp, e * n_up + i, where=(e, i))
                with sp.Fori(0, n_down) as i:
                    down.fetch_round(sp, e * n_down + i, where=(e, i))

        @block.tensor
        def _(pe):
            with pe.Fori(0, EXPERTS) as e:
                with pe.Fori(0, n_up) as i:
                    up.matmul_round(pe, e * n_up + i, lambda k: st.H[:, k, LATS])
                pe.wait_ge(up.free[3].sem, up.free[3].at(e * n_up + n_up))
                pe.sem_inc(passed.sem, 1)
                with pe.Fori(0, n_down) as i:
                    down.matmul_round(pe, e * n_down + i, lambda k: h[:, k])

        @block.scalar
        def _(act):
            with act.Fori(0, EXPERTS) as e:
                with act.Fori(0, n_up) as i:
                    it = e * n_up + i
                    for o in (0, 1):
                        bank = up.wait_bank(act, o, it)
                        act.wait_ge(silu_shared.sem, silu_shared.at(it * 2 + o + 1))
                        up.bank_taken(nc.scalar.activation(silu[:, o], bank[:, 0:LAT], ACT.Silu), o)

        @block.vector
        def _(dve):
            nc.vector.memset(st.Y[:, :, LATS], 0.0).then_inc(silu_shared.sem, 2)
            with dve.Fori(0, EXPERTS) as e:
                with dve.Fori(0, n_up) as i:
                    it = e * n_up + i
                    for o in (0, 1):
                        dve.wait_ge(up.free[o].sem, up.free[o].at(it + 1))
                        nc.vector.tensor_tensor(shared[:, o], silu[:, o], chunk_of(shares, e), ALU.mult).then_inc(silu_shared.sem, 1)
                        bank = up.wait_bank(dve, 2 + o, it)
                        dve.wait_ge(silu_shared.sem, silu_shared.at(it * 2 + o + 3))
                        up.bank_taken(nc.vector.tensor_tensor(chunk_of(h, i * 2 + o), shared[:, o], bank[:, 0:LAT], ALU.mult), 2 + o)
                with dve.Fori(0, n_down) as i:
                    it = e * n_down + i
                    for o in (0, 1):
                        bank = down.wait_bank(dve, o, it)
                        y = chunk_of(st.Y, i * 2 + o, LATS)
                        down.bank_taken(nc.vector.tensor_tensor(y, y, bank[:, 0:LAT], ALU.add), o)
        silu_shared.n += 2 + 2 * EXPERTS * n_up
        passed.n += EXPERTS
        up.settle(EXPERTS * n_up)
        down.settle(EXPERTS * n_down)


def gated_stage(core, st, gate):
    nc = core.nc
    with core.engines_block() as block:
        @block.vector
        def _(dve):
            for k in range(DC):
                x = st.X[:, k, LATS]
                nc.vector.scalar_tensor_tensor(x, st.Y[:, k, LATS], st.mod[:, gate + k, 0:1], x, ALU.mult, ALU.add)


def branch_layer(core, st):
    nc, A = core.nc, st.A
    with ExitStack() as scope:
        sb = lambda name, shape: core.sb(name, shape, ctx=scope)
        pair = lambda name: sb(name, [P, KV_HEADS, LAT])
        value = lambda name: sb(name, [P, 2, KV_HEADS, 3 * HD])
        k_cmp, v_cmp, k_slc, k_win = pair("k_cmp"), pair("v_cmp"), pair("k_slc"), pair("k_win")
        v_slc, v_win = value("v_slc"), value("v_win")
        kc, vc = sb("kc", [P, KV_HEADS, CMP_STRIDE]), sb("vc", [P, 1, KV_HEADS, 3 * HD])
        q, gates, seen = sb("q", [P, HEADS // 2, LAT]), sb("gates", [P, 2, 3 * HEADS]), sb("seen", [P, 2, LAT])
        mod_stage(core, st, A["w_kv_ada_2"], ("b_kv_ada_2", 0), (2, 2), 16)
        coef_stage(core, st, [(0, 0, ("kv_gain_2", 0), 8, 1)])
        norm_in(core, st, 0, 0, (0,))
        w = KV_HEADS * HD
        small_stage(core, st, A["w_kv_2"], [("pair", 0, KV_HEADS, k_cmp), ("pair", w, KV_HEADS, v_cmp)])
        small_stage(core, st, A["w_kv_2"], [("pair", 2 * w, KV_HEADS, k_slc), ("values", 3 * w, KV_HEADS, v_slc),
                                            ("pair", 4 * w, KV_HEADS, k_win), ("values", 5 * w, KV_HEADS, v_win)])
        rope_stage(core, st, [x[:, i] for x in (k_cmp, k_slc, k_win) for i in range(KV_HEADS)])
        compress_stage(core, st, [(k_cmp, "cmp_pe_k_2", A["cmp_w1_k_2"], A["cmp_w2_k_2"], kc, False),
                                  (v_cmp, "cmp_pe_v_2", A["cmp_w1_v_2"], A["cmp_w2_v_2"], vc, True)])
        ada(core, st, 1)
        norm_in(core, st, 0, 0, (0,))
        gemm_stage(core, st, "in", A["b_w_q_2"][0], D, lambda k: st.H[:, k, LATS],
                   lambda act, c, bank: nc.scalar.activation(chunk_of(q, c), bank[:, 0:LAT], ACT.Copy))
        small_stage(core, st, A["b_w_q_2"][0], [("tokens", D, 3 * HEADS, gates, ACT.Sigmoid, 1.0)])
        rope_stage(core, st, [q[:, i] for i in range(8)])
        causal_stage(core, st, seen)
        out = st.Y[:, :, LATS]
        branch = lambda i: gates[:, :, i:3 * HEADS:3]
        cmp_neg, cmp_seen = (st.C(n).rearrange("p (b n) -> p b n", b=2) for n in ("cmp_neg", "cmp_seen"))
        attention_stage(core, st, q, kc, vc, cmp_neg, out, n_keys=CMP_STRIDE, gate=branch(0), some=cmp_seen)
        attention_stage(core, st, q, k_slc, v_slc, seen, out, gate=branch(1), add=True)
        attention_stage(core, st, q, k_win, v_win, seen, out, gate=branch(2), add=True)
        add_gated(core, st, "in", A["b_w_out_2"][0], lambda k: st.Y[:, k, LATS], 16)
    norm_in(core, st, 2, 24, (0,))
    with ExitStack() as scope:
        shares = core.sb("shares", [P, EXPERTS, LAT], ctx=scope)
        router_stage(core, st, shares)
        moe_stage(core, st, shares)
    gated_stage(core, st, 40)
    norm_stage(core, st, [(lambda k: st.X[:, k, LATS], lambda k: st.V("final_gain_2", k), None, lambda k: st.Y[:, k, LATS])])


def finish_stage(core, st, out):
    nc = core.nc
    with ExitStack() as ctx, core.engines_block() as block:
        tokens = core.sb("tokens_out", [P, 2, D], ctx=ctx)
        turned, copied, stored = core.counter("turned"), core.counter("turned_copied"), core.counter("stored")

        @block.tensor
        def _(pe):
            for g in range(4):
                t, k0 = g // 2, g % 2 * 4
                for j in range(4):
                    ins = nc.tensor.transpose(core.bank(g)[:, j * P:(j + 1) * P], st.Y[:, k0 + j, CTX + t * P:CTX + (t + 1) * P], st.C("ident"))
                turned.count(ins)

        @block.vector
        def _(dve):
            for g in range(4):
                dve.wait_ge(turned.sem, turned.at(g + 1))
                copied.count(nc.vector.tensor_copy(tokens[:, g // 2, g % 2 * 512:(g % 2 + 1) * 512], core.bank(g)))

        @block.sync
        def _(sp):
            for t in (0, 1):
                sp.wait_ge(copied.sem, copied.at(2 * t + 2))
                stored.count(sp.dma_start(out[0, t * P:(t + 1) * P, :], tokens[:, t, :]), 16)
            sp.wait_ge(stored.sem, stored.at(stored.n))


def norm_in(core, st, slot, shift, streams):
    seg = (SEGS["lat"], SEGS["ctx"])
    norm_stage(core, st, [(lambda k, v=v: st.X[:, k, seg[v]], lambda k, v=v: st.coef[:, v, slot, k:k + 1],
                           lambda k, v=v: st.mod[:, shift + k, v:v + 1], lambda k, v=v: st.H[:, k, seg[v]]) for v in streams])


def norm_out(core, st, slot, src, streams):
    seg = (SEGS["lat"], SEGS["ctx"])
    norm_stage(core, st, [(lambda k, v=v: src[:, k, seg[v]], lambda k, v=v: st.coef[:, v, slot, k:k + 1],
                           lambda k, v=v: st.X[:, k, seg[v]], lambda k, v=v: st.X[:, k, seg[v]]) for v in streams])


def modulations(core, st, layer, streams):
    mod_stage(core, st, st.A["w_mod"][layer], ("b_mod", layer * 48), (0, 2), 48)
    g = lambda i: ("norm_g", (layer * 4 + i) * DC)
    coef_stage(core, st, [job for v in streams for job in ((v, 0, g(0), 8, 1), (v, 1, g(1), 16, 0), (v, 2, g(2), 32, 1), (v, 3, g(3), 40, 0))])


def build(nc, A, out):
    with ExitStack() as ctx:
        core = Core(nc, ctx)
        st = Store(core, A)
        setup_stage(core, st)
        modulations(core, st, 0, (0, 1))
        norm_in(core, st, 0, 0, (0, 1))
        with ExitStack() as scope:
            ev = Even(core, scope)
            even_project(core, st, ev)
            mlstm_stage(core, st, ev)
            gla_stage(core, st, ev)
            even_gate_stage(core, st, ev)
        gemm_stage(core, st, "in", A["ev_w_out"][0], D, lambda k: st.Y[:, k],
                   lambda act, c, bank: nc.scalar.activation(chunk_of(st.H, c), bank, ACT.Copy))
        norm_out(core, st, 1, st.H, (0, 1))
        norm_in(core, st, 2, 24, (0, 1))
        ffn_stage(core, st, 0, TT, 0)
        norm_out(core, st, 3, st.Y, (0, 1))
        rwkv_layer(core, st)
        sparse_layer(core, st)
        branch_layer(core, st)
        finish_stage(core, st, out)


def kernel(**inputs):
    import concourse.bacc as bacc
    from concourse.bass_utils import run_bass_kernel_spmd

    nc = bacc.Bacc("TRN2", target_bir_lowering=False, num_devices=1)
    arrays = {n: np.ascontiguousarray(a) for n, a in inputs.items()}
    arrays["const"] = CONST
    A = {n: nc.dram_tensor(f"in_{n}", a.shape, mybir.dt.from_np(a.dtype), kind="ExternalInput").ap() for n, a in arrays.items()}
    out = nc.dram_tensor("out", (1, LAT, D), F32, kind="ExternalOutput").ap()
    build(nc, A, out)
    r = run_bass_kernel_spmd(nc, [{f"in_{n}": a for n, a in arrays.items()}], core_ids=[0])
    return r.results[0]["out"]
```

```python
from contextlib import ExitStack, contextmanager

import numpy as np

import concourse.bass as bass
from concourse import mybir

F32 = mybir.dt.float32
I32 = mybir.dt.int32
U32 = mybir.dt.uint32
ALU = mybir.AluOpType
ACT = mybir.ActivationFunctionType
AX = mybir.AxisListType.X
ds = bass.ds

P = 128
D = 1024
DC = D // P
CTX = 256
LAT = 256
TT = CTX + LAT
GRID_W = 64
GRID_H = LAT // GRID_W
SEGS = {"ctx": slice(0, CTX), "lat": slice(CTX, TT)}
EPS = 1e-6

ML_HEADS = 4
ML_DK = 128
GLA_HEADS = 4
GLA_DK = 64
GLA_LR = 16
GLA_TAU = 16.0
RW_HEADS = 16
RW_HEAD = 64
RW_CHUNK = 64
RW_LN_EPS = 64e-5
RW_DECAY = -float(np.exp(-0.5))
FF = 2816
FC = FF // P

HEADS = 16
HD = 64
KV_HEADS = 4
IDX_HEADS = 8
DSA_KEEP = min(256, LAT // 4)
CMP_LEN = 32
CMP_STRIDE = 16
CMP_HIDDEN = 256
N_CMP = (LAT - CMP_LEN) // CMP_STRIDE + 1
SLC_LEN = 64
assert min(16, LAT // SLC_LEN) * SLC_LEN == LAT
assert LAT <= 512
EXPERTS = 8
SEATS = 128
FE = 3584
FEC = FE // P
NEG = -1e30
GONE = -3e38


LEVELS = 8


def level_mask(level, backward):
    s, t = np.arange(P)[:, None], np.arange(P)[None, :]
    if level == 0:
        return (s == t).astype(np.float32)
    h = 1 << (level - 1)
    late, early = (s, t) if backward else (t, s)
    return ((s // (2 * h) == t // (2 * h)) & (late // h % 2 == 1) & (early // h % 2 == 0)).astype(np.float32)


def constant_table():
    s, t = np.arange(P)[:, None], np.arange(P)[None, :]
    block = (s // RW_CHUNK == t // RW_CHUNK)
    parts = {"ident": np.eye(P), "ones": np.ones((P, P)), "head_ones": block}
    rot = np.zeros((P, P))
    for m in range(P):
        if m % HD < HD // 2:
            rot[m + HD // 2, m] = -1.0
        else:
            rot[m - HD // 2, m] = 1.0
    parts["rot"] = rot
    parts["neg_after"] = np.where(t <= s, 0.0, NEG)
    parts["neg_before"] = np.where(t >= s, 0.0, NEG)
    u, c = np.arange(P)[:, None] % RW_CHUNK, np.arange(RW_CHUNK)[None, :]
    for back in (0, 1):
        first, then = (c, u) if back else (u, c)
        parts[f"before_{back}"] = first < then
        parts[f"upto_{back}"] = first <= then
        for level in range(1, 7):
            m = level_mask(level, back)[:RW_CHUNK, :RW_CHUNK]
            parts[f"pair{level}_{back}"] = np.concatenate([m, m])
    parts["pair_ident"] = u == c
    parts["earlier"] = s < t
    parts["column"] = np.broadcast_to(t, (P, P))
    for back in (0, 1):
        for level in range(LEVELS):
            parts[f"level{level}_{back}"] = level_mask(level, back)
    token = np.arange(LAT).reshape(2, P).T
    end = np.arange(CMP_STRIDE) * CMP_STRIDE + CMP_LEN - 1
    seen = (end[None, None, :] <= token[:, :, None]) & (np.arange(CMP_STRIDE) < N_CMP)[None, None, :]
    parts["cmp_seen"] = seen.reshape(P, -1)
    parts["cmp_neg"] = np.where(seen, 0.0, NEG).reshape(P, -1)
    start = (np.arange(TT) % RW_CHUNK != 0)
    parts["keep_fwd"] = np.broadcast_to(start, (P, TT))
    stop = (np.arange(TT) % RW_CHUNK != RW_CHUNK - 1)
    parts["keep_bwd"] = np.broadcast_to(stop, (P, TT))
    inv = np.float32(1.0) / np.power(np.float32(10000.0), np.arange(0, HD, 2, dtype=np.float32) / np.float32(HD)).astype(np.float32)
    parts["inv_freq"] = np.concatenate([inv] * (P // len(inv)))[:, None]
    at, columns = {}, 0
    for name, a in parts.items():
        at[name] = (columns, columns + a.shape[1])
        columns += a.shape[1]
    return np.ascontiguousarray(np.concatenate([np.asarray(a, np.float32) for a in parts.values()], axis=1)), at


CONST, CONST_AT = constant_table()


def vector_rows(shapes):
    names = ("c", "c_ctx", "c_2", "b_mod", "norm_g", "ffn_conv_w", "ffn_conv_b", "ev_conv_w", "ev_conv_b", "ev_gla_b",
             "ev_head_g", "rw_mu", "rw_w0", "rw_a0", "rw_kvec", "rw_lnx", "b_ada_2", "attn_gain_2", "ffn_gain_2",
             "kv_gain_2", "b_kv_ada_2", "final_gain_2", "cmp_pe_k_2", "cmp_pe_v_2")
    at, row = {}, 0
    for n in names:
        k = int(np.prod(shapes[n])) // P
        at[n] = (row, k)
        row += k
    return at, row


class Counter:

    def __init__(self, nc, ctx, name):
        self.sem = ctx.enter_context(nc.semaphore(name))
        self.base = 0
        self.n = 0

    def at(self, n):
        return self.base + n

    def count(self, ins, by=1):
        ins.then_inc(self.sem, by)
        self.n += by
        return ins

    def settle(self):
        self.base += self.n
        self.n = 0


class Core:

    def __init__(self, nc, ctx):
        self.nc = nc
        self.ctx = ctx
        self.counters = {}
        self.spare = []
        self.psum = [ctx.enter_context(nc.psum_tensor(f"bank_pair{i}", [P, 1024], F32)) for i in range(4)]
        self.stage_no = 0

    def bank(self, i):
        return self.psum[i // 2][:, (i % 2) * 512:(i % 2 + 1) * 512]

    def counter(self, name, keep=False):
        if name not in self.counters:
            s = self.spare.pop() if self.spare and not keep else Counter(self.nc, self.ctx, name if keep else f"{name}_{self.stage_no}")
            s.keep = keep
            self.counters[name] = s
        return self.counters[name]

    def sb(self, name, shape, dtype=F32, ctx=None):
        return (ctx or self.ctx).enter_context(self.nc.sbuf_tensor(f"{name}_{self.stage_no}" if ctx else name, shape, dtype))

    @contextmanager
    def engines_block(self):
        with self.nc.Block() as block:
            yield block
        for name, s in list(self.counters.items()):
            s.settle()
            if not s.keep:
                self.spare.append(self.counters.pop(name))
        self.stage_no += 1


    @contextmanager
    def rarely(self, count, more_than):
        outer, spare, self.counters, self.spare = self.counters, self.spare, {}, []
        n = self.nc.values_load(count, min_val=0, max_val=TT)
        nc = self.nc
        with nc.If(n > more_than):
            entered = self.counter("entered")
            for eng in (nc.sync, nc.gpsimd, nc.tensor, nc.vector, nc.scalar):
                eng.sem_inc(entered.sem, 1)
            entered.n += 5
            yield
        self.counters, self.spare = outer, spare


class Chain:

    def __init__(self, eng, signal, it=None, per=0):
        self.eng, self.counter, self.it, self.per, self.k = eng, signal, it, per, signal.n if it is None else 0
        self.start = signal.n

    def ended(self, ins):
        ins.then_inc(self.counter.sem, 1)
        self.k += 1
        if self.it is None:
            self.counter.n += 1
            self.eng.wait_ge(self.counter.sem, self.counter.at(self.k))
        else:
            self.eng.wait_ge(self.counter.sem, self.counter.at(self.start + self.it * self.per + self.k))

    def settle(self, rounds):
        assert self.k == self.per, (self.k, self.per)
        self.counter.n += rounds * self.per


class Gemm:

    def __init__(self, core, ctx, key, tiles, banks, width):
        self.core, self.sources = core, tiles
        nc = core.nc
        kc = max(t[2] for t in tiles)
        self.ring = core.sb(f"ring_{key}", [P, len(tiles), kc, width], ctx=ctx)
        self.banks = {o: core.bank(b) for o, b in banks.items()}
        self.landed = [core.counter(f"{key}_tile{s}_landed", True) for s in range(len(tiles))]
        self.used = [core.counter(f"{key}_tile{s}_used", True) for s in range(len(tiles))]
        self.free = {o: core.counter(f"{key}_bank{o}_free", True) for o in banks}
        self.first = {o: min(s for s, t in enumerate(tiles) if o in t[3]) for o in banks}
        self.last = {o: max(s for s, t in enumerate(tiles) if o in t[3]) for o in banks}

    def fetch_round(self, sp, it, first=False, where=None):
        for s, (src, _, kc, outs) in enumerate(self.sources):
            if not first:
                sp.wait_ge(self.used[s].sem, self.used[s].at(it))
            ap = src(it if where is None else where)
            sp.dma_start(self.ring[:, s, 0:kc, 0:ap.shape[2]], ap).then_inc(self.landed[s].sem, 16)

    def matmul_round(self, pe, it, rhs, first=False):
        for s, (_, k0, kc, outs) in enumerate(self.sources):
            pe.wait_ge(self.landed[s].sem, self.landed[s].at(16 * it + 16))
            for j, o in enumerate(outs):
                if s == self.first[o] and not first:
                    pe.wait_ge(self.free[o].sem, self.free[o].at(it))
                for k in range(kc):
                    x = rhs(k0 + k)
                    ins = self.core.nc.tensor.matmul(self.banks[o][:, 0:x.shape[1]], self.ring[:, s, k, j * P:(j + 1) * P], x,
                                                     start=(s == self.first[o] and k == 0),
                                                     stop=(s == self.last[o] and k == kc - 1))
            ins.then_inc(self.used[s].sem, 1)

    def wait_bank(self, eng, o, it):
        s = self.last[o]
        eng.wait_ge(self.used[s].sem, self.used[s].at(it + 1))
        return self.banks[o]

    def bank_taken(self, ins, o):
        ins.then_inc(self.free[o].sem, 1)

    def settle(self, rounds):
        for s in self.landed:
            s.n += 16 * rounds
        for s in (*self.used, *self.free.values()):
            s.n += rounds


def rounds(eng, n, body):
    body(0, True)
    if n > 1:
        with eng.Fori(1, n) as it:
            body(it, False)


def k_tiles(w, width, splits, outs, col=lambda it: None):
    v = w.rearrange("(k p) n -> p k n", p=P)
    kc = v.shape[1]
    edges = [kc * i // splits for i in range(splits + 1)]
    return [((lambda it, a=a, b=b: v[:, a:b, ds(col(it), width)]), a, b - a, outs) for a, b in zip(edges, edges[1:])]


class Store:

    def __init__(self, core, A):
        sb = core.sb
        self.A = A
        self.rows_at, self.n_rows = vector_rows({n: a.shape for n, a in A.items()})
        self.const = sb("const", [P, CONST.shape[1]])
        self.vec = sb("vec", [P, -(-self.n_rows // P) * P])
        self.X = sb("X", [P, DC, TT])
        self.H = sb("H", [P, DC, TT])
        self.Y = sb("Y", [P, DC, TT])
        self.act = sb("act", [P, DC, 4])
        self.mod = sb("mod", [P, 48, 2])
        self.coef = sb("coef", [P, 2, 4, DC])
        self.cos = sb("cos", [P, LAT])
        self.sin = sb("sin", [P, LAT])

    def C(self, name):
        a, b = CONST_AT[name]
        return self.const[:, a:b]

    def V(self, name, i=0, n=1):
        r, k = self.rows_at[name]
        assert i + n <= k
        return self.vec[:, r + i:r + i + n]


def setup_stage(core, st):
    nc, A = core.nc, st.A
    n_tiles = -(-st.n_rows // P)
    with ExitStack() as ctx, core.engines_block() as block:
        rows = core.sb("rows", [P, n_tiles, P], ctx=ctx)
        tokens = core.sb("tokens", [P, 4, D], ctx=ctx)
        pos_i = core.sb("pos_i", [P, LAT], I32, ctx=ctx)
        ang = core.sb("ang", [P, LAT], ctx=ctx)
        turn = core.sb("turn", [P, 2, LAT], ctx=ctx)
        rest = core.sb("rest", [P, 2, LAT], ctx=ctx)
        sig = core.sb("sig", [P, DC, 4], ctx=ctx)
        const_in, rows_in, tokens_in, pos_in = (core.counter(n) for n in ("const_in", "rows_in", "tokens_in", "pos_in"))
        turned, copied = core.counter("turned"), core.counter("turned_copied")
        vec_chain, angle_ready, sig_ready = core.counter("vector_chain"), core.counter("angle_ready"), core.counter("sig_ready")
        groups = [("rows", t, min(4, n_tiles - t)) for t in range(0, n_tiles, 4)]
        groups += [("tokens", b, k) for b in range(4) for k in (0, 4)]

        @block.sync
        def _(sp):
            const_in.count(sp.dma_start(st.const[:], A["const"]), 16)
            for name, (r, k) in st.rows_at.items():
                axes = " ".join("abcdef"[:len(A[name].shape)])
                src = A[name].rearrange(f"{axes} -> ({axes})").rearrange("(r p) -> r p", p=P)
                done = 0
                while done < k:
                    at = r + done
                    n = min(k - done, P - at % P)
                    rows_in.count(sp.dma_start(rows[at % P:at % P + n, at // P, :], src[done:done + n, :]), 16)
                    done += n

        @block.scalar
        def _(act):
            for b, (name, t) in enumerate((("ctx", 0), ("ctx", 1), ("x", 0), ("x", 1))):
                tokens_in.count(act.dma_start(tokens[:, b, :], A[name][0, t * P:(t + 1) * P, :]), 16)
            pos_in.count(act.dma_start(pos_i[:], A["positions_2"].rearrange("a t -> (a t)").partition_broadcast(P)), 16)
            act.wait_ge(copied.sem, copied.at(1))
            for i, name in enumerate(("c", "c_ctx", "c_2", "c_2")):
                ins = nc.scalar.activation(sig[:, :, i], st.V(name, 0, DC), ACT.Sigmoid)
            sig_ready.count(ins)
            for i, table in enumerate((st.sin, st.cos)):
                act.wait_ge(angle_ready.sem, angle_ready.at(i + 1))
                nc.scalar.activation(table[:], rest[:, i, :], ACT.Sin)

        @block.tensor
        def _(pe):
            pe.wait_ge(const_in.sem, const_in.at(16))
            pe.wait_ge(rows_in.sem, rows_in.at(rows_in.n))
            for g, (kind, a, b) in enumerate(groups):
                if g >= 4:
                    pe.wait_ge(copied.sem, copied.at(g - 3))
                bank = core.bank(g % 4)
                if kind == "rows":
                    for j in range(b):
                        n = min(P, st.n_rows - (a + j) * P)
                        ins = nc.tensor.transpose(bank[:, j * P:j * P + n], rows[0:n, a + j, :], st.C("ident")[0:n, 0:n])
                else:
                    pe.wait_ge(tokens_in.sem, tokens_in.at(64))
                    for j in range(4):
                        ins = nc.tensor.transpose(bank[:, j * P:(j + 1) * P], tokens[:, a, (b + j) * P:(b + j + 1) * P], st.C("ident"))
                turned.count(ins)

        @block.vector
        def _(dve):
            for g, (kind, a, b) in enumerate(groups):
                dve.wait_ge(turned.sem, turned.at(g + 1))
                bank = core.bank(g % 4)
                if kind == "rows":
                    n = min(b * P, st.n_rows - a * P)
                    ins = nc.vector.tensor_copy(st.vec[:, a * P:a * P + n], bank[:, 0:n])
                else:
                    ins = nc.vector.tensor_copy(st.X[:, b:b + 4, a * P:(a + 1) * P], bank.rearrange("p (k t) -> p k t", k=4))
                copied.count(ins)
            c = Chain(dve, vec_chain)
            dve.wait_ge(sig_ready.sem, sig_ready.at(1))
            for i, name in enumerate(("c", "c_ctx", "c_2", "c_2")):
                nc.vector.tensor_tensor(st.act[:, :, i], sig[:, :, i], st.V(name, 0, DC), ALU.mult)
            dve.wait_ge(pos_in.sem, pos_in.at(16))
            c.ended(nc.vector.tensor_copy(ang[:], pos_i[:]))
            c.ended(nc.vector.tensor_scalar(ang[:], ang[:], st.C("inv_freq"), None, ALU.mult))
            for i, quarter in enumerate((0.0, 0.25)):
                n, r = turn[:, i, :], rest[:, i, :]
                c.ended(nc.vector.tensor_scalar(n, ang[:], float(1 / (2 * np.pi)), quarter, ALU.mult, ALU.add))
                c.ended(nc.vector.tensor_scalar(n, n, 12582912.0, None, ALU.add))
                c.ended(nc.vector.tensor_scalar(n, n, -12582912.0, None, ALU.add))
                c.ended(nc.vector.scalar_tensor_tensor(r, n, -6.28125, ang[:], ALU.mult, ALU.add))
                c.ended(nc.vector.scalar_tensor_tensor(r, n, -0.00193500518798828125, r, ALU.mult, ALU.add))
                c.ended(nc.vector.scalar_tensor_tensor(r, n, -3.0199159819e-07, r, ALU.mult, ALU.add))
                c.ended(nc.vector.tensor_scalar(r, r, quarter * float(2 * np.pi), 3.1415925, ALU.add, ALU.min))
                angle_ready.count(nc.vector.tensor_scalar(r, r, -3.1415925, None, ALU.max))


class ModSums:
    WIDE = 512
    TILES = 4
    PART = DC // TILES

    def __init__(self, core, st, scope, key, w, bias, vecs, n_chunks, place=None):
        self.core, self.st, self.key = core, st, key
        self.w = w.rearrange("(k p) n -> p k n", p=P)
        self.bias = st.rows_at[bias[0]][0] + bias[1]
        self.n_chunks, self.groups = n_chunks, n_chunks * P // self.WIDE
        self.vecs = vecs
        self.sums = place.sums if place else core.sb(f"mod_sums_{key}", [P, len(vecs), n_chunks * P], ctx=scope)

    def open(self, ctx):
        core = self.core
        self.ring = core.sb(f"mod_ring_{self.key}", [P, self.TILES, self.PART, self.WIDE], ctx=ctx)
        self.landed = [core.counter(f"mod_{self.key}_tile{s}_landed", True) for s in range(self.TILES)]
        self.added = core.counter(f"mod_{self.key}_added")

    def done(self, g, k):
        return self.added.at(1 + g * (DC * len(self.vecs)) + (k + 1) * len(self.vecs))

    def loads(self, eng):
        def group(g, first):
            for s in range(self.TILES):
                k = s * self.PART
                if not first:
                    eng.wait_ge(self.added.sem, self.done(g - 1, k + self.PART - 1))
                eng.dma_start(self.ring[:, s], self.w[:, k:k + self.PART, ds(g * self.WIDE, self.WIDE)]).then_inc(self.landed[s].sem, 16)
        rounds(eng, self.groups, group)

    def empty(self):
        self.core.nc.vector.memset(self.sums[:], 0.0).then_inc(self.added.sem, 1)

    def add_group(self, dve, g):
        for k in range(DC):
            s = k // self.PART
            if k % self.PART == 0:
                dve.wait_ge(self.landed[s].sem, self.landed[s].at(16 * g + 16))
            dve.wait_ge(self.added.sem, self.done(g, k - 1))
            for v, c in enumerate(self.vecs):
                at = self.sums[:, v, ds(g * self.WIDE, self.WIDE)]
                self.core.nc.vector.scalar_tensor_tensor(at, self.ring[:, s, k % self.PART], self.st.act[:, k, c:c + 1], at,
                                                         ALU.mult, ALU.add).then_inc(self.added.sem, 1)

    def adds(self, dve):
        self.empty()
        with dve.Fori(0, self.groups) as g:
            self.add_group(dve, g)
        self.settle()

    def settle(self):
        self.added.n += 1 + self.groups * DC * len(self.vecs)
        for c in self.landed:
            c.n += 16 * self.groups


def mod_stage(core, st, m, jobs, first=False):
    nc = core.nc
    nv = len(m.vecs)
    n_group = m.n_chunks // m.groups
    with ExitStack() as ctx, core.engines_block() as block:
        whole, chain = core.counter("mod_whole"), core.counter("vector_chain")
        bank = core.bank(0)[:, 0:nv * m.n_chunks].rearrange("p (v n) -> p v n", v=nv)
        if first:
            m.open(ctx)

            @block.sync
            def _(sp):
                m.loads(sp)

        @block.tensor
        def _(pe):
            for n in range(m.n_chunks):
                if first and n % n_group == 0:
                    pe.wait_ge(m.added.sem, m.done(n // n_group, DC - 1))
                for v in range(nv):
                    ins = nc.tensor.matmul(bank[:, v, n:n + 1], m.sums[:, v, n * P:(n + 1) * P], st.C("ones")[:, 0:1], start=True, stop=True)
            whole.count(ins)

        @block.vector
        def _(dve):
            if first:
                m.adds(dve)
            c = Chain(dve, chain)
            dve.wait_ge(whole.sem, whole.at(1))
            for v in range(nv):
                ins = nc.vector.tensor_tensor(st.mod[:, 0:m.n_chunks, v], bank[:, v], st.vec[:, m.bias:m.bias + m.n_chunks], ALU.add)
            c.ended(ins)
            for v, slot, gain, n, one in jobs:
                out = st.coef[:, v, slot, :]
                c.ended(nc.vector.tensor_scalar(out, st.mod[:, n:n + DC, v], float(one), None, ALU.add))
                nc.vector.tensor_tensor(out, out, st.V(gain[0], gain[1], DC), ALU.mult)


def norm_stage(core, st, jobs, T=LAT):
    nc = core.nc
    with ExitStack() as ctx, core.engines_block() as block:
        square = core.sb("square", [P, len(jobs), DC, T], ctx=ctx)
        var = core.sb("var", [P, len(jobs), T], ctx=ctx)
        rstd = core.sb("rstd", [P, len(jobs), T], ctx=ctx)
        unit = core.sb("unit", [P, 2, T], ctx=ctx)
        squared, summed, var_ready, std_ready = (core.counter(n) for n in ("squared", "summed", "var_ready", "std_ready"))
        chain = core.counter("vector_chain")

        @block.scalar
        def _(act):
            for j, (x, *_) in enumerate(jobs):
                for k in range(DC):
                    ins = nc.scalar.activation(square[:, j, k], x(k), ACT.Square)
                squared.count(ins)
            for j in range(len(jobs)):
                act.wait_ge(var_ready.sem, var_ready.at(j + 1))
                std_ready.count(nc.scalar.activation(rstd[:, j], var[:, j], ACT.Sqrt))

        @block.tensor
        def _(pe):
            for j in range(len(jobs)):
                pe.wait_ge(squared.sem, squared.at(j + 1))
                for k in range(DC):
                    ins = nc.tensor.matmul(core.bank(j)[:, 0:T], st.C("ones"), square[:, j, k], start=k == 0, stop=k == DC - 1)
                summed.count(ins)

        @block.vector
        def _(dve):
            c = Chain(dve, chain)
            for j in range(len(jobs)):
                dve.wait_ge(summed.sem, summed.at(j + 1))
                var_ready.count(nc.vector.tensor_scalar(var[:, j], core.bank(j)[:, 0:T], 1.0 / D, EPS, ALU.mult, ALU.add))
            for j, (x, mul, add, dst) in enumerate(jobs):
                dve.wait_ge(std_ready.sem, std_ready.at(j + 1))
                c.ended(nc.vector.reciprocal(rstd[:, j], rstd[:, j]))
                for k in range(DC):
                    u = unit[:, k % 2]
                    c.ended(nc.vector.tensor_tensor(u, x(k), rstd[:, j], ALU.mult))
                    a = add(k) if add else None
                    if a is None:
                        nc.vector.tensor_scalar(dst(k), u, mul(k), None, ALU.mult)
                    elif a.shape[1] == 1:
                        nc.vector.tensor_scalar(dst(k), u, mul(k), a, ALU.mult, ALU.add)
                    else:
                        nc.vector.scalar_tensor_tensor(dst(k), u, mul(k), a, ALU.mult, ALU.add)


def in_background(block, ctx, m):
    if m:
        m.open(ctx)

        @block.gpsimd
        def _(pool):
            m.loads(pool)

        @block.vector
        def _(dve):
            m.adds(dve)


def gemm_stage(core, st, key, w, n_cols, rhs, store, width=512, splits=4, sections=None, mix=None, engine="scalar", background=None):
    nc = core.nc
    n_it = len(sections) if sections else n_cols // width
    outs = tuple(range(width // P))
    col = (lambda it: sections[it]) if sections else (lambda it: it * width)
    with ExitStack() as ctx, core.engines_block() as block:
        g = Gemm(core, ctx, key, k_tiles(w, width, splits, outs, col), {o: o for o in outs}, width)

        def each(eng, body):
            if sections:
                for it in range(n_it):
                    body(it, it == 0)
            else:
                rounds(eng, n_it, body)

        @block.sync
        def _(sp):
            each(sp, lambda it, first: g.fetch_round(sp, it, first))

        in_background(block, ctx, background)
        mixed = core.counter("mixed")
        if mix:
            @block.vector
            def _(dve):
                mixed.count(mix())

        @block.tensor
        def _(pe):
            if mix:
                pe.wait_ge(mixed.sem, mixed.at(1))
            each(pe, lambda it, first: g.matmul_round(pe, it, rhs, first))

        def take(eng):
            def body(it, first):
                for o in outs:
                    bank = g.wait_bank(eng, o, it)
                    g.bank_taken(store(eng, it * len(outs) + o, bank), o)
            each(eng, body)

        if engine == "scalar":
            @block.scalar
            def _(act):
                take(act)
        else:
            @block.vector
            def _(dve):
                take(dve)
        g.settle(n_it)


def chunk_of(tensor, n, tokens=slice(None)):
    return tensor[:, ds(n, 1), tokens].rearrange("p a t -> p (a t)")



IN_MQK, IN_MV, IN_MO, IN_MG, IN_GQK, IN_GV, IN_GG, IN_LR = 0, 1024, 1536, 2048, 2064, 2576, 3088, 3600


class Even:
    def __init__(self, core, ctx):
        sb = lambda name, shape: core.sb(name, shape, ctx=ctx)
        self.q = sb("ml_q", [P, 4, TT])
        self.k = sb("ml_k", [P, 4, TT])
        self.o = sb("ml_o", [P, 4, TT])
        self.gqk = sb("gla_qk", [P, 4, TT])
        self.gg = sb("gla_g", [P, 4, TT])
        self.v = sb("values", [P, 2, 4, 512])
        self.gap = sb("gap", [P, 4, 2, 4])
        self.rowmax = [sb(f"rowmax{d}", [4, TT]) for d in (0, 1)]
        self.floor = [sb(f"floor{d}", [4, TT]) for d in (0, 1)]
        self.decay = sb("decay", [P, 2, 2, TT])


def even_project(core, st, ev):
    nc, w = core.nc, st.A["ev_w_in"][0]

    def store(act, c, bank):
        i, j = c // 4, c % 4
        dst = (ev.q, ev.k, ev.o, ev.gqk, ev.gg)[i][:, j]
        if i == 2:
            return nc.scalar.activation(dst, bank, ACT.Sigmoid)
        return nc.scalar.activation(dst, bank, ACT.Copy, scale=GLA_DK ** -0.5 if i == 3 and j < 2 else 1.0)
    gemm_stage(core, st, "in", w, None, lambda k: st.H[:, k], store, sections=[IN_MQK, IN_MQK + 512, IN_MO, IN_GQK, IN_GG])

    with ExitStack() as ctx, core.engines_block() as block:
        wv = (st.Y, core.sb("wv", [P, DC, 512], ctx=ctx))
        wg = core.sb("wg", [P, DC, 4 * ML_HEADS], ctx=ctx)
        wl = core.sb("wl", [P, DC, 2 * GLA_LR], ctx=ctx)
        w2 = core.sb("gla_w2", [GLA_LR, 2, 256], ctx=ctx)
        bg = core.sb("b_gates", [4, 4], ctx=ctx)
        low = core.sb("low", [GLA_LR, 2, TT], ctx=ctx)
        gate = [core.sb(f"gate{i}", [4, TT], ctx=ctx) for i in range(4)]
        soft = [core.sb(f"soft{i}", [4, TT], ctx=ctx) for i in range(2)]
        raw = ev.decay
        soft2 = core.sb("soft2", [P, 2, 2, TT], ctx=ctx)
        gap = [core.sb(f"gap_rows{d}", [4, TT], ctx=ctx) for d in (0, 1)]
        one = core.sb("one_row", [P, TT], ctx=ctx)
        nul = core.sb("nul_row", [4, TT], ctx=ctx)
        conv = core.sb("conv", [P, 2, TT], ctx=ctx)
        load = [core.counter(f"even_weights{i}") for i in range(3)]
        low_ready, low_copied = core.counter("low_ready"), core.counter("low_copied")
        gates_ready, values_ready, values_copied = core.counter("gates_ready"), core.counter("values_ready"), core.counter("values_copied")
        la_ready, raw_ready, soft_ready = core.counter("la_ready"), core.counter("raw_ready"), core.counter("soft_ready")
        gap_ready, gap_turned, floor_ready = core.counter("gap_ready"), core.counter("gap_turned"), core.counter("floor_ready")
        act_chain, vec_chain, conv_ready = core.counter("scalar_chain"), core.counter("vector_chain"), core.counter("conv_ready")

        @block.sync
        def _(sp):
            v = w.rearrange("(k p) n -> p k n", p=P)
            load[0].count(sp.dma_start(wg[:], v[:, :, IN_MG:IN_MG + 16]), 16)
            load[0].count(sp.dma_start(wl[:], v[:, :, IN_LR:IN_LR + 32]), 16)
            load[0].count(sp.dma_start(w2[:], st.A["ev_gla_w2"][0].rearrange("z r c -> r z c")), 16)
            load[0].count(sp.dma_start(bg[:], st.A["ev_b_gates"][0].rearrange("(g h) -> h g", h=4), allow_slow_non_contiguous=True), 16)
            for i, col in enumerate((IN_MV, IN_GV)):
                load[1 + i].count(sp.dma_start(wv[i][:], v[:, :, col:col + 512]), 16)

        @block.tensor
        def _(pe):
            pe.wait_ge(load[0].sem, load[0].at(64))
            for z in (0, 1):
                for k in range(DC):
                    ins = nc.tensor.matmul(core.bank(4 + z)[0:GLA_LR, :], wl[:, k, z * GLA_LR:(z + 1) * GLA_LR], st.H[:, k],
                                           start=k == 0, stop=k == DC - 1)
                low_ready.count(ins)
            for i in range(4):
                for k in range(DC):
                    ins = nc.tensor.matmul(core.bank(i)[0:4, :], wg[:, k, i * 4:(i + 1) * 4], st.H[:, k], start=k == 0, stop=k == DC - 1)
                gates_ready.count(ins)
            for z in (0, 1):
                pe.wait_ge(low_copied.sem, low_copied.at(2))
                for c in (0, 1):
                    b = 4 + z * 2 + c
                    la_ready.count(nc.tensor.matmul(core.bank(b), w2[:, z, c * P:(c + 1) * P], low[:, z], start=True, stop=True))
            for i in (0, 1):
                pe.wait_ge(load[1 + i].sem, load[1 + i].at(16))
                for t in range(4):
                    n = i * 4 + t
                    if n < 4:
                        pe.wait_ge(raw_ready.sem, raw_ready.at(4))
                    else:
                        pe.wait_ge(values_copied.sem, values_copied.at(n - 3))
                    for k in range(DC):
                        ins = nc.tensor.matmul(core.bank(n % 4), st.H[:, k, t * P:(t + 1) * P], wv[i][:, k], start=k == 0, stop=k == DC - 1)
                    values_ready.count(ins)
            for d in (0, 1):
                pe.wait_ge(gap_ready.sem, gap_ready.at(d + 1))
                if d == 0:
                    pe.wait_ge(raw_ready.sem, raw_ready.at(8))
                for b in range(4):
                    ins = nc.tensor.transpose(core.bank(4)[:, (b * 2 + d) * 4:(b * 2 + d) * 4 + 4], gap[d][:, b * P:(b + 1) * P],
                                              st.C("ident")[0:4, 0:4])
                gap_turned.count(ins)

        @block.scalar
        def _(act):
            c = Chain(act, act_chain)
            act.wait_ge(low_ready.sem, low_ready.at(2))
            for z in (0, 1):
                ins = nc.scalar.activation(low[:, z], core.bank(4 + z)[0:GLA_LR, :], ACT.Copy)
                low_copied.count(ins)
            act.wait_ge(raw_ready.sem, raw_ready.at(4))
            for d in (0, 1):
                s = soft[d][:]
                c.ended(nc.scalar.activation(s, gate[2 * d + 1][:], ACT.Abs))
                c.ended(nc.scalar.activation(s, s, ACT.Exp, scale=-1.0))
                soft_ready.count(nc.scalar.activation(s, s, ACT.Ln, bias=1.0))
            act.wait_ge(raw_ready.sem, raw_ready.at(8))
            c.ended(nc.scalar.activation(soft2[:], raw[:], ACT.Abs))
            c.ended(nc.scalar.activation(soft2[:], soft2[:], ACT.Exp, scale=-1.0))
            soft_ready.count(nc.scalar.activation(soft2[:], soft2[:], ACT.Ln, bias=1.0))
            for i in (0, 1):
                for t in range(4):
                    act.wait_ge(values_ready.sem, values_ready.at(i * 4 + t + 1))
                    values_copied.count(nc.scalar.activation(ev.v[:, i, t], core.bank(t), ACT.Copy))
            for d in (0, 1):
                act.wait_ge(floor_ready.sem, floor_ready.at(d + 1))
                nc.scalar.activation(ev.floor[d][:], ev.floor[d][:], ACT.Exp, scale=-1.0)
            for n in range(8):
                x = (ev.q, ev.k)[n // 4][:, n % 4]
                act.wait_ge(conv_ready.sem, conv_ready.at(n + 1))
                c.ended(nc.scalar.activation(x, conv[:, n % 2], ACT.Silu))

        @block.vector
        def _(dve):
            c = Chain(dve, vec_chain)
            c.ended(nc.vector.memset(one[:], 1.0))
            c.ended(nc.vector.memset(nul[:], 0.0))
            dve.wait_ge(load[0].sem, load[0].at(64))
            for i in range(4):
                dve.wait_ge(gates_ready.sem, gates_ready.at(i + 1))
                raw_ready.count(nc.vector.tensor_scalar(gate[i][:], core.bank(i)[0:4, :], bg[:, i:i + 1], None, ALU.add))
            for z in (0, 1):
                for k in (0, 1):
                    dve.wait_ge(la_ready.sem, la_ready.at(z * 2 + k + 1))
                    raw_ready.count(nc.vector.tensor_scalar(raw[:, z, k], core.bank(4 + z * 2 + k), st.V("ev_gla_b", z * 2 + k), None, ALU.add))
            for d in (0, 1):
                i_gate, f_gate = gate[2 * d][:], gate[2 * d + 1][:]
                dve.wait_ge(soft_ready.sem, soft_ready.at(d + 1))
                c.ended(nc.vector.scalar_tensor_tensor(f_gate, f_gate, 0.0, soft[d][:], ALU.min, ALU.subtract))
                total = soft[d]
                for part in scan_parts(d):
                    c.ended(nc.vector.tensor_tensor_scan(total[:, part[0]], one[0:4, part[0]], f_gate[:, part[0]],
                                                        total[:, part[1]:part[1] + 1] if part[1] is not None else 0.0, ALU.mult, ALU.add))
                gap_ready.count(nc.vector.tensor_tensor(gap[d][:], i_gate, total[:], ALU.subtract))
                dve.wait_ge(gap_ready.sem, gap_ready.at(d + 1))
                for part in scan_parts(d):
                    c.ended(nc.vector.tensor_tensor_scan(ev.rowmax[d][:, part[0]], nul[:, part[0]], gap[d][:, part[0]],
                                                        ev.rowmax[d][:, part[1]:part[1] + 1] if part[1] is not None else 0.0, ALU.max, ALU.max))
                floor_ready.count(nc.vector.tensor_tensor(ev.floor[d][:], total[:], ev.rowmax[d][:], ALU.add))
            dve.wait_ge(soft_ready.sem, soft_ready.at(3))
            for z in (0, 1):
                c.ended(nc.vector.scalar_tensor_tensor(raw[:, z], raw[:, z], 0.0, soft2[:, z], ALU.min, ALU.subtract))
                c.ended(nc.vector.tensor_scalar(raw[:, z], raw[:, z], 1.0 / GLA_TAU, None, ALU.mult))
                for k in (0, 1):
                    for part in scan_parts(z):
                        c.ended(nc.vector.tensor_tensor_scan(ev.decay[:, z, k, part[0]], one[:, part[0]], raw[:, z, k, part[0]],
                                                            ev.decay[:, z, k, part[1]:part[1] + 1] if part[1] is not None else 0.0, ALU.mult, ALU.add))
            dve.wait_ge(gap_turned.sem, gap_turned.at(2))
            c.ended(nc.vector.tensor_copy(ev.gap[:], core.bank(4)[:, 0:32].rearrange("p (b d h) -> p b d h", b=4, d=2)))
            for n in range(8):
                x, y = (ev.q, ev.k)[n // 4][:, n % 4].rearrange("p (s t) -> p s t", s=2), conv[:, n % 2].rearrange("p (s t) -> p s t", s=2)
                if n >= 2:
                    dve.wait_ge(act_chain.sem, act_chain.at(6 + n - 1))
                c.ended(nc.vector.tensor_scalar(y, x, st.V("ev_conv_w", 8 + n), st.V("ev_conv_b", n), ALU.mult, ALU.add))
                c.ended(nc.vector.scalar_tensor_tensor(y[:, :, 1:], x[:, :, :-1], st.V("ev_conv_w", n), y[:, :, 1:], ALU.mult, ALU.add))
                conv_ready.count(nc.vector.scalar_tensor_tensor(y[:, :, :-1], x[:, :, 1:], st.V("ev_conv_w", 16 + n), y[:, :, :-1], ALU.mult, ALU.add))


def scan_parts(backward):
    if backward:
        return [(slice(CTX - 1, None, -1), None), (slice(TT - 1, CTX - 1, -1), 0)]
    return [(slice(0, TT), None)]


def key_blocks(backward):
    if backward:
        return [(1, [(0, 4)]), (0, [(0, 1), (2, 4)]), (3, [(2, 4)]), (2, [(2, 3)])]
    return [(s, [(s, 4)]) for s in range(4)]


def mlstm_stage(core, st, ev):
    nc = core.nc
    units = [(h, d) for h in range(ML_HEADS) for d in (0, 1)]
    items = [(u, s, runs) for u, (h, d) in enumerate(units) for s, runs in key_blocks(d)]
    with ExitStack() as ctx, core.engines_block() as block:
        masked = core.sb("masked", [P, 2, P], ctx=ctx)
        weight = core.sb("weight", [P, 2, TT], ctx=ctx)
        pt = core.sb("pt", [P, 2, TT], ctx=ctx)
        den = core.sb("den", [P, TT], ctx=ctx)
        res = core.sb("res", [P, TT], ctx=ctx)
        names = ("rows_spread", "scores_ready", "masked_ready", "weights_ready", "pt_ready", "pt_used", "den_ready", "unit_done")
        spread, scores, masked_ready, weights, pt_ready, pt_used, den_ready, unit_done = (core.counter("ml_" + n) for n in names)
        chain = core.counter("vector_chain")
        MAXB, FLOORB, NUM, DEN = core.bank(0), core.bank(1), core.bank(4), core.bank(5)
        SC = [core.bank(2), core.bank(3)]

        @block.tensor
        def _(pe):
            for u, (h, d) in enumerate(units):
                if u:
                    pe.wait_ge(unit_done.sem, unit_done.at(u))
                sel = st.C("ident")[0:4, h:h + 1].to_broadcast([4, P])
                nc.tensor.matmul(MAXB, sel, ev.rowmax[d][:], start=True, stop=True)
                spread.count(nc.tensor.matmul(FLOORB, sel, ev.floor[d][:], start=True, stop=True))
                mine = [(n, s, runs) for n, (uu, s, runs) in enumerate(items) if uu == u]

                def score(n, s):
                    if n >= 2:
                        pe.wait_ge(pt_ready.sem, pt_ready.at(n - 1))
                    scores.count(nc.tensor.matmul(SC[n % 2], ev.k[:, h, s * P:(s + 1) * P], ev.q[:, h], start=True, stop=True))
                score(*mine[0][:2])
                for j, (n, s, runs) in enumerate(mine):
                    if j + 1 < len(mine):
                        score(*mine[j + 1][:2])
                    pe.wait_ge(pt_ready.sem, pt_ready.at(n + 1))
                    for r, (a, b) in enumerate(runs):
                        x = pt[:, n % 2, a * P:b * P]
                        flags = dict(start=j == 0 and r == 0, stop=j == 3, skip_group_check=True)
                        nc.tensor.matmul(NUM[:, a * P:b * P], ev.v[:, 0, s, h * P:(h + 1) * P], x, **flags)
                        ins = nc.tensor.matmul(DEN[:, a * P:b * P], st.C("ones"), x, **flags)
                    pt_used.count(ins)

        @block.scalar
        def _(act):
            for n, (u, s, runs) in enumerate(items):
                h, d = units[u]
                bias = ev.gap[:, s, d, h:h + 1]
                act.wait_ge(masked_ready.sem, masked_ready.at(n + 1))
                if n >= 2:
                    act.wait_ge(pt_ready.sem, pt_ready.at(n - 1))
                w = weight[:, n % 2]
                for a, b in runs:
                    for i, j in ((a, s), (s + 1, b)) if a <= s < b else ((a, b),):
                        if i < j:
                            nc.scalar.activation(w[:, i * P:j * P], MAXB[:, i * P:j * P], ACT.Exp, bias=bias, scale=-1.0)
                weights.count(nc.scalar.activation(w[:, s * P:(s + 1) * P], masked[:, n % 2], ACT.Exp, bias=bias))
                if n % 4 == 3:
                    act.wait_ge(pt_used.sem, pt_used.at(n + 1))
                    if u:
                        act.wait_ge(unit_done.sem, unit_done.at(u))
                    den_ready.count(nc.scalar.activation(den[:], DEN, ACT.Abs))

        @block.vector
        def _(dve):
            c = Chain(dve, chain)
            for n, (u, s, runs) in enumerate(items):
                h, d = units[u]
                dve.wait_ge(spread.sem, spread.at(u + 1))
                if n >= 2:
                    dve.wait_ge(weights.sem, weights.at(n - 1))
                masked_ready.count(nc.vector.scalar_tensor_tensor(masked[:, n % 2], MAXB[:, s * P:(s + 1) * P], -1.0,
                                                                st.C("neg_after" if d else "neg_before"), ALU.mult, ALU.add))
                dve.wait_ge(scores.sem, scores.at(n + 1))
                dve.wait_ge(weights.sem, weights.at(n + 1))
                if n >= 2:
                    dve.wait_ge(pt_used.sem, pt_used.at(n - 1))
                for a, b in runs:
                    ins = nc.vector.scalar_tensor_tensor(pt[:, n % 2, a * P:b * P], SC[n % 2][:, a * P:b * P], ML_DK ** -0.5,
                                                         weight[:, n % 2, a * P:b * P], ALU.mult, ALU.mult)
                pt_ready.count(ins)
                if n % 4 == 3:
                    dve.wait_ge(den_ready.sem, den_ready.at(u + 1))
                    c.ended(nc.vector.tensor_tensor(den[:], den[:], FLOORB, ALU.max))
                    c.ended(nc.vector.reciprocal(den[:], den[:]))
                    if d == 0:
                        unit_done.count(nc.vector.tensor_tensor(st.Y[:, h], NUM, den[:], ALU.mult))
                    else:
                        c.ended(nc.vector.tensor_tensor(res[:], NUM, den[:], ALU.mult))
                        unit_done.count(nc.vector.tensor_tensor(st.Y[:, h], st.Y[:, h], res[:], ALU.add))


def gla_stage(core, st, ev):
    nc = core.nc
    units = [(c, d) for c in (0, 1) for d in (0, 1)]
    n_lv = LEVELS + 2
    with ExitStack() as ctx, core.engines_block() as block:
        eq = core.sb("eq", [P, 2, TT], ctx=ctx)
        ek = core.sb("ek", [P, 2, TT], ctx=ctx)
        qs = core.sb("qs", [P, 2, TT], ctx=ctx)
        ks = core.sb("ks", [P, 2, TT], ctx=ctx)
        att = core.sb("att", [P, 2, TT], ctx=ctx)
        part = core.sb("part", [P, 2, TT], ctx=ctx)
        near = core.sb("near", [P, 2, 2 * P], ctx=ctx)
        far = core.sb("far", [P, 2, 2, CTX], ctx=ctx)
        exps_in, exps, scaled, scored, summed, pv = (core.counter("gla_" + n) for n in ("shifts", "exps", "scaled", "scored", "summed", "pv"))
        far_copied, out_taken = core.counter("gla_far_copied"), core.counter("gla_out_taken")
        chain = core.counter("vector_chain")
        OUT = [core.bank(4), core.bank(5)]

        def halves(x, level, d):
            h = 1 << (level - 1)
            v = x.rearrange("p (n two h) -> p n two h", two=2, h=h)
            late, early = (0, 1) if d and h < CTX else (1, 0)
            ref = v[:, :, early, 0:1] if d else v[:, :, early, h - 1:h]
            return v[:, :, late], v[:, :, early], ref.to_broadcast([P, TT // (2 * h), h])

        @block.vector
        def _(dve):
            c = Chain(dve, chain)
            c.ended(nc.vector.memset(qs[:], 0.0))
            c.ended(nc.vector.memset(ks[:], 0.0))
            for u, (ch, d) in enumerate(units):
                b, q, k = ev.decay[:, d, ch], ev.gqk[:, ch], ev.gqk[:, 2 + ch]

                def scale(l):
                    n = u * n_lv + l
                    p = n % 2
                    if n >= 2:
                        dve.wait_ge(scored.sem, scored.at(n - 1))
                    if l == 0:
                        nc.vector.tensor_copy(qs[:, p], q)
                        scaled.count(nc.vector.tensor_copy(ks[:, p], k))
                        return
                    bq, bk, ref = halves(b, l, d)
                    shift_q, _, _ = halves(eq[:, p], l, d)
                    _, shift_k, _ = halves(ek[:, p], l, d)
                    nc.vector.tensor_tensor(shift_q, bq, ref, ALU.subtract)
                    exps_in.count(nc.vector.tensor_tensor(shift_k, ref, bk, ALU.subtract))
                    dve.wait_ge(exps.sem, exps.at(u * (n_lv - 1) + l))
                    nc.vector.tensor_tensor(halves(qs[:, p], l, d)[0], halves(q, l, d)[0], shift_q, ALU.mult)
                    scaled.count(nc.vector.tensor_tensor(halves(ks[:, p], l, d)[1], halves(k, l, d)[1], shift_k, ALU.mult))

                def add_up(l):
                    n = u * n_lv + l
                    dve.wait_ge(scored.sem, scored.at(n + 1))
                    mask = st.C(f"level{l}_{d}").unsqueeze(1).to_broadcast([P, 4, P])
                    if l == 0 and u:
                        dve.wait_ge(pv.sem, pv.at(u))
                    for hh in (0, 1):
                        bank = core.bank((n % 2) * 2 + hh).rearrange("p (b t) -> p b t", b=4)
                        dst = att if l == 0 else part
                        ins = nc.vector.tensor_tensor(dst[:, hh].rearrange("p (b t) -> p b t", b=4), bank, mask, ALU.mult)
                    if l:
                        c.ended(ins)
                        ins = nc.vector.tensor_tensor(att[:], att[:], part[:], ALU.add)
                    summed.count(ins)
                    dve.wait_ge(summed.sem, summed.at(u * LEVELS + l + 1))

                scale(0)
                for l in range(n_lv):
                    if l + 1 < n_lv:
                        scale(l + 1)
                    if l < LEVELS:
                        add_up(l)
                if d:
                    dve.wait_ge(pv.sem, pv.at(u + 1))
                    for hh in (0, 1):
                        ins = nc.vector.tensor_copy(st.Y[:, 4 + 2 * ch + hh], OUT[hh])
                    out_taken.count(ins)

        @block.scalar
        def _(act):
            for u, (ch, d) in enumerate(units):
                for l in range(n_lv):
                    n = u * n_lv + l
                    p = n % 2
                    if l:
                        act.wait_ge(exps_in.sem, exps_in.at(u * (n_lv - 1) + l))
                        x, y = halves(eq[:, p], l, d)[0], halves(ek[:, p], l, d)[1]
                        nc.scalar.activation(x, x, ACT.Exp)
                        exps.count(nc.scalar.activation(y, y, ACT.Exp))
                    if l >= LEVELS + 1:
                        if u:
                            act.wait_ge(pv.sem, pv.at(u))
                        for up in (LEVELS, LEVELS + 1):
                            m = u * n_lv + up
                            act.wait_ge(scored.sem, scored.at(m + 1))
                            for hh in (0, 1):
                                bank = core.bank((m % 2) * 2 + hh)
                                if up == LEVELS:
                                    ins = nc.scalar.activation(near[:, hh], bank[:, 0:2 * P], ACT.Copy)
                                else:
                                    ins = nc.scalar.activation(far[:, hh], bank.rearrange("p (b t) -> p b t", b=2), ACT.Copy)
                            far_copied.count(ins)

        @block.tensor
        def _(pe):
            for u, (ch, d) in enumerate(units):
                for l in range(n_lv):
                    n = u * n_lv + l
                    pe.wait_ge(scaled.sem, scaled.at(n + 1))
                    if n >= 2:
                        m = n - 2
                        if m % n_lv < LEVELS:
                            pe.wait_ge(summed.sem, summed.at(m // n_lv * LEVELS + m % n_lv + 1))
                        else:
                            pe.wait_ge(far_copied.sem, far_copied.at(m // n_lv * 2 + m % n_lv - LEVELS + 1))
                    for hh in (0, 1):
                        bank = core.bank((n % 2) * 2 + hh)
                        k, q = ks[hh * 64:hh * 64 + 64, n % 2], qs[hh * 64:hh * 64 + 64, n % 2]
                        if l < LEVELS:
                            tiles = [(b * P, b * P, b * P, P) for b in range(4)]
                        elif l == LEVELS:
                            tiles = [(i * P, (2 * i + d) * P, (2 * i + 1 - d) * P, P) for i in (0, 1)]
                        else:
                            tiles = [(i * CTX, i * P, CTX, LAT) for i in (0, 1)]
                        for at, s, t, w in tiles:
                            ins = nc.tensor.matmul(bank[:, at:at + w], k[:, s:s + P], q[:, t:t + w], start=True, stop=True)
                    scored.count(ins)
                pe.wait_ge(summed.sem, summed.at((u + 1) * LEVELS))
                pe.wait_ge(far_copied.sem, far_copied.at(2 * u + 2))
                if u == 2:
                    pe.wait_ge(out_taken.sem, out_taken.at(1))
                for hh in (0, 1):
                    v = lambda s: ev.v[:, 1, s, (2 * ch + hh) * P:(2 * ch + hh + 1) * P]
                    prods = [(s, att[:, hh, s * P:(s + 1) * P], s * P, P) for s in range(4)]
                    prods += [(2 * i + d, near[:, hh, i * P:(i + 1) * P], (2 * i + 1 - d) * P, P) for i in (0, 1)]
                    prods += [(i, far[:, hh, i], CTX, LAT) for i in (0, 1)]
                    for j, (s, x, t, w) in enumerate(prods):
                        ins = nc.tensor.matmul(OUT[hh][:, t:t + w], v(s), x, start=d == 0 and j == 0,
                                               stop=d == 1 and j == len(prods) - 1, skip_group_check=True)
                pv.count(ins)


def even_gate_stage(core, st, ev):
    nc = core.nc
    with ExitStack() as ctx, core.engines_block() as block:
        square = core.sb("square", [P, DC, TT], ctx=ctx)
        var = core.sb("var", [P, 2, TT], ctx=ctx)
        unit = core.sb("unit", [P, 2, TT], ctx=ctx)
        squared, summed, var_ready, std_ready, done = (core.counter(n) for n in ("squared", "summed", "var_ready", "std_ready", "head_done"))
        chain = core.counter("vector_chain")

        @block.scalar
        def _(act):
            for k in range(DC):
                squared.count(nc.scalar.activation(square[:, k], st.Y[:, k], ACT.Square))
            for k in range(4):
                ins = nc.scalar.activation(ev.gg[:, k], ev.gg[:, k], ACT.Silu)
            for k in range(DC):
                act.wait_ge(var_ready.sem, var_ready.at(k + 1))
                std_ready.count(nc.scalar.activation(var[:, k % 2], var[:, k % 2], ACT.Sqrt))

        @block.tensor
        def _(pe):
            for k in range(DC):
                pe.wait_ge(squared.sem, squared.at(k + 1))
                summed.count(nc.tensor.matmul(core.bank(k), st.C("ones"), square[:, k], start=True, stop=True))

        @block.vector
        def _(dve):
            c = Chain(dve, chain)

            def spread(k):
                dve.wait_ge(summed.sem, summed.at(k + 1))
                var_ready.count(nc.vector.tensor_scalar(var[:, k % 2], core.bank(k), 1.0 / P, EPS, ALU.mult, ALU.add))
            spread(0)
            for k in range(DC):
                if k + 1 < DC:
                    spread(k + 1)
                dve.wait_ge(std_ready.sem, std_ready.at(k + 1))
                v = var[:, k % 2]
                c.ended(nc.vector.reciprocal(v, v))
                u = unit[:, k % 2]
                c.ended(nc.vector.scalar_tensor_tensor(u, st.Y[:, k], st.V("ev_head_g", k), v, ALU.mult, ALU.mult))
                nc.vector.tensor_tensor(st.Y[:, k], u, (ev.o if k < 4 else ev.gg)[:, k % 4], ALU.mult)


def ffn_stage(core, st, layer, T, t0, beside=None):
    nc, A = core.nc, st.A
    with ExitStack() as outer:
        h = core.sb("ffn_h", [P, FC, T], ctx=outer)
        n_it = FC // 2
        with ExitStack() as ctx, core.engines_block() as block:
            up = A["ffn_w_up"][layer]
            tiles = k_tiles(up, 256, 2, (0, 1), lambda it: it * 256) + k_tiles(up, 256, 2, (2, 3), lambda it: it * 256 + FF)
            g = Gemm(core, ctx, "up", tiles, {o: o for o in range(4)}, 256)
            taps = core.sb("taps", [P, 2, 10], ctx=ctx)
            conv = core.sb("conv", [P, 2, T], ctx=ctx)
            gelu = core.sb("gelu", [P, 2, T], ctx=ctx)
            conv_ready, gelu_ready, chain = core.counter("conv_ready"), core.counter("gelu_ready"), core.counter("vector_chain")
            w0, b0 = st.rows_at["ffn_conv_w"][0] + layer * 9 * FC, st.rows_at["ffn_conv_b"][0] + layer * FC
            tap_order = [(dy, dx) for dy in (-1, 0, 1) for dx in (-1, 0, 1) if (dy, dx) != (0, 0)]
            per = 2 * (1 + len(tap_order)) + (2 * 2 if T == TT else 0)

            @block.sync
            def _(sp):
                rounds(sp, n_it, lambda it, first: g.fetch_round(sp, it, first))

            @block.tensor
            def _(pe):
                rounds(pe, n_it, lambda it, first: g.matmul_round(pe, it, lambda k: st.H[:, k, t0:t0 + T], first))

            @block.vector
            def _(dve):
                def body(it, first):
                    c = Chain(dve, chain, it, per)
                    for o in (0, 1):
                        n = it * 2 + o
                        nc.vector.tensor_copy(taps[:, o, 0:9].unsqueeze(2), st.vec[:, w0:w0 + 9 * FC].rearrange("p (w f) -> p w f", f=FC)[:, :, ds(n, 1)])
                        c.ended(nc.vector.tensor_copy(taps[:, o, 9:10], st.vec[:, ds(b0 + n, 1)]))
                        bank = g.wait_bank(dve, o, it)
                        if not first:
                            dve.wait_ge(gelu_ready.sem, gelu_ready.at(it * 2 + o - 1))
                        y = conv[:, o]
                        c.ended(nc.vector.tensor_scalar(y, bank[:, 0:T], taps[:, o, 4:5], taps[:, o, 9:10], ALU.mult, ALU.add))
                        if T == TT:
                            c.ended(nc.vector.scalar_tensor_tensor(y[:, 1:CTX], bank[:, 0:CTX - 1], taps[:, o, 3:4], y[:, 1:CTX], ALU.mult, ALU.add))
                            c.ended(nc.vector.scalar_tensor_tensor(y[:, 0:CTX - 1], bank[:, 1:CTX], taps[:, o, 5:6], y[:, 0:CTX - 1], ALU.mult, ALU.add))
                        yg = y[:, T - LAT:T].rearrange("p (r w) -> p r w", w=GRID_W)
                        xg = bank[:, T - LAT:T].rearrange("p (r w) -> p r w", w=GRID_W)
                        for i, (dy, dx) in enumerate(tap_order):
                            rows = [slice(max(0, -s), n - max(0, s)) for s, n in ((dy, GRID_H), (dx, GRID_W))]
                            from_ = [slice(r.start + s, r.stop + s) for r, s in zip(rows, (dy, dx))]
                            w = (dy + 1) * 3 + dx + 1
                            ins = nc.vector.scalar_tensor_tensor(yg[:, rows[0], rows[1]], xg[:, from_[0], from_[1]], taps[:, o, w:w + 1],
                                                                 yg[:, rows[0], rows[1]], ALU.mult, ALU.add)
                            if i + 1 < len(tap_order):
                                c.ended(ins)
                        g.bank_taken(ins, o)
                    for o in (0, 1):
                        bank = g.wait_bank(dve, 2 + o, it)
                        dve.wait_ge(gelu_ready.sem, gelu_ready.at(it * 2 + o + 1))
                        g.bank_taken(nc.vector.tensor_tensor(chunk_of(h, it * 2 + o), gelu[:, o], bank[:, 0:T], ALU.mult), 2 + o)
                    return c
                c = [None]

                def run(it, first):
                    c[0] = body(it, first)
                rounds(dve, n_it, run)
                c[0].settle(n_it)

            @block.scalar
            def _(act):
                def body(it, first):
                    for o in (0, 1):
                        act.wait_ge(g.free[o].sem, g.free[o].at(it + 1))
                        if not first:
                            act.wait_ge(g.free[2 + o].sem, g.free[2 + o].at(it))
                        nc.scalar.activation(gelu[:, o], conv[:, o], ACT.Gelu_apprx_tanh).then_inc(gelu_ready.sem, 1)
                rounds(act, n_it, body)
            gelu_ready.n += 2 * n_it
            g.settle(n_it)
        gemm_stage(core, st, "down", A["ffn_w_down"][layer], D, lambda k: h[:, k],
                   lambda act, c, bank: nc.scalar.activation(chunk_of(st.Y, c, slice(t0, t0 + T)), bank[:, 0:T], ACT.Copy), width=256, background=beside)


class Rwkv:
    def __init__(self, core, st, ctx):
        sb = lambda name: core.sb(name, [P, DC, TT], ctx=ctx)
        self.k, self.v, self.kk, self.b = sb("rw_k"), sb("rw_v"), sb("rw_kk"), sb("rw_b")
        self.decay = [sb("rw_decay0"), sb("rw_decay1")]
        self.r = st.X[:, :, 0:CTX]
        self.g = st.Y[:, :, 0:CTX]
        self.y = st.Y[:, :, CTX:TT]


def rwkv_shift_stage(core, st):
    nc = core.nc
    with core.engines_block() as block:
        @block.vector
        def _(dve):
            for quarter in range(4):
                k = slice(2 * quarter, 2 * quarter + 2)
                h, y = st.H[:, k], st.Y[:, k]
                back = quarter % 2 == 0
                to, of, edge = (slice(1, CTX), slice(0, CTX - 1), slice(0, 1)) if back else (slice(0, CTX - 1), slice(1, CTX), slice(CTX - 1, CTX))
                nc.vector.tensor_tensor(y[:, :, to], h[:, :, of], h[:, :, to], ALU.subtract)
                nc.vector.tensor_scalar(y[:, :, edge], h[:, :, edge], -1.0, None, ALU.mult)
                for c in (0, 1):
                    hg, yg = (x[:, c, CTX:TT].rearrange("p (r w) -> p r w", w=GRID_W) for x in (h, y))
                    n = GRID_W if quarter < 2 else GRID_H
                    to, of, edge = (slice(1, n), slice(0, n - 1), slice(0, 1)) if back else (slice(0, n - 1), slice(1, n), slice(n - 1, n))
                    cut = (lambda x, s: x[:, :, s]) if quarter < 2 else (lambda x, s: x[:, s, :])
                    nc.vector.tensor_tensor(cut(yg, to), cut(hg, of), cut(hg, to), ALU.subtract)
                    nc.vector.tensor_scalar(cut(yg, edge), cut(hg, edge), -1.0, None, ALU.mult)


def rwkv_low_rank_stage(core, st, rw, mu, w1_parts, rank, func, w2, parts, store, tokens):
    nc = core.nc
    T = tokens.stop - tokens.start
    with ExitStack() as ctx, core.engines_block() as block:
        w1s = core.sb("w1s", [P, DC, rank], ctx=ctx)
        w2s = core.sb("w2s", [rank, D], ctx=ctx)
        hidden = core.sb("hidden", [rank, T], ctx=ctx)
        loaded, mixed, hid, hid_done, out, taken = (core.counter("low_" + n) for n in ("loaded", "mixed", "hidden", "hidden_done", "out", "taken"))

        @block.sync
        def _(sp):
            each = rank // len(w1_parts)
            for i, w in enumerate(w1_parts):
                loaded.count(sp.dma_start(w1s[:, :, i * each:(i + 1) * each], w.rearrange("(k p) r -> p k r", p=P)), 16)
            loaded.count(sp.dma_start(w2s[:], w2), 16)

        @block.vector
        def _(dve):
            mixed.count(rwkv_mix(core, st, rw, mu, tokens))

        @block.tensor
        def _(pe):
            pe.wait_ge(mixed.sem, mixed.at(1))
            pe.wait_ge(loaded.sem, loaded.at(loaded.n))
            for k in range(DC):
                ins = nc.tensor.matmul(core.bank(0)[0:rank, 0:T], w1s[:, k], rw.kk[:, k, tokens], start=k == 0, stop=k == DC - 1)
            hid.count(ins)
            pe.wait_ge(hid_done.sem, hid_done.at(1))
            for i, rows in enumerate(parts):
                for n in range(DC):
                    m = i * DC + n
                    if m >= 4:
                        pe.wait_ge(taken.sem, taken.at(m - 3))
                    out.count(nc.tensor.matmul(core.bank(4 + m % 4)[:, 0:T], w2s[rows, n * P:(n + 1) * P], hidden[rows], start=True, stop=True))

        @block.scalar
        def _(act):
            act.wait_ge(hid.sem, hid.at(1))
            hid_done.count(nc.scalar.activation(hidden[:], core.bank(0)[0:rank, 0:T], func))
            for m in range(len(parts) * DC):
                act.wait_ge(out.sem, out.at(m + 1))
                taken.count(store(m // DC, m % DC, core.bank(4 + m % 4)[:, 0:T]))


def rwkv_mix(core, st, rw, mu, tokens):
    for k in range(DC):
        ins = core.nc.vector.scalar_tensor_tensor(rw.kk[:, k, tokens], st.Y[:, k, tokens], st.V("rw_mu", mu * DC + k), st.H[:, k, tokens],
                                                  ALU.mult, ALU.add)
    return ins


def rwkv_project(core, st, rw):
    nc, A = core.nc, st.A
    lat, all_ = slice(CTX, TT), slice(0, TT)
    rwkv_shift_stage(core, st)
    copy = lambda dst: lambda act, c, bank: nc.scalar.activation(chunk_of(dst, c), bank[:, 0:dst.shape[2]], ACT.Copy)
    for i, (mu, dst, tokens) in enumerate(((0, rw.r, lat), (2, rw.k, all_), (3, rw.v, all_))):
        gemm_stage(core, st, "in", A["rw_w_rkv"][0, i], D, lambda k, t=tokens: rw.kk[:, k, t], copy(dst),
                   mix=lambda mu=mu, t=tokens: rwkv_mix(core, st, rw, mu, t))
    rwkv_low_rank_stage(core, st, rw, 4, [A["rw_a1"][0]], 64, ACT.Copy, A["rw_a2"][0], [slice(0, 64)],
                        lambda i, n, bank: nc.scalar.activation(rw.b[:, n], bank, ACT.Sigmoid, bias=st.V("rw_a0", n)), all_)
    rwkv_low_rank_stage(core, st, rw, 1, [A["rw_w1"][0, 0], A["rw_w1"][0, 1]], 128, ACT.Tanh, A["rw_w2"][0].rearrange("z r d -> (z r) d"),
                        [slice(0, 64), slice(64, 128)],
                        lambda i, n, bank: nc.scalar.activation(rw.decay[i][:, n], bank, ACT.Sigmoid, bias=st.V("rw_w0", i * DC + n)), all_)
    rwkv_low_rank_stage(core, st, rw, 5, [A["rw_g1"][0]], 128, ACT.Sigmoid, A["rw_g2"][0], [slice(0, 128)],
                        lambda i, n, bank: nc.scalar.activation(rw.g[:, n], bank, ACT.Copy), lat)

    with ExitStack() as ctx, core.engines_block() as block:
        square = core.sb("square", [P, 2, TT], ctx=ctx)
        norm = core.sb("norm", [P, 2, TT], ctx=ctx)
        blend = core.sb("blend", [P, TT], ctx=ctx)
        rest = core.sb("rest", [P, DC], ctx=ctx)
        scaled, squared, summed, rooted = (core.counter("kk_" + n) for n in ("scaled", "squared", "summed", "rooted"))
        chain = core.counter("vector_chain")

        @block.scalar
        def _(act):
            for n in range(DC):
                act.wait_ge(scaled.sem, scaled.at(n + 1))
                squared.count(nc.scalar.activation(square[:, n % 2], rw.kk[:, n], ACT.Square))
                act.wait_ge(summed.sem, summed.at(n + 1))
                if n >= 2:
                    act.wait_ge(scaled.sem, scaled.at(n + 1))
                rooted.count(nc.scalar.activation(norm[:, n % 2], core.bank(n), ACT.Sqrt))

        @block.tensor
        def _(pe):
            for n in range(DC):
                pe.wait_ge(squared.sem, squared.at(n + 1))
                summed.count(nc.tensor.matmul(core.bank(n), st.C("head_ones"), square[:, n % 2], start=True, stop=True))

        @block.vector
        def _(dve):
            c = Chain(dve, chain)
            c.ended(nc.vector.tensor_scalar(rest[:], st.V("rw_kvec", DC, DC), -1.0, 1.0, ALU.mult, ALU.add))
            scale = lambda n: scaled.count(nc.vector.tensor_scalar(rw.kk[:, n], rw.k[:, n], st.V("rw_kvec", n), None, ALU.mult))
            scale(0)
            for n in range(DC):
                if n + 1 < DC:
                    scale(n + 1)
                nc.vector.tensor_tensor_scan(rw.decay[0][:, n], st.C("keep_fwd"), rw.decay[0][:, n], 0.0, ALU.mult, ALU.add)
                nc.vector.tensor_tensor_scan(rw.decay[1][:, n, ::-1], st.C("keep_bwd")[:, ::-1], rw.decay[1][:, n, ::-1], 0.0, ALU.mult, ALU.add)
                c.ended(nc.vector.tensor_scalar(blend[:], rw.b[:, n], st.V("rw_kvec", DC + n), rest[:, n:n + 1], ALU.mult, ALU.add))
                c.ended(nc.vector.tensor_tensor(rw.k[:, n], rw.k[:, n], blend[:], ALU.mult))
                dve.wait_ge(rooted.sem, rooted.at(n + 1))
                v = norm[:, n % 2]
                c.ended(nc.vector.tensor_scalar(v, v, 1e-12, None, ALU.max))
                c.ended(nc.vector.reciprocal(v, v))
                c.ended(nc.vector.tensor_tensor(rw.kk[:, n], rw.kk[:, n], v, ALU.mult))
                c.ended(nc.vector.tensor_tensor(rw.b[:, n], rw.b[:, n], rw.kk[:, n], ALU.mult))


def rwkv_steps(latent):
    levels = range(2, 7)
    out = ["RK", "RB"] if latent else []
    pe = ["V", "K", "B", "C", "CT", "LK"] + out
    for l in levels:
        pe += [f"Y{l}", f"E{l}"] + ([f"D{l}"] if l < 6 else [])
    pe += ["W", "U"] + (["O"] if latent else []) + ["S"]
    act = ["exp", "V", "K", "B", "C"] + [f"Y{l}" for l in levels] + ["W", "U"]
    dve = ["prep", "CT", "D1", "LK"] + out
    for l in levels:
        dve += [f"E{l}"] + ([f"D{l}"] if l < 6 else [])
    dve += (["O"] if latent else []) + ["S"]
    return pe, act, dve


def rwkv_scan_stage(core, st, rw):
    nc = core.nc
    n_chunks = CTX // RW_CHUNK
    C = RW_CHUNK
    with ExitStack() as ctx, core.engines_block() as block:
        taken_h = iter(range(DC))

        def buf(name):
            k = next(taken_h, None)
            t = st.H[:, k] if k is not None else core.sb(name, [P, DC * C], ctx=ctx)[:]
            return t.rearrange("p (n t) -> p n t", n=DC)
        names = ("alpha", "rho", "beta", "kappa", "val", "kappa_t", "beta_t", "val_t", "c", "e", "grow", "fall", "state")
        B = [{n: buf(f"{n}{d}") for n in names} for d in (0, 1)]
        for b in B:
            b.update(lk=b["grow"], rk=b["fall"], rb=b["kappa"], y=b["beta"], w=b["beta"], u=b["c"], d=b["val"])
        last = [core.sb(f"last{d}", [P, DC], ctx=ctx) for d in (0, 1)]
        pe_s, act_s, dve_s = ([core.counter(f"rw_{e}_step{d}") for d in (0, 1)] for e in ("tensor", "scalar", "vector"))
        chain = core.counter("vector_chain")
        passed = core.counter("rw_tensor_passed"), core.counter("rw_vector_passed")
        phases = [(False, 0), (True, CTX)]
        H2 = [slice(0, 64), slice(64, 128)]

        def value(sig, order, off, it, step):
            return sig.at(off + it * len(order) + order.index(step) + 1)

        def start_of(it, d, t0):
            return t0 + (it * C if d == 0 else (n_chunks - 1) * C - it * C)

        offs = []
        off = [1, 1, 1]
        for latent, _ in phases:
            offs.append(list(off))
            off = [o + n_chunks * len(x) for o, x in zip(off, rwkv_steps(latent))]

        @block.tensor
        def _(pe):
            for d in (0, 1):
                pe.sem_inc(pe_s[d].sem, 1)
            for (latent, t0), (po, ao, do) in zip(phases, offs):
                order, act_order, dve_order = rwkv_steps(latent)
                a, v = "act", "dve"
                need = {"V": [(v, "prep"), (a, "exp")], "Y2": [(a, "C"), (v, "CT")], "E2": [(a, "Y2"), (v, "D1")], "W": [(v, "LK"), (a, "V")],
                        "U": [(a, "W"), (v, "E6")], "O": [(a, "U"), (v, "RB")], "S": [(a, "U")]}
                for l in range(3, 7):
                    need[f"Y{l}"] = [(v, f"E{l - 1}")]
                    need[f"E{l}"] = [(a, f"Y{l}"), (v, f"D{l - 1}")]
                with pe.Fori(0, n_chunks) as it:
                    for n, step in enumerate(order):
                        for d in (0, 1):
                            b, bank = B[d], core.bank(4 * d + n % 4).rearrange("p (n t) -> p n t", n=DC)
                            wait = list(need.get(step, []))
                            if n >= 4:
                                p = order[n - 4]
                                wait.append(("act" if p in act_order else "dve", p))
                            on_act = [s for eng, s in wait if eng == "act"]
                            on_dve = [s for eng, s in wait if eng == "dve"]
                            if on_act:
                                pe.wait_ge(act_s[d].sem, value(act_s[d], act_order, ao, it, max(on_act, key=act_order.index)))
                            if on_dve:
                                pe.wait_ge(dve_s[d].sem, value(dve_s[d], dve_order, do, it, max(on_dve, key=dve_order.index)))
                            pe.sem_inc(passed[0].sem, 1)
                            kind = step.rstrip("123456")
                            ident = st.C("ident")
                            for i in range(DC):
                                for h in H2:
                                    turn = ident[h, h]
                                    x = {"V": [("val", turn)], "K": [("kappa", turn)], "B": [("beta", turn)], "C": [("alpha", "beta")],
                                         "CT": [("beta", "alpha")], "LK": [("kappa", "alpha")], "RK": [("kappa", "rho")], "RB": [("beta", "rho")],
                                         "Y": [("c", "e")], "E": [("d", "y")], "D": [("y", "d")], "W": [("alpha", "state"), ("lk", "val_t")],
                                         "U": [("e", "w")], "O": [("state", "rho"), ("val_t", "rk"), ("u", "rb")],
                                         "S": [("kappa_t", "val_t"), ("beta_t", "u")]}[kind]
                                    for j, (lhs, rhs) in enumerate(x):
                                        moving = b[rhs][h, i] if isinstance(rhs, str) else rhs
                                        ins = nc.tensor.matmul(bank[h, i], b[lhs][h, i], moving, start=j == 0, stop=j == len(x) - 1)
                            ins.then_inc(pe_s[d].sem, 1)

        @block.scalar
        def _(act):
            for d in (0, 1):
                act.sem_inc(act_s[d].sem, 1)
            for (latent, t0), (po, ao, do) in zip(phases, offs):
                pe_order, order, _ = rwkv_steps(latent)
                with act.Fori(0, n_chunks) as it:
                    for step in order:
                        for d in (0, 1):
                            b = B[d]
                            if step == "exp":
                                act.wait_ge(pe_s[d].sem, pe_s[d].at(po + it * len(pe_order)))
                                at = ds(start_of(it, d, t0), C)
                                nc.scalar.activation(b["grow"], rw.decay[d][:, :, at], ACT.Exp, scale=RW_DECAY)
                                nc.scalar.activation(b["fall"], rw.decay[d][:, :, at], ACT.Exp, scale=-RW_DECAY)
                                ins = nc.scalar.activation(b["val"], rw.v[:, :, at], ACT.Copy)
                            else:
                                act.wait_ge(pe_s[d].sem, value(pe_s[d], pe_order, po, it, step))
                                bank = core.bank(4 * d + pe_order.index(step) % 4).rearrange("p (n t) -> p n t", n=DC)
                                dst = {"V": "val_t", "K": "kappa_t", "B": "beta_t", "C": "c", "W": "w", "U": "u"}.get(step, "y")
                                ins = nc.scalar.activation(b[dst], bank, ACT.Copy)
                            ins.then_inc(act_s[d].sem, 1)

        @block.vector
        def _(dve):
            for d in (0, 1):
                nc.vector.memset(B[d]["state"], 0.0).then_inc(dve_s[d].sem, 1)
            nc.vector.memset(rw.y, 0.0).then_inc(chain.sem, 1)
            chain.n += 1
            for (latent, t0), (po, ao, do) in zip(phases, offs):
                pe_order, act_order, order = rwkv_steps(latent)
                done = 0
                per = 4
                base = chain.n
                with dve.Fori(0, n_chunks) as it:
                    for step in order:
                        for d in (0, 1):
                            b = B[d]
                            mask = lambda name, u=False: (st.C(name).bitcast(U32) if u else st.C(name)).unsqueeze(1).to_broadcast([P, DC, C])
                            if step == "prep":
                                dve.wait_ge(act_s[d].sem, value(act_s[d], act_order, ao, it, "exp"))
                                dve.wait_ge(dve_s[d].sem, dve_s[d].at(do + it * len(order)))
                                t = start_of(it, d, t0)
                                at = ds(t, C)
                                edge, inner, before = (C - 1, slice(0, C - 1), slice(1, C)) if d else (0, slice(1, C), slice(0, C - 1))
                                shift = 0 if d else 1
                                nc.vector.tensor_copy(last[d][:].unsqueeze(2), b["grow"][:, :, (0 if d else C - 1):(1 if d else C)])
                                nc.vector.scalar_tensor_tensor(b["alpha"][:, :, inner], rw.kk[:, :, ds(t + shift, C - 1)], -1.0,
                                                               b["grow"][:, :, before], ALU.mult, ALU.mult)
                                nc.vector.tensor_scalar(b["alpha"][:, :, edge:edge + 1], rw.kk[:, :, ds(t + edge, 1)], -1.0, None, ALU.mult)
                                if latent:
                                    nc.vector.tensor_tensor(b["rho"], rw.r[:, :, ds(t - CTX, C)], b["grow"], ALU.mult)
                                nc.vector.tensor_tensor(b["beta"], rw.b[:, :, at], b["fall"], ALU.mult)
                                ins = nc.vector.tensor_tensor(b["kappa"], rw.k[:, :, at], b["fall"], ALU.mult)
                            elif step == "D1":
                                dve.wait_ge(act_s[d].sem, value(act_s[d], act_order, ao, it, "C"))
                                nc.vector.tensor_copy(b["d"], mask("pair_ident")).then_inc(chain.sem, 1)
                                done += 1
                                dve.wait_ge(chain.sem, chain.at(base + it * 6 + done))
                                dve.sem_inc(passed[1].sem, 1)
                                ins = nc.vector.copy_predicated(b["d"], mask(f"pair1_{1 - d}", True), b["c"])
                            else:
                                bank = core.bank(4 * d + pe_order.index(step) % 4).rearrange("p (n t) -> p n t", n=DC)
                                if step == "CT":
                                    nc.vector.tensor_copy(b["e"], mask("pair_ident")).then_inc(chain.sem, 1)
                                    done += 1
                                    dve.wait_ge(chain.sem, chain.at(base + it * 6 + done))
                                dve.wait_ge(pe_s[d].sem, value(pe_s[d], pe_order, po, it, step))
                                if step == "CT" or step[0] in "ED":
                                    dve.sem_inc(passed[1].sem, 1)
                                if step == "CT":
                                    ins = nc.vector.copy_predicated(b["e"], mask(f"pair1_{d}", True), bank)
                                elif step in ("LK", "RK", "RB"):
                                    m = "before" if step == "LK" else "upto"
                                    ins = nc.vector.tensor_tensor(b[step.lower()], bank, mask(f"{m}_{d}"), ALU.mult)
                                elif step[0] in "ED":
                                    l = int(step[1])
                                    ins = nc.vector.copy_predicated(b[step[0].lower()], mask(f"pair{l}_{d if step[0] == 'E' else 1 - d}", True), bank)
                                elif step == "O":
                                    y = rw.y[:, :, ds(start_of(it, d, 0), C)]
                                    ins = nc.vector.tensor_tensor(y, y, bank, ALU.add)
                                elif step == "S":
                                    nc.vector.tensor_tensor(b["state"], b["state"], bank, ALU.add).then_inc(chain.sem, 1)
                                    done += 1
                                    dve.wait_ge(chain.sem, chain.at(base + it * 6 + done))
                                    ins = nc.vector.tensor_tensor(b["state"], b["state"], last[d][:].unsqueeze(2).to_broadcast([P, DC, C]), ALU.mult)
                            ins.then_inc(dve_s[d].sem, 1)
                assert done == 6
                chain.n += 6 * n_chunks
        for sigs, n in zip((pe_s, act_s, dve_s), off):
            for s in sigs:
                s.n += n
        for s, per in zip(passed, (lambda x: 2 * len(x[0]), lambda x: 2 * sum(y[0] in "ED" or y == "CT" for y in x[2]))):
            s.n += n_chunks * sum(per(rwkv_steps(latent)) for latent, _ in phases)


def rwkv_out_stage(core, st, rw):
    nc = core.nc
    lat = slice(CTX, TT)
    with ExitStack() as ctx, core.engines_block() as block:
        cen = core.sb("cen", [P, DC, LAT], ctx=ctx)
        square = core.sb("square", [P, DC, LAT], ctx=ctx)
        std = core.sb("std", [P, DC, LAT], ctx=ctx)
        rk = core.sb("rk", [P, DC, LAT], ctx=ctx)
        names = ("rk", "mean", "centred", "squared", "summed", "var", "rooted", "bonus")
        rk_s, mean, centred, squared, summed, var, rooted, bonus = (core.counter("out_" + n) for n in names)
        chain = core.counter("vector_chain")

        def half(i, n):
            return core.bank(i * 4 + n // 2)[:, n % 2 * LAT:(n % 2 + 1) * LAT]

        @block.tensor
        def _(pe):
            for n in range(DC):
                mean.count(nc.tensor.matmul(half(0, n), st.C("head_ones"), rw.y[:, n], start=True, stop=True))
            for n in range(DC):
                pe.wait_ge(rk_s.sem, rk_s.at(n + 1))
                bonus.count(nc.tensor.matmul(half(1, n), st.C("head_ones"), rk[:, n], start=True, stop=True))
            for n in range(DC):
                pe.wait_ge(squared.sem, squared.at(DC))
                summed.count(nc.tensor.matmul(half(0, n), st.C("head_ones"), square[:, n], start=True, stop=True))

        @block.scalar
        def _(act):
            for n in range(DC):
                act.wait_ge(centred.sem, centred.at(n + 1))
                squared.count(nc.scalar.activation(square[:, n], cen[:, n], ACT.Square))
            for n in range(DC):
                act.wait_ge(var.sem, var.at(n + 1))
                rooted.count(nc.scalar.activation(std[:, n], std[:, n], ACT.Sqrt))

        @block.vector
        def _(dve):
            c = Chain(dve, chain)
            for n in range(DC):
                rk_s.count(nc.vector.scalar_tensor_tensor(rk[:, n], rw.r[:, n], st.V("rw_kvec", 2 * DC + n), rw.k[:, n, lat], ALU.mult, ALU.mult))
            for n in range(DC):
                dve.wait_ge(mean.sem, mean.at(n // 2 * 2 + 2))
                centred.count(nc.vector.scalar_tensor_tensor(cen[:, n], half(0, n), -1.0 / RW_HEAD, rw.y[:, n], ALU.mult, ALU.add))
            for n in range(DC):
                dve.wait_ge(summed.sem, summed.at(n // 2 * 2 + 2))
                var.count(nc.vector.tensor_scalar(std[:, n], half(0, n), 1.0 / RW_HEAD, RW_LN_EPS, ALU.mult, ALU.add))
            for n in range(DC):
                dve.wait_ge(rooted.sem, rooted.at(n + 1))
                c.ended(nc.vector.reciprocal(std[:, n], std[:, n]))
                c.ended(nc.vector.tensor_tensor(cen[:, n], cen[:, n], std[:, n], ALU.mult))
                c.ended(nc.vector.tensor_scalar(cen[:, n], cen[:, n], st.V("rw_lnx", n), st.V("rw_lnx", DC + n), ALU.mult, ALU.add))
                dve.wait_ge(bonus.sem, bonus.at(n // 2 * 2 + 2))
                c.ended(nc.vector.tensor_tensor(rk[:, n], half(1, n), rw.v[:, n, lat], ALU.mult))
                c.ended(nc.vector.tensor_tensor(cen[:, n], cen[:, n], rk[:, n], ALU.add))
                nc.vector.tensor_tensor(st.H[:, n, lat], cen[:, n], rw.g[:, n], ALU.mult)


def rwkv_layer(core, st, scope):
    nc, A = core.nc, st.A
    lat = slice(CTX, TT)
    norm_in(core, st, 0, 0, (0, 1))
    with ExitStack() as heads:
        rw = Rwkv(core, st, heads)
        rwkv_project(core, st, rw)
        rwkv_scan_stage(core, st, rw)
        rwkv_out_stage(core, st, rw)
    kv_sums = ModSums(core, st, scope, "kv_ada", A["w_kv_ada_2"], ("b_kv_ada_2", 0), (2,), 16)
    gemm_stage(core, st, "in", A["rw_w_o"][0], D, lambda k: st.H[:, k, lat],
               lambda act, c, bank: nc.scalar.activation(chunk_of(st.Y, c, lat), bank[:, 0:LAT], ACT.Copy), background=kv_sums)
    norm_out(core, st, 1, st.Y, (0,))
    norm_in(core, st, 2, 24, (0,))
    return kv_sums


LATS = slice(CTX, TT)


def ada_sums(core, st, scope, layer, place=None):
    return ModSums(core, st, scope, f"ada{layer}", st.A["w_ada_2"][layer], ("b_ada_2", layer * 48), (2,), 48, place)


def ada(core, st, sums, layer):
    mod_stage(core, st, sums, [(0, 0, ("attn_gain_2", layer * DC), 8, 1), (0, 2, ("ffn_gain_2", layer * DC), 32, 1)])


def add_gated(core, st, key, w, rhs, gate, width=512):
    nc = core.nc

    def store(dve, c, bank):
        x = chunk_of(st.X, c, LATS)
        return nc.vector.scalar_tensor_tensor(x, bank[:, 0:LAT], st.mod[:, ds(gate + c, 1), 0], x, ALU.mult, ALU.add)
    gemm_stage(core, st, key, w, D, rhs, store, width=width, engine="vector")


def small_stage(core, st, w, jobs):
    nc = core.nc
    v = w.rearrange("(k p) n -> p k n", p=P)
    with ExitStack() as ctx, core.engines_block() as block:
        ws, outs = [], []
        for i, (kind, col, n, dst, *more) in enumerate(jobs):
            if kind == "pair":
                t = core.sb(f"w_pair{i}", [P, DC, n, 2, HD], ctx=ctx)
                for g in range(n):
                    outs.append((i, lambda k, t=t, g=g: (t[:, k, g].rearrange("p a d -> p (a d)"), st.H[:, k, LATS]), LAT,
                                 lambda bank, dst=dst, g=g: nc.scalar.activation(dst[:, g], bank, ACT.Copy)))
            else:
                width = n * HD if kind == "values" else n
                t = core.sb(f"w_tokens{i}", [P, DC, width], ctx=ctx)
                for b in (0, 1):
                    if kind == "values":
                        take = lambda bank, dst=dst, b=b, n=n: nc.scalar.activation(dst[:, b, :, HD:2 * HD], bank.rearrange("p (g d) -> p g d", g=n), ACT.Copy)
                    else:
                        take = lambda bank, dst=dst, b=b, more=more: nc.scalar.activation(dst[:, b], bank, more[0], scale=more[1])
                    outs.append((i, lambda k, t=t, b=b: (st.H[:, k, CTX + b * P:CTX + (b + 1) * P], t[:, k]), width, take))
            ws.append(t)
        loaded = [core.counter(f"small_weights{i}") for i in range(len(jobs))]
        ready, taken, zeroed = core.counter("small_ready"), core.counter("small_taken"), core.counter("small_zeroed")

        @block.sync
        def _(sp):
            for i, (kind, col, n, *_) in enumerate(jobs):
                if kind == "pair":
                    for k in range(DC):
                        for a in (0, 1):
                            loaded[i].count(sp.dma_start(ws[i][:, k, :, a], v[:, k, col:col + n * HD].rearrange("p (g d) -> p g d", d=HD)), 16)
                else:
                    width = n * HD if kind == "values" else n
                    loaded[i].count(sp.dma_start(ws[i][:], v[:, :, col:col + width]), 16)

        @block.vector
        def _(dve):
            for kind, _, _, dst, *_ in jobs:
                if kind == "values":
                    zeroed.count(nc.vector.memset(dst[:], 0.0))

        @block.tensor
        def _(pe):
            for m, (i, operands, width, _) in enumerate(outs):
                pe.wait_ge(loaded[i].sem, loaded[i].at(loaded[i].n))
                if m >= 4:
                    pe.wait_ge(taken.sem, taken.at(m - 3))
                for k in range(DC):
                    lhs, rhs = operands(k)
                    ins = nc.tensor.matmul(core.bank(m % 4)[:, 0:width], lhs, rhs, start=k == 0, stop=k == DC - 1)
                ready.count(ins)

        @block.scalar
        def _(act):
            if zeroed.n:
                act.wait_ge(zeroed.sem, zeroed.at(zeroed.n))
            for m, (i, _, width, take) in enumerate(outs):
                act.wait_ge(ready.sem, ready.at(m + 1))
                taken.count(take(core.bank(m % 4)[:, 0:width]))


def rope_stage(core, st, chunks):
    nc = core.nc
    with ExitStack() as ctx, core.engines_block() as block:
        turned = core.sb("turned", [P, 2, LAT], ctx=ctx)
        straight = core.sb("straight", [P, 2, LAT], ctx=ctx)
        swapped, done, chain = core.counter("rope_swapped"), core.counter("rope_done"), core.counter("vector_chain")

        @block.tensor
        def _(pe):
            for i, x in enumerate(chunks):
                if i >= 4:
                    pe.wait_ge(done.sem, done.at(i - 3))
                swapped.count(nc.tensor.matmul(core.bank(i % 4)[:, 0:LAT], st.C("rot"), x, start=True, stop=True))

        @block.vector
        def _(dve):
            c = Chain(dve, chain)
            for i, x in enumerate(chunks):
                nc.vector.tensor_tensor(straight[:, i % 2], x, st.cos[:], ALU.mult)
                dve.wait_ge(swapped.sem, swapped.at(i + 1))
                c.ended(nc.vector.tensor_tensor(turned[:, i % 2], core.bank(i % 4)[:, 0:LAT], st.sin[:], ALU.mult))
                done.count(nc.vector.tensor_tensor(x, straight[:, i % 2], turned[:, i % 2], ALU.add))


def causal_stage(core, st, seen):
    nc = core.nc
    with core.engines_block() as block:
        @block.vector
        def _(dve):
            nc.vector.memset(seen[:, 0, P:LAT], NEG)
            nc.vector.memset(seen[:, 1, 0:P], 0.0)
            for b in (0, 1):
                nc.vector.tensor_copy(seen[:, b, b * P:(b + 1) * P], st.C("neg_after"))


def indexer_stage(core, st, iq, ik, iw, seen, keep):
    nc = core.nc
    with ExitStack() as ctx, core.engines_block() as block:
        score = core.sb("score", [P, 2, LAT], ctx=ctx)
        left = [core.sb(f"left{i}", [P, 2, LAT], ctx=ctx) for i in (0, 1)]
        part = core.sb("part", [P, 2, LAT], ctx=ctx)
        top = core.sb("top", [P, 2, 2, 8], ctx=ctx)
        dots, weighed, chain = core.counter("idx_dots"), core.counter("idx_weighed"), core.counter("vector_chain")

        @block.tensor
        def _(pe):
            for b in (0, 1):
                for h in range(IDX_HEADS):
                    n = b * IDX_HEADS + h
                    if n >= 4:
                        pe.wait_ge(weighed.sem, weighed.at(n - 3))
                    half = slice(h % 2 * HD, (h % 2 + 1) * HD)
                    dots.count(nc.tensor.matmul(core.bank(n % 4)[:, 0:LAT], iq[half, h // 2, b * P:(b + 1) * P], ik[half, 0], start=True, stop=True))

        @block.vector
        def _(dve):
            c = Chain(dve, chain)
            for b in (0, 1):
                for h in range(IDX_HEADS):
                    n = b * IDX_HEADS + h
                    dve.wait_ge(dots.sem, dots.at(n + 1))
                    ins = nc.vector.tensor_scalar(score[:, b] if h == 0 else part[:, h % 2], core.bank(n % 4)[:, 0:LAT], 0.0, iw[:, b, h:h + 1], ALU.max, ALU.mult)
                    weighed.count(ins)
                    dve.wait_ge(weighed.sem, weighed.at(n + 1))
                    if h:
                        c.ended(nc.vector.tensor_tensor(score[:, b], score[:, b], part[:, h % 2], ALU.add))
            c.ended(nc.vector.tensor_tensor(left[0][:], score[:], seen[:], ALU.add))
            for r in range(DSA_KEEP // 8):
                x, y = left[r % 2], left[1 - r % 2]
                for b in (0, 1):
                    ins = nc.vector.max(top[:, b, r % 2], x[:, b])
                c.ended(ins)
                for b in (0, 1):
                    ins = nc.vector.match_replace(y[:, b], top[:, b, r % 2], x[:, b], GONE)
                c.ended(ins)
            x = left[DSA_KEEP // 8 % 2]
            c.ended(nc.vector.tensor_scalar(keep[:], x[:], GONE / 2, NEG, ALU.is_ge, ALU.mult))
            nc.vector.tensor_tensor(keep[:], keep[:], seen[:], ALU.add)


def attention_stage(core, st, q, kd, v, neg, out, n_keys=LAT, gate=None, some=None, add=False):
    nc = core.nc
    items = [(b, hp) for b in (0, 1) for hp in range(HEADS // 2)]
    N = len(items)
    group = HEADS // KV_HEADS
    with ExitStack() as ctx, core.engines_block() as block:
        s = core.sb("scores", [P, 2, 2, n_keys], ctx=ctx)
        low = core.sb("low", [P, 2, 2], ctx=ctx)
        total = core.sb("total", [P, 2, 2], ctx=ctx)
        pt = core.sb("pt", [P, 2, 4, P], ctx=ctx)
        names = ("scored", "masked", "exped", "normed", "turned", "pt_ready", "summed", "out_taken")
        scored, masked, exped, normed, turned, pt_ready, summed, out_taken = (core.counter("at_" + n) for n in names)
        chain = core.counter("vector_chain")
        keys = lambda b: min(n_keys, (b + 1) * P)
        blocks = lambda b: [(i * P, min(P, keys(b) - i * P)) for i in range(-(-keys(b) // P))]
        SC = [core.psum[i].rearrange("p (h s) -> p h s", h=2) for i in (0, 1)]
        TR, OUT = [core.bank(4), core.bank(5)], [core.bank(6), core.bank(7)]

        @block.tensor
        def _(pe):
            for n in range(N + 2):
                if n < N:
                    b, hp = items[n]
                    if n >= 2:
                        pe.wait_ge(masked.sem, masked.at(n - 1))
                    for h in (0, 1):
                        half = slice(h * HD, (h + 1) * HD)
                        ins = nc.tensor.matmul(SC[n % 2][:, h, 0:keys(b)], q[half, hp, b * P:(b + 1) * P],
                                               kd[half, hp * 2 // group, 0:keys(b)], start=True, stop=True)
                    scored.count(ins)
                if 0 <= n - 1 < N:
                    m = n - 1
                    b, hp = items[m]
                    pe.wait_ge(normed.sem, normed.at(m + 1))
                    if m >= 2:
                        pe.wait_ge(pt_ready.sem, pt_ready.at(m - 1))
                    for h in (0, 1):
                        for i, (at, w) in enumerate(blocks(b)):
                            ins = nc.tensor.transpose(TR[m % 2][0:w, (h * 2 + i) * P:(h * 2 + i + 1) * P], s[:, m % 2, h, at:at + w], st.C("ident"))
                    turned.count(ins)
                if 0 <= n - 2:
                    m = n - 2
                    b, hp = items[m]
                    pe.wait_ge(pt_ready.sem, pt_ready.at(m + 1))
                    if m >= 2:
                        pe.wait_ge(out_taken.sem, out_taken.at(m - 1))
                    parts = [(h, i, w) for h in (0, 1) for i, (_, w) in enumerate(blocks(b))]
                    for j, (h, i, w) in enumerate(parts):
                        ins = nc.tensor.matmul(OUT[m % 2][:, 0:P], v[0:w, i, hp * 2 // group, (1 - h) * HD:(1 - h) * HD + P], pt[0:w, m % 2, h * 2 + i],
                                               start=j == 0, stop=j == len(parts) - 1)
                    summed.count(ins)

        @block.scalar
        def _(act):
            for n in range(N + 2):
                if n < N:
                    b, hp = items[n]
                    act.wait_ge(masked.sem, masked.at(n + 1))
                    if n >= 2:
                        act.wait_ge(normed.sem, normed.at(n - 1))
                    for h in (0, 1):
                        x = s[:, n % 2, h, 0:keys(b)]
                        ins = nc.scalar.activation(x, x, ACT.Exp, bias=low[:, n % 2, h:h + 1], accum_out=total[:, n % 2, h:h + 1])
                    exped.count(ins)
                if 0 <= n - 1 < N:
                    m = n - 1
                    b, hp = items[m]
                    act.wait_ge(turned.sem, turned.at(m + 1))
                    if m >= 2:
                        act.wait_ge(summed.sem, summed.at(m - 1))
                    nb, w = len(blocks(b)), blocks(b)[0][1]
                    ins = nc.scalar.activation(pt[0:w, m % 2].rearrange("p (h i) t -> p h i t", h=2)[:, :, 0:nb],
                                               TR[m % 2][0:w].rearrange("p (h i t) -> p h i t", h=2, i=2)[:, :, 0:nb], ACT.Copy)
                    pt_ready.count(ins)
                if 0 <= n - 2 and not add:
                    m = n - 2
                    b, hp = items[m]
                    act.wait_ge(summed.sem, summed.at(m + 1))
                    out_taken.count(nc.scalar.activation(out[:, hp, b * P:(b + 1) * P], OUT[m % 2][:, 0:P], ACT.Copy))

        @block.vector
        def _(dve):
            c = Chain(dve, chain)
            for n in range(N + 3):
                if n < N:
                    b, hp = items[n]
                    K = keys(b)
                    x = s[:, n % 2, :, 0:K]
                    dve.wait_ge(scored.sem, scored.at(n + 1))
                    if n >= 2:
                        dve.wait_ge(turned.sem, turned.at(n - 1))
                    c.ended(nc.vector.scalar_tensor_tensor(x, SC[n % 2][:, :, 0:K], HD ** -0.5,
                                                          neg[:, b, 0:K].unsqueeze(1).to_broadcast([P, 2, K]), ALU.mult, ALU.add))
                    masked.count(nc.vector.tensor_reduce(low[:, n % 2], x, AX, ALU.max, negate=True))
                if 0 <= n - 1 < N:
                    m = n - 1
                    b, hp = items[m]
                    K = keys(b)
                    x = s[:, m % 2, :, 0:K]
                    r = total[:, m % 2]
                    dve.wait_ge(exped.sem, exped.at(m + 1))
                    c.ended(nc.vector.reciprocal(r, r))
                    if gate is not None:
                        c.ended(nc.vector.tensor_tensor(r, r, gate[:, b, 2 * hp:2 * hp + 2], ALU.mult))
                    if some is not None:
                        c.ended(nc.vector.tensor_tensor(x, x, some[:, b, 0:K].unsqueeze(1).to_broadcast([P, 2, K]), ALU.mult))
                    normed.count(nc.vector.tensor_tensor(x, x, r.unsqueeze(2).to_broadcast([P, 2, K]), ALU.mult))
                if 0 <= n - 3 and add:
                    m = n - 3
                    b, hp = items[m]
                    dve.wait_ge(summed.sem, summed.at(m + 1))
                    y = out[:, hp, b * P:(b + 1) * P]
                    out_taken.count(nc.vector.tensor_tensor(y, y, OUT[m % 2][:, 0:P], ALU.add))


def swiglu_stage(core, st, wg, wu, wd, beside):
    nc = core.nc
    fc = wg.shape[1] // P
    n_it = fc // 2
    assert beside.groups == n_it + 1
    with ExitStack() as outer:
        h = core.sb("swiglu_h", [P, fc, LAT], ctx=outer)
        with ExitStack() as ctx, core.engines_block() as block:
            tiles = k_tiles(wg, 256, 2, (0, 1), lambda it: it * 256) + k_tiles(wu, 256, 2, (2, 3), lambda it: it * 256)
            g = Gemm(core, ctx, "up", tiles, {o: o for o in range(4)}, 256)
            silu = core.sb("silu", [P, 2, LAT], ctx=ctx)
            beside.open(ctx)

            @block.gpsimd
            def _(pool):
                beside.loads(pool)

            @block.sync
            def _(sp):
                rounds(sp, n_it, lambda it, first: g.fetch_round(sp, it, first))

            @block.tensor
            def _(pe):
                rounds(pe, n_it, lambda it, first: g.matmul_round(pe, it, lambda k: st.H[:, k, LATS], first))

            @block.scalar
            def _(act):
                def body(it, first):
                    for o in (0, 1):
                        bank = g.wait_bank(act, o, it)
                        if not first:
                            act.wait_ge(g.free[2 + o].sem, g.free[2 + o].at(it))
                        g.bank_taken(nc.scalar.activation(silu[:, o], bank[:, 0:LAT], ACT.Silu), o)
                rounds(act, n_it, body)

            @block.vector
            def _(dve):
                def body(it, first):
                    for o in (0, 1):
                        bank = g.wait_bank(dve, 2 + o, it)
                        dve.wait_ge(g.free[o].sem, g.free[o].at(it + 1))
                        g.bank_taken(nc.vector.tensor_tensor(chunk_of(h, it * 2 + o), silu[:, o], bank[:, 0:LAT], ALU.mult), 2 + o)
                    if first:
                        beside.add_group(dve, 0)
                    beside.add_group(dve, it + 1)
                beside.empty()
                rounds(dve, n_it, body)
                beside.settle()
            g.settle(n_it)
        add_gated(core, st, "down", wd, lambda k: h[:, k], 40, width=256)


def sparse_layer(core, st, beside):
    nc, A = core.nc, st.A
    norm_in(core, st, 0, 0, (0,))
    with ExitStack() as scope:
        sb = lambda name, shape: core.sb(name, shape, ctx=scope)
        q, kd, v = sb("q", [P, HEADS // 2, LAT]), sb("kd", [P, KV_HEADS, LAT]), sb("v", [P, 2, KV_HEADS, 3 * HD])
        iq, ik, iw = sb("iq", [P, IDX_HEADS // 2, LAT]), sb("ik", [P, 1, LAT]), sb("iw", [P, 2, IDX_HEADS])
        seen, keep = sb("seen", [P, 2, LAT]), sb("keep", [P, 2, LAT])
        w = A["a_w_in_2"][0]
        at = np.cumsum([0, HEADS * HD, KV_HEADS * HD, KV_HEADS * HD, IDX_HEADS * HD, HD])
        gemm_stage(core, st, "in", w, None, lambda k: st.H[:, k, LATS],
                   lambda act, c, bank: nc.scalar.activation(q[:, c] if c < 8 else iq[:, c - 8], bank[:, 0:LAT], ACT.Copy),
                   sections=[0, 512, int(at[3])])
        small_stage(core, st, w, [("pair", int(at[1]), KV_HEADS, kd), ("values", int(at[2]), KV_HEADS, v), ("pair", int(at[4]), 1, ik),
                                  ("tokens", int(at[5]), IDX_HEADS, iw, ACT.Copy, IDX_HEADS ** -0.5 * HD ** -0.5)])
        rope_stage(core, st, [q[:, i] for i in range(8)] + [kd[:, i] for i in range(4)] + [iq[:, i] for i in range(4)] + [ik[:, 0]])
        causal_stage(core, st, seen)
        indexer_stage(core, st, iq, ik, iw, seen, keep)
        attention_stage(core, st, q, kd, v, keep, st.Y[:, :, LATS])
        add_gated(core, st, "in", A["a_w_out_2"][0], lambda k: st.Y[:, k, LATS], 16)
    norm_in(core, st, 2, 24, (0,))
    swiglu_stage(core, st, A["ffn_w_gate_2"][0], A["ffn_w_up_2"][0], A["ffn_w_down_2"][0], beside)


def compress_stage(core, st, jobs):
    nc = core.nc
    n_l = CMP_LEN // 2
    with ExitStack() as ctx, core.engines_block() as block:
        loaded = [core.counter(f"cmp_weights{i}") for i in (0, 1)]
        unfolded, hid, hid_done, out, zeroed = (core.counter("cmp_" + n) for n in ("unfolded", "hidden", "hidden_done", "out", "zeroed"))
        chain = core.counter("vector_chain")
        w1s = [core.sb(f"cmp_w1_{i}", [P, n_l, CMP_HIDDEN], ctx=ctx) for i in (0, 1)]
        w2s = [core.sb(f"cmp_w2_{i}", [P, 2, 2, HD], ctx=ctx) for i in (0, 1)]
        blocks = [core.sb(f"cmp_blocks{i}", [P, n_l, KV_HEADS, N_CMP], ctx=ctx) for i in (0, 1)]
        hidden = [core.sb(f"cmp_hidden{i}", [P, 2, KV_HEADS * N_CMP], ctx=ctx) for i in (0, 1)]

        @block.sync
        def _(sp):
            for i, (x, pe_name, w1, w2, dst, by_token) in enumerate(jobs):
                loaded[i].count(sp.dma_start(w1s[i][:], w1.rearrange("(l p) n -> p l n", p=P)), 16)
                for a in (0, 1):
                    loaded[i].count(sp.dma_start(w2s[i][:, :, a], w2.rearrange("(c p) d -> p c d", p=P)), 16)

        @block.vector
        def _(dve):
            c = Chain(dve, chain)
            for i, (x, pe_name, *_, dst, by_token) in enumerate(jobs):
                if by_token:
                    nc.vector.memset(dst[:], 0.0)
                else:
                    nc.vector.memset(dst[:], 0.0)
                for half in (0, 1):
                    rows = slice(half * HD, (half + 1) * HD)
                    for l in range(n_l):
                        at = 2 * l + half
                        src = x[rows, :, at:at + (N_CMP - 1) * CMP_STRIDE + 1:CMP_STRIDE]
                        ins = nc.vector.tensor_scalar(blocks[i][rows, l], src, st.V(pe_name, l)[rows], None, ALU.add)
                unfolded.count(ins)

        @block.tensor
        def _(pe):
            for i, (*_, dst, by_token) in enumerate(jobs):
                pe.wait_ge(loaded[i].sem, loaded[i].at(48))
                pe.wait_ge(unfolded.sem, unfolded.at(i + 1))
                for c in (0, 1):
                    for l in range(n_l):
                        ins = nc.tensor.matmul(core.bank(2 * i + c)[:, 0:KV_HEADS * N_CMP], w1s[i][:, l, c * P:(c + 1) * P],
                                               blocks[i][:, l].rearrange("p g n -> p (g n)"), start=l == 0, stop=l == n_l - 1)
                hid.count(ins)
            for i, (*_, dst, by_token) in enumerate(jobs):
                pe.wait_ge(hid_done.sem, hid_done.at(i + 1))
                bank = core.bank(4 + i)
                if not by_token:
                    for c in (0, 1):
                        ins = nc.tensor.matmul(bank[:, 0:KV_HEADS * N_CMP], w2s[i][:, c].rearrange("p a d -> p (a d)"), hidden[i][:, c], start=c == 0, stop=c == 1)
                else:
                    for g in range(KV_HEADS):
                        for c in (0, 1):
                            ins = nc.tensor.matmul(bank[0:N_CMP, g * HD:(g + 1) * HD], hidden[i][:, c, g * N_CMP:(g + 1) * N_CMP], w2s[i][:, c, 0],
                                                   start=c == 0, stop=c == 1)
                out.count(ins)

        @block.scalar
        def _(act):
            for i in (0, 1):
                act.wait_ge(hid.sem, hid.at(i + 1))
                for c in (0, 1):
                    ins = nc.scalar.activation(hidden[i][:, c], core.bank(2 * i + c)[:, 0:KV_HEADS * N_CMP], ACT.Gelu_apprx_tanh)
                hid_done.count(ins)
            for i, (*_, dst, by_token) in enumerate(jobs):
                act.wait_ge(out.sem, out.at(i + 1))
                bank = core.bank(4 + i)
                if by_token:
                    nc.scalar.activation(dst[0:N_CMP, 0, :, HD:2 * HD], bank[0:N_CMP, 0:KV_HEADS * HD].rearrange("p (g d) -> p g d", g=KV_HEADS), ACT.Copy)
                else:
                    nc.scalar.activation(dst[:, :, 0:N_CMP], bank[:, 0:KV_HEADS * N_CMP].rearrange("p (g n) -> p g n", g=KV_HEADS), ACT.Copy)


class Route:

    def __init__(self, core, scope):
        sb = lambda name, shape, dtype=F32: core.sb(name, shape, dtype, ctx=scope)
        self.share = sb("share", [P, 2, EXPERTS])
        self.goes = sb("goes", [P, 2, EXPERTS])
        self.seat = sb("seat", [P, 2, EXPERTS])
        self.most = sb("most", [P, 1], I32)
        self.seated = sb("seated", [P, EXPERTS, DC, SEATS])
        self.back = sb("back", [SEATS, EXPERTS, LAT])


def router_stage(core, st, route):
    nc = core.nc
    E = EXPERTS
    with ExitStack() as ctx, core.engines_block() as block:
        w = core.sb("w_router", [P, DC, E], ctx=ctx)
        logit, rank = (core.sb(n, [P, 2, E], ctx=ctx) for n in ("logit", "rank"))
        low, total = (core.sb(n, [P, 2, 1], ctx=ctx) for n in ("low", "total"))
        most = core.sb("most_f32", [P, 1], ctx=ctx)
        expo = route.share
        loaded, logits, low_ready, exped, chosen, counted = (
            core.counter("route_" + n) for n in ("loaded", "logits", "low_ready", "exped", "chosen", "counted"))
        chain = core.counter("vector_chain")

        @block.sync
        def _(sp):
            loaded.count(sp.dma_start(w[:], st.A["moe_w_router_2"][0].rearrange("(k p) e -> p k e", p=P)), 16)

        @block.tensor
        def _(pe):
            pe.wait_ge(loaded.sem, loaded.at(16))
            for b in (0, 1):
                for k in range(DC):
                    ins = nc.tensor.matmul(core.bank(b)[:, 0:E], st.H[:, k, CTX + b * P:CTX + (b + 1) * P], w[:, k], start=k == 0, stop=k == DC - 1)
            logits.count(ins)
            pe.wait_ge(chosen.sem, chosen.at(1))
            nc.tensor.matmul(core.bank(2)[:, 0:E], st.C("earlier"), route.goes[:, 0], start=True, stop=True)
            nc.tensor.matmul(core.bank(3)[:, 0:E], st.C("ones"), route.goes[:, 0], start=True, stop=False)
            nc.tensor.matmul(core.bank(3)[:, 0:E], st.C("earlier"), route.goes[:, 1], start=False, stop=True)
            for b in (0, 1):
                ins = nc.tensor.matmul(core.bank(4)[:, 0:E], st.C("ones"), route.goes[:, b], start=b == 0, stop=b == 1)
            counted.count(ins)

        @block.scalar
        def _(act):
            act.wait_ge(low_ready.sem, low_ready.at(1))
            for b in (0, 1):
                ins = nc.scalar.activation(expo[:, b], logit[:, b], ACT.Exp, bias=low[:, b])
            exped.count(ins)

        @block.vector
        def _(dve):
            c = Chain(dve, chain)
            dve.wait_ge(logits.sem, logits.at(1))
            nc.vector.memset(rank[:], 0.0)
            for b in (0, 1):
                c.ended(nc.vector.tensor_copy(logit[:, b], core.bank(b)[:, 0:E]))
            low_ready.count(nc.vector.tensor_reduce(low[:], logit[:], AX, ALU.max, negate=True))
            for j in range(E):
                for b in (0, 1):
                    x = logit[:, b, j:j + 1]
                    ins = nc.vector.scalar_tensor_tensor(rank[:, b], logit[:, b], x, rank[:, b], ALU.is_lt, ALU.add)
                c.ended(ins)
                if j + 1 < E:
                    for b in (0, 1):
                        x, later = logit[:, b, j:j + 1], rank[:, b, j + 1:]
                        ins = nc.vector.scalar_tensor_tensor(later, logit[:, b, j + 1:], x, later, ALU.is_equal, ALU.add)
                    c.ended(ins)
            chosen.count(nc.vector.tensor_scalar(route.goes[:], rank[:], 2.0, None, ALU.is_lt))
            dve.wait_ge(chosen.sem, chosen.at(1))
            dve.wait_ge(exped.sem, exped.at(1))
            c.ended(nc.vector.tensor_tensor(expo[:], expo[:], route.goes[:], ALU.mult))
            c.ended(nc.vector.tensor_reduce(total[:], expo[:], AX, ALU.add))
            c.ended(nc.vector.reciprocal(total[:], total[:]))
            nc.vector.tensor_tensor(expo[:], expo[:], total[:].to_broadcast([P, 2, E]), ALU.mult)
            dve.wait_ge(counted.sem, counted.at(1))
            for b in (0, 1):
                nc.vector.tensor_copy(route.seat[:, b], core.bank(2 + b)[:, 0:E])
            c.ended(nc.vector.tensor_reduce(most[:], core.bank(4)[:, 0:E], AX, ALU.max))
            nc.vector.tensor_copy(route.most[:], most[:])
            nc.vector.memset(st.Y[:, :, LATS], 0.0)


def seat_stage(core, st, route, turn):
    nc = core.nc
    E = EXPERTS
    with ExitStack() as ctx, core.engines_block() as block:
        tokens = core.sb("tokens", [P, 2, D], ctx=ctx)
        sits = core.sb("sits", [P, 2, E, SEATS], ctx=ctx)
        weighed = core.sb("weighed", [P, 2, E, SEATS], ctx=ctx)
        at = core.sb("at", [P, 2, E], ctx=ctx)
        turned, copied, sits_ready, weighed_ready, gathered, stored = (
            core.counter("seat_" + n) for n in ("turned", "copied", "sits_ready", "weighed_ready", "gathered", "stored"))
        chain = core.counter("vector_chain")
        picks = [(k, g) for k in range(DC) for g in (0, 1)]

        @block.tensor
        def _(pe):
            for n in range(4):
                b, k0 = n // 2, n % 2 * 4
                for j in range(4):
                    ins = nc.tensor.transpose(core.bank(n)[:, j * P:(j + 1) * P], st.H[:, k0 + j, CTX + b * P:CTX + (b + 1) * P], st.C("ident"))
                turned.count(ins)
            pe.wait_ge(copied.sem, copied.at(4))
            pe.wait_ge(sits_ready.sem, sits_ready.at(1))
            for n, (k, g) in enumerate(picks):
                if n >= 4:
                    pe.wait_ge(stored.sem, stored.at(n - 3))
                for b in (0, 1):
                    ins = nc.tensor.matmul(core.bank(n % 4), tokens[:, b, k * P:(k + 1) * P], sits[:, b, g * 4:(g + 1) * 4].rearrange("p e s -> p (e s)"),
                                           start=b == 0, stop=b == 1)
                gathered.count(ins)
            pe.wait_ge(weighed_ready.sem, weighed_ready.at(1))
            for n in range(4):
                for j in range(4):
                    e, b = n * 2 + j // 2, j % 2
                    ins = nc.tensor.transpose(core.bank(4 + n)[:, j * P:(j + 1) * P], weighed[:, b, e], st.C("ident"))
                turned.count(ins)

        @block.vector
        def _(dve):
            c = Chain(dve, chain)
            c.ended(nc.vector.tensor_scalar(at[:], route.seat[:], float(-turn * SEATS), None, ALU.add))
            for n in range(4):
                dve.wait_ge(turned.sem, turned.at(n + 1))
                copied.count(nc.vector.tensor_copy(tokens[:, n // 2, n % 2 * 512:(n % 2 + 1) * 512], core.bank(n)))
            for b in (0, 1):
                for e in range(E):
                    ins = nc.vector.tensor_scalar(sits[:, b, e], st.C("column"), at[:, b, e:e + 1], route.goes[:, b, e:e + 1], ALU.is_equal, ALU.mult)
            sits_ready.count(ins)
            dve.wait_ge(sits_ready.sem, sits_ready.at(1))
            for b in (0, 1):
                for e in range(E):
                    ins = nc.vector.tensor_scalar(weighed[:, b, e], sits[:, b, e], route.share[:, b, e:e + 1], None, ALU.mult)
            weighed_ready.count(ins)
            for n in range(4):
                dve.wait_ge(turned.sem, turned.at(4 + n + 1))
                nc.vector.tensor_copy(route.back[:, 2 * n:2 * n + 2].rearrange("p e t -> p (e t)"), core.bank(4 + n))

        @block.scalar
        def _(act):
            for n, (k, g) in enumerate(picks):
                act.wait_ge(gathered.sem, gathered.at(n + 1))
                stored.count(nc.scalar.activation(route.seated[:, g * 4:(g + 1) * 4, k], core.bank(n % 4).rearrange("p (e s) -> p e s", e=4), ACT.Copy))


def moe_stage(core, st, route):
    nc, A = core.nc, st.A
    WIDE = 512
    groups = FE // WIDE
    parts = 2
    kc = DC // parts
    per = 1
    DOWN = 7
    turns = FEC // per // DOWN
    with ExitStack() as ctx, core.engines_block() as block:
        x = core.sb("expert_x", [P, DC, SEATS], ctx=ctx)
        silu = core.sb("silu", [SEATS, WIDE], ctx=ctx)
        rows = core.sb("hidden_rows", [SEATS, WIDE], ctx=ctx)
        h = core.sb("hidden", [P, FEC, SEATS], ctx=ctx)
        y = core.sb("expert_y", [SEATS, D], ctx=ctx)
        up_ring = core.sb("up_ring", [P, 2 * parts, kc, WIDE], ctx=ctx)
        down_ring = core.sb("down_ring", [P, DOWN, per, D], ctx=ctx)
        up_in = [core.counter(f"moe_up{s}_in") for s in range(2 * parts)]
        up_free = [core.counter(f"moe_up{s}_free") for s in range(2 * parts)]
        down_in = [core.counter(f"moe_down{s}_in") for s in range(DOWN)]
        down_free = [core.counter(f"moe_down{s}_free") for s in range(DOWN)]
        names = ("x_ready", "silu_done", "rows_ready", "turned", "h_copied", "y_copied", "scattered", "y_added")
        x_ready, silu_done, rows_ready, turned, h_copied, y_copied, scattered, y_added = (core.counter("moe_" + n) for n in names)
        GATE, UP, TURN, DN, SC = core.bank(0), core.bank(1), core.bank(2), (core.bank(4), core.bank(5)), (core.bank(3), core.bank(6), core.bank(7))
        w_up = [A[n][0].rearrange("e (k p) n -> p e k n", p=P) for n in ("moe_w_gate_2", "moe_w_up_2")]
        w_down = A["moe_w_down_2"][0].rearrange("e (k p) n -> p e k n", p=P)
        gate_done, up_done, down_done = up_free[parts - 1], up_free[2 * parts - 1], down_free[DOWN - 1]
        START = 1

        @block.sync
        def _(sp):
            with sp.Fori(0, EXPERTS) as e:
                with sp.Fori(0, groups) as i:
                    for s in range(2 * parts):
                        k0 = s % parts * kc
                        sp.wait_ge(up_free[s].sem, up_free[s].at(START + e * groups + i))
                        src = w_up[s // parts][:, ds(e, 1), k0:k0 + kc, ds(i * WIDE, WIDE)]
                        sp.dma_start(up_ring[:, s], src.rearrange("p e k n -> p (e k) n")).then_inc(up_in[s].sem, 16)
                for n in range(turns * DOWN):
                    s, r = n % DOWN, n // DOWN
                    sp.wait_ge(down_free[s].sem, down_free[s].at(START + e * turns + r))
                    src = w_down[:, ds(e, 1), n * per:(n + 1) * per, :]
                    sp.dma_start(down_ring[:, s], src.rearrange("p e k n -> p (e k) n")).then_inc(down_in[s].sem, 16)

        @block.gpsimd
        def _(pool):
            with pool.Fori(0, EXPERTS) as e:
                pool.wait_ge(up_done.sem, up_done.at(START + e * groups))
                nc.gpsimd.tensor_copy(x[:].rearrange("p k s -> p (k s)"),
                                      route.seated[:, ds(e, 1)].rearrange("p e k s -> p (e k s)")).then_inc(x_ready.sem, 1)

        @block.tensor
        def _(pe):
            for c in (*up_free, *down_free):
                pe.sem_inc(c.sem, START)

            def turn():
                for j in range(WIDE // P):
                    ins = nc.tensor.transpose(TURN[:, j * P:(j + 1) * P], rows[:, j * P:(j + 1) * P], st.C("ident"))
                ins.then_inc(turned.sem, 1)

            def product(bank, it, slots):
                for s in slots:
                    pe.wait_ge(up_in[s].sem, up_in[s].at(16 * it + 16))
                    for k in range(kc):
                        k0 = s % parts * kc
                        ins = nc.tensor.matmul(bank, x[:, k0 + k], up_ring[:, s, k], start=k0 + k == 0, stop=k0 + k == DC - 1)
                    ins.then_inc(up_free[s].sem, 1)

            with pe.Fori(0, EXPERTS) as e:
                pe.wait_ge(x_ready.sem, x_ready.at(e + 1))

                def group(i, first):
                    it = e * groups + i
                    pe.wait_ge(silu_done.sem, silu_done.at(START + it))
                    product(GATE, it, range(parts))
                    pe.wait_ge(rows_ready.sem, rows_ready.at(START + it))
                    if not first:
                        pe.wait_ge(h_copied.sem, h_copied.at(START + it - 1))
                        turn()
                    product(UP, it, range(parts, 2 * parts))
                rounds(pe, groups, group)
                pe.wait_ge(rows_ready.sem, rows_ready.at(START + e * groups + groups))
                pe.wait_ge(h_copied.sem, h_copied.at(START + e * groups + groups - 1))
                turn()
                pe.wait_ge(y_copied.sem, y_copied.at(2 * START + 2 * e))
                for c in range(FEC):
                    n, q = c // per, c % per
                    s = n % DOWN
                    if q == 0:
                        pe.wait_ge(down_in[s].sem, down_in[s].at(16 * (e * turns + n // DOWN) + 16))
                    if c % (WIDE // P) == 0:
                        pe.wait_ge(h_copied.sem, h_copied.at(START + e * groups + c // (WIDE // P) + 1))
                    for half in (0, 1):
                        ins = nc.tensor.matmul(DN[half], h[:, c], down_ring[:, s, q, half * 512:(half + 1) * 512], start=c == 0, stop=c == FEC - 1)
                    if q == per - 1:
                        ins.then_inc(down_free[s].sem, 1)
                pe.wait_ge(y_copied.sem, y_copied.at(2 * START + 2 * e + 2))
                for r in range(DC // 2):
                    pe.wait_ge(y_added.sem, y_added.at(START + e * (DC // 2) + max(0, r - 2)))
                    for j in (0, 1):
                        k = 2 * r + j
                        ins = nc.tensor.matmul(SC[r % 3][:, j * LAT:(j + 1) * LAT], y[:, k * P:(k + 1) * P], chunk_of(route.back, e), start=True, stop=True)
                    ins.then_inc(scattered.sem, 1)

        @block.scalar
        def _(act):
            for c, by in ((silu_done, START), (h_copied, START), (y_copied, START)):
                act.sem_inc(c.sem, by)

            def copy(i, it):
                act.wait_ge(turned.sem, turned.at(it + 1))
                nc.scalar.activation(h[:, ds(i * (WIDE // P), WIDE // P)].rearrange("p c s -> p (c s)"), TURN, ACT.Copy).then_inc(h_copied.sem, 1)

            with act.Fori(0, EXPERTS) as e:
                def group(i, first):
                    it = e * groups + i
                    act.wait_ge(gate_done.sem, gate_done.at(START + it + 1))
                    act.wait_ge(rows_ready.sem, rows_ready.at(START + it))
                    nc.scalar.activation(silu[:], GATE, ACT.Silu).then_inc(silu_done.sem, 1)
                    if not first:
                        copy(i - 1, it - 1)
                rounds(act, groups, group)
                copy(groups - 1, e * groups + groups - 1)
                act.wait_ge(down_done.sem, down_done.at(START + e * turns + turns))
                nc.scalar.activation(y[:, 0:512], DN[0], ACT.Copy).then_inc(y_copied.sem, 1)

        @block.vector
        def _(dve):
            for c, by in ((rows_ready, START), (y_added, START), (y_copied, START)):
                dve.sem_inc(c.sem, by)
            with dve.Fori(0, EXPERTS) as e:
                with dve.Fori(0, groups) as i:
                    it = e * groups + i
                    dve.wait_ge(silu_done.sem, silu_done.at(START + it + 1))
                    dve.wait_ge(up_done.sem, up_done.at(START + it + 1))
                    nc.vector.tensor_tensor(rows[:], silu[:], UP, ALU.mult).then_inc(rows_ready.sem, 1)
                dve.wait_ge(down_done.sem, down_done.at(START + e * turns + turns))
                nc.vector.tensor_copy(y[:, 512:D], DN[1]).then_inc(y_copied.sem, 1)
                for r in range(DC // 2):
                    dve.wait_ge(scattered.sem, scattered.at(e * (DC // 2) + r + 1))
                    out = st.Y[:, 2 * r:2 * r + 2, LATS]
                    nc.vector.tensor_tensor(out, out, SC[r % 3].rearrange("p (k t) -> p k t", k=2), ALU.add).then_inc(y_added.sem, 1)

        n = EXPERTS * groups
        for c, total in ((x_ready, EXPERTS), (silu_done, START + n), (rows_ready, START + n), (turned, n),
                         (h_copied, START + n), (y_copied, 2 * START + 2 * EXPERTS), (scattered, EXPERTS * DC // 2),
                         (y_added, START + EXPERTS * DC // 2), *((c, 16 * n) for c in up_in), *((c, START + n) for c in up_free),
                         *((c, 16 * EXPERTS * turns) for c in down_in), *((c, START + EXPERTS * turns) for c in down_free)):
            c.n += total


def gated_stage(core, st, gate):
    nc = core.nc
    with core.engines_block() as block:
        @block.vector
        def _(dve):
            for k in range(DC):
                x = st.X[:, k, LATS]
                nc.vector.scalar_tensor_tensor(x, st.Y[:, k, LATS], st.mod[:, gate + k, 0:1], x, ALU.mult, ALU.add)


def branch_layer(core, st, kv_sums, sums):
    nc, A = core.nc, st.A
    with ExitStack() as scope:
        sb = lambda name, shape: core.sb(name, shape, ctx=scope)
        pair = lambda name: sb(name, [P, KV_HEADS, LAT])
        value = lambda name: sb(name, [P, 2, KV_HEADS, 3 * HD])
        k_cmp, v_cmp, k_slc, k_win = pair("k_cmp"), pair("v_cmp"), pair("k_slc"), pair("k_win")
        v_slc, v_win = value("v_slc"), value("v_win")
        kc, vc = sb("kc", [P, KV_HEADS, CMP_STRIDE]), sb("vc", [P, 1, KV_HEADS, 3 * HD])
        q, gates, seen = sb("q", [P, HEADS // 2, LAT]), sb("gates", [P, 2, 3 * HEADS]), sb("seen", [P, 2, LAT])
        mod_stage(core, st, kv_sums, [(0, 0, ("kv_gain_2", 0), 8, 1)])
        norm_in(core, st, 0, 0, (0,))
        w = KV_HEADS * HD
        small_stage(core, st, A["w_kv_2"], [("pair", 0, KV_HEADS, k_cmp), ("pair", w, KV_HEADS, v_cmp)])
        small_stage(core, st, A["w_kv_2"], [("pair", 2 * w, KV_HEADS, k_slc), ("values", 3 * w, KV_HEADS, v_slc),
                                            ("pair", 4 * w, KV_HEADS, k_win), ("values", 5 * w, KV_HEADS, v_win)])
        rope_stage(core, st, [x[:, i] for x in (k_cmp, k_slc, k_win) for i in range(KV_HEADS)])
        compress_stage(core, st, [(k_cmp, "cmp_pe_k_2", A["cmp_w1_k_2"], A["cmp_w2_k_2"], kc, False),
                                  (v_cmp, "cmp_pe_v_2", A["cmp_w1_v_2"], A["cmp_w2_v_2"], vc, True)])
        ada(core, st, sums, 1)
        norm_in(core, st, 0, 0, (0,))
        gemm_stage(core, st, "in", A["b_w_q_2"][0], D, lambda k: st.H[:, k, LATS],
                   lambda act, c, bank: nc.scalar.activation(chunk_of(q, c), bank[:, 0:LAT], ACT.Copy))
        small_stage(core, st, A["b_w_q_2"][0], [("tokens", D, 3 * HEADS, gates, ACT.Sigmoid, 1.0)])
        rope_stage(core, st, [q[:, i] for i in range(8)])
        causal_stage(core, st, seen)
        out = st.Y[:, :, LATS]
        branch = lambda i: gates[:, :, i:3 * HEADS:3]
        cmp_neg, cmp_seen = (st.C(n).rearrange("p (b n) -> p b n", b=2) for n in ("cmp_neg", "cmp_seen"))
        attention_stage(core, st, q, kc, vc, cmp_neg, out, n_keys=CMP_STRIDE, gate=branch(0), some=cmp_seen)
        attention_stage(core, st, q, k_slc, v_slc, seen, out, gate=branch(1), add=True)
        attention_stage(core, st, q, k_win, v_win, seen, out, gate=branch(2), add=True)
        add_gated(core, st, "in", A["b_w_out_2"][0], lambda k: st.Y[:, k, LATS], 16)


def moe_layer(core, st):
    norm_in(core, st, 2, 24, (0,))
    with ExitStack() as scope:
        route = Route(core, scope)
        router_stage(core, st, route)
        seat_stage(core, st, route, 0)
        moe_stage(core, st, route)
        with core.rarely(route.most[0:1, 0:1], SEATS):
            seat_stage(core, st, route, 1)
            moe_stage(core, st, route)
    gated_stage(core, st, 40)
    norm_stage(core, st, [(lambda k: st.X[:, k, LATS], lambda k: st.V("final_gain_2", k), None, lambda k: st.Y[:, k, LATS])])


def finish_stage(core, st, out):
    nc = core.nc
    with ExitStack() as ctx, core.engines_block() as block:
        tokens = core.sb("tokens_out", [P, 2, D], ctx=ctx)
        turned, copied, stored = core.counter("turned"), core.counter("turned_copied"), core.counter("stored")

        @block.tensor
        def _(pe):
            for g in range(4):
                t, k0 = g // 2, g % 2 * 4
                for j in range(4):
                    ins = nc.tensor.transpose(core.bank(g)[:, j * P:(j + 1) * P], st.Y[:, k0 + j, CTX + t * P:CTX + (t + 1) * P], st.C("ident"))
                turned.count(ins)

        @block.vector
        def _(dve):
            for g in range(4):
                dve.wait_ge(turned.sem, turned.at(g + 1))
                copied.count(nc.vector.tensor_copy(tokens[:, g // 2, g % 2 * 512:(g % 2 + 1) * 512], core.bank(g)))

        @block.sync
        def _(sp):
            for t in (0, 1):
                sp.wait_ge(copied.sem, copied.at(2 * t + 2))
                stored.count(sp.dma_start(out[0, t * P:(t + 1) * P, :], tokens[:, t, :]), 16)
            sp.wait_ge(stored.sem, stored.at(stored.n))


def norm_in(core, st, slot, shift, streams):
    seg = (SEGS["lat"], SEGS["ctx"])
    norm_stage(core, st, [(lambda k, v=v: st.X[:, k, seg[v]], lambda k, v=v: st.coef[:, v, slot, k:k + 1],
                           lambda k, v=v: st.mod[:, shift + k, v:v + 1], lambda k, v=v: st.H[:, k, seg[v]]) for v in streams])


def norm_out(core, st, slot, src, streams):
    seg = (SEGS["lat"], SEGS["ctx"])
    norm_stage(core, st, [(lambda k, v=v: src[:, k, seg[v]], lambda k, v=v: st.coef[:, v, slot, k:k + 1],
                           lambda k, v=v: st.X[:, k, seg[v]], lambda k, v=v: st.X[:, k, seg[v]]) for v in streams])


def decoder_sums(core, st, scope, layer):
    return ModSums(core, st, scope, f"mod{layer}", st.A["w_mod"][layer], ("b_mod", layer * 48), (0, 1), 48)


def modulations(core, st, sums, layer, first=False):
    g = lambda i: ("norm_g", (layer * 4 + i) * DC)
    mod_stage(core, st, sums, [job for v in (0, 1) for job in ((v, 0, g(0), 8, 1), (v, 1, g(1), 16, 0), (v, 2, g(2), 32, 1), (v, 3, g(3), 40, 0))], first)


def build(nc, A, out):
    with ExitStack() as ctx:
        core = Core(nc, ctx)
        st = Store(core, A)
        setup_stage(core, st)
        with ExitStack() as scope:
            modulations(core, st, decoder_sums(core, st, scope, 0), 0, first=True)
        norm_in(core, st, 0, 0, (0, 1))
        with ExitStack() as scope:
            ev = Even(core, scope)
            even_project(core, st, ev)
            mlstm_stage(core, st, ev)
            gla_stage(core, st, ev)
            even_gate_stage(core, st, ev)
        gemm_stage(core, st, "in", A["ev_w_out"][0], D, lambda k: st.Y[:, k],
                   lambda act, c, bank: nc.scalar.activation(chunk_of(st.H, c), bank, ACT.Copy))
        norm_out(core, st, 1, st.H, (0, 1))
        norm_in(core, st, 2, 24, (0, 1))
        with ExitStack() as scope:
            sums = decoder_sums(core, st, scope, 1)
            ffn_stage(core, st, 0, TT, 0, beside=sums)
            norm_out(core, st, 3, st.Y, (0, 1))
            modulations(core, st, sums, 1)
        with ExitStack() as scope:
            kv_sums = rwkv_layer(core, st, scope)
            sums = ada_sums(core, st, scope, 0)
            ffn_stage(core, st, 1, LAT, CTX, beside=sums)
            norm_out(core, st, 3, st.Y, (0,))
            ada(core, st, sums, 0)
            last_sums = ada_sums(core, st, scope, 1, place=sums)
            sparse_layer(core, st, last_sums)
            branch_layer(core, st, kv_sums, last_sums)
        moe_layer(core, st)
        finish_stage(core, st, out)


def kernel(**inputs):
    import concourse.bacc as bacc
    from concourse.bass_utils import run_bass_kernel_spmd

    nc = bacc.Bacc("TRN2", target_bir_lowering=False, num_devices=1)
    arrays = {n: np.ascontiguousarray(a) for n, a in inputs.items()}
    arrays["const"] = CONST
    A = {n: nc.dram_tensor(f"in_{n}", a.shape, mybir.dt.from_np(a.dtype), kind="ExternalInput").ap() for n, a in arrays.items()}
    out = nc.dram_tensor("out", (1, LAT, D), F32, kind="ExternalOutput").ap()
    build(nc, A, out)
    r = run_bass_kernel_spmd(nc, [{f"in_{n}": a for n, a in arrays.items()}], core_ids=[0])
    return r.results[0]["out"]
```

```python
from contextlib import ExitStack, contextmanager

import numpy as np

import concourse.bass as bass
from concourse import mybir

F32 = mybir.dt.float32
I32 = mybir.dt.int32
U32 = mybir.dt.uint32
F32R = mybir.dt.float32r
ALU = mybir.AluOpType
ACT = mybir.ActivationFunctionType
AX = mybir.AxisListType.X
ds = bass.ds

P = 128
D = 1024
DC = D // P
CTX = 256
LAT = 256
TT = CTX + LAT
GRID_W = 64
GRID_H = LAT // GRID_W
SEGS = {"ctx": slice(0, CTX), "lat": slice(CTX, TT)}
EPS = 1e-6

ML_HEADS = 4
ML_DK = 128
GLA_HEADS = 4
GLA_DK = 64
GLA_LR = 16
GLA_TAU = 16.0
RW_HEADS = 16
RW_HEAD = 64
RW_CHUNK = 64
RW_LN_EPS = 64e-5
RW_DECAY = -float(np.exp(-0.5))
FF = 2816
FC = FF // P

HEADS = 16
HD = 64
KV_HEADS = 4
IDX_HEADS = 8
DSA_KEEP = min(256, LAT // 4)
CMP_LEN = 32
CMP_STRIDE = 16
CMP_HIDDEN = 256
N_CMP = (LAT - CMP_LEN) // CMP_STRIDE + 1
SLC_LEN = 64
assert min(16, LAT // SLC_LEN) * SLC_LEN == LAT
assert LAT <= 512
EXPERTS = 8
SEATS = 128
FE = 3584
FEC = FE // P
NEG = -1e30
GONE = -3e38


LEVELS = 8


def level_mask(level, backward):
    s, t = np.arange(P)[:, None], np.arange(P)[None, :]
    if level == 0:
        return (s == t).astype(np.float32)
    h = 1 << (level - 1)
    late, early = (s, t) if backward else (t, s)
    return ((s // (2 * h) == t // (2 * h)) & (late // h % 2 == 1) & (early // h % 2 == 0)).astype(np.float32)


def constant_table():
    s, t = np.arange(P)[:, None], np.arange(P)[None, :]
    block = (s // RW_CHUNK == t // RW_CHUNK)
    parts = {"ident": np.eye(P), "ones": np.ones((P, P)), "head_ones": block}
    rot = np.zeros((P, P))
    for m in range(P):
        if m % HD < HD // 2:
            rot[m + HD // 2, m] = -1.0
        else:
            rot[m - HD // 2, m] = 1.0
    parts["rot"] = rot
    parts["neg_after"] = np.where(t <= s, 0.0, NEG)
    parts["neg_before"] = np.where(t >= s, 0.0, NEG)
    u, c = np.arange(P)[:, None] % RW_CHUNK, np.arange(RW_CHUNK)[None, :]
    for back in (0, 1):
        first, then = (c, u) if back else (u, c)
        parts[f"before_{back}"] = first < then
        parts[f"upto_{back}"] = first <= then
        for level in range(1, 7):
            m = level_mask(level, back)[:RW_CHUNK, :RW_CHUNK]
            parts[f"pair{level}_{back}"] = np.concatenate([m, m])
    parts["pair_ident"] = u == c
    parts["earlier"] = s < t
    parts["column"] = np.broadcast_to(t, (P, P))
    for back in (0, 1):
        for level in range(LEVELS):
            parts[f"level{level}_{back}"] = level_mask(level, back)
    token = np.arange(LAT).reshape(2, P).T
    end = np.arange(CMP_STRIDE) * CMP_STRIDE + CMP_LEN - 1
    seen = (end[None, None, :] <= token[:, :, None]) & (np.arange(CMP_STRIDE) < N_CMP)[None, None, :]
    parts["cmp_seen"] = seen.reshape(P, -1)
    parts["cmp_neg"] = np.where(seen, 0.0, NEG).reshape(P, -1)
    start = (np.arange(TT) % RW_CHUNK != 0)
    parts["keep_fwd"] = np.broadcast_to(start, (P, TT))
    stop = (np.arange(TT) % RW_CHUNK != RW_CHUNK - 1)
    parts["keep_bwd"] = np.broadcast_to(stop, (P, TT))
    inv = np.float32(1.0) / np.power(np.float32(10000.0), np.arange(0, HD, 2, dtype=np.float32) / np.float32(HD)).astype(np.float32)
    parts["inv_freq"] = np.concatenate([inv] * (P // len(inv)))[:, None]
    at, columns = {}, 0
    for name, a in parts.items():
        at[name] = (columns, columns + a.shape[1])
        columns += a.shape[1]
    return np.ascontiguousarray(np.concatenate([np.asarray(a, np.float32) for a in parts.values()], axis=1)), at


CONST, CONST_AT = constant_table()


def vector_rows(shapes):
    names = ("c", "c_ctx", "c_2", "b_mod", "norm_g", "ffn_conv_w", "ffn_conv_b", "ev_conv_w", "ev_conv_b", "ev_gla_b",
             "ev_head_g", "rw_mu", "rw_w0", "rw_a0", "rw_kvec", "rw_lnx", "b_ada_2", "attn_gain_2", "ffn_gain_2",
             "kv_gain_2", "b_kv_ada_2", "final_gain_2", "cmp_pe_k_2", "cmp_pe_v_2")
    at, row = {}, 0
    for n in names:
        k = int(np.prod(shapes[n])) // P
        at[n] = (row, k)
        row += k
    return at, row


class Counter:

    def __init__(self, nc, ctx, name):
        self.sem = ctx.enter_context(nc.semaphore(name))
        self.base = 0
        self.n = 0

    def at(self, n):
        return self.base + n

    def count(self, ins, by=1):
        ins.then_inc(self.sem, by)
        self.n += by
        return ins

    def settle(self):
        self.base += self.n
        self.n = 0


class Core:

    def __init__(self, nc, ctx):
        self.nc = nc
        self.ctx = ctx
        self.counters = {}
        self.spare = []
        self.psum = [ctx.enter_context(nc.psum_tensor(f"bank_pair{i}", [P, 1024], F32)) for i in range(4)]
        self.stage_no = 0

    def bank(self, i):
        return self.psum[i // 2][:, (i % 2) * 512:(i % 2 + 1) * 512]

    def counter(self, name, keep=False):
        if name not in self.counters:
            s = self.spare.pop() if self.spare and not keep else Counter(self.nc, self.ctx, name if keep else f"{name}_{self.stage_no}")
            s.keep = keep
            self.counters[name] = s
        return self.counters[name]

    def sb(self, name, shape, dtype=F32, ctx=None):
        return (ctx or self.ctx).enter_context(self.nc.sbuf_tensor(f"{name}_{self.stage_no}" if ctx else name, shape, dtype))

    @contextmanager
    def engines_block(self):
        with self.nc.Block() as block:
            yield block
        for name, s in list(self.counters.items()):
            s.settle()
            if not s.keep:
                self.spare.append(self.counters.pop(name))
        self.stage_no += 1


    @contextmanager
    def rarely(self, count, more_than):
        outer, spare, self.counters, self.spare = self.counters, self.spare, {}, []
        n = self.nc.values_load(count, min_val=0, max_val=TT)
        nc = self.nc
        with nc.If(n > more_than):
            entered = self.counter("entered")
            for eng in (nc.sync, nc.gpsimd, nc.tensor, nc.vector, nc.scalar):
                eng.sem_inc(entered.sem, 1)
            entered.n += 5
            yield
        self.counters, self.spare = outer, spare


class Chain:

    def __init__(self, eng, signal, it=None, per=0):
        self.eng, self.counter, self.it, self.per, self.k = eng, signal, it, per, signal.n if it is None else 0
        self.start = signal.n

    def ended(self, ins):
        ins.then_inc(self.counter.sem, 1)
        self.k += 1
        if self.it is None:
            self.counter.n += 1
            self.eng.wait_ge(self.counter.sem, self.counter.at(self.k))
        else:
            self.eng.wait_ge(self.counter.sem, self.counter.at(self.start + self.it * self.per + self.k))

    def settle(self, rounds):
        assert self.k == self.per, (self.k, self.per)
        self.counter.n += rounds * self.per


def leading(nc, hi, x):
    return nc.vector.tensor_copy(hi.bitcast(F32R), x)


class Gemm:

    def __init__(self, core, ctx, key, tiles, banks, width, split=False):
        self.core, self.sources, self.split = core, tiles, split
        nc = core.nc
        kc = max(t[2] for t in tiles)
        self.ring = core.sb(f"ring_{key}", [P, len(tiles), kc, width], ctx=ctx)
        self.banks = {o: core.bank(b) for o, b in banks.items()}
        self.landed = [core.counter(f"{key}_tile{s}_landed", True) for s in range(len(tiles))]
        self.used = [core.counter(f"{key}_tile{s}_used", True) for s in range(len(tiles))]
        self.free = {o: core.counter(f"{key}_bank{o}_free", True) for o in banks}
        self.first = {o: min(s for s, t in enumerate(tiles) if o in t[3]) for o in banks}
        self.last = {o: max(s for s, t in enumerate(tiles) if o in t[3]) for o in banks}
        if split:
            self.hi, self.lo = (core.sb(f"ring_{n}_{key}", [P, len(tiles), kc, width], ctx=ctx) for n in ("hi", "lo"))
            self.cut = [core.counter(f"{key}_tile{s}_cut", True) for s in range(len(tiles))]
            self.parted = [core.counter(f"{key}_tile{s}_parted", True) for s in range(len(tiles))]

    def fetch_round(self, sp, it, first=False, where=None):
        for s, (src, _, kc, outs) in enumerate(self.sources):
            if not first:
                done = self.parted if self.split else self.used
                sp.wait_ge(done[s].sem, done[s].at(it))
            ap = src(it if where is None else where)
            sp.dma_start(self.ring[:, s, 0:kc, 0:ap.shape[2]], ap).then_inc(self.landed[s].sem, 16)

    def part_tile(self, dve, it, s, first=False, rest=True):
        kc = self.sources[s][2]
        if not first:
            dve.wait_ge(self.used[s].sem, self.used[s].at(it))
        dve.wait_ge(self.landed[s].sem, self.landed[s].at(16 * it + 16))
        leading(self.core.nc, self.hi[:, s, 0:kc], self.ring[:, s, 0:kc]).then_inc(self.cut[s].sem, 1)
        if rest:
            self.rest_of_tile(dve, self.core.nc.vector, it, s)

    def rest_of_tile(self, eng, ns, it, s):
        kc = self.sources[s][2]
        eng.wait_ge(self.cut[s].sem, self.cut[s].at(it + 1))
        ns.tensor_tensor(self.lo[:, s, 0:kc].bitcast(F32R), self.ring[:, s, 0:kc], self.hi[:, s, 0:kc], ALU.subtract).then_inc(self.parted[s].sem, 1)

    def matmul_round(self, pe, it, rhs, first=False, wait_x=None):
        for s, (_, k0, kc, outs) in enumerate(self.sources):
            if self.split:
                pe.wait_ge(self.parted[s].sem, self.parted[s].at(it + 1))
            else:
                pe.wait_ge(self.landed[s].sem, self.landed[s].at(16 * it + 16))
            if first and wait_x:
                wait_x(k0 + kc - 1)
            for j, o in enumerate(outs):
                if s == self.first[o] and not first:
                    pe.wait_ge(self.free[o].sem, self.free[o].at(it))
                for k in range(kc):
                    x = rhs(k0 + k)
                    cols = slice(j * P, (j + 1) * P)
                    w = self.ring[:, s, k, cols]
                    if self.split:
                        hi, lo = self.hi[:, s, k, cols].bitcast(F32R), self.lo[:, s, k, cols].bitcast(F32R)
                        x_hi, x_lo = (part.bitcast(F32R) for part in x)
                        passes = [(hi, x_hi), (hi, x_lo), (lo, x_hi)]
                    else:
                        passes = [(w, x)]
                    for i, (lhs, moving) in enumerate(passes):
                        ins = self.core.nc.tensor.matmul(self.banks[o][:, 0:moving.shape[1]], lhs, moving,
                                                         start=(s == self.first[o] and k == 0 and i == 0),
                                                         stop=(s == self.last[o] and k == kc - 1 and i == len(passes) - 1))
            ins.then_inc(self.used[s].sem, 1)

    def wait_bank(self, eng, o, it):
        s = self.last[o]
        eng.wait_ge(self.used[s].sem, self.used[s].at(it + 1))
        return self.banks[o]

    def bank_taken(self, ins, o):
        ins.then_inc(self.free[o].sem, 1)

    def settle(self, rounds):
        for s in self.landed:
            s.n += 16 * rounds
        for s in (*self.used, *self.free.values(), *((*self.cut, *self.parted) if self.split else ())):
            s.n += rounds


class Parts:

    def __init__(self, core, ctx, key, chunks, T):
        self.core = core
        self.hi, self.lo = (core.sb(f"{key}_{n}", [P, chunks, T], ctx=ctx) for n in ("hi", "lo"))
        self.cut, self.ready = core.counter(f"{key}_cut"), core.counter(f"{key}_parted")

    def part(self, dve, k, x):
        self.cut.count(leading(self.core.nc, self.hi[:, k], x))
        dve.wait_ge(self.cut.sem, self.cut.at(self.cut.n))
        self.ready.count(self.core.nc.vector.tensor_tensor(self.lo[:, k].bitcast(F32R), x, self.hi[:, k], ALU.subtract))

    def __call__(self, k):
        return self.hi[:, k], self.lo[:, k]

    def wait(self, eng, k):
        eng.wait_ge(self.ready.sem, self.ready.at(k + 1))


def rounds(eng, n, body):
    body(0, True)
    if n > 1:
        with eng.Fori(1, n) as it:
            body(it, False)


def rounds_ahead(eng, n, body):
    body(0, True, n == 1)
    if n > 2:
        with eng.Fori(1, n - 1) as it:
            body(it, False, False)
    if n > 1:
        body(n - 1, False, True)


def k_tiles(w, width, splits, outs, col=lambda it: None):
    v = w.rearrange("(k p) n -> p k n", p=P)
    kc = v.shape[1]
    edges = [kc * i // splits for i in range(splits + 1)]
    return [((lambda it, a=a, b=b: v[:, a:b, ds(col(it), width)]), a, b - a, outs) for a, b in zip(edges, edges[1:])]


class Store:

    def __init__(self, core, A):
        sb = core.sb
        self.A = A
        self.rows_at, self.n_rows = vector_rows({n: a.shape for n, a in A.items()})
        self.const = sb("const", [P, CONST.shape[1]])
        self.vec = sb("vec", [P, -(-self.n_rows // P) * P])
        self.X = sb("X", [P, DC, TT])
        self.H = sb("H", [P, DC, TT])
        self.Y = sb("Y", [P, DC, TT])
        self.act = sb("act", [P, DC, 4])
        self.mod = sb("mod", [P, 48, 2])
        self.coef = sb("coef", [P, 2, 4, DC])
        self.cos = sb("cos", [P, LAT])
        self.sin = sb("sin", [P, LAT])

    def C(self, name):
        a, b = CONST_AT[name]
        return self.const[:, a:b]

    def V(self, name, i=0, n=1):
        r, k = self.rows_at[name]
        assert i + n <= k
        return self.vec[:, r + i:r + i + n]


def setup_stage(core, st):
    nc, A = core.nc, st.A
    n_tiles = -(-st.n_rows // P)
    with ExitStack() as ctx, core.engines_block() as block:
        rows = core.sb("rows", [P, n_tiles, P], ctx=ctx)
        tokens = core.sb("tokens", [P, 4, D], ctx=ctx)
        pos_i = core.sb("pos_i", [P, LAT], I32, ctx=ctx)
        ang = core.sb("ang", [P, LAT], ctx=ctx)
        turn = core.sb("turn", [P, 2, LAT], ctx=ctx)
        rest = core.sb("rest", [P, 2, LAT], ctx=ctx)
        sig = core.sb("sig", [P, DC, 4], ctx=ctx)
        const_in, rows_in, tokens_in, pos_in = (core.counter(n) for n in ("const_in", "rows_in", "tokens_in", "pos_in"))
        turned, copied = core.counter("turned"), core.counter("turned_copied")
        vec_chain, angle_ready, sig_ready = core.counter("vector_chain"), core.counter("angle_ready"), core.counter("sig_ready")
        groups = [("rows", t, min(4, n_tiles - t)) for t in range(0, n_tiles, 4)]
        groups += [("tokens", b, k) for b in range(4) for k in (0, 4)]

        @block.sync
        def _(sp):
            const_in.count(sp.dma_start(st.const[:], A["const"]), 16)
            for name, (r, k) in st.rows_at.items():
                axes = " ".join("abcdef"[:len(A[name].shape)])
                src = A[name].rearrange(f"{axes} -> ({axes})").rearrange("(r p) -> r p", p=P)
                done = 0
                while done < k:
                    at = r + done
                    n = min(k - done, P - at % P)
                    rows_in.count(sp.dma_start(rows[at % P:at % P + n, at // P, :], src[done:done + n, :]), 16)
                    done += n

        @block.scalar
        def _(act):
            for b, (name, t) in enumerate((("ctx", 0), ("ctx", 1), ("x", 0), ("x", 1))):
                tokens_in.count(act.dma_start(tokens[:, b, :], A[name][0, t * P:(t + 1) * P, :]), 16)
            pos_in.count(act.dma_start(pos_i[:], A["positions_2"].rearrange("a t -> (a t)").partition_broadcast(P)), 16)
            act.wait_ge(copied.sem, copied.at(1))
            for i, name in enumerate(("c", "c_ctx", "c_2", "c_2")):
                ins = nc.scalar.activation(sig[:, :, i], st.V(name, 0, DC), ACT.Sigmoid)
            sig_ready.count(ins)
            for i, table in enumerate((st.sin, st.cos)):
                act.wait_ge(angle_ready.sem, angle_ready.at(i + 1))
                nc.scalar.activation(table[:], rest[:, i, :], ACT.Sin)

        @block.tensor
        def _(pe):
            pe.wait_ge(const_in.sem, const_in.at(16))
            pe.wait_ge(rows_in.sem, rows_in.at(rows_in.n))
            for g, (kind, a, b) in enumerate(groups):
                if g >= 4:
                    pe.wait_ge(copied.sem, copied.at(g - 3))
                bank = core.bank(g % 4)
                if kind == "rows":
                    for j in range(b):
                        n = min(P, st.n_rows - (a + j) * P)
                        ins = nc.tensor.transpose(bank[:, j * P:j * P + n], rows[0:n, a + j, :], st.C("ident")[0:n, 0:n])
                else:
                    pe.wait_ge(tokens_in.sem, tokens_in.at(64))
                    for j in range(4):
                        ins = nc.tensor.transpose(bank[:, j * P:(j + 1) * P], tokens[:, a, (b + j) * P:(b + j + 1) * P], st.C("ident"))
                turned.count(ins)

        @block.vector
        def _(dve):
            for g, (kind, a, b) in enumerate(groups):
                dve.wait_ge(turned.sem, turned.at(g + 1))
                bank = core.bank(g % 4)
                if kind == "rows":
                    n = min(b * P, st.n_rows - a * P)
                    ins = nc.vector.tensor_copy(st.vec[:, a * P:a * P + n], bank[:, 0:n])
                else:
                    ins = nc.vector.tensor_copy(st.X[:, b:b + 4, a * P:(a + 1) * P], bank.rearrange("p (k t) -> p k t", k=4))
                copied.count(ins)
            c = Chain(dve, vec_chain)
            dve.wait_ge(sig_ready.sem, sig_ready.at(1))
            for i, name in enumerate(("c", "c_ctx", "c_2", "c_2")):
                nc.vector.tensor_tensor(st.act[:, :, i], sig[:, :, i], st.V(name, 0, DC), ALU.mult)
            dve.wait_ge(pos_in.sem, pos_in.at(16))
            c.ended(nc.vector.tensor_copy(ang[:], pos_i[:]))
            c.ended(nc.vector.tensor_scalar(ang[:], ang[:], st.C("inv_freq"), None, ALU.mult))
            for i, quarter in enumerate((0.0, 0.25)):
                n, r = turn[:, i, :], rest[:, i, :]
                c.ended(nc.vector.tensor_scalar(n, ang[:], float(1 / (2 * np.pi)), quarter, ALU.mult, ALU.add))
                c.ended(nc.vector.tensor_scalar(n, n, 12582912.0, None, ALU.add))
                c.ended(nc.vector.tensor_scalar(n, n, -12582912.0, None, ALU.add))
                c.ended(nc.vector.scalar_tensor_tensor(r, n, -6.28125, ang[:], ALU.mult, ALU.add))
                c.ended(nc.vector.scalar_tensor_tensor(r, n, -0.00193500518798828125, r, ALU.mult, ALU.add))
                c.ended(nc.vector.scalar_tensor_tensor(r, n, -3.0199159819e-07, r, ALU.mult, ALU.add))
                c.ended(nc.vector.tensor_scalar(r, r, quarter * float(2 * np.pi), 3.1415925, ALU.add, ALU.min))
                angle_ready.count(nc.vector.tensor_scalar(r, r, -3.1415925, None, ALU.max))


class ModSums:
    WIDE = 512
    TILES = 4
    PART = DC // TILES

    def __init__(self, core, st, scope, key, w, bias, vecs, n_chunks, place=None):
        self.core, self.st, self.key = core, st, key
        self.w = w.rearrange("(k p) n -> p k n", p=P)
        self.bias = st.rows_at[bias[0]][0] + bias[1]
        self.n_chunks, self.groups = n_chunks, n_chunks * P // self.WIDE
        self.vecs = vecs
        self.sums = place.sums if place else core.sb(f"mod_sums_{key}", [P, len(vecs), n_chunks * P], ctx=scope)

    def open(self, ctx):
        core = self.core
        self.ring = core.sb(f"mod_ring_{self.key}", [P, self.TILES, self.PART, self.WIDE], ctx=ctx)
        self.landed = [core.counter(f"mod_{self.key}_tile{s}_landed", True) for s in range(self.TILES)]
        self.added = core.counter(f"mod_{self.key}_added")

    def done(self, g, k):
        return self.added.at(1 + g * (DC * len(self.vecs)) + (k + 1) * len(self.vecs))

    def loads(self, eng):
        def group(g, first):
            for s in range(self.TILES):
                k = s * self.PART
                if not first:
                    eng.wait_ge(self.added.sem, self.done(g - 1, k + self.PART - 1))
                eng.dma_start(self.ring[:, s], self.w[:, k:k + self.PART, ds(g * self.WIDE, self.WIDE)]).then_inc(self.landed[s].sem, 16)
        rounds(eng, self.groups, group)

    def empty(self):
        self.core.nc.vector.memset(self.sums[:], 0.0).then_inc(self.added.sem, 1)

    def add_group(self, dve, g):
        for k in range(DC):
            s = k // self.PART
            if k % self.PART == 0:
                dve.wait_ge(self.landed[s].sem, self.landed[s].at(16 * g + 16))
            dve.wait_ge(self.added.sem, self.done(g, k - 1))
            for v, c in enumerate(self.vecs):
                at = self.sums[:, v, ds(g * self.WIDE, self.WIDE)]
                self.core.nc.vector.scalar_tensor_tensor(at, self.ring[:, s, k % self.PART], self.st.act[:, k, c:c + 1], at,
                                                         ALU.mult, ALU.add).then_inc(self.added.sem, 1)

    def adds(self, dve):
        self.empty()
        with dve.Fori(0, self.groups) as g:
            self.add_group(dve, g)
        self.settle()

    def settle(self):
        self.added.n += 1 + self.groups * DC * len(self.vecs)
        for c in self.landed:
            c.n += 16 * self.groups


def mod_stage(core, st, m, jobs, first=False):
    nc = core.nc
    nv = len(m.vecs)
    n_group = m.n_chunks // m.groups
    with ExitStack() as ctx, core.engines_block() as block:
        whole, chain = core.counter("mod_whole"), core.counter("vector_chain")
        bank = core.bank(0)[:, 0:nv * m.n_chunks].rearrange("p (v n) -> p v n", v=nv)
        if first:
            m.open(ctx)

            @block.sync
            def _(sp):
                m.loads(sp)

        @block.tensor
        def _(pe):
            for n in range(m.n_chunks):
                if first and n % n_group == 0:
                    pe.wait_ge(m.added.sem, m.done(n // n_group, DC - 1))
                for v in range(nv):
                    ins = nc.tensor.matmul(bank[:, v, n:n + 1], m.sums[:, v, n * P:(n + 1) * P], st.C("ones")[:, 0:1], start=True, stop=True)
            whole.count(ins)

        @block.vector
        def _(dve):
            if first:
                m.adds(dve)
            c = Chain(dve, chain)
            dve.wait_ge(whole.sem, whole.at(1))
            for v in range(nv):
                ins = nc.vector.tensor_tensor(st.mod[:, 0:m.n_chunks, v], bank[:, v], st.vec[:, m.bias:m.bias + m.n_chunks], ALU.add)
            c.ended(ins)
            for v, slot, gain, n, one in jobs:
                out = st.coef[:, v, slot, :]
                c.ended(nc.vector.tensor_scalar(out, st.mod[:, n:n + DC, v], float(one), None, ALU.add))
                nc.vector.tensor_tensor(out, out, st.V(gain[0], gain[1], DC), ALU.mult)


def norm_stage(core, st, jobs, T=LAT):
    nc = core.nc
    with ExitStack() as ctx, core.engines_block() as block:
        square = core.sb("square", [P, len(jobs), DC, T], ctx=ctx)
        var = core.sb("var", [P, len(jobs), T], ctx=ctx)
        rstd = core.sb("rstd", [P, len(jobs), T], ctx=ctx)
        unit = core.sb("unit", [P, 2, T], ctx=ctx)
        squared, summed, var_ready, std_ready = (core.counter(n) for n in ("squared", "summed", "var_ready", "std_ready"))
        chain = core.counter("vector_chain")

        @block.scalar
        def _(act):
            for j, (x, *_) in enumerate(jobs):
                for k in range(DC):
                    ins = nc.scalar.activation(square[:, j, k], x(k), ACT.Square)
                squared.count(ins)
            for j in range(len(jobs)):
                act.wait_ge(var_ready.sem, var_ready.at(j + 1))
                std_ready.count(nc.scalar.activation(rstd[:, j], var[:, j], ACT.Sqrt))

        @block.tensor
        def _(pe):
            for j in range(len(jobs)):
                pe.wait_ge(squared.sem, squared.at(j + 1))
                for k in range(DC):
                    ins = nc.tensor.matmul(core.bank(j)[:, 0:T], st.C("ones"), square[:, j, k], start=k == 0, stop=k == DC - 1)
                summed.count(ins)

        @block.vector
        def _(dve):
            c = Chain(dve, chain)
            for j in range(len(jobs)):
                dve.wait_ge(summed.sem, summed.at(j + 1))
                var_ready.count(nc.vector.tensor_scalar(var[:, j], core.bank(j)[:, 0:T], 1.0 / D, EPS, ALU.mult, ALU.add))
            for j, (x, mul, add, dst) in enumerate(jobs):
                dve.wait_ge(std_ready.sem, std_ready.at(j + 1))
                c.ended(nc.vector.reciprocal(rstd[:, j], rstd[:, j]))
                for k in range(DC):
                    u = unit[:, k % 2]
                    c.ended(nc.vector.tensor_tensor(u, x(k), rstd[:, j], ALU.mult))
                    a = add(k) if add else None
                    if a is None:
                        nc.vector.tensor_scalar(dst(k), u, mul(k), None, ALU.mult)
                    elif a.shape[1] == 1:
                        nc.vector.tensor_scalar(dst(k), u, mul(k), a, ALU.mult, ALU.add)
                    else:
                        nc.vector.scalar_tensor_tensor(dst(k), u, mul(k), a, ALU.mult, ALU.add)


def in_background(block, ctx, m):
    if m:
        m.open(ctx)

        @block.gpsimd
        def _(pool):
            m.loads(pool)

        @block.vector
        def _(dve):
            m.adds(dve)


def gemm_stage(core, st, key, w, n_cols, rhs, store, width=512, splits=4, sections=None, mix=None, engine="scalar", background=None, split=False):
    nc = core.nc
    n_it = len(sections) if sections else n_cols // width
    outs = tuple(range(width // P))
    col = (lambda it: sections[it]) if sections else (lambda it: it * width)
    assert not (split and (background or engine == "vector"))
    with ExitStack() as ctx, core.engines_block() as block:
        tiles = k_tiles(w, width, splits, outs, col)
        g = Gemm(core, ctx, key, tiles, {o: o for o in outs}, width, split)

        def each(eng, body):
            if sections:
                for it in range(n_it):
                    body(it, it == 0)
            else:
                rounds(eng, n_it, body)

        @block.sync
        def _(sp):
            each(sp, lambda it, first: g.fetch_round(sp, it, first))

        if split:
            x = Parts(core, ctx, "x", DC, rhs(0).shape[1])
            mixed = core.counter("mixed")

            @block.vector
            def _(dve):
                def body(it, first):
                    for s, (_, k0, kc, _) in enumerate(tiles):
                        if first:
                            for k in range(k0, k0 + kc):
                                if mix:
                                    mixed.count(mix(k))
                                    dve.wait_ge(mixed.sem, mixed.at(k + 1))
                                x.part(dve, k, rhs(k))
                        g.part_tile(dve, it, s, first)
                each(dve, body)
        else:
            in_background(block, ctx, background)

        @block.tensor
        def _(pe):
            each(pe, lambda it, first: g.matmul_round(pe, it, x if split else rhs, first, (lambda k: x.wait(pe, k)) if split else None))

        def take(eng):
            def body(it, first):
                for o in outs:
                    bank = g.wait_bank(eng, o, it)
                    g.bank_taken(store(eng, it * len(outs) + o, bank), o)
            each(eng, body)

        if engine == "scalar":
            @block.scalar
            def _(act):
                take(act)
        else:
            @block.vector
            def _(dve):
                take(dve)
        g.settle(n_it)


def chunk_of(tensor, n, tokens=slice(None)):
    return tensor[:, ds(n, 1), tokens].rearrange("p a t -> p (a t)")



IN_MQK, IN_MV, IN_MO, IN_MG, IN_GQK, IN_GV, IN_GG, IN_LR = 0, 1024, 1536, 2048, 2064, 2576, 3088, 3600


class Even:
    def __init__(self, core, ctx):
        sb = lambda name, shape: core.sb(name, shape, ctx=ctx)
        self.q = sb("ml_q", [P, 4, TT])
        self.k = sb("ml_k", [P, 4, TT])
        self.o = sb("ml_o", [P, 4, TT])
        self.gqk = sb("gla_qk", [P, 4, TT])
        self.gg = sb("gla_g", [P, 4, TT])
        self.v = sb("values", [P, 2, 4, 512])
        self.gap = sb("gap", [P, 4, 2, 4])
        self.rowmax = [sb(f"rowmax{d}", [4, TT]) for d in (0, 1)]
        self.floor = [sb(f"floor{d}", [4, TT]) for d in (0, 1)]
        self.decay = sb("decay", [P, 2, 2, TT])


def even_project(core, st, ev):
    nc, w = core.nc, st.A["ev_w_in"][0]

    def store(act, c, bank):
        i, j = c // 4, c % 4
        dst = (ev.q, ev.k, ev.o, ev.gqk, ev.gg)[i][:, j]
        if i == 2:
            return nc.scalar.activation(dst, bank, ACT.Sigmoid)
        return nc.scalar.activation(dst, bank, ACT.Copy, scale=GLA_DK ** -0.5 if i == 3 and j < 2 else 1.0)
    gemm_stage(core, st, "in", w, None, lambda k: st.H[:, k], store, width=256,
               sections=[a + i for a in (IN_MQK, IN_MQK + 512, IN_MO, IN_GQK, IN_GG) for i in (0, 256)], split=True)

    with ExitStack() as ctx, core.engines_block() as block:
        wv = (st.Y, core.sb("wv", [P, DC, 512], ctx=ctx))
        wg = core.sb("wg", [P, DC, 4 * ML_HEADS], ctx=ctx)
        wl = core.sb("wl", [P, DC, 2 * GLA_LR], ctx=ctx)
        w2 = core.sb("gla_w2", [GLA_LR, 2, 256], ctx=ctx)
        bg = core.sb("b_gates", [4, 4], ctx=ctx)
        low = core.sb("low", [GLA_LR, 2, TT], ctx=ctx)
        gate = [core.sb(f"gate{i}", [4, TT], ctx=ctx) for i in range(4)]
        soft = [core.sb(f"soft{i}", [4, TT], ctx=ctx) for i in range(2)]
        raw = ev.decay
        soft2 = core.sb("soft2", [P, 2, 2, TT], ctx=ctx)
        gap = [core.sb(f"gap_rows{d}", [4, TT], ctx=ctx) for d in (0, 1)]
        one = core.sb("one_row", [P, TT], ctx=ctx)
        nul = core.sb("nul_row", [4, TT], ctx=ctx)
        conv = core.sb("conv", [P, 2, TT], ctx=ctx)
        load = [core.counter(f"even_weights{i}") for i in range(3)]
        low_ready, low_copied = core.counter("low_ready"), core.counter("low_copied")
        gates_ready, values_ready, values_copied = core.counter("gates_ready"), core.counter("values_ready"), core.counter("values_copied")
        la_ready, raw_ready, soft_ready = core.counter("la_ready"), core.counter("raw_ready"), core.counter("soft_ready")
        gap_ready, gap_turned, floor_ready = core.counter("gap_ready"), core.counter("gap_turned"), core.counter("floor_ready")
        act_chain, vec_chain, conv_ready = core.counter("scalar_chain"), core.counter("vector_chain"), core.counter("conv_ready")

        @block.sync
        def _(sp):
            v = w.rearrange("(k p) n -> p k n", p=P)
            load[0].count(sp.dma_start(wg[:], v[:, :, IN_MG:IN_MG + 16]), 16)
            load[0].count(sp.dma_start(wl[:], v[:, :, IN_LR:IN_LR + 32]), 16)
            load[0].count(sp.dma_start(w2[:], st.A["ev_gla_w2"][0].rearrange("z r c -> r z c")), 16)
            load[0].count(sp.dma_start(bg[:], st.A["ev_b_gates"][0].rearrange("(g h) -> h g", h=4), allow_slow_non_contiguous=True), 16)
            for i, col in enumerate((IN_MV, IN_GV)):
                load[1 + i].count(sp.dma_start(wv[i][:], v[:, :, col:col + 512]), 16)

        @block.tensor
        def _(pe):
            pe.wait_ge(load[0].sem, load[0].at(64))
            for z in (0, 1):
                for k in range(DC):
                    ins = nc.tensor.matmul(core.bank(4 + z)[0:GLA_LR, :], wl[:, k, z * GLA_LR:(z + 1) * GLA_LR], st.H[:, k],
                                           start=k == 0, stop=k == DC - 1)
                low_ready.count(ins)
            for i in range(4):
                for k in range(DC):
                    ins = nc.tensor.matmul(core.bank(i)[0:4, :], wg[:, k, i * 4:(i + 1) * 4], st.H[:, k], start=k == 0, stop=k == DC - 1)
                gates_ready.count(ins)
            for z in (0, 1):
                pe.wait_ge(low_copied.sem, low_copied.at(2))
                for c in (0, 1):
                    b = 4 + z * 2 + c
                    la_ready.count(nc.tensor.matmul(core.bank(b), w2[:, z, c * P:(c + 1) * P], low[:, z], start=True, stop=True))
            for i in (0, 1):
                pe.wait_ge(load[1 + i].sem, load[1 + i].at(16))
                for t in range(4):
                    n = i * 4 + t
                    if n < 4:
                        pe.wait_ge(raw_ready.sem, raw_ready.at(4))
                    else:
                        pe.wait_ge(values_copied.sem, values_copied.at(n - 3))
                    for k in range(DC):
                        ins = nc.tensor.matmul(core.bank(n % 4), st.H[:, k, t * P:(t + 1) * P], wv[i][:, k], start=k == 0, stop=k == DC - 1)
                    values_ready.count(ins)
            for d in (0, 1):
                pe.wait_ge(gap_ready.sem, gap_ready.at(d + 1))
                if d == 0:
                    pe.wait_ge(raw_ready.sem, raw_ready.at(8))
                for b in range(4):
                    ins = nc.tensor.transpose(core.bank(4)[:, (b * 2 + d) * 4:(b * 2 + d) * 4 + 4], gap[d][:, b * P:(b + 1) * P],
                                              st.C("ident")[0:4, 0:4])
                gap_turned.count(ins)

        @block.scalar
        def _(act):
            c = Chain(act, act_chain)
            act.wait_ge(low_ready.sem, low_ready.at(2))
            for z in (0, 1):
                ins = nc.scalar.activation(low[:, z], core.bank(4 + z)[0:GLA_LR, :], ACT.Copy)
                low_copied.count(ins)
            act.wait_ge(raw_ready.sem, raw_ready.at(4))
            for d in (0, 1):
                s = soft[d][:]
                c.ended(nc.scalar.activation(s, gate[2 * d + 1][:], ACT.Abs))
                c.ended(nc.scalar.activation(s, s, ACT.Exp, scale=-1.0))
                soft_ready.count(nc.scalar.activation(s, s, ACT.Ln, bias=1.0))
            act.wait_ge(raw_ready.sem, raw_ready.at(8))
            c.ended(nc.scalar.activation(soft2[:], raw[:], ACT.Abs))
            c.ended(nc.scalar.activation(soft2[:], soft2[:], ACT.Exp, scale=-1.0))
            soft_ready.count(nc.scalar.activation(soft2[:], soft2[:], ACT.Ln, bias=1.0))
            for i in (0, 1):
                for t in range(4):
                    act.wait_ge(values_ready.sem, values_ready.at(i * 4 + t + 1))
                    values_copied.count(nc.scalar.activation(ev.v[:, i, t], core.bank(t), ACT.Copy))
            for d in (0, 1):
                act.wait_ge(floor_ready.sem, floor_ready.at(d + 1))
                nc.scalar.activation(ev.floor[d][:], ev.floor[d][:], ACT.Exp, scale=-1.0)
            for n in range(8):
                x = (ev.q, ev.k)[n // 4][:, n % 4]
                act.wait_ge(conv_ready.sem, conv_ready.at(n + 1))
                c.ended(nc.scalar.activation(x, conv[:, n % 2], ACT.Silu))

        @block.vector
        def _(dve):
            c = Chain(dve, vec_chain)
            c.ended(nc.vector.memset(one[:], 1.0))
            c.ended(nc.vector.memset(nul[:], 0.0))
            dve.wait_ge(load[0].sem, load[0].at(64))
            for i in range(4):
                dve.wait_ge(gates_ready.sem, gates_ready.at(i + 1))
                raw_ready.count(nc.vector.tensor_scalar(gate[i][:], core.bank(i)[0:4, :], bg[:, i:i + 1], None, ALU.add))
            for z in (0, 1):
                for k in (0, 1):
                    dve.wait_ge(la_ready.sem, la_ready.at(z * 2 + k + 1))
                    raw_ready.count(nc.vector.tensor_scalar(raw[:, z, k], core.bank(4 + z * 2 + k), st.V("ev_gla_b", z * 2 + k), None, ALU.add))
            for d in (0, 1):
                i_gate, f_gate = gate[2 * d][:], gate[2 * d + 1][:]
                dve.wait_ge(soft_ready.sem, soft_ready.at(d + 1))
                c.ended(nc.vector.scalar_tensor_tensor(f_gate, f_gate, 0.0, soft[d][:], ALU.min, ALU.subtract))
                total = soft[d]
                for part in scan_parts(d):
                    c.ended(nc.vector.tensor_tensor_scan(total[:, part[0]], one[0:4, part[0]], f_gate[:, part[0]],
                                                        total[:, part[1]:part[1] + 1] if part[1] is not None else 0.0, ALU.mult, ALU.add))
                gap_ready.count(nc.vector.tensor_tensor(gap[d][:], i_gate, total[:], ALU.subtract))
                dve.wait_ge(gap_ready.sem, gap_ready.at(d + 1))
                for part in scan_parts(d):
                    c.ended(nc.vector.tensor_tensor_scan(ev.rowmax[d][:, part[0]], nul[:, part[0]], gap[d][:, part[0]],
                                                        ev.rowmax[d][:, part[1]:part[1] + 1] if part[1] is not None else 0.0, ALU.max, ALU.max))
                floor_ready.count(nc.vector.tensor_tensor(ev.floor[d][:], total[:], ev.rowmax[d][:], ALU.add))
            dve.wait_ge(soft_ready.sem, soft_ready.at(3))
            for z in (0, 1):
                c.ended(nc.vector.scalar_tensor_tensor(raw[:, z], raw[:, z], 0.0, soft2[:, z], ALU.min, ALU.subtract))
                c.ended(nc.vector.tensor_scalar(raw[:, z], raw[:, z], 1.0 / GLA_TAU, None, ALU.mult))
                for k in (0, 1):
                    for part in scan_parts(z):
                        c.ended(nc.vector.tensor_tensor_scan(ev.decay[:, z, k, part[0]], one[:, part[0]], raw[:, z, k, part[0]],
                                                            ev.decay[:, z, k, part[1]:part[1] + 1] if part[1] is not None else 0.0, ALU.mult, ALU.add))
            dve.wait_ge(gap_turned.sem, gap_turned.at(2))
            c.ended(nc.vector.tensor_copy(ev.gap[:], core.bank(4)[:, 0:32].rearrange("p (b d h) -> p b d h", b=4, d=2)))
            for n in range(8):
                x, y = (ev.q, ev.k)[n // 4][:, n % 4].rearrange("p (s t) -> p s t", s=2), conv[:, n % 2].rearrange("p (s t) -> p s t", s=2)
                if n >= 2:
                    dve.wait_ge(act_chain.sem, act_chain.at(6 + n - 1))
                c.ended(nc.vector.tensor_scalar(y, x, st.V("ev_conv_w", 8 + n), st.V("ev_conv_b", n), ALU.mult, ALU.add))
                c.ended(nc.vector.scalar_tensor_tensor(y[:, :, 1:], x[:, :, :-1], st.V("ev_conv_w", n), y[:, :, 1:], ALU.mult, ALU.add))
                conv_ready.count(nc.vector.scalar_tensor_tensor(y[:, :, :-1], x[:, :, 1:], st.V("ev_conv_w", 16 + n), y[:, :, :-1], ALU.mult, ALU.add))


def scan_parts(backward):
    if backward:
        return [(slice(CTX - 1, None, -1), None), (slice(TT - 1, CTX - 1, -1), 0)]
    return [(slice(0, TT), None)]


def key_blocks(backward):
    if backward:
        return [(1, [(0, 4)]), (0, [(0, 1), (2, 4)]), (3, [(2, 4)]), (2, [(2, 3)])]
    return [(s, [(s, 4)]) for s in range(4)]


def mlstm_stage(core, st, ev):
    nc = core.nc
    units = [(h, d) for h in range(ML_HEADS) for d in (0, 1)]
    items = [(u, s, runs) for u, (h, d) in enumerate(units) for s, runs in key_blocks(d)]
    with ExitStack() as ctx, core.engines_block() as block:
        masked = core.sb("masked", [P, 2, P], ctx=ctx)
        weight = core.sb("weight", [P, 2, TT], ctx=ctx)
        pt = core.sb("pt", [P, 2, TT], ctx=ctx)
        den = core.sb("den", [P, TT], ctx=ctx)
        num = core.sb("num", [P, TT], ctx=ctx)
        names = ("rows_spread", "scores_ready", "masked_ready", "weights_ready", "pt_ready", "pt_used", "den_ready", "unit_done")
        spread, scores, masked_ready, weights, pt_ready, pt_used, den_ready, unit_done = (core.counter("ml_" + n) for n in names)
        chain = core.counter("vector_chain")
        MAXB, FLOORB = [core.bank(0), core.bank(6)], [core.bank(1), core.bank(7)]
        NUM, DEN = core.bank(4), core.bank(5)
        SC = [core.bank(2), core.bank(3)]

        @block.tensor
        def _(pe):
            def spread_rows(u):
                h, d = units[u]
                if u >= 2:
                    pe.wait_ge(unit_done.sem, unit_done.at(u - 1))
                sel = st.C("ident")[0:4, h:h + 1].to_broadcast([4, P])
                nc.tensor.matmul(MAXB[u % 2], sel, ev.rowmax[d][:], start=True, stop=True)
                spread.count(nc.tensor.matmul(FLOORB[u % 2], sel, ev.floor[d][:], start=True, stop=True))

            def score(n):
                u, s, _ = items[n]
                h = units[u][0]
                if n >= 2:
                    pe.wait_ge(pt_ready.sem, pt_ready.at(n - 1))
                scores.count(nc.tensor.matmul(SC[n % 2], ev.k[:, h, s * P:(s + 1) * P], ev.q[:, h], start=True, stop=True))

            spread_rows(0)
            score(0)
            for n, (u, s, runs) in enumerate(items):
                h, d = units[u]
                j = n % 4
                if j == 2 and u + 1 < len(units):
                    spread_rows(u + 1)
                if n + 1 < len(items):
                    score(n + 1)
                pe.wait_ge(pt_ready.sem, pt_ready.at(n + 1))
                if j == 0 and u:
                    pe.wait_ge(den_ready.sem, den_ready.at(u))
                for r, (a, b) in enumerate(runs):
                    x = pt[:, n % 2, a * P:b * P]
                    flags = dict(start=j == 0 and r == 0, stop=j == 3, skip_group_check=True)
                    nc.tensor.matmul(NUM[:, a * P:b * P], ev.v[:, 0, s, h * P:(h + 1) * P], x, **flags)
                    ins = nc.tensor.matmul(DEN[:, a * P:b * P], st.C("ones"), x, **flags)
                pt_used.count(ins)

        @block.scalar
        def _(act):
            def copy_sums(u):
                act.wait_ge(pt_used.sem, pt_used.at(4 * u + 4))
                if u:
                    act.wait_ge(unit_done.sem, unit_done.at(u))
                nc.scalar.activation(num[:], NUM, ACT.Copy)
                den_ready.count(nc.scalar.activation(den[:], DEN, ACT.Abs))

            for n, (u, s, runs) in enumerate(items):
                h, d = units[u]
                bias = ev.gap[:, s, d, h:h + 1]
                act.wait_ge(masked_ready.sem, masked_ready.at(n + 1))
                if n >= 2:
                    act.wait_ge(pt_ready.sem, pt_ready.at(n - 1))
                w = weight[:, n % 2]
                for a, b in runs:
                    for i, j in ((a, s), (s + 1, b)) if a <= s < b else ((a, b),):
                        if i < j:
                            nc.scalar.activation(w[:, i * P:j * P], MAXB[u % 2][:, i * P:j * P], ACT.Exp, bias=bias, scale=-1.0)
                weights.count(nc.scalar.activation(w[:, s * P:(s + 1) * P], masked[:, n % 2], ACT.Exp, bias=bias))
                if n % 4 == 0 and u:
                    copy_sums(u - 1)
            copy_sums(len(units) - 1)

        @block.vector
        def _(dve):
            c = Chain(dve, chain)

            def finish(u):
                h, d = units[u]
                dve.wait_ge(den_ready.sem, den_ready.at(u + 1))
                c.ended(nc.vector.tensor_tensor(den[:], den[:], FLOORB[u % 2], ALU.max))
                c.ended(nc.vector.reciprocal(den[:], den[:]))
                if d == 0:
                    unit_done.count(nc.vector.tensor_tensor(st.Y[:, h], num[:], den[:], ALU.mult))
                else:
                    c.ended(nc.vector.tensor_tensor(num[:], num[:], den[:], ALU.mult))
                    unit_done.count(nc.vector.tensor_tensor(st.Y[:, h], st.Y[:, h], num[:], ALU.add))

            for n, (u, s, runs) in enumerate(items):
                h, d = units[u]
                dve.wait_ge(spread.sem, spread.at(u + 1))
                if n >= 2:
                    dve.wait_ge(weights.sem, weights.at(n - 1))
                masked_ready.count(nc.vector.scalar_tensor_tensor(masked[:, n % 2], MAXB[u % 2][:, s * P:(s + 1) * P], -1.0,
                                                                st.C("neg_after" if d else "neg_before"), ALU.mult, ALU.add))
                dve.wait_ge(scores.sem, scores.at(n + 1))
                dve.wait_ge(weights.sem, weights.at(n + 1))
                if n >= 2:
                    dve.wait_ge(pt_used.sem, pt_used.at(n - 1))
                for a, b in runs:
                    ins = nc.vector.scalar_tensor_tensor(pt[:, n % 2, a * P:b * P], SC[n % 2][:, a * P:b * P], ML_DK ** -0.5,
                                                         weight[:, n % 2, a * P:b * P], ALU.mult, ALU.mult)
                pt_ready.count(ins)
                if n % 4 == 0 and u:
                    finish(u - 1)
            finish(len(units) - 1)


def gla_stage(core, st, ev):
    nc = core.nc
    units = [(c, d) for c in (0, 1) for d in (0, 1)]
    n_lv = LEVELS + 2
    with ExitStack() as ctx, core.engines_block() as block:
        eq = core.sb("eq", [P, 2, TT], ctx=ctx)
        ek = core.sb("ek", [P, 2, TT], ctx=ctx)
        qs = core.sb("qs", [P, 2, TT], ctx=ctx)
        ks = core.sb("ks", [P, 2, TT], ctx=ctx)
        att = core.sb("att", [P, 2, TT], ctx=ctx)
        part = core.sb("part", [P, 2, TT], ctx=ctx)
        near = core.sb("near", [P, 2, 2 * P], ctx=ctx)
        far = core.sb("far", [P, 2, 2, CTX], ctx=ctx)
        exps_in, exps, scaled, scored, summed, pv = (core.counter("gla_" + n) for n in ("shifts", "exps", "scaled", "scored", "summed", "pv"))
        far_copied, out_taken = core.counter("gla_far_copied"), core.counter("gla_out_taken")
        chain = core.counter("vector_chain")
        OUT = [core.bank(4), core.bank(5)]

        def halves(x, level, d):
            h = 1 << (level - 1)
            v = x.rearrange("p (n two h) -> p n two h", two=2, h=h)
            late, early = (0, 1) if d and h < CTX else (1, 0)
            ref = v[:, :, early, 0:1] if d else v[:, :, early, h - 1:h]
            return v[:, :, late], v[:, :, early], ref.to_broadcast([P, TT // (2 * h), h])

        @block.vector
        def _(dve):
            c = Chain(dve, chain)
            c.ended(nc.vector.memset(qs[:], 0.0))
            c.ended(nc.vector.memset(ks[:], 0.0))
            for u, (ch, d) in enumerate(units):
                b, q, k = ev.decay[:, d, ch], ev.gqk[:, ch], ev.gqk[:, 2 + ch]

                def scale(l):
                    n = u * n_lv + l
                    p = n % 2
                    if n >= 2:
                        dve.wait_ge(scored.sem, scored.at(n - 1))
                    if l == 0:
                        nc.vector.tensor_copy(qs[:, p], q)
                        scaled.count(nc.vector.tensor_copy(ks[:, p], k))
                        return
                    bq, bk, ref = halves(b, l, d)
                    shift_q, _, _ = halves(eq[:, p], l, d)
                    _, shift_k, _ = halves(ek[:, p], l, d)
                    nc.vector.tensor_tensor(shift_q, bq, ref, ALU.subtract)
                    exps_in.count(nc.vector.tensor_tensor(shift_k, ref, bk, ALU.subtract))
                    dve.wait_ge(exps.sem, exps.at(u * (n_lv - 1) + l))
                    nc.vector.tensor_tensor(halves(qs[:, p], l, d)[0], halves(q, l, d)[0], shift_q, ALU.mult)
                    scaled.count(nc.vector.tensor_tensor(halves(ks[:, p], l, d)[1], halves(k, l, d)[1], shift_k, ALU.mult))

                def add_up(l):
                    n = u * n_lv + l
                    dve.wait_ge(scored.sem, scored.at(n + 1))
                    mask = st.C(f"level{l}_{d}").unsqueeze(1).to_broadcast([P, 4, P])
                    if l == 0 and u:
                        dve.wait_ge(pv.sem, pv.at(u))
                    for hh in (0, 1):
                        bank = core.bank((n % 2) * 2 + hh).rearrange("p (b t) -> p b t", b=4)
                        dst = att if l == 0 else part
                        ins = nc.vector.tensor_tensor(dst[:, hh].rearrange("p (b t) -> p b t", b=4), bank, mask, ALU.mult)
                    if l:
                        c.ended(ins)
                        ins = nc.vector.tensor_tensor(att[:], att[:], part[:], ALU.add)
                    summed.count(ins)
                    dve.wait_ge(summed.sem, summed.at(u * LEVELS + l + 1))

                scale(0)
                for l in range(n_lv):
                    if l + 1 < n_lv:
                        scale(l + 1)
                    if l < LEVELS:
                        add_up(l)
                if d:
                    dve.wait_ge(pv.sem, pv.at(u + 1))
                    for hh in (0, 1):
                        ins = nc.vector.tensor_copy(st.Y[:, 4 + 2 * ch + hh], OUT[hh])
                    out_taken.count(ins)

        @block.scalar
        def _(act):
            for u, (ch, d) in enumerate(units):
                for l in range(n_lv):
                    n = u * n_lv + l
                    p = n % 2
                    if l:
                        act.wait_ge(exps_in.sem, exps_in.at(u * (n_lv - 1) + l))
                        x, y = halves(eq[:, p], l, d)[0], halves(ek[:, p], l, d)[1]
                        nc.scalar.activation(x, x, ACT.Exp)
                        exps.count(nc.scalar.activation(y, y, ACT.Exp))
                    if l >= LEVELS + 1:
                        if u:
                            act.wait_ge(pv.sem, pv.at(u))
                        for up in (LEVELS, LEVELS + 1):
                            m = u * n_lv + up
                            act.wait_ge(scored.sem, scored.at(m + 1))
                            for hh in (0, 1):
                                bank = core.bank((m % 2) * 2 + hh)
                                if up == LEVELS:
                                    ins = nc.scalar.activation(near[:, hh], bank[:, 0:2 * P], ACT.Copy)
                                else:
                                    ins = nc.scalar.activation(far[:, hh], bank.rearrange("p (b t) -> p b t", b=2), ACT.Copy)
                            far_copied.count(ins)

        @block.tensor
        def _(pe):
            for u, (ch, d) in enumerate(units):
                for l in range(n_lv):
                    n = u * n_lv + l
                    pe.wait_ge(scaled.sem, scaled.at(n + 1))
                    if n >= 2:
                        m = n - 2
                        if m % n_lv < LEVELS:
                            pe.wait_ge(summed.sem, summed.at(m // n_lv * LEVELS + m % n_lv + 1))
                        else:
                            pe.wait_ge(far_copied.sem, far_copied.at(m // n_lv * 2 + m % n_lv - LEVELS + 1))
                    for hh in (0, 1):
                        bank = core.bank((n % 2) * 2 + hh)
                        k, q = ks[hh * 64:hh * 64 + 64, n % 2], qs[hh * 64:hh * 64 + 64, n % 2]
                        if l < LEVELS:
                            tiles = [(b * P, b * P, b * P, P) for b in range(4)]
                        elif l == LEVELS:
                            tiles = [(i * P, (2 * i + d) * P, (2 * i + 1 - d) * P, P) for i in (0, 1)]
                        else:
                            tiles = [(i * CTX, i * P, CTX, LAT) for i in (0, 1)]
                        for at, s, t, w in tiles:
                            ins = nc.tensor.matmul(bank[:, at:at + w], k[:, s:s + P], q[:, t:t + w], start=True, stop=True)
                    scored.count(ins)
                pe.wait_ge(summed.sem, summed.at((u + 1) * LEVELS))
                pe.wait_ge(far_copied.sem, far_copied.at(2 * u + 2))
                if u == 2:
                    pe.wait_ge(out_taken.sem, out_taken.at(1))
                for hh in (0, 1):
                    v = lambda s: ev.v[:, 1, s, (2 * ch + hh) * P:(2 * ch + hh + 1) * P]
                    prods = [(s, att[:, hh, s * P:(s + 1) * P], s * P, P) for s in range(4)]
                    prods += [(2 * i + d, near[:, hh, i * P:(i + 1) * P], (2 * i + 1 - d) * P, P) for i in (0, 1)]
                    prods += [(i, far[:, hh, i], CTX, LAT) for i in (0, 1)]
                    for j, (s, x, t, w) in enumerate(prods):
                        ins = nc.tensor.matmul(OUT[hh][:, t:t + w], v(s), x, start=d == 0 and j == 0,
                                               stop=d == 1 and j == len(prods) - 1, skip_group_check=True)
                pv.count(ins)


def even_gate_stage(core, st, ev):
    nc = core.nc
    with ExitStack() as ctx, core.engines_block() as block:
        square = core.sb("square", [P, DC, TT], ctx=ctx)
        var = core.sb("var", [P, 2, TT], ctx=ctx)
        unit = core.sb("unit", [P, 2, TT], ctx=ctx)
        squared, summed, var_ready, std_ready, done = (core.counter(n) for n in ("squared", "summed", "var_ready", "std_ready", "head_done"))
        chain = core.counter("vector_chain")

        @block.scalar
        def _(act):
            for k in range(DC):
                squared.count(nc.scalar.activation(square[:, k], st.Y[:, k], ACT.Square))
            for k in range(4):
                ins = nc.scalar.activation(ev.gg[:, k], ev.gg[:, k], ACT.Silu)
            for k in range(DC):
                act.wait_ge(var_ready.sem, var_ready.at(k + 1))
                std_ready.count(nc.scalar.activation(var[:, k % 2], var[:, k % 2], ACT.Sqrt))

        @block.tensor
        def _(pe):
            for k in range(DC):
                pe.wait_ge(squared.sem, squared.at(k + 1))
                summed.count(nc.tensor.matmul(core.bank(k), st.C("ones"), square[:, k], start=True, stop=True))

        @block.vector
        def _(dve):
            c = Chain(dve, chain)

            def spread(k):
                dve.wait_ge(summed.sem, summed.at(k + 1))
                var_ready.count(nc.vector.tensor_scalar(var[:, k % 2], core.bank(k), 1.0 / P, EPS, ALU.mult, ALU.add))
            spread(0)
            for k in range(DC):
                if k + 1 < DC:
                    spread(k + 1)
                dve.wait_ge(std_ready.sem, std_ready.at(k + 1))
                v = var[:, k % 2]
                c.ended(nc.vector.reciprocal(v, v))
                u = unit[:, k % 2]
                c.ended(nc.vector.scalar_tensor_tensor(u, st.Y[:, k], st.V("ev_head_g", k), v, ALU.mult, ALU.mult))
                nc.vector.tensor_tensor(st.Y[:, k], u, (ev.o if k < 4 else ev.gg)[:, k % 4], ALU.mult)


def ffn_stage(core, st, scope, layer, T, t0, beside):
    nc, A = core.nc, st.A
    h = core.sb("ffn_h", [P, FC, T], ctx=scope)
    n_it = FC // 2
    with ExitStack() as ctx, core.engines_block() as block:
        up = A["ffn_w_up"][layer]
        split = T == TT
        tiles = k_tiles(up, 256, 2, (0, 1), lambda it: it * 256) + k_tiles(up, 256, 2, (2, 3), lambda it: it * 256 + FF)
        g = Gemm(core, ctx, "up", tiles, {o: o for o in range(4)}, 256, split)
        x = Parts(core, ctx, "x", DC, T) if split else None
        taps = core.sb("taps", [P, 2, 10], ctx=ctx)
        conv = core.sb("conv", [P, 2, T], ctx=ctx)
        gelu = core.sb("gelu", [P, 2, T], ctx=ctx)
        conv_ready, gelu_ready, chain = core.counter("conv_ready"), core.counter("gelu_ready"), core.counter("vector_chain")
        w0, b0 = st.rows_at["ffn_conv_w"][0] + layer * 9 * FC, st.rows_at["ffn_conv_b"][0] + layer * FC
        tap_order = [(dy, dx) for dy in (-1, 0, 1) for dx in (-1, 0, 1) if (dy, dx) != (0, 0)]
        per = 2 * (1 + len(tap_order)) + (2 * 2 if T == TT else 0)

        @block.sync
        def _(sp):
            rounds(sp, n_it, lambda it, first: g.fetch_round(sp, it, first))

        @block.tensor
        def _(pe):
            if split:
                rounds(pe, n_it, lambda it, first: g.matmul_round(pe, it, x, first, lambda k: x.wait(pe, k)))
            else:
                rounds(pe, n_it, lambda it, first: g.matmul_round(pe, it, lambda k: st.H[:, k, t0:t0 + T], first))

        if split:
            @block.gpsimd
            def _(pool):
                def body(it, first):
                    for s in range(len(tiles)):
                        g.rest_of_tile(pool, nc.gpsimd, it, s)
                rounds(pool, n_it, body)

        @block.vector
        def _(dve):
            def body(it, first, last):
                c = Chain(dve, chain, it, per)
                if first and split:
                    for s, (_, k0, kc, _) in enumerate(tiles):
                        g.part_tile(dve, 0, s, True, rest=False)
                        for k in range(k0, k0 + kc) if s < 2 else ():
                            x.part(dve, k, st.H[:, k])
                ahead = lambda s: None if last or not split else g.part_tile(dve, it + 1, s, rest=False)
                ahead(0)
                for o in (0, 1):
                    n = it * 2 + o
                    nc.vector.tensor_copy(taps[:, o, 0:9].unsqueeze(2), st.vec[:, w0:w0 + 9 * FC].rearrange("p (w f) -> p w f", f=FC)[:, :, ds(n, 1)])
                    c.ended(nc.vector.tensor_copy(taps[:, o, 9:10], st.vec[:, ds(b0 + n, 1)]))
                    bank = g.wait_bank(dve, o, it)
                    if not first:
                        dve.wait_ge(gelu_ready.sem, gelu_ready.at(it * 2 + o - 1))
                    y = conv[:, o]
                    c.ended(nc.vector.tensor_scalar(y, bank[:, 0:T], taps[:, o, 4:5], taps[:, o, 9:10], ALU.mult, ALU.add))
                    if T == TT:
                        c.ended(nc.vector.scalar_tensor_tensor(y[:, 1:CTX], bank[:, 0:CTX - 1], taps[:, o, 3:4], y[:, 1:CTX], ALU.mult, ALU.add))
                        c.ended(nc.vector.scalar_tensor_tensor(y[:, 0:CTX - 1], bank[:, 1:CTX], taps[:, o, 5:6], y[:, 0:CTX - 1], ALU.mult, ALU.add))
                    yg = y[:, T - LAT:T].rearrange("p (r w) -> p r w", w=GRID_W)
                    xg = bank[:, T - LAT:T].rearrange("p (r w) -> p r w", w=GRID_W)
                    for i, (dy, dx) in enumerate(tap_order):
                        rows = [slice(max(0, -s), n - max(0, s)) for s, n in ((dy, GRID_H), (dx, GRID_W))]
                        from_ = [slice(r.start + s, r.stop + s) for r, s in zip(rows, (dy, dx))]
                        w = (dy + 1) * 3 + dx + 1
                        ins = nc.vector.scalar_tensor_tensor(yg[:, rows[0], rows[1]], xg[:, from_[0], from_[1]], taps[:, o, w:w + 1],
                                                             yg[:, rows[0], rows[1]], ALU.mult, ALU.add)
                        if i + 1 < len(tap_order):
                            c.ended(ins)
                    g.bank_taken(ins, o)
                ahead(1)
                for o in (0, 1):
                    bank = g.wait_bank(dve, 2 + o, it)
                    dve.wait_ge(gelu_ready.sem, gelu_ready.at(it * 2 + o + 1))
                    g.bank_taken(nc.vector.tensor_tensor(chunk_of(h, it * 2 + o), gelu[:, o], bank[:, 0:T], ALU.mult), 2 + o)
                ahead(2)
                ahead(3)
                links.append(c)
            links = []
            rounds_ahead(dve, n_it, body)
            links[-1].settle(n_it)

        @block.scalar
        def _(act):
            def body(it, first):
                for o in (0, 1):
                    act.wait_ge(g.free[o].sem, g.free[o].at(it + 1))
                    if not first:
                        act.wait_ge(g.free[2 + o].sem, g.free[2 + o].at(it))
                    nc.scalar.activation(gelu[:, o], conv[:, o], ACT.Gelu_apprx_tanh).then_inc(gelu_ready.sem, 1)
            rounds(act, n_it, body)
        gelu_ready.n += 2 * n_it
        g.settle(n_it)
    sums = beside()
    gemm_stage(core, st, "down", A["ffn_w_down"][layer], D, lambda k: h[:, k],
               lambda act, c, bank: nc.scalar.activation(chunk_of(st.Y, c, slice(t0, t0 + T)), bank[:, 0:T], ACT.Copy), width=256, background=sums)
    return sums


class Rwkv:
    def __init__(self, core, st, ctx):
        sb = lambda name: core.sb(name, [P, DC, TT], ctx=ctx)
        self.k, self.v, self.kk = sb("rw_k"), sb("rw_v"), sb("rw_kk")
        self.r = st.X[:, :, 0:CTX]
        self.g = st.Y[:, :, 0:CTX]
        self.y = st.Y[:, :, CTX:TT]

    def rest(self, core, ctx):
        sb = lambda name: core.sb(name, [P, DC, TT], ctx=ctx)
        self.b = sb("rw_b")
        self.decay = [sb("rw_decay0"), sb("rw_decay1")]


def rwkv_shift_stage(core, st):
    nc = core.nc
    with core.engines_block() as block:
        @block.vector
        def _(dve):
            for quarter in range(4):
                k = slice(2 * quarter, 2 * quarter + 2)
                h, y = st.H[:, k], st.Y[:, k]
                back = quarter % 2 == 0
                to, of, edge = (slice(1, CTX), slice(0, CTX - 1), slice(0, 1)) if back else (slice(0, CTX - 1), slice(1, CTX), slice(CTX - 1, CTX))
                nc.vector.tensor_tensor(y[:, :, to], h[:, :, of], h[:, :, to], ALU.subtract)
                nc.vector.tensor_scalar(y[:, :, edge], h[:, :, edge], -1.0, None, ALU.mult)
                for c in (0, 1):
                    hg, yg = (x[:, c, CTX:TT].rearrange("p (r w) -> p r w", w=GRID_W) for x in (h, y))
                    n = GRID_W if quarter < 2 else GRID_H
                    to, of, edge = (slice(1, n), slice(0, n - 1), slice(0, 1)) if back else (slice(0, n - 1), slice(1, n), slice(n - 1, n))
                    cut = (lambda x, s: x[:, :, s]) if quarter < 2 else (lambda x, s: x[:, s, :])
                    nc.vector.tensor_tensor(cut(yg, to), cut(hg, of), cut(hg, to), ALU.subtract)
                    nc.vector.tensor_scalar(cut(yg, edge), cut(hg, edge), -1.0, None, ALU.mult)


def rwkv_low_rank_stage(core, st, rw, mu, w1_parts, rank, func, w2, parts, store, tokens):
    nc = core.nc
    T = tokens.stop - tokens.start
    with ExitStack() as ctx, core.engines_block() as block:
        w1s = core.sb("w1s", [P, DC, rank], ctx=ctx)
        w2s = core.sb("w2s", [rank, D], ctx=ctx)
        hidden = core.sb("hidden", [rank, T], ctx=ctx)
        loaded, mixed, hid, hid_done, out, taken = (core.counter("low_" + n) for n in ("loaded", "mixed", "hidden", "hidden_done", "out", "taken"))

        @block.sync
        def _(sp):
            each = rank // len(w1_parts)
            for i, w in enumerate(w1_parts):
                loaded.count(sp.dma_start(w1s[:, :, i * each:(i + 1) * each], w.rearrange("(k p) r -> p k r", p=P)), 16)
            loaded.count(sp.dma_start(w2s[:], w2), 16)

        @block.vector
        def _(dve):
            for k in range(DC):
                ins = rwkv_mix(core, st, rw, mu, tokens, k)
            mixed.count(ins)

        @block.tensor
        def _(pe):
            pe.wait_ge(mixed.sem, mixed.at(1))
            pe.wait_ge(loaded.sem, loaded.at(loaded.n))
            for k in range(DC):
                ins = nc.tensor.matmul(core.bank(0)[0:rank, 0:T], w1s[:, k], rw.kk[:, k, tokens], start=k == 0, stop=k == DC - 1)
            hid.count(ins)
            pe.wait_ge(hid_done.sem, hid_done.at(1))
            for i, rows in enumerate(parts):
                for n in range(DC):
                    m = i * DC + n
                    if m >= 4:
                        pe.wait_ge(taken.sem, taken.at(m - 3))
                    out.count(nc.tensor.matmul(core.bank(4 + m % 4)[:, 0:T], w2s[rows, n * P:(n + 1) * P], hidden[rows], start=True, stop=True))

        @block.scalar
        def _(act):
            act.wait_ge(hid.sem, hid.at(1))
            hid_done.count(nc.scalar.activation(hidden[:], core.bank(0)[0:rank, 0:T], func))
            for m in range(len(parts) * DC):
                act.wait_ge(out.sem, out.at(m + 1))
                taken.count(store(m // DC, m % DC, core.bank(4 + m % 4)[:, 0:T]))


def rwkv_mix(core, st, rw, mu, tokens, k):
    return core.nc.vector.scalar_tensor_tensor(rw.kk[:, k, tokens], st.Y[:, k, tokens], st.V("rw_mu", mu * DC + k), st.H[:, k, tokens],
                                               ALU.mult, ALU.add)


def rwkv_project(core, st, rw, scope):
    nc, A = core.nc, st.A
    lat, all_ = slice(CTX, TT), slice(0, TT)
    rwkv_shift_stage(core, st)
    copy = lambda dst: lambda act, c, bank: nc.scalar.activation(chunk_of(dst, c), bank[:, 0:dst.shape[2]], ACT.Copy)
    for i, (mu, dst, tokens) in enumerate(((0, rw.r, lat), (2, rw.k, all_), (3, rw.v, all_))):
        gemm_stage(core, st, "in", A["rw_w_rkv"][0, i], D, lambda k, t=tokens: rw.kk[:, k, t], copy(dst),
                   mix=lambda k, mu=mu, t=tokens: rwkv_mix(core, st, rw, mu, t, k), split=True)
    rw.rest(core, scope)
    rwkv_low_rank_stage(core, st, rw, 4, [A["rw_a1"][0]], 64, ACT.Copy, A["rw_a2"][0], [slice(0, 64)],
                        lambda i, n, bank: nc.scalar.activation(rw.b[:, n], bank, ACT.Sigmoid, bias=st.V("rw_a0", n)), all_)
    rwkv_low_rank_stage(core, st, rw, 1, [A["rw_w1"][0, 0], A["rw_w1"][0, 1]], 128, ACT.Tanh, A["rw_w2"][0].rearrange("z r d -> (z r) d"),
                        [slice(0, 64), slice(64, 128)],
                        lambda i, n, bank: nc.scalar.activation(rw.decay[i][:, n], bank, ACT.Sigmoid, bias=st.V("rw_w0", i * DC + n)), all_)
    rwkv_low_rank_stage(core, st, rw, 5, [A["rw_g1"][0]], 128, ACT.Sigmoid, A["rw_g2"][0], [slice(0, 128)],
                        lambda i, n, bank: nc.scalar.activation(rw.g[:, n], bank, ACT.Copy), lat)

    with ExitStack() as ctx, core.engines_block() as block:
        square = core.sb("square", [P, 2, TT], ctx=ctx)
        norm = core.sb("norm", [P, 2, TT], ctx=ctx)
        blend = core.sb("blend", [P, TT], ctx=ctx)
        rest = core.sb("rest", [P, DC], ctx=ctx)
        scaled, squared, summed, rooted = (core.counter("kk_" + n) for n in ("scaled", "squared", "summed", "rooted"))
        chain = core.counter("vector_chain")

        @block.scalar
        def _(act):
            for n in range(DC):
                act.wait_ge(scaled.sem, scaled.at(n + 1))
                squared.count(nc.scalar.activation(square[:, n % 2], rw.kk[:, n], ACT.Square))
                act.wait_ge(summed.sem, summed.at(n + 1))
                if n >= 2:
                    act.wait_ge(scaled.sem, scaled.at(n + 1))
                rooted.count(nc.scalar.activation(norm[:, n % 2], core.bank(n), ACT.Sqrt))

        @block.tensor
        def _(pe):
            for n in range(DC):
                pe.wait_ge(squared.sem, squared.at(n + 1))
                summed.count(nc.tensor.matmul(core.bank(n), st.C("head_ones"), square[:, n % 2], start=True, stop=True))

        @block.vector
        def _(dve):
            c = Chain(dve, chain)
            c.ended(nc.vector.tensor_scalar(rest[:], st.V("rw_kvec", DC, DC), -1.0, 1.0, ALU.mult, ALU.add))
            scale = lambda n: scaled.count(nc.vector.tensor_scalar(rw.kk[:, n], rw.k[:, n], st.V("rw_kvec", n), None, ALU.mult))
            scale(0)
            for n in range(DC):
                if n + 1 < DC:
                    scale(n + 1)
                nc.vector.tensor_tensor_scan(rw.decay[0][:, n], st.C("keep_fwd"), rw.decay[0][:, n], 0.0, ALU.mult, ALU.add)
                nc.vector.tensor_tensor_scan(rw.decay[1][:, n, ::-1], st.C("keep_bwd")[:, ::-1], rw.decay[1][:, n, ::-1], 0.0, ALU.mult, ALU.add)
                c.ended(nc.vector.tensor_scalar(blend[:], rw.b[:, n], st.V("rw_kvec", DC + n), rest[:, n:n + 1], ALU.mult, ALU.add))
                c.ended(nc.vector.tensor_tensor(rw.k[:, n], rw.k[:, n], blend[:], ALU.mult))
                dve.wait_ge(rooted.sem, rooted.at(n + 1))
                v = norm[:, n % 2]
                c.ended(nc.vector.tensor_scalar(v, v, 1e-12, None, ALU.max))
                c.ended(nc.vector.reciprocal(v, v))
                c.ended(nc.vector.scalar_tensor_tensor(rw.kk[:, n], rw.kk[:, n], -1.0, v, ALU.mult, ALU.mult))
                c.ended(nc.vector.scalar_tensor_tensor(rw.b[:, n], rw.b[:, n], -1.0, rw.kk[:, n], ALU.mult, ALU.mult))


def rwkv_steps(latent):
    levels = range(2, 7)
    out = ["RK", "RB"] if latent else []
    pe = ["V", "K", "B", "CT", "C", "LK"] + out
    act = ["exp", "diagonal", "V", "K", "B", "C"]
    dve = ["last"] + (["rho"] if latent else []) + ["CT", "LK"] + out
    for l in levels:
        pe += [f"Y{l}", f"D{l - 1}", f"E{l}"]
        act += [f"Y{l}", f"D{l - 1}"]
        dve += [f"E{l}"]
    pe += ["W", "U"] + (["O"] if latent else []) + ["S"]
    act += ["W", "U"]
    dve += (["O"] if latent else []) + ["S"]
    return pe, act, dve, ["prep"]


def of_both_groups(steps, order):
    place = lambda step: order.index(step) if step in order else steps.index(step) - len(steps)
    return sorted(((step, g) for step in steps for g in (0, 1)), key=lambda x: (place(x[0]), x[1]))


def rwkv_scan_stage(core, st, rw):
    nc = core.nc
    n_chunks = CTX // RW_CHUNK
    C = RW_CHUNK
    N = DC // 2
    H2 = [slice(0, C), slice(C, 2 * C)]
    with ExitStack() as ctx, core.engines_block() as block:
        masks = CONST_AT["level0_0"][0]
        assert CONST_AT[f"level{LEVELS - 1}_1"][1] - masks == 2 * LEVELS * P
        size = N * P
        used_up = iter([st.H[:, k] for k in range(DC)] + [st.const[:, masks + i * size:masks + (i + 1) * size] for i in range(2 * LEVELS * P // size)])

        def blocks(name):
            t = next(used_up, None)
            t = core.sb(name, [P, size], ctx=ctx)[:] if t is None else t
            return t.rearrange("p (n t) -> p n t", n=N)
        plain = ("alpha", "beta", "kappa", "val", "kappa_t", "beta_t", "val_t", "c", "e", "fall")
        diagonal = ("alpha", "beta", "rho", "e", "val_t", "state", "rk", "rb")
        B = [{n: core.sb(f"{n}{g}", [P, N, C], ctx=ctx)[:] for n in plain} for g in (0, 1)]
        X = [{n: blocks(f"{n}_blocks{g}") for n in diagonal} for g in (0, 1)]
        wide = [core.sb(f"grow{g}", [P, N, C + 2], ctx=ctx)[:] for g in (0, 1)]
        for g in (0, 1):
            B[g]["grow"] = B[g]["lk"] = wide[g][:, :, 1:C + 1]
            B[g].update(w=B[g]["beta"], u=B[g]["c"], d=B[g]["val"])
            X[g].update(y=X[g]["beta"], u=X[g]["e"])
        last = [core.sb(f"last{g}", [P, N], ctx=ctx) for g in (0, 1)]
        pe_s, act_s, dve_s, pool_s = ([core.counter(f"rw_{e}_step{g}") for g in (0, 1)] for e in ("tensor", "scalar", "vector", "gpsimd"))
        chain = core.counter("vector_chain")
        pe_passed, dve_passed, pool_passed = (core.counter(f"rw_{e}_passed") for e in ("tensor", "vector", "gpsimd"))
        phases = [(d, latent, t0) for d in (0, 1) for latent, t0 in ((False, 0), (True, CTX))]
        on_diagonal = lambda x, h: x[H2[h], :, H2[h]]
        mine = lambda g: slice(g * N, (g + 1) * N)
        bank_of = lambda g, n: core.bank(4 * g + n % 4)[:, 0:N * C].rearrange("p (n t) -> p n t", n=N)

        def value(sig, order, off, it, step):
            return sig.at(off + it * len(order) + order.index(step) + 1)

        def half_columns(x, level, which):
            return x.rearrange("p n (b two h) -> p n b two h", two=2, h=1 << (level - 1))[:, :, :, which]

        def start_of(it, d, t0):
            return t0 + (it * C if d == 0 else (n_chunks - 1) * C - it * C)

        offs = []
        off = [1, 1, 0, 0]
        for d, latent, _ in phases:
            off[2] += not latent
            offs.append(list(off))
            off = [o + n_chunks * len(x) for o, x in zip(off, rwkv_steps(latent))]

        @block.tensor
        def _(pe):
            for g in (0, 1):
                pe.sem_inc(pe_s[g].sem, 1)
            for (_, latent, t0), (po, ao, do, go) in zip(phases, offs):
                order, act_order, dve_order, pool_order = rwkv_steps(latent)
                a, v, p_ = "act", "dve", "pool"
                need = {"V": [(a, "exp")], "K": [(p_, "prep")], "CT": [(a, "diagonal")], "RK": [(v, "rho")],
                        "W": [(v, "LK"), (a, "V")], "U": [(a, "W"), (v, "E6")], "O": [(a, "U"), (v, "RB")], "S": [(a, "U")]}
                for l in range(2, 7):
                    e = f"E{l - 1}" if l > 2 else "CT"
                    need[f"Y{l}"] = [(a, "C"), (v, e)]
                    need[f"D{l - 1}"] = [(v, e)]
                    need[f"E{l}"] = [(a, f"D{l - 1}")]
                with pe.Fori(0, n_chunks) as it:
                    for step, g in of_both_groups(order, order):
                        n = order.index(step)
                        b, x, bank = B[g], X[g], bank_of(g, n)
                        wait = list(need.get(step, []))
                        if n >= 4:
                            p = order[n - 4]
                            wait.append(("act" if p in act_order else "dve", p))
                        on_act, on_dve, on_pool = ([s for eng, s in wait if eng == e] for e in (a, v, p_))
                        if step == "V" and latent:
                            pe.wait_ge(dve_s[g].sem, dve_s[g].at(do - 1 + it * len(dve_order)))
                        elif step == ("K" if latent else "V"):
                            pe.wait_ge(dve_s[g].sem, dve_s[g].at(do + it * len(dve_order)))
                        if on_act:
                            pe.wait_ge(act_s[g].sem, value(act_s[g], act_order, ao, it, max(on_act, key=act_order.index)))
                        if on_dve:
                            pe.wait_ge(dve_s[g].sem, value(dve_s[g], dve_order, do, it, max(on_dve, key=dve_order.index)))
                        if on_pool:
                            pe.wait_ge(pool_s[g].sem, value(pool_s[g], pool_order, go, it, on_pool[-1]))
                        pe.sem_inc(pe_passed.sem, 1)
                        kind = step.rstrip("123456")
                        ident = st.C("ident")
                        crossing = {"V": [("val", None)], "K": [("kappa", None)], "B": [("beta", None)], "C": [("alpha", "beta")],
                                    "CT": [("beta", "alpha")], "LK": [("kappa", "alpha")], "RK": [("kappa", "rho")], "RB": [("beta", "rho")],
                                    "Y": [("c", "e")], "E": [("d", "y")], "D": [("e", None)], "W": [("alpha", "state")], "U": [],
                                    "O": [("val_t", "rk"), ("u", "rb")], "S": [("kappa_t", "val_t"), ("beta_t", "u")]}[kind]

                        own = {"W": (lambda i, h: b["lk"][H2[h], i], lambda i, h: x["val_t"][H2[h], i, H2[h]]),
                               "U": (lambda i, h: b["e"][H2[h], i], lambda i, h: b["w"][H2[h], i]),
                               "O": (lambda i, h: x["state"][H2[h], i, H2[h]], lambda i, h: x["rho"][H2[h], i, H2[h]])}.get(step)
                        for i0 in range(0, N, 2):
                            for j, (turned, by) in enumerate(crossing):
                                for i in (i0, i0 + 1):
                                    ins = nc.tensor.matmul(bank[H2[i % 2], i0:i0 + 2], b[turned][:, i], x[by][:, i] if by else ident,
                                                           start=j == 0, stop=j == len(crossing) - 1 and not own)
                            if own:
                                for i in (i0, i0 + 1):
                                    for h in (0, 1):
                                        ins = nc.tensor.matmul(bank[H2[h], i], own[0](i, h), own[1](i, h), start=not crossing, stop=not crossing or i > i0)
                        ins.then_inc(pe_s[g].sem, 1)

        @block.scalar
        def _(act):
            for g in (0, 1):
                act.wait_ge(dve_s[g].sem, dve_s[g].at(1))
                act.sem_inc(act_s[g].sem, 1)
            for (d, latent, t0), (po, ao, do, go) in zip(phases, offs):
                pe_order, order, _, pool_order = rwkv_steps(latent)
                with act.Fori(0, n_chunks) as it:
                    for step, g in of_both_groups(order, pe_order):
                        b, x = B[g], X[g]
                        if step == "exp":
                            at = ds(start_of(it, d, t0), C)
                            nc.scalar.activation(b["grow"], rw.decay[d][:, mine(g), at], ACT.Exp, scale=RW_DECAY)
                            nc.scalar.activation(b["fall"], rw.decay[d][:, mine(g), at], ACT.Exp, scale=-RW_DECAY)
                            ins = nc.scalar.activation(b["val"], rw.v[:, mine(g), at], ACT.Copy)
                        elif step == "diagonal":
                            act.wait_ge(pool_s[g].sem, value(pool_s[g], pool_order, go, it, "prep"))
                            for name in ("alpha", "beta"):
                                for h in (0, 1):
                                    ins = nc.scalar.activation(on_diagonal(x[name], h), b[name][H2[h]], ACT.Copy)
                        else:
                            act.wait_ge(pe_s[g].sem, value(pe_s[g], pe_order, po, it, step))
                            bank = bank_of(g, pe_order.index(step))
                            dst = {"V": "val_t", "K": "kappa_t", "B": "beta_t", "C": "c", "W": "w", "U": "u"}.get(step, step[0].lower())
                            part = lambda x: x
                            if step[0] == "Y":
                                part = lambda x: half_columns(x, int(step[1]), 1 - d)
                            elif step[0] == "D" and step != "D1":
                                part = lambda x: half_columns(x, int(step[1]), d)
                            if step[0] != "Y":
                                ins = nc.scalar.activation(part(b[dst]), part(bank), ACT.Copy)
                            if step[0] in "YVU":
                                for h in (0, 1):
                                    ins = nc.scalar.activation(part(on_diagonal(x[dst], h)), part(bank[H2[h]]), ACT.Copy)
                        ins.then_inc(act_s[g].sem, 1)

        @block.gpsimd
        def _(pool):
            for g in (0, 1):
                pool.wait_ge(dve_s[g].sem, dve_s[g].at(1))
            for (d, latent, t0), (po, ao, do, go) in zip(phases, offs):
                pe_order, act_order, _, order = rwkv_steps(latent)
                with pool.Fori(0, n_chunks) as it:
                    for g in (0, 1):
                        b = B[g]
                        at = ds(start_of(it, d, t0), C)
                        pool.wait_ge(act_s[g].sem, value(act_s[g], act_order, ao, it, "exp"))
                        pool.sem_inc(pool_passed.sem, 1)
                        nc.gpsimd.tensor_tensor(b["kappa"], rw.k[:, mine(g), at], b["fall"], ALU.mult)
                        nc.gpsimd.tensor_tensor(b["beta"], rw.b[:, mine(g), at], b["fall"], ALU.mult)
                        nc.gpsimd.tensor_tensor(b["alpha"], rw.kk[:, mine(g), at], wide[g][:, :, 2 * d:2 * d + C], ALU.mult).then_inc(pool_s[g].sem, 1)

        @block.vector
        def _(dve):
            for g in (0, 1):
                for edge in (0, C + 1):
                    nc.vector.memset(wide[g][:, :, edge:edge + 1], 1.0)
                for name in diagonal:
                    ins = nc.vector.memset(X[g][name], 0.0)
                ins.then_inc(dve_s[g].sem, 1)
            nc.vector.memset(rw.y, 0.0).then_inc(chain.sem, 1)
            chain.n += 1
            spread = lambda name, h=None: st.C(name)[slice(0, P) if h is None else H2[h]].unsqueeze(1).to_broadcast([P if h is None else C, N, C])
            for ph, ((d, latent, t0), (po, ao, do, go)) in enumerate(zip(phases, offs)):
                pe_order, act_order, order, _ = rwkv_steps(latent)
                done = 0
                per = 4
                if ph and not latent:
                    for g in (0, 1):
                        dve.wait_ge(dve_s[g].sem, dve_s[g].at(do - 1))
                        nc.vector.memset(X[g]["state"], 0.0).then_inc(dve_s[g].sem, 1)
                base = chain.n
                with dve.Fori(0, n_chunks) as it:
                    for step, g in of_both_groups(order, pe_order):
                        b, x = B[g], X[g]
                        if step == "last":
                            dve.wait_ge(act_s[g].sem, value(act_s[g], act_order, ao, it, "exp"))
                            dve.wait_ge(dve_s[g].sem, dve_s[g].at(do + it * len(order)))
                            dve.sem_inc(dve_passed.sem, 1)
                            ins = nc.vector.tensor_copy(last[g][:].unsqueeze(2), b["grow"][:, :, (0 if d else C - 1):(1 if d else C)])
                        elif step == "rho":
                            at = ds(start_of(it, d, 0), C)
                            for h in (0, 1):
                                ins = nc.vector.tensor_tensor(on_diagonal(x["rho"], h), rw.r[H2[h], mine(g), at], b["grow"][H2[h]], ALU.mult)
                        else:
                            bank = bank_of(g, pe_order.index(step))
                            if step == "CT":
                                nc.vector.tensor_copy(b["e"], spread("pair_ident"))
                                for h in (0, 1):
                                    ins = nc.vector.tensor_copy(on_diagonal(x["e"], h), spread("pair_ident", h))
                                ins.then_inc(chain.sem, 1)
                                done += 1
                                dve.wait_ge(chain.sem, chain.at(base + it * per + done))
                            dve.wait_ge(pe_s[g].sem, value(pe_s[g], pe_order, po, it, step))
                            if step != "O":
                                dve.sem_inc(dve_passed.sem, 1)
                            if step == "CT" or step[0] == "E":
                                level = 1 if step == "CT" else int(step[1])
                                queries = lambda x: half_columns(x, level, 1 - d)
                                mask = lambda rows: queries(st.C(f"pair{level}_{d}").bitcast(U32)[rows].unsqueeze(1).to_broadcast([rows.stop - rows.start, N, C]))
                                nc.vector.copy_predicated(queries(b["e"]), mask(slice(0, P)), queries(bank))
                                for h in (0, 1):
                                    ins = nc.vector.copy_predicated(queries(on_diagonal(x["e"], h)), mask(H2[h]), queries(bank[H2[h]]))
                            elif step == "LK":
                                ins = nc.vector.tensor_tensor(b["lk"], bank, spread(f"before_{d}"), ALU.mult)
                            elif step in ("RK", "RB"):
                                for h in (0, 1):
                                    ins = nc.vector.tensor_tensor(on_diagonal(x[step.lower()], h), bank[H2[h]], spread(f"upto_{d}", h), ALU.mult)
                            elif step == "O":
                                y = rw.y[:, mine(g), ds(start_of(it, d, 0), C)]
                                ins = nc.vector.tensor_tensor(y, y, bank, ALU.add)
                            elif step == "S":
                                for h in (0, 1):
                                    s = on_diagonal(x["state"], h)
                                    ins = nc.vector.tensor_tensor(s, s, bank[H2[h]], ALU.add)
                                ins.then_inc(chain.sem, 1)
                                done += 1
                                dve.wait_ge(chain.sem, chain.at(base + it * per + done))
                                for h in (0, 1):
                                    s = on_diagonal(x["state"], h)
                                    ins = nc.vector.tensor_tensor(s, s, last[g][H2[h]].unsqueeze(2).to_broadcast([C, N, C]), ALU.mult)
                        ins.then_inc(dve_s[g].sem, 1)
                assert done == per
                chain.n += per * n_chunks

        for sigs, n in zip((pe_s, act_s, dve_s, pool_s), off):
            for s in sigs:
                s.n += n
        for s, per in zip((pe_passed, dve_passed, pool_passed), (lambda x: 2 * len(x[0]), lambda x: 2 * sum(y not in ("O", "rho") for y in x[2]), lambda x: 2 * len(x[3]))):
            s.n += n_chunks * sum(per(rwkv_steps(latent)) for _, latent, _ in phases)


def rwkv_out_stage(core, st, rw):
    nc = core.nc
    lat = slice(CTX, TT)
    with ExitStack() as ctx, core.engines_block() as block:
        cen = core.sb("cen", [P, DC, LAT], ctx=ctx)
        square = core.sb("square", [P, DC, LAT], ctx=ctx)
        std = core.sb("std", [P, DC, LAT], ctx=ctx)
        rk = core.sb("rk", [P, DC, LAT], ctx=ctx)
        names = ("rk", "mean", "centred", "squared", "summed", "var", "rooted", "bonus")
        rk_s, mean, centred, squared, summed, var, rooted, bonus = (core.counter("out_" + n) for n in names)
        chain = core.counter("vector_chain")

        def half(i, n):
            return core.bank(i * 4 + n // 2)[:, n % 2 * LAT:(n % 2 + 1) * LAT]

        @block.tensor
        def _(pe):
            for n in range(DC):
                mean.count(nc.tensor.matmul(half(0, n), st.C("head_ones"), rw.y[:, n], start=True, stop=True))
            for n in range(DC):
                pe.wait_ge(rk_s.sem, rk_s.at(n + 1))
                bonus.count(nc.tensor.matmul(half(1, n), st.C("head_ones"), rk[:, n], start=True, stop=True))
            for n in range(DC):
                pe.wait_ge(squared.sem, squared.at(DC))
                summed.count(nc.tensor.matmul(half(0, n), st.C("head_ones"), square[:, n], start=True, stop=True))

        @block.scalar
        def _(act):
            for n in range(DC):
                act.wait_ge(centred.sem, centred.at(n + 1))
                squared.count(nc.scalar.activation(square[:, n], cen[:, n], ACT.Square))
            for n in range(DC):
                act.wait_ge(var.sem, var.at(n + 1))
                rooted.count(nc.scalar.activation(std[:, n], std[:, n], ACT.Sqrt))

        @block.vector
        def _(dve):
            c = Chain(dve, chain)
            for n in range(DC):
                rk_s.count(nc.vector.scalar_tensor_tensor(rk[:, n], rw.r[:, n], st.V("rw_kvec", 2 * DC + n), rw.k[:, n, lat], ALU.mult, ALU.mult))
            for n in range(DC):
                dve.wait_ge(mean.sem, mean.at(n // 2 * 2 + 2))
                centred.count(nc.vector.scalar_tensor_tensor(cen[:, n], half(0, n), -1.0 / RW_HEAD, rw.y[:, n], ALU.mult, ALU.add))
            for n in range(DC):
                dve.wait_ge(summed.sem, summed.at(n // 2 * 2 + 2))
                var.count(nc.vector.tensor_scalar(std[:, n], half(0, n), 1.0 / RW_HEAD, RW_LN_EPS, ALU.mult, ALU.add))
            for n in range(DC):
                dve.wait_ge(rooted.sem, rooted.at(n + 1))
                c.ended(nc.vector.reciprocal(std[:, n], std[:, n]))
                c.ended(nc.vector.tensor_tensor(cen[:, n], cen[:, n], std[:, n], ALU.mult))
                c.ended(nc.vector.tensor_scalar(cen[:, n], cen[:, n], st.V("rw_lnx", n), st.V("rw_lnx", DC + n), ALU.mult, ALU.add))
                dve.wait_ge(bonus.sem, bonus.at(n // 2 * 2 + 2))
                c.ended(nc.vector.tensor_tensor(rk[:, n], half(1, n), rw.v[:, n, lat], ALU.mult))
                c.ended(nc.vector.tensor_tensor(cen[:, n], cen[:, n], rk[:, n], ALU.add))
                nc.vector.tensor_tensor(st.H[:, n, lat], cen[:, n], rw.g[:, n], ALU.mult)


def rwkv_layer(core, st, scope):
    nc, A = core.nc, st.A
    lat = slice(CTX, TT)
    norm_in(core, st, 0, 0, (0, 1))
    with ExitStack() as heads:
        rw = Rwkv(core, st, heads)
        rwkv_project(core, st, rw, heads)
        rwkv_scan_stage(core, st, rw)
        rwkv_out_stage(core, st, rw)
    kv_sums = ModSums(core, st, scope, "kv_ada", A["w_kv_ada_2"], ("b_kv_ada_2", 0), (2,), 16)
    gemm_stage(core, st, "in", A["rw_w_o"][0], D, lambda k: st.H[:, k, lat],
               lambda act, c, bank: nc.scalar.activation(chunk_of(st.Y, c, lat), bank[:, 0:LAT], ACT.Copy), background=kv_sums)
    norm_out(core, st, 1, st.Y, (0,))
    norm_in(core, st, 2, 24, (0,))
    return kv_sums


LATS = slice(CTX, TT)


def ada_sums(core, st, scope, layer, place=None):
    return ModSums(core, st, scope, f"ada{layer}", st.A["w_ada_2"][layer], ("b_ada_2", layer * 48), (2,), 48, place)


def ada(core, st, sums, layer):
    mod_stage(core, st, sums, [(0, 0, ("attn_gain_2", layer * DC), 8, 1), (0, 2, ("ffn_gain_2", layer * DC), 32, 1)])


def add_gated(core, st, key, w, rhs, gate, width=512):
    nc = core.nc

    def store(dve, c, bank):
        x = chunk_of(st.X, c, LATS)
        return nc.vector.scalar_tensor_tensor(x, bank[:, 0:LAT], st.mod[:, ds(gate + c, 1), 0], x, ALU.mult, ALU.add)
    gemm_stage(core, st, key, w, D, rhs, store, width=width, engine="vector")


def small_stage(core, st, w, jobs):
    nc = core.nc
    v = w.rearrange("(k p) n -> p k n", p=P)
    with ExitStack() as ctx, core.engines_block() as block:
        ws, outs = [], []
        for i, (kind, col, n, dst, *more) in enumerate(jobs):
            if kind == "pair":
                t = core.sb(f"w_pair{i}", [P, DC, n, 2, HD], ctx=ctx)
                for g in range(n):
                    outs.append((i, lambda k, t=t, g=g: (t[:, k, g].rearrange("p a d -> p (a d)"), st.H[:, k, LATS]), LAT,
                                 lambda bank, dst=dst, g=g: nc.scalar.activation(dst[:, g], bank, ACT.Copy)))
            else:
                width = n * HD if kind == "values" else n
                t = core.sb(f"w_tokens{i}", [P, DC, width], ctx=ctx)
                for b in (0, 1):
                    if kind == "values":
                        take = lambda bank, dst=dst, b=b, n=n: nc.scalar.activation(dst[:, b, :, HD:2 * HD], bank.rearrange("p (g d) -> p g d", g=n), ACT.Copy)
                    else:
                        take = lambda bank, dst=dst, b=b, more=more: nc.scalar.activation(dst[:, b], bank, more[0], scale=more[1])
                    outs.append((i, lambda k, t=t, b=b: (st.H[:, k, CTX + b * P:CTX + (b + 1) * P], t[:, k]), width, take))
            ws.append(t)
        loaded = [core.counter(f"small_weights{i}") for i in range(len(jobs))]
        ready, taken, zeroed = core.counter("small_ready"), core.counter("small_taken"), core.counter("small_zeroed")

        @block.sync
        def _(sp):
            for i, (kind, col, n, *_) in enumerate(jobs):
                if kind == "pair":
                    for k in range(DC):
                        for a in (0, 1):
                            loaded[i].count(sp.dma_start(ws[i][:, k, :, a], v[:, k, col:col + n * HD].rearrange("p (g d) -> p g d", d=HD)), 16)
                else:
                    width = n * HD if kind == "values" else n
                    loaded[i].count(sp.dma_start(ws[i][:], v[:, :, col:col + width]), 16)

        @block.vector
        def _(dve):
            for kind, _, _, dst, *_ in jobs:
                if kind == "values":
                    zeroed.count(nc.vector.memset(dst[:], 0.0))

        @block.tensor
        def _(pe):
            for m, (i, operands, width, _) in enumerate(outs):
                pe.wait_ge(loaded[i].sem, loaded[i].at(loaded[i].n))
                if m >= 4:
                    pe.wait_ge(taken.sem, taken.at(m - 3))
                for k in range(DC):
                    lhs, rhs = operands(k)
                    ins = nc.tensor.matmul(core.bank(m % 4)[:, 0:width], lhs, rhs, start=k == 0, stop=k == DC - 1)
                ready.count(ins)

        @block.scalar
        def _(act):
            if zeroed.n:
                act.wait_ge(zeroed.sem, zeroed.at(zeroed.n))
            for m, (i, _, width, take) in enumerate(outs):
                act.wait_ge(ready.sem, ready.at(m + 1))
                taken.count(take(core.bank(m % 4)[:, 0:width]))


def rope_stage(core, st, chunks):
    nc = core.nc
    with ExitStack() as ctx, core.engines_block() as block:
        turned = core.sb("turned", [P, 2, LAT], ctx=ctx)
        straight = core.sb("straight", [P, 2, LAT], ctx=ctx)
        swapped, done, chain = core.counter("rope_swapped"), core.counter("rope_done"), core.counter("vector_chain")

        @block.tensor
        def _(pe):
            for i, x in enumerate(chunks):
                if i >= 4:
                    pe.wait_ge(done.sem, done.at(i - 3))
                swapped.count(nc.tensor.matmul(core.bank(i % 4)[:, 0:LAT], st.C("rot"), x, start=True, stop=True))

        @block.vector
        def _(dve):
            c = Chain(dve, chain)
            for i, x in enumerate(chunks):
                nc.vector.tensor_tensor(straight[:, i % 2], x, st.cos[:], ALU.mult)
                dve.wait_ge(swapped.sem, swapped.at(i + 1))
                c.ended(nc.vector.tensor_tensor(turned[:, i % 2], core.bank(i % 4)[:, 0:LAT], st.sin[:], ALU.mult))
                done.count(nc.vector.tensor_tensor(x, straight[:, i % 2], turned[:, i % 2], ALU.add))


def causal_stage(core, st, seen):
    nc = core.nc
    with core.engines_block() as block:
        @block.vector
        def _(dve):
            nc.vector.memset(seen[:, 0, P:LAT], NEG)
            nc.vector.memset(seen[:, 1, 0:P], 0.0)
            for b in (0, 1):
                nc.vector.tensor_copy(seen[:, b, b * P:(b + 1) * P], st.C("neg_after"))


def indexer_stage(core, st, iq, ik, iw, seen, keep):
    nc = core.nc
    with ExitStack() as ctx, core.engines_block() as block:
        score = core.sb("score", [P, 2, LAT], ctx=ctx)
        left = [core.sb(f"left{i}", [P, 2, LAT], ctx=ctx) for i in (0, 1)]
        part = core.sb("part", [P, 2, LAT], ctx=ctx)
        top = core.sb("top", [P, 2, 2, 8], ctx=ctx)
        dots, weighed, chain = core.counter("idx_dots"), core.counter("idx_weighed"), core.counter("vector_chain")

        @block.tensor
        def _(pe):
            for b in (0, 1):
                for h in range(IDX_HEADS):
                    n = b * IDX_HEADS + h
                    if n >= 4:
                        pe.wait_ge(weighed.sem, weighed.at(n - 3))
                    half = slice(h % 2 * HD, (h % 2 + 1) * HD)
                    dots.count(nc.tensor.matmul(core.bank(n % 4)[:, 0:LAT], iq[half, h // 2, b * P:(b + 1) * P], ik[half, 0], start=True, stop=True))

        @block.vector
        def _(dve):
            c = Chain(dve, chain)
            for b in (0, 1):
                for h in range(IDX_HEADS):
                    n = b * IDX_HEADS + h
                    dve.wait_ge(dots.sem, dots.at(n + 1))
                    ins = nc.vector.tensor_scalar(score[:, b] if h == 0 else part[:, h % 2], core.bank(n % 4)[:, 0:LAT], 0.0, iw[:, b, h:h + 1], ALU.max, ALU.mult)
                    weighed.count(ins)
                    dve.wait_ge(weighed.sem, weighed.at(n + 1))
                    if h:
                        c.ended(nc.vector.tensor_tensor(score[:, b], score[:, b], part[:, h % 2], ALU.add))
            c.ended(nc.vector.tensor_tensor(left[0][:], score[:], seen[:], ALU.add))
            for r in range(DSA_KEEP // 8):
                x, y = left[r % 2], left[1 - r % 2]
                for b in (0, 1):
                    ins = nc.vector.max(top[:, b, r % 2], x[:, b])
                c.ended(ins)
                for b in (0, 1):
                    ins = nc.vector.match_replace(y[:, b], top[:, b, r % 2], x[:, b], GONE)
                c.ended(ins)
            x = left[DSA_KEEP // 8 % 2]
            c.ended(nc.vector.tensor_scalar(keep[:], x[:], GONE / 2, NEG, ALU.is_ge, ALU.mult))
            nc.vector.tensor_tensor(keep[:], keep[:], seen[:], ALU.add)


def attention_stage(core, st, q, kd, v, neg, out, n_keys=LAT, gate=None, some=None, add=False):
    nc = core.nc
    items = [(b, hp) for b in (0, 1) for hp in range(HEADS // 2)]
    N = len(items)
    group = HEADS // KV_HEADS
    with ExitStack() as ctx, core.engines_block() as block:
        s = core.sb("scores", [P, 2, 2, n_keys], ctx=ctx)
        low = core.sb("low", [P, 2, 2], ctx=ctx)
        total = core.sb("total", [P, 2, 2], ctx=ctx)
        pt = core.sb("pt", [P, 2, 4, P], ctx=ctx)
        names = ("scored", "masked", "exped", "normed", "turned", "pt_ready", "summed", "out_taken")
        scored, masked, exped, normed, turned, pt_ready, summed, out_taken = (core.counter("at_" + n) for n in names)
        chain = core.counter("vector_chain")
        keys = lambda b: min(n_keys, (b + 1) * P)
        blocks = lambda b: [(i * P, min(P, keys(b) - i * P)) for i in range(-(-keys(b) // P))]
        SC = [core.psum[i].rearrange("p (h s) -> p h s", h=2) for i in (0, 1)]
        TR, OUT = [core.bank(4), core.bank(5)], [core.bank(6), core.bank(7)]

        @block.tensor
        def _(pe):
            for n in range(N + 2):
                if n < N:
                    b, hp = items[n]
                    if n >= 2:
                        pe.wait_ge(masked.sem, masked.at(n - 1))
                    for h in (0, 1):
                        half = slice(h * HD, (h + 1) * HD)
                        ins = nc.tensor.matmul(SC[n % 2][:, h, 0:keys(b)], q[half, hp, b * P:(b + 1) * P],
                                               kd[half, hp * 2 // group, 0:keys(b)], start=True, stop=True)
                    scored.count(ins)
                if 0 <= n - 1 < N:
                    m = n - 1
                    b, hp = items[m]
                    pe.wait_ge(normed.sem, normed.at(m + 1))
                    if m >= 2:
                        pe.wait_ge(pt_ready.sem, pt_ready.at(m - 1))
                    for h in (0, 1):
                        for i, (at, w) in enumerate(blocks(b)):
                            ins = nc.tensor.transpose(TR[m % 2][0:w, (h * 2 + i) * P:(h * 2 + i + 1) * P], s[:, m % 2, h, at:at + w], st.C("ident"))
                    turned.count(ins)
                if 0 <= n - 2:
                    m = n - 2
                    b, hp = items[m]
                    pe.wait_ge(pt_ready.sem, pt_ready.at(m + 1))
                    if m >= 2:
                        pe.wait_ge(out_taken.sem, out_taken.at(m - 1))
                    parts = [(h, i, w) for h in (0, 1) for i, (_, w) in enumerate(blocks(b))]
                    for j, (h, i, w) in enumerate(parts):
                        ins = nc.tensor.matmul(OUT[m % 2][:, 0:P], v[0:w, i, hp * 2 // group, (1 - h) * HD:(1 - h) * HD + P], pt[0:w, m % 2, h * 2 + i],
                                               start=j == 0, stop=j == len(parts) - 1)
                    summed.count(ins)

        @block.scalar
        def _(act):
            for n in range(N + 3):
                if 0 <= n - 1 < N:
                    m = n - 1
                    b, hp = items[m]
                    act.wait_ge(turned.sem, turned.at(m + 1))
                    if m >= 2:
                        act.wait_ge(summed.sem, summed.at(m - 1))
                    nb, w = len(blocks(b)), blocks(b)[0][1]
                    ins = nc.scalar.activation(pt[0:w, m % 2].rearrange("p (h i) t -> p h i t", h=2)[:, :, 0:nb],
                                               TR[m % 2][0:w].rearrange("p (h i t) -> p h i t", h=2, i=2)[:, :, 0:nb], ACT.Copy)
                    pt_ready.count(ins)
                if 0 <= n - 3 and not add:
                    m = n - 3
                    b, hp = items[m]
                    act.wait_ge(summed.sem, summed.at(m + 1))
                    out_taken.count(nc.scalar.activation(out[:, hp, b * P:(b + 1) * P], OUT[m % 2][:, 0:P], ACT.Copy))
                if n < N:
                    b, hp = items[n]
                    act.wait_ge(masked.sem, masked.at(n + 1))
                    if n >= 2:
                        act.wait_ge(normed.sem, normed.at(n - 1))
                    for h in (0, 1):
                        x = s[:, n % 2, h, 0:keys(b)]
                        ins = nc.scalar.activation(x, x, ACT.Exp, bias=low[:, n % 2, h:h + 1], accum_out=total[:, n % 2, h:h + 1])
                    exped.count(ins)

        @block.vector
        def _(dve):
            c = Chain(dve, chain)
            for n in range(N + 3):
                if 0 <= n - 1 < N:
                    m = n - 1
                    b, hp = items[m]
                    K = keys(b)
                    x = s[:, m % 2, :, 0:K]
                    r = total[:, m % 2]
                    dve.wait_ge(exped.sem, exped.at(m + 1))
                    c.ended(nc.vector.reciprocal(r, r))
                    if gate is not None:
                        c.ended(nc.vector.tensor_tensor(r, r, gate[:, b, 2 * hp:2 * hp + 2], ALU.mult))
                    if some is not None:
                        c.ended(nc.vector.tensor_tensor(x, x, some[:, b, 0:K].unsqueeze(1).to_broadcast([P, 2, K]), ALU.mult))
                    normed.count(nc.vector.tensor_tensor(x, x, r.unsqueeze(2).to_broadcast([P, 2, K]), ALU.mult))
                if n < N:
                    b, hp = items[n]
                    K = keys(b)
                    x = s[:, n % 2, :, 0:K]
                    dve.wait_ge(scored.sem, scored.at(n + 1))
                    if n >= 2:
                        dve.wait_ge(turned.sem, turned.at(n - 1))
                    c.ended(nc.vector.scalar_tensor_tensor(x, SC[n % 2][:, :, 0:K], HD ** -0.5,
                                                          neg[:, b, 0:K].unsqueeze(1).to_broadcast([P, 2, K]), ALU.mult, ALU.add))
                    masked.count(nc.vector.tensor_reduce(low[:, n % 2], x, AX, ALU.max, negate=True))
                if 0 <= n - 3 and add:
                    m = n - 3
                    b, hp = items[m]
                    dve.wait_ge(summed.sem, summed.at(m + 1))
                    y = out[:, hp, b * P:(b + 1) * P]
                    out_taken.count(nc.vector.tensor_tensor(y, y, OUT[m % 2][:, 0:P], ALU.add))


def swiglu_stage(core, st, wg, wu, wd, beside):
    nc = core.nc
    fc = wg.shape[1] // P
    n_it = fc // 2
    assert beside.groups == n_it + 1
    with ExitStack() as outer:
        h = core.sb("swiglu_h", [P, fc, LAT], ctx=outer)
        with ExitStack() as ctx, core.engines_block() as block:
            tiles = k_tiles(wg, 256, 2, (0, 1), lambda it: it * 256) + k_tiles(wu, 256, 2, (2, 3), lambda it: it * 256)
            g = Gemm(core, ctx, "up", tiles, {o: o for o in range(4)}, 256)
            silu = core.sb("silu", [P, 2, LAT], ctx=ctx)
            beside.open(ctx)

            @block.gpsimd
            def _(pool):
                beside.loads(pool)

            @block.sync
            def _(sp):
                rounds(sp, n_it, lambda it, first: g.fetch_round(sp, it, first))

            @block.tensor
            def _(pe):
                rounds(pe, n_it, lambda it, first: g.matmul_round(pe, it, lambda k: st.H[:, k, LATS], first))

            @block.scalar
            def _(act):
                def body(it, first):
                    for o in (0, 1):
                        bank = g.wait_bank(act, o, it)
                        if not first:
                            act.wait_ge(g.free[2 + o].sem, g.free[2 + o].at(it))
                        g.bank_taken(nc.scalar.activation(silu[:, o], bank[:, 0:LAT], ACT.Silu), o)
                rounds(act, n_it, body)

            @block.vector
            def _(dve):
                def body(it, first):
                    for o in (0, 1):
                        bank = g.wait_bank(dve, 2 + o, it)
                        dve.wait_ge(g.free[o].sem, g.free[o].at(it + 1))
                        g.bank_taken(nc.vector.tensor_tensor(chunk_of(h, it * 2 + o), silu[:, o], bank[:, 0:LAT], ALU.mult), 2 + o)
                    if first:
                        beside.add_group(dve, 0)
                    beside.add_group(dve, it + 1)
                beside.empty()
                rounds(dve, n_it, body)
                beside.settle()
            g.settle(n_it)
        add_gated(core, st, "down", wd, lambda k: h[:, k], 40, width=256)


def sparse_layer(core, st, beside):
    nc, A = core.nc, st.A
    norm_in(core, st, 0, 0, (0,))
    with ExitStack() as scope:
        sb = lambda name, shape: core.sb(name, shape, ctx=scope)
        q, kd, v = sb("q", [P, HEADS // 2, LAT]), sb("kd", [P, KV_HEADS, LAT]), sb("v", [P, 2, KV_HEADS, 3 * HD])
        iq, ik, iw = sb("iq", [P, IDX_HEADS // 2, LAT]), sb("ik", [P, 1, LAT]), sb("iw", [P, 2, IDX_HEADS])
        seen, keep = sb("seen", [P, 2, LAT]), sb("keep", [P, 2, LAT])
        w = A["a_w_in_2"][0]
        at = np.cumsum([0, HEADS * HD, KV_HEADS * HD, KV_HEADS * HD, IDX_HEADS * HD, HD])
        gemm_stage(core, st, "in", w, None, lambda k: st.H[:, k, LATS],
                   lambda act, c, bank: nc.scalar.activation(q[:, c] if c < 8 else iq[:, c - 8], bank[:, 0:LAT], ACT.Copy),
                   sections=[0, 512, int(at[3])], split=True)
        small_stage(core, st, w, [("pair", int(at[1]), KV_HEADS, kd), ("values", int(at[2]), KV_HEADS, v), ("pair", int(at[4]), 1, ik),
                                  ("tokens", int(at[5]), IDX_HEADS, iw, ACT.Copy, IDX_HEADS ** -0.5 * HD ** -0.5)])
        rope_stage(core, st, [q[:, i] for i in range(8)] + [kd[:, i] for i in range(4)] + [iq[:, i] for i in range(4)] + [ik[:, 0]])
        causal_stage(core, st, seen)
        indexer_stage(core, st, iq, ik, iw, seen, keep)
        attention_stage(core, st, q, kd, v, keep, st.Y[:, :, LATS])
        add_gated(core, st, "in", A["a_w_out_2"][0], lambda k: st.Y[:, k, LATS], 16)
    norm_in(core, st, 2, 24, (0,))
    swiglu_stage(core, st, A["ffn_w_gate_2"][0], A["ffn_w_up_2"][0], A["ffn_w_down_2"][0], beside)


def compress_stage(core, st, jobs):
    nc = core.nc
    n_l = CMP_LEN // 2
    with ExitStack() as ctx, core.engines_block() as block:
        loaded = [core.counter(f"cmp_weights{i}") for i in (0, 1)]
        unfolded, hid, hid_done, out, zeroed = (core.counter("cmp_" + n) for n in ("unfolded", "hidden", "hidden_done", "out", "zeroed"))
        chain = core.counter("vector_chain")
        w1s = [core.sb(f"cmp_w1_{i}", [P, n_l, CMP_HIDDEN], ctx=ctx) for i in (0, 1)]
        w2s = [core.sb(f"cmp_w2_{i}", [P, 2, 2, HD], ctx=ctx) for i in (0, 1)]
        blocks = [core.sb(f"cmp_blocks{i}", [P, n_l, KV_HEADS, N_CMP], ctx=ctx) for i in (0, 1)]
        hidden = [core.sb(f"cmp_hidden{i}", [P, 2, KV_HEADS * N_CMP], ctx=ctx) for i in (0, 1)]

        @block.sync
        def _(sp):
            for i, (x, pe_name, w1, w2, dst, by_token) in enumerate(jobs):
                loaded[i].count(sp.dma_start(w1s[i][:], w1.rearrange("(l p) n -> p l n", p=P)), 16)
                for a in (0, 1):
                    loaded[i].count(sp.dma_start(w2s[i][:, :, a], w2.rearrange("(c p) d -> p c d", p=P)), 16)

        @block.vector
        def _(dve):
            c = Chain(dve, chain)
            for i, (x, pe_name, *_, dst, by_token) in enumerate(jobs):
                if by_token:
                    nc.vector.memset(dst[:], 0.0)
                else:
                    nc.vector.memset(dst[:], 0.0)
                for half in (0, 1):
                    rows = slice(half * HD, (half + 1) * HD)
                    for l in range(n_l):
                        at = 2 * l + half
                        src = x[rows, :, at:at + (N_CMP - 1) * CMP_STRIDE + 1:CMP_STRIDE]
                        ins = nc.vector.tensor_scalar(blocks[i][rows, l], src, st.V(pe_name, l)[rows], None, ALU.add)
                unfolded.count(ins)

        @block.tensor
        def _(pe):
            for i, (*_, dst, by_token) in enumerate(jobs):
                pe.wait_ge(loaded[i].sem, loaded[i].at(48))
                pe.wait_ge(unfolded.sem, unfolded.at(i + 1))
                for c in (0, 1):
                    for l in range(n_l):
                        ins = nc.tensor.matmul(core.bank(2 * i + c)[:, 0:KV_HEADS * N_CMP], w1s[i][:, l, c * P:(c + 1) * P],
                                               blocks[i][:, l].rearrange("p g n -> p (g n)"), start=l == 0, stop=l == n_l - 1)
                hid.count(ins)
            for i, (*_, dst, by_token) in enumerate(jobs):
                pe.wait_ge(hid_done.sem, hid_done.at(i + 1))
                bank = core.bank(4 + i)
                if not by_token:
                    for c in (0, 1):
                        ins = nc.tensor.matmul(bank[:, 0:KV_HEADS * N_CMP], w2s[i][:, c].rearrange("p a d -> p (a d)"), hidden[i][:, c], start=c == 0, stop=c == 1)
                else:
                    for g in range(KV_HEADS):
                        for c in (0, 1):
                            ins = nc.tensor.matmul(bank[0:N_CMP, g * HD:(g + 1) * HD], hidden[i][:, c, g * N_CMP:(g + 1) * N_CMP], w2s[i][:, c, 0],
                                                   start=c == 0, stop=c == 1)
                out.count(ins)

        @block.scalar
        def _(act):
            for i in (0, 1):
                act.wait_ge(hid.sem, hid.at(i + 1))
                for c in (0, 1):
                    ins = nc.scalar.activation(hidden[i][:, c], core.bank(2 * i + c)[:, 0:KV_HEADS * N_CMP], ACT.Gelu_apprx_tanh)
                hid_done.count(ins)
            for i, (*_, dst, by_token) in enumerate(jobs):
                act.wait_ge(out.sem, out.at(i + 1))
                bank = core.bank(4 + i)
                if by_token:
                    nc.scalar.activation(dst[0:N_CMP, 0, :, HD:2 * HD], bank[0:N_CMP, 0:KV_HEADS * HD].rearrange("p (g d) -> p g d", g=KV_HEADS), ACT.Copy)
                else:
                    nc.scalar.activation(dst[:, :, 0:N_CMP], bank[:, 0:KV_HEADS * N_CMP].rearrange("p (g n) -> p g n", g=KV_HEADS), ACT.Copy)


class Route:

    def __init__(self, core, scope):
        sb = lambda name, shape, dtype=F32: core.sb(name, shape, dtype, ctx=scope)
        self.share = sb("share", [P, 2, EXPERTS])
        self.goes = sb("goes", [P, 2, EXPERTS])
        self.seat = sb("seat", [P, 2, EXPERTS])
        self.most = sb("most", [P, 1], I32)
        self.seated = sb("seated", [P, EXPERTS, DC, SEATS])
        self.back = sb("back", [SEATS, EXPERTS, LAT])


def router_stage(core, st, route):
    nc = core.nc
    E = EXPERTS
    with ExitStack() as ctx, core.engines_block() as block:
        w = core.sb("w_router", [P, DC, E], ctx=ctx)
        logit, rank = (core.sb(n, [P, 2, E], ctx=ctx) for n in ("logit", "rank"))
        low, total = (core.sb(n, [P, 2, 1], ctx=ctx) for n in ("low", "total"))
        most = core.sb("most_f32", [P, 1], ctx=ctx)
        expo = route.share
        loaded, logits, low_ready, exped, chosen, counted = (
            core.counter("route_" + n) for n in ("loaded", "logits", "low_ready", "exped", "chosen", "counted"))
        chain = core.counter("vector_chain")

        @block.sync
        def _(sp):
            loaded.count(sp.dma_start(w[:], st.A["moe_w_router_2"][0].rearrange("(k p) e -> p k e", p=P)), 16)

        @block.tensor
        def _(pe):
            pe.wait_ge(loaded.sem, loaded.at(16))
            for b in (0, 1):
                for k in range(DC):
                    ins = nc.tensor.matmul(core.bank(b)[:, 0:E], st.H[:, k, CTX + b * P:CTX + (b + 1) * P], w[:, k], start=k == 0, stop=k == DC - 1)
            logits.count(ins)
            pe.wait_ge(chosen.sem, chosen.at(1))
            nc.tensor.matmul(core.bank(2)[:, 0:E], st.C("earlier"), route.goes[:, 0], start=True, stop=True)
            nc.tensor.matmul(core.bank(3)[:, 0:E], st.C("ones"), route.goes[:, 0], start=True, stop=False)
            nc.tensor.matmul(core.bank(3)[:, 0:E], st.C("earlier"), route.goes[:, 1], start=False, stop=True)
            for b in (0, 1):
                ins = nc.tensor.matmul(core.bank(4)[:, 0:E], st.C("ones"), route.goes[:, b], start=b == 0, stop=b == 1)
            counted.count(ins)

        @block.scalar
        def _(act):
            act.wait_ge(low_ready.sem, low_ready.at(1))
            for b in (0, 1):
                ins = nc.scalar.activation(expo[:, b], logit[:, b], ACT.Exp, bias=low[:, b])
            exped.count(ins)

        @block.vector
        def _(dve):
            c = Chain(dve, chain)
            dve.wait_ge(logits.sem, logits.at(1))
            nc.vector.memset(rank[:], 0.0)
            for b in (0, 1):
                c.ended(nc.vector.tensor_copy(logit[:, b], core.bank(b)[:, 0:E]))
            low_ready.count(nc.vector.tensor_reduce(low[:], logit[:], AX, ALU.max, negate=True))
            for j in range(E):
                for b in (0, 1):
                    x = logit[:, b, j:j + 1]
                    ins = nc.vector.scalar_tensor_tensor(rank[:, b], logit[:, b], x, rank[:, b], ALU.is_lt, ALU.add)
                c.ended(ins)
                if j + 1 < E:
                    for b in (0, 1):
                        x, later = logit[:, b, j:j + 1], rank[:, b, j + 1:]
                        ins = nc.vector.scalar_tensor_tensor(later, logit[:, b, j + 1:], x, later, ALU.is_equal, ALU.add)
                    c.ended(ins)
            chosen.count(nc.vector.tensor_scalar(route.goes[:], rank[:], 2.0, None, ALU.is_lt))
            dve.wait_ge(chosen.sem, chosen.at(1))
            dve.wait_ge(exped.sem, exped.at(1))
            c.ended(nc.vector.tensor_tensor(expo[:], expo[:], route.goes[:], ALU.mult))
            c.ended(nc.vector.tensor_reduce(total[:], expo[:], AX, ALU.add))
            c.ended(nc.vector.reciprocal(total[:], total[:]))
            nc.vector.tensor_tensor(expo[:], expo[:], total[:].to_broadcast([P, 2, E]), ALU.mult)
            dve.wait_ge(counted.sem, counted.at(1))
            for b in (0, 1):
                nc.vector.tensor_copy(route.seat[:, b], core.bank(2 + b)[:, 0:E])
            c.ended(nc.vector.tensor_reduce(most[:], core.bank(4)[:, 0:E], AX, ALU.max))
            nc.vector.tensor_copy(route.most[:], most[:])
            nc.vector.memset(st.Y[:, :, LATS], 0.0)


def seat_stage(core, st, route, turn):
    nc = core.nc
    E = EXPERTS
    with ExitStack() as ctx, core.engines_block() as block:
        tokens = core.sb("tokens", [P, 2, D], ctx=ctx)
        sits = core.sb("sits", [P, 2, E, SEATS], ctx=ctx)
        weighed = core.sb("weighed", [P, 2, E, SEATS], ctx=ctx)
        at = core.sb("at", [P, 2, E], ctx=ctx)
        turned, copied, sits_ready, weighed_ready, gathered, stored = (
            core.counter("seat_" + n) for n in ("turned", "copied", "sits_ready", "weighed_ready", "gathered", "stored"))
        chain = core.counter("vector_chain")
        picks = [(k, g) for k in range(DC) for g in (0, 1)]

        @block.tensor
        def _(pe):
            for n in range(4):
                b, k0 = n // 2, n % 2 * 4
                for j in range(4):
                    ins = nc.tensor.transpose(core.bank(n)[:, j * P:(j + 1) * P], st.H[:, k0 + j, CTX + b * P:CTX + (b + 1) * P], st.C("ident"))
                turned.count(ins)
            pe.wait_ge(copied.sem, copied.at(4))
            pe.wait_ge(sits_ready.sem, sits_ready.at(1))
            for n, (k, g) in enumerate(picks):
                if n >= 4:
                    pe.wait_ge(stored.sem, stored.at(n - 3))
                for b in (0, 1):
                    ins = nc.tensor.matmul(core.bank(n % 4), tokens[:, b, k * P:(k + 1) * P], sits[:, b, g * 4:(g + 1) * 4].rearrange("p e s -> p (e s)"),
                                           start=b == 0, stop=b == 1)
                gathered.count(ins)
            pe.wait_ge(weighed_ready.sem, weighed_ready.at(1))
            for n in range(4):
                for j in range(4):
                    e, b = n * 2 + j // 2, j % 2
                    ins = nc.tensor.transpose(core.bank(4 + n)[:, j * P:(j + 1) * P], weighed[:, b, e], st.C("ident"))
                turned.count(ins)

        @block.vector
        def _(dve):
            c = Chain(dve, chain)
            c.ended(nc.vector.tensor_scalar(at[:], route.seat[:], float(-turn * SEATS), None, ALU.add))
            for n in range(4):
                dve.wait_ge(turned.sem, turned.at(n + 1))
                copied.count(nc.vector.tensor_copy(tokens[:, n // 2, n % 2 * 512:(n % 2 + 1) * 512], core.bank(n)))
            for b in (0, 1):
                for e in range(E):
                    ins = nc.vector.tensor_scalar(sits[:, b, e], st.C("column"), at[:, b, e:e + 1], route.goes[:, b, e:e + 1], ALU.is_equal, ALU.mult)
            sits_ready.count(ins)
            dve.wait_ge(sits_ready.sem, sits_ready.at(1))
            for b in (0, 1):
                for e in range(E):
                    ins = nc.vector.tensor_scalar(weighed[:, b, e], sits[:, b, e], route.share[:, b, e:e + 1], None, ALU.mult)
            weighed_ready.count(ins)
            for n in range(4):
                dve.wait_ge(turned.sem, turned.at(4 + n + 1))
                nc.vector.tensor_copy(route.back[:, 2 * n:2 * n + 2].rearrange("p e t -> p (e t)"), core.bank(4 + n))

        @block.scalar
        def _(act):
            for n, (k, g) in enumerate(picks):
                act.wait_ge(gathered.sem, gathered.at(n + 1))
                stored.count(nc.scalar.activation(route.seated[:, g * 4:(g + 1) * 4, k], core.bank(n % 4).rearrange("p (e s) -> p e s", e=4), ACT.Copy))


def moe_stage(core, st, route):
    nc, A = core.nc, st.A
    WIDE = 512
    groups = FE // WIDE
    parts = 2
    kc = DC // parts
    per = 1
    DOWN = 7
    turns = FEC // per // DOWN
    with ExitStack() as ctx, core.engines_block() as block:
        x = core.sb("expert_x", [P, DC, SEATS], ctx=ctx)
        silu = core.sb("silu", [SEATS, WIDE], ctx=ctx)
        rows = core.sb("hidden_rows", [SEATS, WIDE], ctx=ctx)
        h = core.sb("hidden", [P, FEC, SEATS], ctx=ctx)
        y = core.sb("expert_y", [SEATS, D], ctx=ctx)
        up_ring = core.sb("up_ring", [P, 2 * parts, kc, WIDE], ctx=ctx)
        down_ring = core.sb("down_ring", [P, DOWN, per, D], ctx=ctx)
        up_in = [core.counter(f"moe_up{s}_in") for s in range(2 * parts)]
        up_free = [core.counter(f"moe_up{s}_free") for s in range(2 * parts)]
        down_in = [core.counter(f"moe_down{s}_in") for s in range(DOWN)]
        down_free = [core.counter(f"moe_down{s}_free") for s in range(DOWN)]
        names = ("x_ready", "silu_done", "rows_ready", "turned", "h_copied", "y_copied", "scattered", "y_added")
        x_ready, silu_done, rows_ready, turned, h_copied, y_copied, scattered, y_added = (core.counter("moe_" + n) for n in names)
        GATE, UP, TURN, DN, SC = core.bank(0), core.bank(1), core.bank(2), (core.bank(4), core.bank(5)), (core.bank(3), core.bank(6), core.bank(7))
        w_up = [A[n][0].rearrange("e (k p) n -> p e k n", p=P) for n in ("moe_w_gate_2", "moe_w_up_2")]
        w_down = A["moe_w_down_2"][0].rearrange("e (k p) n -> p e k n", p=P)
        gate_done, up_done, down_done = up_free[parts - 1], up_free[2 * parts - 1], down_free[DOWN - 1]
        START = 1

        @block.sync
        def _(sp):
            with sp.Fori(0, EXPERTS) as e:
                with sp.Fori(0, groups) as i:
                    for s in range(2 * parts):
                        k0 = s % parts * kc
                        sp.wait_ge(up_free[s].sem, up_free[s].at(START + e * groups + i))
                        src = w_up[s // parts][:, ds(e, 1), k0:k0 + kc, ds(i * WIDE, WIDE)]
                        sp.dma_start(up_ring[:, s], src.rearrange("p e k n -> p (e k) n")).then_inc(up_in[s].sem, 16)
                for n in range(turns * DOWN):
                    s, r = n % DOWN, n // DOWN
                    sp.wait_ge(down_free[s].sem, down_free[s].at(START + e * turns + r))
                    src = w_down[:, ds(e, 1), n * per:(n + 1) * per, :]
                    sp.dma_start(down_ring[:, s], src.rearrange("p e k n -> p (e k) n")).then_inc(down_in[s].sem, 16)

        @block.gpsimd
        def _(pool):
            with pool.Fori(0, EXPERTS) as e:
                pool.wait_ge(up_done.sem, up_done.at(START + e * groups))
                nc.gpsimd.tensor_copy(x[:].rearrange("p k s -> p (k s)"),
                                      route.seated[:, ds(e, 1)].rearrange("p e k s -> p (e k s)")).then_inc(x_ready.sem, 1)

        @block.tensor
        def _(pe):
            for c in (*up_free, *down_free):
                pe.sem_inc(c.sem, START)

            def turn():
                for j in range(WIDE // P):
                    ins = nc.tensor.transpose(TURN[:, j * P:(j + 1) * P], rows[:, j * P:(j + 1) * P], st.C("ident"))
                ins.then_inc(turned.sem, 1)

            def product(bank, it, slots):
                for s in slots:
                    pe.wait_ge(up_in[s].sem, up_in[s].at(16 * it + 16))
                    for k in range(kc):
                        k0 = s % parts * kc
                        ins = nc.tensor.matmul(bank, x[:, k0 + k], up_ring[:, s, k], start=k0 + k == 0, stop=k0 + k == DC - 1)
                    ins.then_inc(up_free[s].sem, 1)

            with pe.Fori(0, EXPERTS) as e:
                pe.wait_ge(x_ready.sem, x_ready.at(e + 1))

                def group(i, first):
                    it = e * groups + i
                    pe.wait_ge(silu_done.sem, silu_done.at(START + it))
                    product(GATE, it, range(parts))
                    pe.wait_ge(rows_ready.sem, rows_ready.at(START + it))
                    if not first:
                        pe.wait_ge(h_copied.sem, h_copied.at(START + it - 1))
                        turn()
                    product(UP, it, range(parts, 2 * parts))
                rounds(pe, groups, group)
                pe.wait_ge(rows_ready.sem, rows_ready.at(START + e * groups + groups))
                pe.wait_ge(h_copied.sem, h_copied.at(START + e * groups + groups - 1))
                turn()
                pe.wait_ge(y_copied.sem, y_copied.at(2 * START + 2 * e))
                for c in range(FEC):
                    n, q = c // per, c % per
                    s = n % DOWN
                    if q == 0:
                        pe.wait_ge(down_in[s].sem, down_in[s].at(16 * (e * turns + n // DOWN) + 16))
                    if c % (WIDE // P) == 0:
                        pe.wait_ge(h_copied.sem, h_copied.at(START + e * groups + c // (WIDE // P) + 1))
                    for half in (0, 1):
                        ins = nc.tensor.matmul(DN[half], h[:, c], down_ring[:, s, q, half * 512:(half + 1) * 512], start=c == 0, stop=c == FEC - 1)
                    if q == per - 1:
                        ins.then_inc(down_free[s].sem, 1)
                pe.wait_ge(y_copied.sem, y_copied.at(2 * START + 2 * e + 2))
                for r in range(DC // 2):
                    pe.wait_ge(y_added.sem, y_added.at(START + e * (DC // 2) + max(0, r - 2)))
                    for j in (0, 1):
                        k = 2 * r + j
                        ins = nc.tensor.matmul(SC[r % 3][:, j * LAT:(j + 1) * LAT], y[:, k * P:(k + 1) * P], chunk_of(route.back, e), start=True, stop=True)
                    ins.then_inc(scattered.sem, 1)

        @block.scalar
        def _(act):
            for c, by in ((silu_done, START), (h_copied, START), (y_copied, START)):
                act.sem_inc(c.sem, by)

            def copy(i, it):
                act.wait_ge(turned.sem, turned.at(it + 1))
                nc.scalar.activation(h[:, ds(i * (WIDE // P), WIDE // P)].rearrange("p c s -> p (c s)"), TURN, ACT.Copy).then_inc(h_copied.sem, 1)

            with act.Fori(0, EXPERTS) as e:
                def group(i, first):
                    it = e * groups + i
                    act.wait_ge(gate_done.sem, gate_done.at(START + it + 1))
                    act.wait_ge(rows_ready.sem, rows_ready.at(START + it))
                    nc.scalar.activation(silu[:], GATE, ACT.Silu).then_inc(silu_done.sem, 1)
                    if not first:
                        copy(i - 1, it - 1)
                rounds(act, groups, group)
                copy(groups - 1, e * groups + groups - 1)
                act.wait_ge(down_done.sem, down_done.at(START + e * turns + turns))
                nc.scalar.activation(y[:, 0:512], DN[0], ACT.Copy).then_inc(y_copied.sem, 1)

        @block.vector
        def _(dve):
            for c, by in ((rows_ready, START), (y_added, START), (y_copied, START)):
                dve.sem_inc(c.sem, by)
            with dve.Fori(0, EXPERTS) as e:
                with dve.Fori(0, groups) as i:
                    it = e * groups + i
                    dve.wait_ge(silu_done.sem, silu_done.at(START + it + 1))
                    dve.wait_ge(up_done.sem, up_done.at(START + it + 1))
                    nc.vector.tensor_tensor(rows[:], silu[:], UP, ALU.mult).then_inc(rows_ready.sem, 1)
                dve.wait_ge(down_done.sem, down_done.at(START + e * turns + turns))
                nc.vector.tensor_copy(y[:, 512:D], DN[1]).then_inc(y_copied.sem, 1)
                for r in range(DC // 2):
                    dve.wait_ge(scattered.sem, scattered.at(e * (DC // 2) + r + 1))
                    out = st.Y[:, 2 * r:2 * r + 2, LATS]
                    nc.vector.tensor_tensor(out, out, SC[r % 3].rearrange("p (k t) -> p k t", k=2), ALU.add).then_inc(y_added.sem, 1)

        n = EXPERTS * groups
        for c, total in ((x_ready, EXPERTS), (silu_done, START + n), (rows_ready, START + n), (turned, n),
                         (h_copied, START + n), (y_copied, 2 * START + 2 * EXPERTS), (scattered, EXPERTS * DC // 2),
                         (y_added, START + EXPERTS * DC // 2), *((c, 16 * n) for c in up_in), *((c, START + n) for c in up_free),
                         *((c, 16 * EXPERTS * turns) for c in down_in), *((c, START + EXPERTS * turns) for c in down_free)):
            c.n += total


def gated_stage(core, st, gate):
    nc = core.nc
    with core.engines_block() as block:
        @block.vector
        def _(dve):
            for k in range(DC):
                x = st.X[:, k, LATS]
                nc.vector.scalar_tensor_tensor(x, st.Y[:, k, LATS], st.mod[:, gate + k, 0:1], x, ALU.mult, ALU.add)


def branch_layer(core, st, kv_sums, sums):
    nc, A = core.nc, st.A
    with ExitStack() as scope:
        sb = lambda name, shape: core.sb(name, shape, ctx=scope)
        pair = lambda name: sb(name, [P, KV_HEADS, LAT])
        value = lambda name: sb(name, [P, 2, KV_HEADS, 3 * HD])
        k_cmp, v_cmp, k_slc, k_win = pair("k_cmp"), pair("v_cmp"), pair("k_slc"), pair("k_win")
        v_slc, v_win = value("v_slc"), value("v_win")
        kc, vc = sb("kc", [P, KV_HEADS, CMP_STRIDE]), sb("vc", [P, 1, KV_HEADS, 3 * HD])
        q, gates, seen = sb("q", [P, HEADS // 2, LAT]), sb("gates", [P, 2, 3 * HEADS]), sb("seen", [P, 2, LAT])
        mod_stage(core, st, kv_sums, [(0, 0, ("kv_gain_2", 0), 8, 1)])
        norm_in(core, st, 0, 0, (0,))
        w = KV_HEADS * HD
        small_stage(core, st, A["w_kv_2"], [("pair", 0, KV_HEADS, k_cmp), ("pair", w, KV_HEADS, v_cmp)])
        small_stage(core, st, A["w_kv_2"], [("pair", 2 * w, KV_HEADS, k_slc), ("values", 3 * w, KV_HEADS, v_slc),
                                            ("pair", 4 * w, KV_HEADS, k_win), ("values", 5 * w, KV_HEADS, v_win)])
        rope_stage(core, st, [x[:, i] for x in (k_cmp, k_slc, k_win) for i in range(KV_HEADS)])
        compress_stage(core, st, [(k_cmp, "cmp_pe_k_2", A["cmp_w1_k_2"], A["cmp_w2_k_2"], kc, False),
                                  (v_cmp, "cmp_pe_v_2", A["cmp_w1_v_2"], A["cmp_w2_v_2"], vc, True)])
        ada(core, st, sums, 1)
        norm_in(core, st, 0, 0, (0,))
        gemm_stage(core, st, "in", A["b_w_q_2"][0], D, lambda k: st.H[:, k, LATS],
                   lambda act, c, bank: nc.scalar.activation(chunk_of(q, c), bank[:, 0:LAT], ACT.Copy), width=256, split=True)
        small_stage(core, st, A["b_w_q_2"][0], [("tokens", D, 3 * HEADS, gates, ACT.Sigmoid, 1.0)])
        rope_stage(core, st, [q[:, i] for i in range(8)])
        causal_stage(core, st, seen)
        out = st.Y[:, :, LATS]
        branch = lambda i: gates[:, :, i:3 * HEADS:3]
        cmp_neg, cmp_seen = (st.C(n).rearrange("p (b n) -> p b n", b=2) for n in ("cmp_neg", "cmp_seen"))
        attention_stage(core, st, q, kc, vc, cmp_neg, out, n_keys=CMP_STRIDE, gate=branch(0), some=cmp_seen)
        attention_stage(core, st, q, k_slc, v_slc, seen, out, gate=branch(1), add=True)
        attention_stage(core, st, q, k_win, v_win, seen, out, gate=branch(2), add=True)
        add_gated(core, st, "in", A["b_w_out_2"][0], lambda k: st.Y[:, k, LATS], 16)


def moe_layer(core, st):
    norm_in(core, st, 2, 24, (0,))
    with ExitStack() as scope:
        route = Route(core, scope)
        router_stage(core, st, route)
        seat_stage(core, st, route, 0)
        moe_stage(core, st, route)
        with core.rarely(route.most[0:1, 0:1], SEATS):
            seat_stage(core, st, route, 1)
            moe_stage(core, st, route)
    gated_stage(core, st, 40)
    norm_stage(core, st, [(lambda k: st.X[:, k, LATS], lambda k: st.V("final_gain_2", k), None, lambda k: st.Y[:, k, LATS])])


def finish_stage(core, st, out):
    nc = core.nc
    with ExitStack() as ctx, core.engines_block() as block:
        tokens = core.sb("tokens_out", [P, 2, D], ctx=ctx)
        turned, copied, stored = core.counter("turned"), core.counter("turned_copied"), core.counter("stored")

        @block.tensor
        def _(pe):
            for g in range(4):
                t, k0 = g // 2, g % 2 * 4
                for j in range(4):
                    ins = nc.tensor.transpose(core.bank(g)[:, j * P:(j + 1) * P], st.Y[:, k0 + j, CTX + t * P:CTX + (t + 1) * P], st.C("ident"))
                turned.count(ins)

        @block.vector
        def _(dve):
            for g in range(4):
                dve.wait_ge(turned.sem, turned.at(g + 1))
                copied.count(nc.vector.tensor_copy(tokens[:, g // 2, g % 2 * 512:(g % 2 + 1) * 512], core.bank(g)))

        @block.sync
        def _(sp):
            for t in (0, 1):
                sp.wait_ge(copied.sem, copied.at(2 * t + 2))
                stored.count(sp.dma_start(out[0, t * P:(t + 1) * P, :], tokens[:, t, :]), 16)
            sp.wait_ge(stored.sem, stored.at(stored.n))


def norm_in(core, st, slot, shift, streams):
    seg = (SEGS["lat"], SEGS["ctx"])
    norm_stage(core, st, [(lambda k, v=v: st.X[:, k, seg[v]], lambda k, v=v: st.coef[:, v, slot, k:k + 1],
                           lambda k, v=v: st.mod[:, shift + k, v:v + 1], lambda k, v=v: st.H[:, k, seg[v]]) for v in streams])


def norm_out(core, st, slot, src, streams):
    seg = (SEGS["lat"], SEGS["ctx"])
    norm_stage(core, st, [(lambda k, v=v: src[:, k, seg[v]], lambda k, v=v: st.coef[:, v, slot, k:k + 1],
                           lambda k, v=v: st.X[:, k, seg[v]], lambda k, v=v: st.X[:, k, seg[v]]) for v in streams])


def decoder_sums(core, st, scope, layer):
    return ModSums(core, st, scope, f"mod{layer}", st.A["w_mod"][layer], ("b_mod", layer * 48), (0, 1), 48)


def modulations(core, st, sums, layer, first=False):
    g = lambda i: ("norm_g", (layer * 4 + i) * DC)
    mod_stage(core, st, sums, [job for v in (0, 1) for job in ((v, 0, g(0), 8, 1), (v, 1, g(1), 16, 0), (v, 2, g(2), 32, 1), (v, 3, g(3), 40, 0))], first)


def build(nc, A, out):
    with ExitStack() as ctx:
        core = Core(nc, ctx)
        st = Store(core, A)
        setup_stage(core, st)
        with ExitStack() as scope:
            modulations(core, st, decoder_sums(core, st, scope, 0), 0, first=True)
        norm_in(core, st, 0, 0, (0, 1))
        with ExitStack() as scope:
            ev = Even(core, scope)
            even_project(core, st, ev)
            mlstm_stage(core, st, ev)
            gla_stage(core, st, ev)
            even_gate_stage(core, st, ev)
        gemm_stage(core, st, "in", A["ev_w_out"][0], D, lambda k: st.Y[:, k],
                   lambda act, c, bank: nc.scalar.activation(chunk_of(st.H, c), bank, ACT.Copy), split=True)
        norm_out(core, st, 1, st.H, (0, 1))
        norm_in(core, st, 2, 24, (0, 1))
        with ExitStack() as scope:
            sums = ffn_stage(core, st, scope, 0, TT, 0, lambda: decoder_sums(core, st, scope, 1))
            norm_out(core, st, 3, st.Y, (0, 1))
            modulations(core, st, sums, 1)
        with ExitStack() as scope:
            kv_sums = rwkv_layer(core, st, scope)
            sums = ada_sums(core, st, scope, 0)
            with ExitStack() as inner:
                ffn_stage(core, st, inner, 1, LAT, CTX, lambda: sums)
            norm_out(core, st, 3, st.Y, (0,))
            ada(core, st, sums, 0)
            last_sums = ada_sums(core, st, scope, 1, place=sums)
            sparse_layer(core, st, last_sums)
            branch_layer(core, st, kv_sums, last_sums)
        moe_layer(core, st)
        finish_stage(core, st, out)


def kernel(**inputs):
    import concourse.bacc as bacc
    from concourse.bass_utils import run_bass_kernel_spmd

    nc = bacc.Bacc("TRN2", target_bir_lowering=False, num_devices=1)
    arrays = {n: np.ascontiguousarray(a) for n, a in inputs.items()}
    arrays["const"] = CONST
    A = {n: nc.dram_tensor(f"in_{n}", a.shape, mybir.dt.from_np(a.dtype), kind="ExternalInput").ap() for n, a in arrays.items()}
    out = nc.dram_tensor("out", (1, LAT, D), F32, kind="ExternalOutput").ap()
    build(nc, A, out)
    r = run_bass_kernel_spmd(nc, [{f"in_{n}": a for n, a in arrays.items()}], core_ids=[0])
    return r.results[0]["out"]
```
